# Optimizing a Trainium2 kernel written in Bass

```python
import math
import jax
import jax.numpy as jnp
from jax import lax
import numpy as np

D_MODEL = 1024
BATCH = 1
SEQ = 512
DEPTH = 2
DEC_BATCH = 8
DEC_SEQ = 8
PAST_LEN = 4096
PAGE_SIZE = 128

N_EVEN = (DEPTH + 1) // 2
N_ODD = DEPTH // 2
MIX_W = D_MODEL
GROUP_W = MIX_W // 2
H_A = 4
DK_A = GROUP_W // H_A
DV_A = GROUP_W // H_A
CONV_W = 4
CHUNK_A = 64
HD_B = 64
H_B = GROUP_W // HD_B
LR_W = 64
LR_A = 64
LR_G = 128
GN_EPS = 64e-5
H_C = 4
DV_C = GROUP_W // H_C
DK_C = DV_C // 2
LR_GK = 16
GLA_NORM = 16.0
CHUNK_C = 16
H_D = 4
DV_D = GROUP_W // H_D
DK_D = DV_D // 2
CHUNK_D = 64
D_FF = ((8 * D_MODEL // 3 + 255) // 256) * 256
N_MOD = 9
EPS = 1e-6

QK_A = H_A * DK_A
V_A = H_A * DV_A
A_WIDTHS = (QK_A, QK_A, V_A, H_A, H_A, V_A)
V_B = H_B * HD_B
B_WIDTHS = (V_B, V_B, V_B, LR_W, LR_A, LR_G)
QK_C = H_C * DK_C
V_C = H_C * DV_C
C_WIDTHS = (QK_C, QK_C, V_C, LR_GK, V_C)
QK_D = H_D * DK_D
V_D = H_D * DV_D
D_WIDTHS = (QK_D, QK_D, V_D, H_D, H_D, V_D)
P_A = sum(A_WIDTHS)
P_B = sum(B_WIDTHS)
P_C = sum(C_WIDTHS)
P_D = sum(D_WIDTHS)
P_EVEN = P_A + P_B
P_ODD = P_C + P_D

kernel_name = 'hybrid_delta_rwkv7_gla_mlstm_macaron_adaln_step'

def _split(x, widths):
    idx = [int(s) for s in np.cumsum(widths)[:-1]]
    return jnp.split(x, idx, axis=-1)

def _chunk_len(t, cap):
    n = min(cap, t)
    while t % n:
        n -= 1
    return n

def _rms(x, eps=EPS):
    return x * lax.rsqrt(jnp.mean(jnp.square(x), -1, keepdims=True) + eps)

def _l2n(x):
    return x * lax.rsqrt(jnp.sum(jnp.square(x), -1, keepdims=True) + 1e-6)

def _heads(x, h):
    return x.reshape(*x.shape[:-1], h, x.shape[-1] // h)

def _to_blocks(x, n):
    b, t = x.shape[:2]
    x = x.reshape(b, t // n, n, *x.shape[2:])
    return jnp.moveaxis(x, 3, 2)

def _from_blocks(x):
    x = jnp.moveaxis(x, 2, 3)
    return x.reshape(x.shape[0], -1, *x.shape[3:])

def _adaln(x, gain, mod, j):
    n = _rms(x.astype(jnp.float32)) * gain
    return (n * (1.0 + mod[:, 3 * j + 1]) + mod[:, 3 * j]).astype(x.dtype)

def _swiglu(h, w_gate, w_up, w_down):
    return (jax.nn.silu(h @ w_gate) * (h @ w_up)) @ w_down

def _gated_delta(q, k, v, g, beta, s0):
    n = _chunk_len(q.shape[1], CHUNK_A)
    q, k, v = (_to_blocks(z, n) for z in (q, k, v))
    g, beta = _to_blocks(g, n), _to_blocks(beta, n)
    gc = jnp.cumsum(g, -1)
    causal = jnp.tril(jnp.ones((n, n), bool))
    strict = jnp.tril(jnp.ones((n, n), bool), -1)
    decay = jnp.exp(jnp.where(causal, gc[..., :, None] - gc[..., None, :], -jnp.inf))
    kb = k * beta[..., None]
    a_low = jnp.where(strict, jnp.einsum('bnhik,bnhjk->bnhij', kb, k) * decay, 0.0)
    eye = jnp.eye(n, dtype=a_low.dtype)
    rhs = jnp.concatenate([v * beta[..., None], kb * jnp.exp(gc)[..., None]], -1)
    sol = lax.linalg.triangular_solve(a_low + eye, rhs, left_side=True, lower=True, unit_diagonal=True)
    dv = v.shape[-1]
    value, kcum = sol[..., :dv], sol[..., dv:]
    qk = jnp.einsum('bnhik,bnhjk->bnhij', q, k) * decay
    qg = q * jnp.exp(gc)[..., None]
    kd = k * jnp.exp(gc[..., -1:] - gc)[..., None]
    gl = jnp.exp(gc[..., -1])

    def step(s, xs):
        qk_c, qg_c, kcum_c, val_c, kd_c, gl_c = xs
        u = val_c - jnp.einsum('bhlk,bhkv->bhlv', kcum_c, s)
        o = jnp.einsum('bhlk,bhkv->bhlv', qg_c, s) + jnp.einsum('bhij,bhjv->bhiv', qk_c, u)
        s = s * gl_c[..., None, None] + jnp.einsum('bhlk,bhlv->bhkv', kd_c, u)
        return s, o

    xs = tuple(jnp.moveaxis(z, 1, 0) for z in (qk, qg, kcum, value, kd, gl))
    s, o = lax.scan(step, s0, xs)
    return _from_blocks(jnp.moveaxis(o, 0, 1)), s

def _rwkv7(r, w, k, v, a, b, s0):
    def step(s, xs):
        r_t, w_t, k_t, v_t, a_t, b_t = xs
        sa = jnp.einsum('bhvk,bhk->bhv', s, a_t)
        s = s * w_t[:, :, None, :] + sa[..., None] * b_t[:, :, None, :] + v_t[..., None] * k_t[:, :, None, :]
        return s, jnp.einsum('bhvk,bhk->bhv', s, r_t)

    xs = tuple(jnp.moveaxis(z, 1, 0) for z in (r, w, k, v, a, b))
    s, y = lax.scan(step, s0, xs)
    return jnp.moveaxis(y, 0, 1), s

def _gla(q, k, v, gk, s0):
    n = _chunk_len(q.shape[1], CHUNK_C)
    q, k, v, gk = (_to_blocks(z, n) for z in (q, k, v, gk))
    bc = jnp.cumsum(gk, -2)
    causal = jnp.tril(jnp.ones((n, n), bool))
    qd = q * jnp.exp(bc)
    att = jnp.where(causal, jnp.einsum('bnhik,bnhjk->bnhij', qd, k * jnp.exp(-bc)), 0.0)
    intra = jnp.einsum('bnhij,bnhjv->bnhiv', att, v)
    kd = k * jnp.exp(bc[..., -1:, :] - bc)
    gl = jnp.exp(bc[..., -1, :])

    def step(s, xs):
        qd_c, kd_c, v_c, gl_c, in_c = xs
        o = in_c + jnp.einsum('bhlk,bhkv->bhlv', qd_c, s)
        s = s * gl_c[..., None] + jnp.einsum('bhlk,bhlv->bhkv', kd_c, v_c)
        return s, o

    xs = tuple(jnp.moveaxis(z, 1, 0) for z in (qd, kd, v, gl, intra))
    s, o = lax.scan(step, s0, xs)
    return _from_blocks(jnp.moveaxis(o, 0, 1)), s

def _mlstm(q, k, v, ig, fg, c0, n0, m0):
    n = _chunk_len(q.shape[1], CHUNK_D)
    q, k, v = (_to_blocks(z, n) for z in (q, k, v))
    ig = _to_blocks(ig, n)
    fcum = jnp.cumsum(_to_blocks(jax.nn.log_sigmoid(fg), n), -1)
    causal = jnp.tril(jnp.ones((n, n), bool))
    log_d = jnp.where(causal, fcum[..., :, None] - fcum[..., None, :] + ig[..., None, :], -jnp.inf)
    m_in = jnp.max(log_d, -1)
    log_e = fcum[..., -1:] - fcum + ig
    m_e = jnp.max(log_e, -1)
    qk = jnp.einsum('bnhik,bnhjk->bnhij', q, k)

    def step(carry, xs):
        c, nn, m = carry
        f_c, ld_c, mi_c, me_c, le_c, qk_c, q_c, k_c, v_c = xs
        m_t = jnp.maximum(f_c + m[..., None], mi_c)
        w_in = jnp.exp(f_c + m[..., None] - m_t)
        dm = jnp.exp(ld_c - m_t[..., None]) * qk_c
        num = w_in[..., None] * jnp.einsum('bhlk,bhkv->bhlv', q_c, c) + jnp.einsum('bhij,bhjv->bhiv', dm, v_c)
        den = w_in * jnp.einsum('bhlk,bhk->bhl', q_c, nn) + jnp.sum(dm, -1)
        h_out = num / jnp.maximum(jnp.abs(den), jnp.exp(-m_t))[..., None]
        m_new = jnp.maximum(f_c[..., -1] + m, me_c)
        carry_decay = jnp.exp(f_c[..., -1] + m - m_new)
        ke = k_c * jnp.exp(le_c - m_new[..., None])[..., None]
        c = c * carry_decay[..., None, None] + jnp.einsum('bhlk,bhlv->bhkv', ke, v_c)
        nn = nn * carry_decay[..., None] + jnp.sum(ke, -2)
        return (c, nn, m_new), h_out

    xs = tuple(jnp.moveaxis(z, 1, 0) for z in (fcum, log_d, m_in, m_e, log_e, qk, q, k, v))
    (c, nn, m), hs = lax.scan(step, (c0, n0, m0), xs)
    return _from_blocks(jnp.moveaxis(hs, 0, 1)), c, nn, m

def _even_mixer(h, xbuf, s_delta, s_rwkv, w, i):
    f32 = jnp.float32
    b, t, _ = h.shape
    hx = jnp.concatenate([xbuf.astype(h.dtype), h], axis=1)
    proj = (hx @ w['w_in_even'][i]).astype(f32)
    pa, pb = proj[..., :P_A], proj[..., P_A:]
    n_qkv = 2 * QK_A + V_A
    cw = w['conv_w'][i].astype(f32)
    conv = sum(cw[j] * pa[:, j:j + t, :n_qkv] for j in range(CONV_W))
    q, k, v = _split(jax.nn.silu(conv), (QK_A, QK_A, V_A))
    _, _, _, a_in, b_in, z = _split(pa[:, CONV_W - 1:], A_WIDTHS)
    q = _l2n(_heads(q, H_A)) * (DK_A ** -0.5)
    k = _l2n(_heads(k, H_A))
    g = -jnp.exp(w['a_log'][i].astype(f32)) * jax.nn.softplus(a_in + w['dt_bias'][i])
    o_a, s_delta = _gated_delta(q, k, _heads(v, H_A), g, jax.nn.sigmoid(b_in), s_delta.astype(f32))
    o_a = (_rms(o_a) * w['gain_a'][i]).reshape(b, t, V_A) * jax.nn.silu(z)
    cur, prev = pb[:, CONV_W - 1:], pb[:, CONV_W - 2:-1]
    xm = cur + (prev - cur) * w['mu_b'][i]
    r, kb, vb, w_lr, a_lr, g_lr = _split(xm, B_WIDTHS)
    w_raw = w['w0_b'][i] + jnp.tanh(w_lr) @ w['w_w2'][i]
    decay = jnp.exp(-jnp.exp(-jax.nn.softplus(-w_raw) - 0.5))
    a = jax.nn.sigmoid(w['a0_b'][i] + a_lr @ w['w_a2'][i])
    gb = jax.nn.sigmoid(g_lr) @ w['w_g2'][i]
    kk = _l2n(_heads(kb * w['k_k'][i], H_B))
    kb = kb * (1.0 + (a - 1.0) * w['k_a'][i])
    r_h, k_h, v_h, a_h = (_heads(z_, H_B) for z_ in (r, kb, vb, a))
    y, s_rwkv = _rwkv7(r_h, _heads(decay, H_B), k_h, v_h, -kk, kk * a_h, s_rwkv.astype(f32))
    yc = y - jnp.mean(y, -1, keepdims=True)
    y = yc * lax.rsqrt(jnp.mean(jnp.square(yc), -1, keepdims=True) + GN_EPS)
    y = y.reshape(b, t, V_B) * w['lnx_gain'][i] + w['lnx_bias'][i]
    bonus = jnp.sum(r_h * k_h * w['r_k'][i], -1, keepdims=True) * v_h
    y = (y + bonus.reshape(b, t, V_B)) * gb
    out = jnp.concatenate([o_a, y], -1).astype(h.dtype) @ w['w_out_even'][i]
    return out, hx[:, -(CONV_W - 1):], s_delta.astype(h.dtype), s_rwkv.astype(h.dtype)

def _odd_mixer(h, s_gla, s_c, s_n, s_m, w, i):
    f32 = jnp.float32
    b, t, _ = h.shape
    proj = (h @ w['w_in_odd'][i]).astype(f32)
    pc, pd = proj[..., :P_C], proj[..., P_C:]
    q, k, v, gk_lr, z = _split(pc, C_WIDTHS)
    gk = jax.nn.log_sigmoid(gk_lr @ w['w_gk2'][i] + w['b_gk'][i]) / GLA_NORM
    o_c, s_gla = _gla(_heads(q, H_C) * (DK_C ** -0.5), _heads(k, H_C), _heads(v, H_C),
                      _heads(gk, H_C), s_gla.astype(f32))
    o_c = (_rms(o_c) * w['gain_c'][i]).reshape(b, t, V_C) * jax.nn.silu(z)
    q, k, v, i_in, f_in, o_in = _split(pd, D_WIDTHS)
    hd, s_c, s_n, s_m = _mlstm(_heads(q, H_D), _heads(k, H_D) * (DK_D ** -0.5), _heads(v, H_D),
                               i_in + w['b_i'][i], f_in + w['b_f'][i],
                               s_c.astype(f32), s_n.astype(f32), s_m.astype(f32))
    o_d = jax.nn.sigmoid(o_in) * (_rms(hd) * w['gain_d'][i]).reshape(b, t, V_D)
    out = jnp.concatenate([o_c, o_d], -1).astype(h.dtype) @ w['w_out_odd'][i]
    return out, s_gla.astype(h.dtype), s_c.astype(h.dtype), s_n.astype(h.dtype), s_m.astype(h.dtype)

def _trunk(x, c, states, w):
    xbuf, s_delta, s_rwkv, s_gla, s_mc, s_mn, s_mm = states
    new_even = ([], [], [])
    new_odd = ([], [], [], [])
    cs = jax.nn.silu(c.astype(jnp.float32))
    for l in range(DEPTH):
        mod = (cs @ w['w_mod'][l] + w['b_mod'][l]).reshape(c.shape[0], N_MOD, 1, D_MODEL)
        h = _adaln(x, w['norm_gain'][l, 0], mod, 0)
        f1 = _swiglu(h, w['w_ffn_gate'][l, 0], w['w_ffn_up'][l, 0], w['w_ffn_down'][l, 0])
        x = x + (0.5 * (1.0 + mod[:, 2]) * f1).astype(x.dtype)
        h = _adaln(x, w['norm_gain'][l, 1], mod, 1)
        if l % 2 == 0:
            i = l // 2
            o, xb, sd, sr = _even_mixer(h, xbuf[i], s_delta[i], s_rwkv[i], w, i)
            for lst, val in zip(new_even, (xb, sd, sr)):
                lst.append(val)
        else:
            i = l // 2
            o, sg, sc, sn, sm = _odd_mixer(h, s_gla[i], s_mc[i], s_mn[i], s_mm[i], w, i)
            for lst, val in zip(new_odd, (sg, sc, sn, sm)):
                lst.append(val)
        x = x + ((1.0 + mod[:, 5]) * o).astype(x.dtype)
        h = _adaln(x, w['norm_gain'][l, 2], mod, 2)
        f2 = _swiglu(h, w['w_ffn_gate'][l, 1], w['w_ffn_up'][l, 1], w['w_ffn_down'][l, 1])
        x = x + (0.5 * (1.0 + mod[:, 8]) * f2).astype(x.dtype)
    y = (_rms(x.astype(jnp.float32)) * w['final_gain']).astype(x.dtype)
    stacked = [jnp.stack(lst) for lst in new_even + new_odd]
    return (y, *stacked)

def setup_inputs(seed: int = 0) -> dict:
    key = jax.random.key(seed)
    ks = iter(jax.random.split(key, 64))
    f32 = jnp.float32

    def nrm(shape, scale):
        return jax.random.normal(next(ks), shape, f32) * scale

    def unif(shape, lo, hi):
        return jax.random.uniform(next(ks), shape, f32, lo, hi)

    d = D_MODEL
    dt = jnp.exp(unif((N_EVEN, H_A), math.log(1e-3), math.log(1e-1)))
    return {
        'x_prompt': nrm((BATCH, SEQ, d), 1.0),
        'x_sample': nrm((DEC_BATCH, DEC_SEQ, d), 1.0),
        'c_prompt': nrm((BATCH, d), 1.0),
        'c_sample': nrm((DEC_BATCH, d), 1.0),
        'state_xbuf_even': nrm((N_EVEN, DEC_BATCH, CONV_W - 1, d), 1.0),
        'state_delta': nrm((N_EVEN, DEC_BATCH, H_A, DK_A, DV_A), 0.3),
        'state_rwkv': nrm((N_EVEN, DEC_BATCH, H_B, HD_B, HD_B), 0.3),
        'state_gla': nrm((N_ODD, DEC_BATCH, H_C, DK_C, DV_C), 0.3),
        'state_mlstm_c': nrm((N_ODD, DEC_BATCH, H_D, DK_D, DV_D), 0.3),
        'state_mlstm_n': nrm((N_ODD, DEC_BATCH, H_D, DK_D), 0.3),
        'state_mlstm_m': nrm((N_ODD, DEC_BATCH, H_D), 1.0),
        'w_mod': nrm((DEPTH, d, N_MOD * d), 0.1 * d ** -0.5),
        'b_mod': nrm((DEPTH, N_MOD * d), 0.02),
        'norm_gain': 1.0 + nrm((DEPTH, 3, d), 0.02),
        'final_gain': 1.0 + nrm((d,), 0.02),
        'w_ffn_gate': nrm((DEPTH, 2, d, D_FF), d ** -0.5),
        'w_ffn_up': nrm((DEPTH, 2, d, D_FF), d ** -0.5),
        'w_ffn_down': nrm((DEPTH, 2, D_FF, d), D_FF ** -0.5),
        'w_in_even': nrm((N_EVEN, d, P_EVEN), d ** -0.5),
        'w_out_even': nrm((N_EVEN, MIX_W, d), MIX_W ** -0.5),
        'conv_w': nrm((N_EVEN, CONV_W, 2 * QK_A + V_A), CONV_W ** -0.5),
        'a_log': jnp.log(unif((N_EVEN, H_A), 1.0, 16.0)),
        'dt_bias': dt + jnp.log(-jnp.expm1(-dt)),
        'gain_a': 1.0 + nrm((N_EVEN, DV_A), 0.02),
        'mu_b': unif((N_EVEN, P_B), 0.0, 1.0),
        'w0_b': unif((N_EVEN, V_B), -6.0, -1.0),
        'w_w2': nrm((N_EVEN, LR_W, V_B), 0.5 * LR_W ** -0.5),
        'a0_b': nrm((N_EVEN, V_B), 0.1),
        'w_a2': nrm((N_EVEN, LR_A, V_B), LR_A ** -0.5),
        'w_g2': nrm((N_EVEN, LR_G, V_B), LR_G ** -0.5),
        'k_k': 0.85 + nrm((N_EVEN, V_B), 0.05),
        'k_a': 1.0 + nrm((N_EVEN, V_B), 0.05),
        'r_k': nrm((N_EVEN, H_B, HD_B), 0.1),
        'lnx_gain': 1.0 + nrm((N_EVEN, V_B), 0.02),
        'lnx_bias': nrm((N_EVEN, V_B), 0.02),
        'w_in_odd': nrm((N_ODD, d, P_ODD), d ** -0.5),
        'w_out_odd': nrm((N_ODD, MIX_W, d), MIX_W ** -0.5),
        'w_gk2': nrm((N_ODD, LR_GK, QK_C), LR_GK ** -0.5),
        'b_gk': nrm((N_ODD, QK_C), 0.1),
        'gain_c': 1.0 + nrm((N_ODD, DV_C), 0.02),
        'b_i': nrm((N_ODD, H_D), 0.1),
        'b_f': unif((N_ODD, H_D), 3.0, 6.0),
        'gain_d': 1.0 + nrm((N_ODD, DV_D), 0.02),
    }

def reference(x_prompt, x_sample, c_prompt, c_sample,
              state_xbuf_even, state_delta, state_rwkv, state_gla,
              state_mlstm_c, state_mlstm_n, state_mlstm_m,
              w_mod, b_mod, norm_gain, final_gain, w_ffn_gate, w_ffn_up, w_ffn_down,
              w_in_even, w_out_even, conv_w, a_log, dt_bias, gain_a,
              mu_b, w0_b, w_w2, a0_b, w_a2, w_g2, k_k, k_a, r_k, lnx_gain, lnx_bias,
              w_in_odd, w_out_odd, w_gk2, b_gk, gain_c, b_i, b_f, gain_d):
    w = dict(w_mod=w_mod, b_mod=b_mod, norm_gain=norm_gain, final_gain=final_gain,
             w_ffn_gate=w_ffn_gate, w_ffn_up=w_ffn_up, w_ffn_down=w_ffn_down,
             w_in_even=w_in_even, w_out_even=w_out_even, conv_w=conv_w, a_log=a_log,
             dt_bias=dt_bias, gain_a=gain_a, mu_b=mu_b, w0_b=w0_b, w_w2=w_w2, a0_b=a0_b,
             w_a2=w_a2, w_g2=w_g2, k_k=k_k, k_a=k_a, r_k=r_k, lnx_gain=lnx_gain,
             lnx_bias=lnx_bias, w_in_odd=w_in_odd, w_out_odd=w_out_odd, w_gk2=w_gk2,
             b_gk=b_gk, gain_c=gain_c, b_i=b_i, b_f=b_f, gain_d=gain_d)
    bp = x_prompt.shape[0]
    dtp = x_prompt.dtype
    zero_states = (
        jnp.zeros((N_EVEN, bp, CONV_W - 1, D_MODEL), dtp),
        jnp.zeros((N_EVEN, bp, H_A, DK_A, DV_A), dtp),
        jnp.zeros((N_EVEN, bp, H_B, HD_B, HD_B), dtp),
        jnp.zeros((N_ODD, bp, H_C, DK_C, DV_C), dtp),
        jnp.zeros((N_ODD, bp, H_D, DK_D, DV_D), dtp),
        jnp.zeros((N_ODD, bp, H_D, DK_D), dtp),
        jnp.zeros((N_ODD, bp, H_D), dtp),
    )
    y_p, xb_p, dl_p, rw_p, gl_p, mc_p, mn_p, mm_p = _trunk(x_prompt, c_prompt, zero_states, w)
    sample_states = (state_xbuf_even, state_delta, state_rwkv, state_gla,
                     state_mlstm_c, state_mlstm_n, state_mlstm_m)
    y_s, xb_s, dl_s, rw_s, gl_s, mc_s, mn_s, mm_s = _trunk(x_sample, c_sample, sample_states, w)
    return (y_p, y_s, xb_p, xb_s, dl_p, dl_s, rw_p, rw_s, gl_p, gl_s, mc_p, mc_s, mn_p, mn_s, mm_p, mm_s)


_drawn_inputs = setup_inputs


def setup_inputs(seed=0):
    import zlib

    import numpy as np

    out = dict(_drawn_inputs(seed))
    spreads = {}
    factors = {'final_gain': 8.131,
     'gain_a': 3.806,
     'lnx_gain': 4.998,
     'gain_c': 34.409,
     'gain_d': 35.501,
     'lnx_bias': 3.898}
    for name, (base, spread) in spreads.items():
        noise = np.random.default_rng([zlib.crc32(name.encode()), seed]).standard_normal(out[name].shape)
        drawn = base * np.exp(spread * noise) if base else spread * noise
        out[name] = jnp.asarray(drawn.astype(out[name].dtype))
    for name, factor in factors.items():
        out[name] = (out[name] * factor).astype(out[name].dtype)
    return out
```

```python
import concourse.bass as bass
from concourse import mybir

F32 = mybir.dt.float32
ACT = mybir.ActivationFunctionType
ALU = mybir.AluOpType

P = 128
D = 1024
KT = D // P
TP = 512
NSEQ = 8
TS = 8
T = TP + NSEQ * TS
NC = 1 + NSEQ
CONV_W = 4
PAD = CONV_W - 1
TX = TP + NSEQ * (TS + PAD)
HALF = T // 2
HALFX = TX // 2
DFF = 2816
FT = DFF // P
DEPTH = 2
MT = 3 * KT
EPS = 1e-6
GN_EPS = 64e-5
BIG = 1e30
CH = 128
NCH = TP // CH
NEG_E_HALF = -0.6065306597126334

PARAM_WIDTHS = [
    ("b_mod", DEPTH * 9 * KT), ("norm_gain", DEPTH * 3 * KT), ("final_gain", KT),
    ("conv_w", 12 * CONV_W), ("mu", 14), ("w0", 4), ("a0", 4), ("k_k", 4), ("k_a", 4), ("r_k", 4),
    ("lnx_gain", 4), ("lnx_bias", 4), ("gain_a", 1), ("a_log", 1), ("dt_bias", 1),
    ("b_gk", 2), ("gain_c", 1), ("gain_d", 1), ("b_i", 1), ("b_f", 1),
]
PARAM = {}
_at = 0
for _n, _w in PARAM_WIDTHS:
    PARAM[_n] = (_at, _w)
    _at += _w
N_PARAM = _at

WORK = 24750
ARENA = WORK - KT * T
RING = 12288


def two_halves(bank_pair, width):
    return bank_pair[:, :, 0:width]


class Phase:

    def __init__(self, nc):
        self.nc, self.sems = nc, {}

    def sem(self, name):
        if name not in self.sems:
            self.sems[name] = self.nc.alloc_semaphore(f"{name}_{self.nc.next_id()}")
        return self.sems[name]


def setup(k):
    nc = k.nc
    with nc.cleanup_on_exit():
        s = Phase(nc)
        loaded, ones_ready, base_ready, masks_ready, sig_ready, cs_ready = (
            s.sem(n) for n in ("loaded", "ones_ready", "base_ready", "masks_ready", "sig_ready", "cs_ready"))
        with nc.Block() as block:
            @block.sync
            def _(sp):
                sp.dma_start(k.cs, k.io["c_in"]).then_inc(loaded, 16)
                sp.dma_start(k.x, k.io["x_in"]).then_inc(loaded, 16)
                sp.dma_start(k.params, k.io["params_in"]).then_inc(loaded, 16)
                sp.dma_start(k.selection, k.io["selection_in"]).then_inc(loaded, 16)
                sp.wait_ge(loaded, 64)

            @block.gpsimd
            def _(pool):
                m = k.masks
                pool.memset(k.eps[:, 0:1], EPS)
                pool.memset(k.eps[:, 1:2], GN_EPS)
                pool.memset(k.eps[:, 2:3], 1.0)
                pool.memset(m[:, 0:N_MASK * P], 1.0).then_inc(ones_ready, 1)
                pool.memset(k.resets, 1.0).then_inc(ones_ready, 1)
                pool.memset(k.bigs, 0.0).then_inc(ones_ready, 1)
                pool.wait_ge(ones_ready, 3)

                def keep(name, op, base, cm, step, fill=0.0, view=None):
                    v = view if view is not None else k.mask(name)
                    return pool.affine_select(out=v, in_=v, compare_op=op, fill=fill, base=base,
                                              pattern=[[step, P]], channel_multiplier=cm)
                keep("ident", ALU.is_equal, 0, 1, -1)
                keep("below", ALU.is_gt, 0, 1, -1)
                keep("above", ALU.is_gt, 0, -1, 1)
                keep("above_eq", ALU.is_ge, 0, -1, 1)
                keep(None, ALU.is_gt, 0, 1, -1, fill=BIG, view=k.big("not_below"))
                keep(None, ALU.is_ge, 0, -1, 1, fill=BIG, view=k.big("not_above_eq"))
                for w in (8, 16, 32, 64):
                    v = k.mask(f"block{w}").rearrange("p (b i) -> p b i", i=w)
                    pool.affine_select(out=v, in_=v, compare_op=ALU.is_ge, fill=0.0, base=0,
                                       pattern=[[-w, P // w], [0, w]], channel_multiplier=1)
                last = pool.memset(k.resets[:, 0:TP].rearrange("p (c i) -> p c i", i=CH)[:, :, 0:1], 0.0)
                last = pool.memset(k.resets[:, TP:T].rearrange("p (c i) -> p c i", i=TS)[:, :, 0:1], 0.0)
                last.then_inc(base_ready, 1)
                pool.wait_ge(base_ready, 1)
                for w in (8, 16, 32, 64):
                    v = k.mask(f"block{w}").rearrange("p (b i) -> p b i", i=w)
                    last = pool.affine_select(out=v, in_=v, compare_op=ALU.is_ge, fill=0.0, base=w - 1,
                                              pattern=[[w, P // w], [0, w]], channel_multiplier=-1)
                last.then_inc(base_ready, 1)
                pool.wait_ge(base_ready, 2)
                for w in (16, 32, 64):
                    outer = k.mask("ones") if w == 64 else k.mask(f"block{2 * w}")
                    pool.tensor_tensor(k.mask(f"level{w}"), outer, k.mask(f"block{w}"), ALU.subtract)
                pool.tensor_tensor(k.mask("below8"), k.mask("below"), k.mask("block8"), ALU.mult)
                pool.tensor_tensor(k.mask("above8"), k.mask("above"), k.mask("block8"), ALU.mult)
                pool.tensor_tensor(k.mask("above_eq8"), k.mask("above_eq"), k.mask("block8"), ALU.mult)
                pool.tensor_tensor(k.mask("above_eq16"), k.mask("above_eq"), k.mask("block16"), ALU.mult)
                pool.tensor_tensor(k.mask("above16"), k.mask("above"), k.mask("block16"), ALU.mult)
                pool.tensor_scalar(k.big("outside8"), k.mask("block8"), -BIG, BIG, ALU.mult, ALU.add)\
                    .then_inc(base_ready, 1)
                pool.wait_ge(base_ready, 3)
                for w in (16, 32, 64):
                    pool.tensor_tensor(k.mask(f"above_level{w}"), k.mask("above"), k.mask(f"level{w}"), ALU.mult)
                for a, b in (("not_below8", "not_below"), ("not_above_eq8", "not_above_eq")):
                    last = pool.tensor_tensor(k.big(a), k.big("outside8"), k.big(b), ALU.add)
                last.then_inc(masks_ready, 1)

            @block.scalar
            def _(act):
                act.wait_ge(loaded, 64)
                act.activation(k.cs_tmp, k.cs, ACT.Sigmoid).then_inc(sig_ready, 1)

            @block.vector
            def _(dve):
                dve.wait_ge(sig_ready, 1)
                dve.tensor_tensor(k.cs, k.cs, k.cs_tmp, ALU.mult).then_inc(cs_ready, 1)


MASKS = ("ident ones below above above_eq block8 block16 block32 block64 level16 level32 level64 "
         "below8 above8 above_eq8 above16 above_eq16 above_level16 above_level32 above_level64").split()
N_MASK = len(MASKS)
BIGS = "not_below not_above_eq outside8 not_below8 not_above_eq8".split()


MOD_W = MT * P // 2
MOD_G = MOD_W // 4
MOD_STEPS = 2 * KT


class Modulation:

    def __init__(self, k, s, sublayer, slots, room):
        self.k, self.sublayer, self.slots = k, sublayer, slots
        self.landed = [s.sem(f"mod_landed{b}") for b in range(slots)]
        self.done, self.cleared, self.copied, self.turned, self.biased, self.finished = (
            s.sem(n) for n in ("mod_done", "mod_cleared", "mod_copied", "mod_turned", "mod_biased",
                               "mod_finished"))
        self.slot = [room[:, b * MOD_W:(b + 1) * MOD_W] for b in range(slots)]
        at = slots * MOD_W
        self.by_vector = room[:, at:at + 2 * MOD_G]
        self.row0 = sublayer * MOD_STEPS

    def load(self, sp, slot, step):
        at = self.row0 + step
        src = self.k.io["w_mod"][at] if isinstance(step, int) else \
            self.k.io["w_mod"][bass.ds(at, 1)].rearrange("a p n -> (a p) n")
        sp.dma_start(self.slot[slot], src).then_inc(self.landed[slot], 16)

    def clear(self, pool):
        pool.memset(self.by_vector, 0.0).then_inc(self.cleared, 1)

    def products(self, pe, kt, slot, half, wait_landed):
        k = self.k
        pe.wait_ge(self.landed[slot], wait_landed)
        for j in range(4):
            last = pe.matmul(k.psum[6 + half][32 * j:32 * j + NC, 0:MOD_G], k.cs[:, kt * NC:(kt + 1) * NC],
                             self.slot[slot][:, j * MOD_G:(j + 1) * MOD_G], start=kt == 0, stop=kt == KT - 1)
        last.then_inc(self.done, 1)

    def copy(self, act):
        act.wait_ge(self.cleared, 1)
        act.wait_ge(self.done, MOD_STEPS)
        for j in range(4):
            at = slice(32 * j, 32 * j + NC)
            last = act.activation(self.by_vector[at].rearrange("p (a n) -> p a n", a=2),
                                  self.k.psum_pair(3)[at, :, 0:MOD_G], ACT.Copy)
        last.then_inc(self.copied, 1)

    def turn(self, pe):
        pe.wait_ge(self.copied, 1)
        for half in range(2):
            for b in range(3):
                at = half * MOD_G + b * P
                last = pe.transpose(self.k.psum[4 + half][:, b * P:(b + 1) * P], self.by_vector[:, at:at + P],
                                    self.k.mask("ident"))
        last.then_inc(self.turned, 1)

    def finish(self, dve):
        k, mod = self.k, self.k.mods[self.sublayer % 2]
        bias = k.par("b_mod")[:, self.sublayer * MT:(self.sublayer + 1) * MT]
        dve.wait_ge(self.turned, 1)
        for half in range(2):
            tiles = slice(half * MT // 2, (half + 1) * MT // 2)
            dve.tensor_tensor(
                mod[:, tiles.start * NC:tiles.stop * NC].rearrange("p (j b s) -> p j b s", j=4, s=NC),
                k.psum[4 + half][:, 0:3 * P].rearrange("p (b j i) -> p j b i", b=3, i=32)[:, :, :, 0:NC],
                bias[:, tiles].rearrange("p (j b) -> p j b", j=4)[:, :, :, None].to_broadcast([P, 4, 3, NC]),
                ALU.add).then_inc(self.biased, 1)
        dve.wait_ge(self.biased, 2)
        mod = mod.rearrange("p (m s) -> p m s", s=NC)
        gain = k.par("norm_gain")[:, self.sublayer * KT:(self.sublayer + 1) * KT, None].to_broadcast([P, KT, NC])
        dve.scalar_tensor_tensor(out=mod[:, KT:2 * KT], in0=mod[:, KT:2 * KT], scalar=1.0, in1=gain,
                                 op0=ALU.add, op1=ALU.mult).then_inc(self.finished, 1)
        weight = 1.0 if self.sublayer % 3 == 1 else 0.5
        dve.tensor_scalar(mod[:, 2 * KT:3 * KT], mod[:, 2 * KT:3 * KT], 1.0, weight, ALU.add, ALU.mult)\
            .then_inc(self.finished, 1)


def first_modulation(k):
    nc = k.nc
    SLOTS = 8
    with nc.cleanup_on_exit():
        s = Phase(nc)
        mod = Modulation(k, s, 0, SLOTS, k.arena)
        with nc.Block() as block:
            @block.sync
            def _(sp):
                for i in range(SLOTS):
                    mod.load(sp, i, i)
                with sp.Fori(1, MOD_STEPS // SLOTS) as r:
                    for b in range(SLOTS):
                        sp.wait_ge(mod.done, (r - 1) * SLOTS + b + 1)
                        mod.load(sp, b, r * SLOTS + b)

            @block.gpsimd
            def _(pool):
                mod.clear(pool)

            @block.tensor
            def _(pe):
                for i in range(MOD_STEPS):
                    mod.products(pe, i // 2, i % SLOTS, i % 2, (i // SLOTS + 1) * 16)
                mod.turn(pe)

            @block.scalar
            def _(act):
                mod.copy(act)

            @block.vector
            def _(dve):
                mod.finish(dve)


def normalise(k, sublayer, final=False, wide=False):
    nc = k.nc
    with nc.cleanup_on_exit():
        s = Phase(nc)
        squared, summed, rooted, inverse, scaled, shifted, stored, loaded = (
            s.sem(n) for n in ("squared", "summed", "rooted", "inverse", "scaled", "shifted", "stored", "loaded"))
        x = k.x.rearrange("p (k t) -> p k t", t=T)
        sq = k.big_buf[:, 0:KT * T].rearrange("p (k t) -> p k t", t=T)
        rstd = k.arena[:, 0:T]
        root = k.arena[:, T:2 * T]
        h = k.h.rearrange("p (k t) -> p k t", t=TX)
        hs = h[:, :, TP:TX].rearrange("p k (s t) -> p k s t", s=NSEQ)[:, :, :, PAD:] if wide else \
            h[:, :, TP:T].rearrange("p k (s t) -> p k s t", s=NSEQ)
        mod = k.mods[sublayer % 2].rearrange("p (m s) -> p m s", s=NC)
        pair = k.psum_pair(0)
        with nc.Block() as block:
            @block.scalar
            def _(act):
                for kt in range(KT):
                    act.activation(sq[:, kt], x[:, kt], ACT.Square).then_inc(squared, 1)
                act.wait_ge(summed, 1)
                act.activation(root.rearrange("p (a t) -> p a t", a=2), two_halves(pair, HALF), ACT.Sqrt,
                               bias=k.eps[:, 0:1], scale=1.0 / D).then_inc(rooted, 1)

            @block.tensor
            def _(pe):
                for kt in range(KT):
                    pe.wait_ge(squared, kt + 1)
                    for a in range(2):
                        last = pe.matmul(pair[:, a, 0:HALF], k.mask("ones"), sq[:, kt, a * HALF:(a + 1) * HALF],
                                         start=kt == 0, stop=kt == KT - 1)
                last.then_inc(summed, 1)

            @block.vector
            def _(dve):
                dve.wait_ge(rooted, 1)
                dve.reciprocal(rstd, root).then_inc(inverse, 1)
                dve.wait_ge(inverse, 1)
                rs = rstd[:, None, TP:T].to_broadcast([P, KT, T - TP]).rearrange("p k (s t) -> p k s t", s=NSEQ)
                for kt in range(KT):
                    gain = k.par("final_gain")[:, kt:kt + 1] if final else mod[:, KT + kt, 0:1]
                    dve.scalar_tensor_tensor(out=h[:, kt, 0:TP], in0=x[:, kt, 0:TP], scalar=gain,
                                             in1=rstd[:, 0:TP], op0=ALU.mult, op1=ALU.mult).then_inc(scaled, 1)
                dve.tensor_tensor(hs, x[:, :, TP:T].rearrange("p k (s t) -> p k s t", s=NSEQ), rs, ALU.mult)\
                    .then_inc(scaled, 1)
                if final:
                    g = k.par("final_gain")[:, :, None, None].to_broadcast([P, KT, NSEQ, TS])
                else:
                    g = mod[:, KT:2 * KT, 1:NC, None].to_broadcast([P, KT, NSEQ, TS])
                dve.wait_ge(scaled, KT + 1)
                dve.tensor_tensor(hs, hs, g, ALU.mult).then_inc(scaled, 1)
                if not final:
                    for kt in range(KT):
                        dve.tensor_scalar(h[:, kt, 0:TP], h[:, kt, 0:TP], mod[:, kt, 0:1], None, ALU.add)\
                            .then_inc(shifted, 1)
                    dve.wait_ge(scaled, KT + 2)
                    dve.tensor_tensor(hs, hs, mod[:, 0:KT, 1:NC, None].to_broadcast([P, KT, NSEQ, TS]), ALU.add)\
                        .then_inc(shifted, 1)

            @block.sync
            def _(sp):
                if final:
                    sp.wait_ge(scaled, KT + 2)
                    sp.dma_start(k.io["y_out"], h[:, :, 0:T]).then_inc(stored, 16)
                    sp.wait_ge(stored, 16)
                if wide:
                    for kt in range(KT):
                        sp.dma_start(h[:, kt, TP:TX].rearrange("p (s t) -> p s t", s=NSEQ)[:, :, 0:PAD],
                                     k.io["xbuf_in"][:, kt]).then_inc(loaded, 16)
                    sp.wait_ge(loaded, 16 * KT)
                    sp.wait_ge(shifted, KT + 1)
                    sp.dma_start(k.io["xbuf_p_out"], h[:, :, TP - PAD:TP]).then_inc(stored, 16)
                    for kt in range(KT):
                        sp.dma_start(k.io["xbuf_s_out"][:, kt], h[:, kt, TP:TX].rearrange("p (s t) -> p s t", s=NSEQ)
                                     [:, :, TS:]).then_inc(stored, 16)
                    sp.wait_ge(stored, 16 + 16 * KT)


def add_gated(dve, k, product, gate, m, scratch, prompt_done, sample_done):
    x = k.x[:, bass.ds(m * T, T)]
    g = gate[:, bass.ds(m * NC, NC)]
    dve.scalar_tensor_tensor(out=x[:, 0:HALF], in0=product[:, 0, 0:HALF], scalar=g[:, 0:1],
                             in1=x[:, 0:HALF], op0=ALU.mult, op1=ALU.add)
    dve.scalar_tensor_tensor(out=x[:, HALF:TP], in0=product[:, 1, 0:TP - HALF], scalar=g[:, 0:1],
                             in1=x[:, HALF:TP], op0=ALU.mult, op1=ALU.add).then_inc(prompt_done, 1)
    per_token = g[:, 1:NC, None].to_broadcast([P, NSEQ, TS])
    dve.tensor_tensor(scratch.rearrange("p (s t) -> p s t", s=NSEQ),
                      product[:, 1, TP - HALF:HALF].rearrange("p (s t) -> p s t", s=NSEQ),
                      per_token, ALU.mult).then_inc(sample_done, 1)


def residual_product(k, weights, row0, source, n_in, sublayer):
    nc = k.nc
    SLOTS = 4
    W = n_in * P
    with nc.cleanup_on_exit():
        s = Phase(nc)
        landed = [s.sem(f"out_landed{b}") for b in range(SLOTS)]
        product, prompt_done, sample_done, taken = (
            s.sem(n) for n in ("product", "prompt_done", "sample_done", "taken"))
        slot = [k.arena[:, b * W:(b + 1) * W] for b in range(SLOTS)]
        gate = k.mods[sublayer % 2][:, 2 * KT * NC:3 * KT * NC]
        mod = Modulation(k, s, sublayer + 1, 2, k.h) if sublayer + 1 < DEPTH * 3 else None
        with nc.Block() as block:
            @block.sync
            def _(sp):
                for m in range(KT):
                    if mod:
                        for half in range(2):
                            if m > 0:
                                sp.wait_ge(mod.done, 2 * (m - 1) + half + 1)
                            mod.load(sp, half, 2 * m + half)
                    if m >= SLOTS:
                        sp.wait_ge(product, m - SLOTS + 1)
                    sp.dma_start(slot[m % SLOTS], weights[row0 + m]).then_inc(landed[m % SLOTS], 16)

            @block.gpsimd
            def _(pool):
                if mod:
                    mod.clear(pool)

            @block.tensor
            def _(pe):
                for m in range(KT):
                    if mod:
                        for half in range(2):
                            mod.products(pe, m, half, half, (m + 1) * 16)
                    pe.wait_ge(landed[m % SLOTS], (m // SLOTS + 1) * 16)
                    if m >= 2:
                        pe.wait_ge(taken, m - 1)
                    for kt in range(n_in):
                        for a in range(2):
                            last = pe.matmul(k.psum_pair(m % 2)[:, a, 0:HALF], slot[m % SLOTS][:, kt * P:(kt + 1) * P],
                                             source(kt)[:, a * HALF:(a + 1) * HALF],
                                             start=kt == 0, stop=kt == n_in - 1)
                    last.then_inc(product, 1)
                if mod:
                    mod.turn(pe)

            @block.scalar
            def _(act):
                if mod:
                    mod.copy(act)

            @block.vector
            def _(dve):
                for m in range(KT):
                    dve.wait_ge(product, m + 1)
                    scratch = k.gated[:, m % 4 * (T - TP):(m % 4 + 1) * (T - TP)]
                    add_gated(dve, k, k.psum_pair(m % 2), gate, m, scratch, prompt_done, sample_done)
                    dve.wait_ge(sample_done, m + 1)
                    xs = k.x[:, m * T + TP:(m + 1) * T]
                    dve.tensor_tensor(xs, xs, scratch, ALU.add).then_inc(taken, 1)
                if mod:
                    mod.finish(dve)


def feed_forward(k, sublayer):
    nc = k.nc
    SLOTS = 4
    W = 2 * D
    which = sublayer // 3 * 2 + sublayer % 3 // 2
    row0 = which * FT
    with nc.cleanup_on_exit():
        s = Phase(nc)
        landed = [s.sem(f"ff_landed{b}") for b in range(SLOTS)]
        product, silu_done, act_done = (s.sem(n) for n in ("product", "silu_done", "act_done"))
        slot = [k.arena[:, b * W:(b + 1) * W] for b in range(SLOTS)]
        silu = [k.arena[:, RING + b * T:RING + (b + 1) * T] for b in range(2)]
        MAIN = FT // SLOTS
        REST = FT % SLOTS
        with nc.Block() as block:
            @block.sync
            def _(sp):
                for b in range(SLOTS):
                    sp.dma_start(slot[b], k.io["w_ff"][row0 + b]).then_inc(landed[b], 16)
                with sp.Fori(1, MAIN) as r:
                    for b in range(SLOTS):
                        sp.wait_ge(product, (r - 1) * SLOTS + b + 1)
                        sp.dma_start(slot[b], k.io["w_ff"][bass.ds(row0 + b + r * SLOTS, 1)]
                                     .rearrange("a p n -> (a p) n")).then_inc(landed[b], 16)
                for b in range(REST):
                    sp.wait_ge(product, (MAIN - 1) * SLOTS + b + 1)
                    sp.dma_start(slot[b], k.io["w_ff"][row0 + MAIN * SLOTS + b]).then_inc(landed[b], 16)

            @block.tensor
            def _(pe):
                def tile(b, wait_landed, wait_taken):
                    pe.wait_ge(landed[b], wait_landed)
                    if wait_taken is not None:
                        pe.wait_ge(act_done, wait_taken)
                    for g in range(2):
                        pair = k.psum_pair(2 * (b % 2) + g)
                        for kt in range(KT):
                            for a in range(2):
                                at = kt * TX + a * HALF
                                last = pe.matmul(pair[:, a, 0:HALF], slot[b][:, g * D + kt * P:g * D + (kt + 1) * P],
                                                 k.h[:, at:at + HALF], start=kt == 0, stop=kt == KT - 1)
                    last.then_inc(product, 1)
                for b in range(SLOTS):
                    tile(b, 16, None if b < 2 else b - 1)
                with pe.Fori(1, MAIN) as r:
                    for b in range(SLOTS):
                        tile(b, (r + 1) * 16, r * SLOTS + b - 1)
                for b in range(REST):
                    tile(b, (MAIN + 1) * 16, MAIN * SLOTS + b - 1)

            @block.scalar
            def _(act):
                def tile(b, m, wait_free):
                    act.wait_ge(product, m + 1)
                    if wait_free is not None:
                        act.wait_ge(act_done, wait_free)
                    act.activation(silu[b].rearrange("p (a t) -> p a t", a=2), two_halves(k.psum_pair(2 * b), HALF),
                                   ACT.Silu).then_inc(silu_done, 1)
                for b in range(2):
                    tile(b, b, None)
                with act.Fori(1, FT // 2) as r:
                    for b in range(2):
                        tile(b, 2 * r + b, 2 * r + b - 1)

            @block.vector
            def _(dve):
                with dve.Fori(0, FT // 2) as r:
                    for b in range(2):
                        dve.wait_ge(silu_done, 2 * r + b + 1)
                        out = k.big_buf[:, bass.ds((2 * r + b) * T, T)].rearrange("p (a t) -> p a t", a=2)
                        dve.tensor_tensor(out, silu[b].rearrange("p (a t) -> p a t", a=2),
                                          two_halves(k.psum_pair(2 * b + 1), HALF), ALU.mult).then_inc(act_done, 1)
    residual_product(k, k.io["w_down"], which * KT, lambda kt: k.big_buf[:, kt * T:(kt + 1) * T], FT, sublayer)


class Schedule:

    def __init__(self, phase, **steps):
        self.count = {e: {n: i + 1 for i, n in enumerate(names)} for e, names in steps.items()}
        for e, names in steps.items():
            assert len(set(names)) == len(names), (e, [n for n in names if names.count(n) > 1])
        self.sems = {e: phase.sem(f"{e}_steps") for e in steps}
        self.said = {e: 0 for e in steps}

    def did(self, engine, name):
        self.said[engine] += 1
        assert self.count[engine][name] == self.said[engine], (engine, name)
        return self.sems[engine], 1

    def after(self, engine, name):
        return self.sems[engine], self.count[engine][name]


def halves_of(tile_count, n):
    return [(t, half) for t in range(tile_count) for half in range(2)]


def project_even(k):
    nc = k.nc
    SLOTS, NCONV, NMIX, NZ = 4, 12, 14, 4
    TILES = NCONV + NMIX + NZ + 1
    ROUNDS = TILES // SLOTS
    REST = TILES % SLOTS
    with nc.cleanup_on_exit():
        s = Phase(nc)
        landed = [s.sem(f"in_landed{b}") for b in range(SLOTS)]
        product, cleared, staged, tile_done, chain = (
            s.sem(n) for n in ("product", "cleared", "staged", "tile_done", "chain"))
        slot = [k.arena[:, b * D:(b + 1) * D] for b in range(SLOTS)]
        SW = PAD + TX + 5
        stage = [k.arena[:, RING + b * SW:RING + (b + 1) * SW] for b in range(2)]
        delta = k.arena[:, RING + 2 * SW:RING + 2 * SW + T]
        rows = k.rows
        with nc.Block() as block:
            @block.sync
            def _(sp):
                for b in range(SLOTS):
                    sp.dma_start(slot[b], k.io["w_in_even"][b]).then_inc(landed[b], 16)
                with sp.Fori(1, ROUNDS) as r:
                    for b in range(SLOTS):
                        sp.wait_ge(product, (r - 1) * SLOTS + b + 1)
                        sp.dma_start(slot[b], k.io["w_in_even"][bass.ds(b + r * SLOTS, 1)]
                                     .rearrange("a p n -> (a p) n")).then_inc(landed[b], 16)
                for b in range(REST):
                    sp.wait_ge(product, (ROUNDS - 1) * SLOTS + b + 1)
                    sp.dma_start(slot[b], k.io["w_in_even"][ROUNDS * SLOTS + b]).then_inc(landed[b], 16)

            @block.tensor
            def _(pe):
                def tile(b, wait_landed, wait_staged):
                    pe.wait_ge(landed[b], wait_landed)
                    if wait_staged is not None:
                        pe.wait_ge(staged, wait_staged)
                    for kt in range(KT):
                        for a in range(2):
                            at = kt * TX + a * HALFX
                            last = pe.matmul(k.psum_pair(b)[:, a, 0:HALFX], slot[b][:, kt * P:(kt + 1) * P],
                                             k.h[:, at:at + HALFX], start=kt == 0, stop=kt == KT - 1)
                    last.then_inc(product, 1)
                for b in range(SLOTS):
                    tile(b, 16, None)
                with pe.Fori(1, ROUNDS) as r:
                    for b in range(SLOTS):
                        tile(b, (r + 1) * 16, (r - 1) * SLOTS + b + 1)
                for b in range(REST):
                    tile(b, (ROUNDS + 1) * 16, (ROUNDS - 1) * SLOTS + b + 1)

            @block.scalar
            def _(act):
                def to_stage(b, pair, m, wait_free):
                    act.wait_ge(product, m + 1)
                    if wait_free is not None:
                        act.wait_ge(tile_done, wait_free)
                    act.activation(stage[b][:, PAD:PAD + TX].rearrange("p (a t) -> p a t", a=2),
                                   two_halves(k.psum_pair(pair), HALFX), ACT.Copy).then_inc(staged, 1)

                def compact(out, pair, rows_out):
                    ps = k.psum_pair(pair)[0:rows_out]
                    act.activation(out[0:rows_out, 0:HALFX], ps[:, 0, 0:HALFX], ACT.Copy)
                    act.activation(out[0:rows_out, HALFX:TP], ps[:, 1, 0:TP - HALFX], ACT.Copy)
                    return act.activation(
                        out[0:rows_out, TP:T].rearrange("p (s t) -> p s t", s=NSEQ),
                        ps[:, 1, TP - HALFX:HALFX].rearrange("p (s t) -> p s t", s=NSEQ)[:, :, PAD:], ACT.Copy)
                act.wait_ge(cleared, 2)
                to_stage(0, 0, 0, None)
                to_stage(1, 1, 1, None)
                to_stage(0, 2, 2, 1)
                to_stage(1, 3, 3, 2)
                with act.Fori(1, (NCONV + NMIX) // 4) as r:
                    for b in range(4):
                        to_stage(b % 2, b, 4 * r + b, 4 * r + b - 1)
                for m in range((NCONV + NMIX) // 4 * 4, NCONV + NMIX):
                    to_stage(m % 2, m % 4, m, m - 1)
                for i in range(NZ):
                    m = NCONV + NMIX + i
                    act.wait_ge(product, m + 1)
                    compact(k.big_buf[:, (NCONV + i) * T:(NCONV + i + 1) * T], m % 4, P).then_inc(staged, 1)
                act.wait_ge(product, TILES)
                compact(rows, (TILES - 1) % 4, 64).then_inc(staged, 1)

            @block.vector
            def _(dve):
                for b in range(2):
                    dve.memset(stage[b][:, 0:PAD], 0.0).then_inc(cleared, 1)

                def views(b, shift):
                    return (stage[b][:, shift:shift + TP],
                            stage[b][:, PAD + TP:PAD + TX].rearrange("p (s t) -> p s t", s=NSEQ)
                            [:, :, shift:shift + TS])

                def conv(b, m):
                    dve.wait_ge(staged, m + 1)
                    out = k.big_buf[:, bass.ds(m * T, T)]
                    out_s = out[:, TP:T].rearrange("p (s t) -> p s t", s=NSEQ)
                    w = k.par("conv_w")[:, bass.ds(m * CONV_W, CONV_W)]
                    for j in range(CONV_W):
                        in_p, in_s = views(b, j)
                        if j == 0:
                            dve.tensor_scalar(out[:, 0:TP], in_p, w[:, 0:1], None, ALU.mult)
                            last = dve.tensor_scalar(out_s, in_s, w[:, 0:1], None, ALU.mult)
                        else:
                            dve.wait_ge(chain, m * (CONV_W - 1) + j)
                            dve.scalar_tensor_tensor(out=out[:, 0:TP], in0=in_p, scalar=w[:, j:j + 1],
                                                     in1=out[:, 0:TP], op0=ALU.mult, op1=ALU.add)
                            last = dve.scalar_tensor_tensor(out=out_s, in0=in_s, scalar=w[:, j:j + 1],
                                                            in1=out_s, op0=ALU.mult, op1=ALU.add)
                        if j < CONV_W - 1:
                            last.then_inc(chain, 1)
                        else:
                            last.then_inc(tile_done, 1)

                def mix(b, i):
                    dve.wait_ge(staged, NCONV + i + 1)
                    cur_p, cur_s = views(b, PAD)
                    prev_p, prev_s = views(b, PAD - 1)
                    out = k.big_buf[:, bass.ds((i + NCONV + NZ) * T, T)]
                    d_s = delta[:, TP:T].rearrange("p (s t) -> p s t", s=NSEQ)
                    dve.wait_ge(tile_done, NCONV + i)
                    dve.tensor_tensor(delta[:, 0:TP], prev_p, cur_p, ALU.subtract)
                    dve.tensor_tensor(d_s, prev_s, cur_s, ALU.subtract).then_inc(chain, 1)
                    dve.wait_ge(chain, NCONV * (CONV_W - 1) + i + 1)
                    mu = k.par("mu")[:, bass.ds(i, 1)]
                    dve.scalar_tensor_tensor(out=out[:, 0:TP], in0=delta[:, 0:TP], scalar=mu, in1=cur_p,
                                             op0=ALU.mult, op1=ALU.add)
                    dve.scalar_tensor_tensor(out=out[:, TP:T].rearrange("p (s t) -> p s t", s=NSEQ), in0=d_s,
                                             scalar=mu, in1=cur_s, op0=ALU.mult, op1=ALU.add)\
                        .then_inc(tile_done, 1)
                with dve.Fori(0, NCONV // 2) as r:
                    for b in range(2):
                        conv(b, 2 * r + b)
                with dve.Fori(0, NMIX // 2) as r:
                    for b in range(2):
                        mix(b, 2 * r + b)


Q_A, K_A, V_A, Z_A, R_B, K_B, V_B, LR_B, G_B = 0, 4, 8, 12, 16, 20, 24, 28, 29
NEG_KK, KK_A = 0, 4
ROW_GC, ROW_BETA, ROW_TO_END, COL_BETA_GC = 0, 1, 2, 3


def prepare_even(k):
    nc = k.nc
    big = lambda t, n=1: k.big_buf[:, t * T:(t + n) * T]
    hb = lambda t, n=1: k.h[:, t * T:(t + n) * T]
    sq = lambda i: k.arena[:, i * T:(i + 1) * T]
    rate = lambda i: k.arena[:, (12 + i) * T:(13 + i) * T]
    spare = lambda i: k.arena[:, (16 + i) * T:(17 + i) * T]
    w2 = k.arena[:, 20 * T:20 * T + 512]
    neg = k.arena[:, 20 * T + 512:20 * T + 520]
    ea = k.arena[:, 20 * T + 520:20 * T + 521]
    softp = k.arena[0:4, 21 * T:22 * T]
    rows = k.rows
    N = range(12)
    act_steps = ([f"silu{i}" for i in range(4)] + ["tanh"] + [f"square{i}" for i in N]
                 + ["abs", "exp", "ln", "exp_a_log", "exp_b", "exp_g"]
                 + [f"exp_w{i}" for i in range(4)] + [f"exp_r{i}" for i in range(4)] + ["exp_to_end", "cols", "exp_gc"]
                 + [f"root{i}" for i in N])
    dve_steps = (["neg_w0", "neg_a0", "rows_b", "rows_clear"] + [f"kk_raw{i}" for i in range(4)]
                 + ["relu", "softplus", "g", "gc", "to_end_p", "to_end_s", "beta1", "beta", "sig1", "sig"]
                 + [f"{n}{i}" for i in range(4) for n in ("w1_", "w2_", "w3_", "lc")]
                 + [f"{n}{i}" for i in range(4) for n in ("r1_", "r2_", "t1_", "k")]
                 + ["beta_gc"]
                 + [f"{n}{i}" for i in N for n in ("inv", "unit")] + [f"kka{i}" for i in range(4)])
    with nc.cleanup_on_exit():
        s = Phase(nc)
        q = Schedule(s, act=act_steps, dve=dve_steps,
                     pe=[f"w{i}" for i in range(4)] + [f"r{i}" for i in range(4)] + ["cols"] + [f"sum{i}" for i in N])
        did, after = q.did, q.after
        loaded, kept = s.sem("w2_loaded"), s.sem("x_kept")
        with nc.Block() as block:
            @block.sync
            def _(sp):
                sp.dma_start(w2, k.io["w_wa2"]).then_inc(loaded, 16)
                sp.dma_start(k.x_kept, k.x).then_inc(kept, 16)
                sp.wait_ge(loaded, 16)
                sp.wait_ge(kept, 16)

            @block.scalar
            def _(act):
                for i in range(4):
                    act.activation(big(4 * i, 4), big(4 * i, 4), ACT.Silu).then_inc(*did("act", f"silu{i}"))
                act.activation(k.big_buf[0:64, LR_B * T:(LR_B + 1) * T], k.big_buf[0:64, LR_B * T:(LR_B + 1) * T],
                               ACT.Tanh).then_inc(*did("act", "tanh"))
                act.wait_ge(*after("act", "silu1"))
                for i in range(8):
                    act.activation(sq(i), big(Q_A + i), ACT.Square).then_inc(*did("act", f"square{i}"))
                for i in range(4):
                    act.wait_ge(*after("dve", f"kk_raw{i}"))
                    act.activation(sq(8 + i), hb(NEG_KK + i), ACT.Square).then_inc(*did("act", f"square{8 + i}"))
                act.wait_ge(*after("dve", "rows_b"))
                act.activation(softp, rows[0:4, :], ACT.Abs, bias=k.par("dt_bias")[0:4, :]).then_inc(*did("act", "abs"))
                act.wait_ge(*after("act", "abs"))
                act.activation(softp, softp, ACT.Exp, scale=-1.0).then_inc(*did("act", "exp"))
                act.wait_ge(*after("act", "exp"))
                act.activation(softp, softp, ACT.Ln, bias=1.0).then_inc(*did("act", "ln"))
                act.activation(ea[0:4, :], k.par("a_log")[0:4, :], ACT.Exp).then_inc(*did("act", "exp_a_log"))
                act.activation(k.rows_b[0:4, :], k.rows_b[0:4, :], ACT.Exp, scale=-1.0).then_inc(*did("act", "exp_b"))
                act.activation(big(G_B), big(G_B), ACT.Exp, scale=-1.0).then_inc(*did("act", "exp_g"))
                for n, first, sem_name in (("w", 0, "exp_w"), ("r", 4, "exp_r")):
                    for i in range(4):
                        act.wait_ge(*after("pe", f"{n}{i}"))
                        dst = spare(i) if n == "w" else rate(i)
                        act.activation(dst.rearrange("p (a t) -> p a t", a=2), two_halves(k.psum_pair(i), HALF),
                                       ACT.Exp, scale=-1.0, bias=neg[:, first + i:first + i + 1])\
                            .then_inc(*did("act", f"{sem_name}{i}"))
                act.wait_ge(*after("dve", "to_end_s"))
                act.activation(rows[64:68, :], rows[64:68, :], ACT.Exp).then_inc(*did("act", "exp_to_end"))
                act.wait_ge(*after("pe", "cols"))
                cols = k.cols.rearrange("p (c r h) -> p c r h", c=5, r=4)
                act.activation(cols[:, 0:4, 0:3], k.psum[0].rearrange("p (c r h) -> p c r h", c=4, r=4)
                               [:, :, 0:3, 0:4], ACT.Copy)
                act.activation(cols[0:64, 4, 0:3], k.psum[1][0:64, 0:128].rearrange("p (r h) -> p r h", r=4)
                               [:, 0:3, 0:4], ACT.Copy).then_inc(*did("act", "cols"))
                act.wait_ge(*after("act", "cols"))
                act.activation(cols[:, 0:4, 3], cols[:, 0:4, 0], ACT.Exp)
                act.activation(cols[0:64, 4, 3], cols[0:64, 4, 0], ACT.Exp).then_inc(*did("act", "exp_gc"))
                for i in N:
                    act.wait_ge(*after("pe", f"sum{i}"))
                    act.activation(sq(i).rearrange("p (a t) -> p a t", a=2), two_halves(k.psum_pair(1 + i % 3), HALF),
                                   ACT.Sqrt, bias=k.eps[:, 0:1]).then_inc(*did("act", f"root{i}"))

            @block.tensor
            def _(pe):
                pe.wait_ge(loaded, 16)
                pe.wait_ge(*after("act", "tanh"))
                for n, lo in (("w", 0), ("r", 64)):
                    for i in range(4):
                        if n == "r":
                            pe.wait_ge(*after("act", f"exp_w{i}"))
                        for a in range(2):
                            at = LR_B * T + a * HALF
                            last = pe.matmul(k.psum_pair(i)[:, a, 0:HALF], w2[lo:lo + 64, i * P:(i + 1) * P],
                                             k.big_buf[lo:lo + 64, at:at + HALF], start=True, stop=True)
                        last.then_inc(*did("pe", f"{n}{i}"))
                pe.wait_ge(*after("act", "exp_to_end"))
                pe.wait_ge(*after("dve", "beta"))
                pe.wait_ge(*after("act", "exp_r3"))
                for c in range(NCH):
                    pe.transpose(k.psum[0][:, c * P:(c + 1) * P], rows[:, c * P:(c + 1) * P], k.mask("ident"))
                pe.transpose(k.psum[1][0:64, 0:P], rows[:, TP:T], k.mask("ident")).then_inc(*did("pe", "cols"))
                for i in N:
                    pe.wait_ge(*after("act", f"square{i}"))
                    if i >= 3:
                        pe.wait_ge(*after("act", f"root{i - 3}"))
                    ones = k.mask("ones") if i < 8 else k.mask("block64")
                    for a in range(2):
                        last = pe.matmul(k.psum_pair(1 + i % 3)[:, a, 0:HALF], ones, sq(i)[:, a * HALF:(a + 1) * HALF],
                                         start=True, stop=True)
                    last.then_inc(*did("pe", f"sum{i}"))

            @block.vector
            def _(dve):
                dve.tensor_scalar(neg[:, 0:4], k.par("w0"), -1.0, None, ALU.mult).then_inc(*did("dve", "neg_w0"))
                dve.tensor_scalar(neg[:, 4:8], k.par("a0"), -1.0, None, ALU.mult).then_inc(*did("dve", "neg_a0"))
                dve.tensor_copy(k.rows_b[0:4, :], rows[32:36, :]).then_inc(*did("dve", "rows_b"))
                dve.wait_ge(*after("dve", "rows_b"))
                dve.memset(rows[32:64, :], 0.0)
                dve.memset(rows[64:128, :], 0.0).then_inc(*did("dve", "rows_clear"))
                for i in range(4):
                    dve.tensor_scalar(hb(NEG_KK + i), big(K_B + i), k.par("k_k")[:, i:i + 1], None, ALU.mult)\
                        .then_inc(*did("dve", f"kk_raw{i}"))
                dve.wait_ge(*after("act", "abs"))
                dve.tensor_scalar(rows[0:4, :], rows[0:4, :], k.par("dt_bias")[0:4, :], 0.0, ALU.add, ALU.max)\
                    .then_inc(*did("dve", "relu"))
                dve.wait_ge(*after("act", "exp_a_log"))
                dve.wait_ge(*after("dve", "relu"))
                dve.tensor_tensor(softp, rows[0:4, :], softp, ALU.add).then_inc(*did("dve", "softplus"))
                dve.wait_ge(*after("dve", "softplus"))
                dve.tensor_scalar(softp, softp, ea[0:4, :], -1.0, ALU.mult, ALU.mult).then_inc(*did("dve", "g"))
                dve.wait_ge(*after("dve", "g"))
                dve.tensor_tensor_scan(rows[0:4, :], k.resets[0:4, :], softp, 0.0, ALU.mult, ALU.add)\
                    .then_inc(*did("dve", "gc"))
                dve.wait_ge(*after("dve", "gc"))
                dve.wait_ge(*after("dve", "rows_clear"))
                for name, lo, hi, w in (("to_end_p", 0, TP, CH), ("to_end_s", TP, T, TS)):
                    v = rows[0:4, lo:hi].rearrange("p (c i) -> p c i", i=w)
                    dve.tensor_tensor(rows[64:68, lo:hi].rearrange("p (c i) -> p c i", i=w),
                                      v[:, :, w - 1:w].to_broadcast([4, (hi - lo) // w, w]), v, ALU.subtract)\
                        .then_inc(*did("dve", name))
                dve.wait_ge(*after("act", "exp_b"))
                dve.tensor_scalar(k.rows_b[0:4, :], k.rows_b[0:4, :], 1.0, None, ALU.add)\
                    .then_inc(*did("dve", "beta1"))
                dve.wait_ge(*after("dve", "beta1"))
                dve.reciprocal(rows[32:36, :], k.rows_b[0:4, :]).then_inc(*did("dve", "beta"))
                dve.wait_ge(*after("act", "exp_g"))
                dve.tensor_scalar(big(G_B), big(G_B), 1.0, None, ALU.add).then_inc(*did("dve", "sig1"))
                dve.wait_ge(*after("dve", "sig1"))
                dve.reciprocal(big(G_B), big(G_B)).then_inc(*did("dve", "sig"))
                for i in range(4):
                    w = spare(i)
                    dve.wait_ge(*after("act", f"exp_w{i}"))
                    dve.tensor_scalar(w, w, 1.0, None, ALU.add).then_inc(*did("dve", f"w1_{i}"))
                    dve.wait_ge(*after("dve", f"w1_{i}"))
                    dve.reciprocal(w, w).then_inc(*did("dve", f"w2_{i}"))
                    dve.wait_ge(*after("dve", f"w2_{i}"))
                    dve.tensor_scalar(w, w, NEG_E_HALF, None, ALU.mult).then_inc(*did("dve", f"w3_{i}"))
                    dve.wait_ge(*after("dve", f"w3_{i}"))
                    dve.tensor_tensor_scan(k.lc[:, i * T:(i + 1) * T], k.resets, w, 0.0, ALU.mult, ALU.add)\
                        .then_inc(*did("dve", f"lc{i}"))
                for i in range(4):
                    a = rate(i)
                    dve.wait_ge(*after("act", f"exp_r{i}"))
                    dve.tensor_scalar(a, a, 1.0, None, ALU.add).then_inc(*did("dve", f"r1_{i}"))
                    dve.wait_ge(*after("dve", f"r1_{i}"))
                    dve.reciprocal(a, a).then_inc(*did("dve", f"r2_{i}"))
                    dve.wait_ge(*after("dve", f"r2_{i}"))
                    dve.tensor_scalar(spare(i), a, 1.0, k.par("k_a")[:, i:i + 1], ALU.subtract, ALU.mult)\
                        .then_inc(*did("dve", f"t1_{i}"))
                    dve.wait_ge(*after("dve", f"t1_{i}"))
                    dve.scalar_tensor_tensor(out=big(K_B + i), in0=spare(i), scalar=1.0, in1=big(K_B + i),
                                             op0=ALU.add, op1=ALU.mult).then_inc(*did("dve", f"k{i}"))
                dve.wait_ge(*after("act", "exp_gc"))
                cols = k.cols.rearrange("p (c r h) -> p c r h", c=5, r=4)
                dve.tensor_tensor(cols[:, 0:4, 3], cols[:, 0:4, 3], cols[:, 0:4, 1], ALU.mult)
                dve.tensor_tensor(cols[0:64, 4, 3], cols[0:64, 4, 3], cols[0:64, 4, 1], ALU.mult)\
                    .then_inc(*did("dve", "beta_gc"))
                for i in N:
                    dve.wait_ge(*after("act", f"root{i}"))
                    dve.reciprocal(sq(i), sq(i)).then_inc(*did("dve", f"inv{i}"))
                    dve.wait_ge(*after("dve", f"inv{i}"))
                    x, scale = (big(Q_A + i), 128.0 ** -0.5 if i < 4 else 1.0) if i < 8 else (hb(NEG_KK + i - 8), -1.0)
                    dve.scalar_tensor_tensor(out=x, in0=x, scalar=scale, in1=sq(i), op0=ALU.mult, op1=ALU.mult)\
                        .then_inc(*did("dve", f"unit{i}"))
                for i in range(4):
                    dve.wait_ge(*after("dve", f"unit{8 + i}"))
                    dve.scalar_tensor_tensor(out=hb(KK_A + i), in0=hb(NEG_KK + i), scalar=-1.0, in1=rate(i),
                                             op0=ALU.mult, op1=ALU.mult).then_inc(*did("dve", f"kka{i}"))


def carve(region, at=0):
    def take(n):
        nonlocal at
        at += n
        assert at <= region.shape[-1], (at, region.shape)
        return region[:, at - n:at]
    return take


def heads4(ap, n):
    return ap.rearrange("p (h n) -> p h n", n=n)


STREAMS = 3
LEVELS = (16, 32, 64)


def inverse_jobs(sample):
    jobs = []
    G = range(STREAMS)
    for g in G:
        jobs += [(f"sq1_{g}", ("act", f"C1_{g}")), (f"sqt1_{g}", ("dve", f"CT1_{g}"))]
    for g in G:
        jobs += [(f"x1_{g}", ("dve", f"P1_{g}")), (f"sq2_{g}", ("act", f"B2_{g}"))]
        if not sample:
            jobs += [(f"sqt2_{g}", ("act", f"BT2_{g}"))]
    for g in G:
        jobs += [(f"x2_{g}", ("dve", f"P2_{g}"))]
        if not sample:
            jobs += [(f"sq3_{g}", ("act", f"C3_{g}"))]
    if sample:
        return jobs
    for g in G:
        jobs += [(f"x3_{g}", ("dve", f"P3_{g}"))]
    for w in LEVELS:
        for g in G:
            jobs += [(f"y{w}_{g}", ("act", f"Y{w}_{g}")), (f"tr{w}_{g}", ("dve", f"T{w}_{g}"))]
        for g in G:
            jobs += [(f"z{w}_{g}", ("dve", f"PZ{w}_{g}"))]
    return jobs


def even_jobs(sample):
    rw = [(f"{n}_{g}", ("dve", f"{n}m_{g}")) for g in (1, 2) for n in ("m", "mt", "rb", "ka", "kr")]
    jobs = [("R", ("act", "eR")), ("kk", ("dve", "M0")), ("kq", ("dve", "KQD")), ("mt_0", ("dve", "mtm_0"))] + rw + [
        ("vt", ("dve", "VB")), ("kt", ("dve", "KD")), ("rvt", ("act", "RVt")), ("rbt", ("act", "RBt")),
        ("rkt", ("act", "RKt"))]
    jobs += inverse_jobs(sample)
    if not sample:
        jobs += [("ks", ("dve", "W1")), ("rw_1", ("act", "RW_1")), ("rw_2", ("act", "RW_2")), ("u", ("act", "U")),
                 ("ru", ("dve", "RU")), ("o", ("act", "O")), ("s", ("dve", "S3")), ("ry", ("act", "RY")), ("rs", ("dve", "RS1"))]
    else:
        jobs += [("ko", ("act", "KO")), ("rko", ("act", "RKO")), ("kst", ("dve", "W1")), ("rwt", ("act", "RWt")),
                 ("rw", ("dve", "RW")), ("u", ("act", "U")), ("ru", ("act", "RU")), ("o", ("dve", "O")),
                 ("ry", ("dve", "RY"))]
        for h in range(4):
            jobs += [(f"s{h}a", ("dve", f"S{h}a")), (f"s{h}b", ("dve", f"S{h}b"))]
        jobs += [(f"rs{t}", ("dve", f"RS{t}")) for t in range(4)]
    return jobs


def even_chunks(k, sample):
    nc = k.nc
    n = NSEQ * TS if sample else CH
    chunks = [NCH] if sample else list(range(NCH))
    G = range(STREAMS)
    jobs1 = even_jobs(sample)
    names = lambda base, c: f"{base}@{c}"
    pe_steps, bank_freed_by = [], []
    act_steps, dve_steps = [], []
    inv_act = lambda: [f"C1_{g}" for g in G] + [x for g in G for x in ([f"B2_{g}"] if sample else [f"B2_{g}", f"BT2_{g}"])]
    for c in chunks:
        pe_steps += [names(j, c) for j, _ in jobs1]
        bank_freed_by += [(e, names(st, c)) for _, (e, st) in jobs1]
        a = ["eR", "DT", "D", "E"] + ([] if sample else ["exp_ref"]) + ["exp_E", "RVt", "RBt", "RKt"] + inv_act()
        d = ["d", "dU", "dL", "Et", "Eref", "Aq", "Rq", "Bq", "Kq"] + (["k_copy"] if sample else []) \
            + ["M0", "M1", "M2", "KQD"]
        d += ["mtm_0", "P0_0"]
        d += [f"{x}_{g}" for g in (1, 2) for x in ("mm", "mtm", "rbm", "kam", "krm", "P0")]
        d += ["VB", "KD", "QG"]
        if sample:
            a += ["KO", "RKO", "RWt", "U", "RU"]
            d += [f"CT1_{g}" for g in G] + [f"P1_{g}" for g in G] + [f"P2_{g}" for g in G]
            d += ["W1", "W2", "RW"] + ["O", "RY"]
            for h in range(4):
                d += [f"Um{h}", f"Sg{h}", f"S{h}a", f"S{h}b"]
            for t in range(4):
                d += [f"RUm{t}", f"RVm{t}", f"RS{t}", f"RSd{t}"]
        else:
            a += [f"C3_{g}" for g in G] + [f"Y{w}_{g}" for w in LEVELS for g in G] + ["RW_1", "RW_2", "U", "O", "RY"]
            d += [f"B_{g}" for g in G] + [f"CT1_{g}" for g in G] + [f"P1_{g}" for g in G] + [f"P2_{g}" for g in G] \
                + [f"P3_{g}" for g in G]
            for w in LEVELS:
                d += [f"T{w}_{g}" for g in G] + [f"PZ{w}_{g}" for g in G]
            d += ["S0s", "W1", "W2", "RU", "S1", "S3", "RS1", "RSn"]
        act_steps += [names(x, c) for x in a]
        dve_steps += [names(x, c) for x in d]
    pool_steps = [] if sample else [names(f"Ms{w}_{g}", c) for c in chunks for w in LEVELS for g in G]

    take = carve(k.work[:, 0:WORK - 4 * T])
    H = 4 * n
    new = lambda cols=H: take(cols)
    eR, KQD = new(), new()
    qg, KD, W, U = (None,) * 4 if sample else (new() for _ in range(4))
    Em = take(4 * (n + 1) if not sample else 4 * NSEQ * (TS + 1))
    AR, BK = take(2 * H), take(2 * H)
    Vt, Bt, Kt = take(512), take(512), take(512)
    if sample:
        Wd, Ud = take(512), take(512)
        KDt, VBt = take(512), take(512)
    else:
        Wd, Ud, KDt, VBt = W, U, KD, take(512)
    RW, RU = take(512), take(512)
    KA, KR, RB = ([None, new(), new()] for _ in range(3))
    A, B, BT, C, CT, Pt = ([new() for _ in G] for _ in range(6))
    Dm, DT, En = C[0], CT[0], C[1]
    if sample:
        S = take(32 * P)
        RS = take(4 * NSEQ * 64)
        KQg = take(2 * H)
        KO, RKO = take(2 * H), take(2 * H)
        RUw, RVw = take(1024), take(1024)
        Uw = RUw
    else:
        S, RS, S0s = take(512), take(256), take(256)
        eref = take(4)
    mask = lambda nm, part=n: k.mask(nm)[0:part, 0:n]
    bc = lambda m: m[:, None, :].to_broadcast([n, 4, n])
    v4 = lambda ap, part=P: ap[0:part].rearrange("p (h n) -> p h n", h=4)
    sfx = "8" if sample else ""

    with nc.cleanup_on_exit():
        ph = Phase(nc)
        sched = Schedule(ph, pe=pe_steps, act=act_steps, dve=dve_steps, pool=pool_steps)
        job_number = {j: i for i, j in enumerate(pe_steps)}
        states_in, states_out, zeroed = ph.sem("states_in"), ph.sem("states_out"), ph.sem("zeroed")

        def bank(job, c):
            return k.psum[job_number[names(job, c)] % 8]

        def tokens(t, c, count=4):
            return k.big_buf[:, t * T:(t + count) * T].rearrange("p (h t) -> p h t", t=T)[:, :, c * CH:c * CH + n]

        def htokens(t, c, count=4):
            return k.h[:, t * T:(t + count) * T].rearrange("p (h t) -> p h t", t=T)[:, :, c * CH:c * CH + n]

        def col(c, r):
            v = k.cols[0:n].rearrange("p (c r h) -> p c r h", c=5, r=4)[:, c, r, :]
            return lambda w: v[:, :, None].to_broadcast([n, 4, w])

        with nc.Block() as block:
            @block.sync
            def _(sp):
                if sample:
                    sp.dma_start(S, k.io["delta_in"]).then_inc(states_in, 16)
                    sp.dma_start(RS, k.io["rwkv_in"]).then_inc(states_in, 16)
                    sp.wait_ge(*sched.after("dve", names("S3b", NCH)))
                    sp.dma_start(k.io["delta_s_out"], S).then_inc(states_out, 16)
                    sp.wait_ge(*sched.after("dve", names("RSd3", NCH)))
                    sp.dma_start(k.io["rwkv_s_out"], RS).then_inc(states_out, 16)
                else:
                    sp.wait_ge(*sched.after("dve", names("S3", NCH - 1)))
                    sp.dma_start(k.io["delta_p_out"], S).then_inc(states_out, 16)
                    sp.wait_ge(*sched.after("dve", names("RSn", NCH - 1)))
                    sp.dma_start(k.io["rwkv_p_out"], RS).then_inc(states_out, 16)
                sp.wait_ge(states_out, 32)

            @block.gpsimd
            def _(pool):
                if not sample:
                    pool.memset(S, 0.0).then_inc(zeroed, 1)
                    pool.memset(RS, 0.0).then_inc(zeroed, 1)
                    for c in chunks:
                        after = lambda e, nm: sched.after(e, names(nm, c))
                        for w, dst, free in ((16, CT, "sqt2"), (32, BT, "sq3"), (64, B, None)):
                            for g in G:
                                if free:
                                    pool.wait_ge(*after("pe", f"{free}_{g}"))
                                else:
                                    pool.wait_ge(*after("pe", f"z16_{g}"))
                                pool.tensor_tensor(v4(dst[g]), v4(A[g]), bc(k.mask(f"level{w}")), ALU.mult)\
                                    .then_inc(*sched.did("pool", names(f"Ms{w}_{g}", c)))

            @block.tensor
            def _(pe):
                for c in chunks:
                    after = lambda e, nm: sched.after(e, names(nm, c))

                    def claim(job):
                        i = job_number[names(job, c)]
                        if i >= 8:
                            pe.wait_ge(*sched.after(*bank_freed_by[i - 8]))
                        return bank(job, c)

                    def done(job, ins):
                        ins.then_inc(*sched.did("pe", names(job, c)))

                    def four(job, lhsT, rhs, out_part=n, width=n):
                        b = claim(job)
                        for h in range(4):
                            last = pe.matmul(b[0:out_part, h * width:(h + 1) * width], lhsT(h), rhs(h),
                                             start=True, stop=True)
                        done(job, last)

                    def four_transposes(job, source, cols=P):
                        b = claim(job)
                        for h in range(4):
                            src = source(h)
                            last = pe.transpose(b[0:src.shape[1], h * cols:(h + 1) * cols], src,
                                                k.mask("ident")[0:src.shape[0], 0:src.shape[0]])
                        done(job, last)

                    def of(buf, w=n, part=n):
                        return lambda h: buf[0:part, h * w:(h + 1) * w]

                    kc, qc, vc = (tokens(t, c) for t in (K_A, Q_A, V_A))
                    def place(g, h):
                        return h, 64 * (g - 1)

                    def ar(g, h, which):
                        t, p = place(g, h)
                        return AR[p:p + 64, (2 * t + which) * n:(2 * t + which + 1) * n]

                    def bk(g, h, which):
                        t, p = place(g, h)
                        return BK[p:p + 64, (2 * t + which) * n:(2 * t + which + 1) * n]

                    b = claim("R")
                    for h in range(4):
                        last = pe.matmul(b[:, h * n:(h + 1) * n], k.select(h)[0:4],
                                         k.rows[0:4, c * CH:c * CH + n], start=True, stop=True)
                    done("R", last)
                    four("kk", lambda h: kc[:, h], lambda h: kc[:, h])
                    four("kq", lambda h: kc[:, h], lambda h: qc[:, h])
                    pe.wait_ge(*after("dve", "M2"))
                    four_transposes("mt_0", lambda h: A[0][0:n, h * n:(h + 1) * n], n)
                    pe.wait_ge(*after("dve", "Kq"))
                    for g in (1, 2):
                        four(f"m_{g}", lambda h: ar(g, h, 0), lambda h: bk(g, h, 0))
                        four(f"mt_{g}", lambda h: bk(g, h, 0), lambda h: ar(g, h, 0))
                        four(f"rb_{g}", lambda h: bk(g, h, 0), lambda h: ar(g, h, 1))
                        four(f"ka_{g}", lambda h: bk(g, h, 1), lambda h: ar(g, h, 0))
                        four(f"kr_{g}", lambda h: bk(g, h, 1), lambda h: ar(g, h, 1))
                    four_transposes("vt", lambda h: vc[:, h])
                    four_transposes("kt", lambda h: kc[:, h])
                    rv = tokens(V_B, c)
                    four_transposes("rvt", lambda h: rv[:, h])
                    four_transposes("rbt", lambda h: BK[:, 2 * h * n:(2 * h + 1) * n])
                    four_transposes("rkt", lambda h: BK[:, (2 * h + 1) * n:(2 * h + 2) * n])

                    Bs = A if sample else B
                    for g in G:
                        pe.wait_ge(*after("dve", f"P0_{g}"))
                        if not sample:
                            pe.wait_ge(*after("dve", f"B_{g}"))
                        four(f"sq1_{g}", of(BT[g]), of(Bs[g]))
                        four(f"sqt1_{g}", of(Bs[g]), of(BT[g]))
                    for g in G:
                        pe.wait_ge(*after("act", f"C1_{g}"))
                        pe.wait_ge(*after("dve", f"CT1_{g}"))
                        four(f"x1_{g}", of(C[g]), of(Pt[g]))
                        four(f"sq2_{g}", of(CT[g]), of(C[g]))
                        if not sample:
                            four(f"sqt2_{g}", of(C[g]), of(CT[g]))
                    for g in G:
                        pe.wait_ge(*after("dve", f"P1_{g}"))
                        pe.wait_ge(*after("act", f"B2_{g}" if sample else f"BT2_{g}"))
                        four(f"x2_{g}", of(B[g]), of(Pt[g]))
                        if not sample:
                            four(f"sq3_{g}", of(BT[g]), of(B[g]))
                    if not sample:
                        for g in G:
                            pe.wait_ge(*after("act", f"C3_{g}"))
                            pe.wait_ge(*after("dve", f"P2_{g}"))
                            four(f"x3_{g}", of(C[g]), of(Pt[g]))
                        before = "P3"
                        for w, Ms, Tb in ((16, CT, B), (32, BT, CT), (64, B, CT)):
                            for g in G:
                                pe.wait_ge(*after("pool", f"Ms{w}_{g}"))
                                pe.wait_ge(*after("dve", f"{before}_{g}"))
                                four(f"y{w}_{g}", of(Ms[g]), of(Pt[g]))
                                four_transposes(f"tr{w}_{g}", of(Pt[g]), n)
                            for g in G:
                                pe.wait_ge(*after("act", f"Y{w}_{g}"))
                                pe.wait_ge(*after("dve", f"T{w}_{g}"))
                                four(f"z{w}_{g}", of(Tb[g]), of(C[g]))
                            before = f"PZ{w}"

                    last_p = "P2" if sample else "PZ64"

                    def rwkv_u():
                        for g in (1, 2):
                            pe.wait_ge(*after("dve", f"{last_p}_{g}"))
                        b = claim("ru")
                        for g in (1, 2):
                            for h in range(4):
                                hd = 2 * h + g - 1
                                last = pe.matmul(b[0:n, hd * 64:(hd + 1) * 64], Pt[g][0:n, h * n:(h + 1) * n],
                                                 RW[0:n, hd * 64:(hd + 1) * 64], start=True, stop=True)
                        done("ru", last)

                    def head_place(hd):
                        return hd // 2, 64 * (hd % 2), hd % 2 + 1, hd // 2

                    if not sample:
                        if c == 0:
                            pe.wait_ge(zeroed, 2)
                        else:
                            pe.wait_ge(*sched.after("dve", names("S3", c - 1)))
                        four("ks", lambda h: kc[:, h], lambda h: S[:, h * P:(h + 1) * P])
                        pe.wait_ge(*after("dve", "S0s"))
                        pe.wait_ge(*after("act", "RVt"))
                        for g in (1, 2):
                            b = claim(f"rw_{g}")
                            for h in range(4):
                                out = b[:, h * 64:(h + 1) * 64]
                                t, p = place(g, h)
                                hd = 2 * h + g - 1
                                pe.matmul(out, ar(g, h, 0), S0s[p:p + 64, t * 64:(t + 1) * 64],
                                          start=True, stop=False)
                                last = pe.matmul(out, KA[g][:, h * n:(h + 1) * n], Vt[:, hd * 64:(hd + 1) * 64],
                                                 start=False, stop=True)
                            done(f"rw_{g}", last)
                        pe.wait_ge(*after("dve", "W2"))
                        four("u", of(Pt[0]), lambda h: W[:, h * P:(h + 1) * P], width=P)
                        pe.wait_ge(*after("act", "RW_2"))
                        rwkv_u()
                        pe.wait_ge(*after("act", "U"))
                        pe.wait_ge(*after("dve", "QG"))
                        b = claim("o")
                        for h in range(4):
                            out = b[:, h * n:(h + 1) * n]
                            pe.matmul(out, S[:, h * P:(h + 1) * P], qg[:, h * n:(h + 1) * n], start=True, stop=False)
                            last = pe.matmul(out, U[:, h * P:(h + 1) * P], KQD[:, h * n:(h + 1) * n],
                                             start=False, stop=True)
                        done("o", last)
                        four("s", lambda h: KD[:, h * P:(h + 1) * P], lambda h: U[:, h * P:(h + 1) * P],
                             out_part=P, width=P)
                        pe.wait_ge(*after("dve", "RU"))
                        b = claim("ry")
                        for hd in range(8):
                            t, p, g, h = head_place(hd)
                            out = b[p:p + 64, t * n:(t + 1) * n]
                            hc = slice(hd * 64, (hd + 1) * 64)
                            pe.matmul(out, RU[:, hc], RB[g][:, h * n:(h + 1) * n], start=True, stop=False)
                            pe.matmul(out, Vt[:, hc], KR[g][:, h * n:(h + 1) * n], start=False, stop=False)
                            last = pe.matmul(out, S0s[p:p + 64, t * 64:(t + 1) * 64], ar(g, h, 1),
                                             start=False, stop=True)
                        done("ry", last)
                        b = claim("rs")
                        for hd in range(8):
                            t, p, g, h = head_place(hd)
                            out = b[p:p + 64, t * 64:(t + 1) * 64]
                            hc = slice(hd * 64, (hd + 1) * 64)
                            pe.matmul(out, Bt[:, hc], RU[:, hc], start=True, stop=False)
                            last = pe.matmul(out, Kt[:, hc], Vt[:, hc], start=False, stop=True)
                        done("rs", last)
                    else:
                        pe.wait_ge(states_in, 32)
                        pe.wait_ge(*after("dve", "QG"))
                        b = claim("ko")
                        out4 = b.rearrange("p (h a t) -> p h a t", h=4, a=2)
                        in4 = KQg.rearrange("p (h a t) -> p h a t", h=4, a=2)
                        S4 = S.rearrange("p (h s v) -> p h s v", h=4, s=NSEQ)
                        for h in range(4):
                            for q in range(NSEQ):
                                last = pe.matmul(out4[:, h, :, q * TS:(q + 1) * TS], S4[:, h, q],
                                                 in4[:, h, :, q * TS:(q + 1) * TS], start=True, stop=True)
                        done("ko", last)
                        b = claim("rko")
                        out4 = b.rearrange("p (t a i) -> p t a i", t=4, a=2)
                        in4 = AR.rearrange("p (t a i) -> p t a i", t=4, a=2)
                        S4 = RS.rearrange("p (t s v) -> p t s v", t=4, s=NSEQ)
                        for hd in range(8):
                            t, p, g, h = head_place(hd)
                            for q in range(NSEQ):
                                last = pe.matmul(out4[p:p + 64, t, :, q * TS:(q + 1) * TS], S4[p:p + 64, t, q],
                                                 in4[p:p + 64, t, :, q * TS:(q + 1) * TS], start=True, stop=True)
                        done("rko", last)
                        pe.wait_ge(*after("act", "RKO"))
                        ko4 = KO.rearrange("p (h a t) -> p h a t", h=4, a=2)
                        rko4 = RKO.rearrange("p (t a i) -> p t a i", t=4, a=2)
                        four_transposes("kst", lambda h: ko4[:, h, 0])
                        four_transposes("rwt", lambda h: rko4[:, h, 0])
                        b = claim("rw")
                        for hd in range(8):
                            t, p, g, h = head_place(hd)
                            last = pe.matmul(b[0:n, hd * 64:(hd + 1) * 64], KA[g][0:n, h * n:(h + 1) * n],
                                             Vt[0:n, hd * 64:(hd + 1) * 64], start=True, stop=True)
                        done("rw", last)
                        pe.wait_ge(*after("dve", "W2"))
                        four("u", of(Pt[0]), lambda h: Wd[0:n, h * P:(h + 1) * P], width=P)
                        pe.wait_ge(*after("dve", "RW"))
                        rwkv_u()
                        pe.wait_ge(*after("act", "U"))
                        four("o", lambda h: Ud[0:n, h * P:(h + 1) * P], lambda h: KQD[0:n, h * n:(h + 1) * n], out_part=P)
                        pe.wait_ge(*after("act", "RU"))
                        b = claim("ry")
                        for hd in range(8):
                            t, p, g, h = head_place(hd)
                            out = b[p:p + 64, t * n:(t + 1) * n]
                            hc = slice(hd * 64, (hd + 1) * 64)
                            pe.matmul(out, RU[0:n, hc], RB[g][0:n, h * n:(h + 1) * n], start=True, stop=False)
                            last = pe.matmul(out, Vt[0:n, hc], KR[g][0:n, h * n:(h + 1) * n], start=False, stop=True)
                        done("ry", last)
                        for h in range(4):
                            pe.wait_ge(*after("dve", f"Um{h}"))
                            for part in range(2):
                                b = claim(f"s{h}{'ab'[part]}")
                                done(f"s{h}{'ab'[part]}",
                                     pe.matmul(b[:, :], KDt[0:n, h * P:(h + 1) * P],
                                               Uw[0:n, part * 512:(part + 1) * 512], start=True, stop=True))
                        for t in range(4):
                            pe.wait_ge(*after("dve", f"RVm{t}"))
                            b = claim(f"rs{t}")
                            for half in range(2):
                                hc = slice((2 * t + half) * 64, (2 * t + half + 1) * 64)
                                out = b[half * 64:half * 64 + 64, :]
                                pe.matmul(out, Bt[0:n, hc], RUw[0:n, half * 512:(half + 1) * 512],
                                          start=True, stop=False)
                                last = pe.matmul(out, Kt[0:n, hc], RVw[0:n, half * 512:(half + 1) * 512],
                                                 start=False, stop=True)
                            done(f"rs{t}", last)

            @block.scalar
            def _(act):
                for c in chunks:
                    after = lambda e, nm: sched.after(e, names(nm, c))
                    did = lambda nm: sched.did("act", names(nm, c))
                    prev = lambda e, nm: sched.after(e, names(nm, c - 1))
                    psum = lambda job, part=n: bank(job, c)[0:part]

                    def copy(step, job, dst, part=n, cols=H):
                        act.wait_ge(*after("pe", job))
                        act.activation(dst[0:part, 0:cols], psum(job, part)[:, 0:cols], ACT.Copy).then_inc(*did(step))

                    act.wait_ge(*after("pe", "R"))
                    act.wait_ge(*after("dve", "d"))
                    act.activation(eR[:, 0:H], psum("R", P)[:, 0:H], ACT.Exp).then_inc(*did("eR"))
                    act.wait_ge(*after("dve", "dU"))
                    act.activation(DT[0:n], DT[0:n], ACT.Exp).then_inc(*did("DT"))
                    act.wait_ge(*after("dve", "dL"))
                    act.activation(Dm[0:n], Dm[0:n], ACT.Exp, scale=-1.0).then_inc(*did("D"))
                    act.wait_ge(*after("dve", "Eref"))
                    if sample:
                        e = Em.rearrange("p (b i) -> p b i", i=TS + 1)
                        act.activation(En.rearrange("p (b i) -> p b i", i=TS), e[:, :, 1:], ACT.Exp, scale=-1.0)\
                            .then_inc(*did("E"))
                    else:
                        e = Em.rearrange("p (t i) -> p t i", t=4)
                        act.activation(v4(En), e[:, :, 1:], ACT.Exp, scale=-1.0).then_inc(*did("E"))
                        act.activation(eref.rearrange("p (t i) -> p t i", t=4), e[:, :, 0:1], ACT.Exp, scale=-1.0)\
                            .then_inc(*did("exp_ref"))
                    act.wait_ge(*after("act", "E" if sample else "exp_ref"))
                    act.activation(Em, Em, ACT.Exp).then_inc(*did("exp_E"))
                    copy("RVt", "rvt", Vt, cols=512)
                    copy("RBt", "rbt", Bt, cols=512)
                    copy("RKt", "rkt", Kt, cols=512)
                    for g in G:
                        if g == 0:
                            act.wait_ge(*after("dve", "KQD"))
                            act.wait_ge(*after("dve", "M0"))
                        if g == 1:
                            act.wait_ge(*after("dve", "Kq"))
                        copy(f"C1_{g}", f"sq1_{g}", C[g])
                    for g in G:
                        copy(f"B2_{g}", f"sq2_{g}", B[g])
                        if not sample:
                            copy(f"BT2_{g}", f"sqt2_{g}", BT[g])
                    if not sample:
                        for g in G:
                            copy(f"C3_{g}", f"sq3_{g}", C[g])
                        for w in LEVELS:
                            for g in G:
                                copy(f"Y{w}_{g}", f"y{w}_{g}", C[g])
                        for g in (1, 2):
                            act.wait_ge(*after("pe", f"rw_{g}"))
                            act.activation(RW.rearrange("p (h g v) -> p h g v", h=4, g=2)[:, :, g - 1],
                                           v4(psum(f"rw_{g}")[:, 0:256]), ACT.Copy).then_inc(*did(f"RW_{g}"))
                        copy("U", "u", U, cols=512)
                        act.wait_ge(*after("pe", "o"))
                        act.activation(tokens(Q_A, c), v4(psum("o", P)), ACT.Copy).then_inc(*did("O"))
                        act.wait_ge(*after("pe", "ry"))
                        act.activation(htokens(NEG_KK, c), v4(psum("ry", P)), ACT.Copy).then_inc(*did("RY"))
                    else:
                        copy("KO", "ko", KO, part=P, cols=512)
                        copy("RKO", "rko", RKO, part=P, cols=512)
                        copy("RWt", "rwt", RW, cols=512)
                        copy("U", "u", Ud, cols=512)
                        copy("RU", "ru", RU, cols=512)

            @block.vector
            def _(dve):
                for c in chunks:
                    after = lambda e, nm: sched.after(e, names(nm, c))
                    did = lambda nm: sched.did("dve", names(nm, c))
                    psum = lambda job, part=n: bank(job, c)[0:part]
                    if c > chunks[0]:
                        dve.wait_ge(*sched.after("pe", names("rs", c - 1)))
                        dve.wait_ge(*sched.after("act", names("RY", c - 1)))
                        dve.wait_ge(*sched.after("dve", names("RSn", c - 1)))
                    dve.wait_ge(*after("pe", "R"))
                    dve.tensor_tensor(v4(Dm, n), v4(psum("R")[:, 0:H], n), col(c, ROW_GC)(n), ALU.subtract)\
                        .then_inc(*did("d"))
                    dve.wait_ge(*after("dve", "d"))
                    big = lambda nm: k.big(nm)[0:n, 0:n][:, None, :].to_broadcast([n, 4, n])
                    dve.tensor_tensor(v4(DT, n), v4(Dm, n), big("not_above_eq" + sfx), ALU.subtract)\
                        .then_inc(*did("dU"))
                    dve.wait_ge(*after("dve", "dU"))
                    dve.tensor_tensor(v4(Dm, n), v4(Dm, n), big("not_below" + sfx), ALU.add).then_inc(*did("dL"))
                    if sample:
                        lcs = k.lc.rearrange("p (t i) -> p t i", t=4)[:, :, TP:T].rearrange("p t (s i) -> p t s i", s=NSEQ)
                        E4 = Em.rearrange("p (t s i) -> p t s i", t=4, s=NSEQ)
                        dve.memset(Em, 0.0).then_inc(*did("Et"))
                        dve.wait_ge(*after("dve", "Et"))
                        dve.tensor_copy(E4[:, :, :, 1:], lcs).then_inc(*did("Eref"))
                        E0, E1 = E4[:, :, :, 0:TS], E4[:, :, :, 1:]
                        v = lambda ap: ap.rearrange("p t (s i) -> p t s i", s=NSEQ)
                    else:
                        lcc = k.lc.rearrange("p (t i) -> p t i", t=4)[:, :, c * CH:(c + 1) * CH]
                        mid = lcc[:, :, CH // 2 - 1:CH // 2]
                        E4 = Em.rearrange("p (t i) -> p t i", t=4)
                        dve.tensor_tensor(E4[:, :, 1:], lcc, mid.to_broadcast([P, 4, CH]), ALU.subtract)\
                            .then_inc(*did("Et"))
                        dve.tensor_scalar(E4[:, :, 0:1], mid, -1.0, None, ALU.mult).then_inc(*did("Eref"))
                        E0, E1 = E4[:, :, 0:n], E4[:, :, 1:]
                        v = lambda ap: ap
                    dve.wait_ge(*after("act", "exp_E"))
                    ar4 = AR.rearrange("p (t a i) -> p t a i", t=4, a=2)
                    bk4 = BK.rearrange("p (t a i) -> p t a i", t=4, a=2)
                    dve.tensor_tensor(v(ar4[:, :, 0]), v(htokens(NEG_KK, c)), E0, ALU.mult).then_inc(*did("Aq"))
                    dve.tensor_tensor(v(ar4[:, :, 1]), v(tokens(R_B, c)), E1, ALU.mult).then_inc(*did("Rq"))
                    dve.tensor_tensor(bk4[:, :, 0], htokens(KK_A, c), v4(En), ALU.mult).then_inc(*did("Bq"))
                    dve.tensor_tensor(bk4[:, :, 1], tokens(K_B, c), v4(En), ALU.mult).then_inc(*did("Kq"))
                    if sample:
                        kq4 = KQg.rearrange("p (h a t) -> p h a t", h=4, a=2)
                        dve.tensor_copy(kq4[:, :, 0], tokens(K_A, c)).then_inc(*did("k_copy"))
                    dve.wait_ge(*after("pe", "kk"))
                    dve.wait_ge(*after("act", "D"))
                    dve.tensor_tensor(v4(A[0], n), v4(psum("kk")[:, 0:H], n), v4(Dm, n), ALU.mult).then_inc(*did("M0"))
                    dve.wait_ge(*after("dve", "M0"))
                    dve.tensor_tensor(v4(A[0], n), v4(A[0], n), col(c, ROW_BETA)(n), ALU.mult).then_inc(*did("M1"))
                    dve.wait_ge(*after("dve", "M1"))
                    dve.tensor_scalar(A[0][0:n], A[0][0:n], -1.0, None, ALU.mult).then_inc(*did("M2"))
                    dve.wait_ge(*after("pe", "kq"))
                    dve.tensor_tensor(v4(KQD, n), v4(psum("kq")[:, 0:H], n), v4(DT, n), ALU.mult).then_inc(*did("KQD"))

                    def masked(step, job, dst, mask_name):
                        dve.wait_ge(*after("pe", job))
                        dve.tensor_tensor(v4(dst, n), v4(psum(job)[:, 0:H], n), bc(mask(mask_name)), ALU.mult)\
                            .then_inc(*did(step))

                    def start_inverse(g):
                        dve.wait_ge(*after("dve", f"mtm_{g}"))
                        dve.tensor_tensor(v4(Pt[g], n), v4(BT[g], n), bc(mask("ident")), ALU.add).then_inc(*did(f"P0_{g}"))
                    masked("mtm_0", "mt_0", BT[0], "block8" if sample else "block16")
                    start_inverse(0)
                    for g in (1, 2):
                        masked(f"mm_{g}", f"m_{g}", A[g], "below" + sfx)
                        masked(f"mtm_{g}", f"mt_{g}", BT[g], "above8" if sample else "above16")
                        masked(f"rbm_{g}", f"rb_{g}", RB[g], "above_eq" + sfx)
                        masked(f"kam_{g}", f"ka_{g}", KA[g], "above" + sfx)
                        masked(f"krm_{g}", f"kr_{g}", KR[g], "above_eq" + sfx)
                        start_inverse(g)
                    dve.wait_ge(*after("pe", "vt"))
                    dve.tensor_tensor(v4(VBt, n), v4(psum("vt"), n), col(c, ROW_BETA)(P), ALU.mult).then_inc(*did("VB"))
                    dve.wait_ge(*after("pe", "kt"))
                    dve.tensor_tensor(v4(KDt, n), v4(psum("kt"), n), col(c, ROW_TO_END)(P), ALU.mult).then_inc(*did("KD"))
                    dve.wait_ge(*after("act", "eR"))
                    qg_out = KQg.rearrange("p (h a t) -> p h a t", h=4, a=2)[:, :, 1] if sample else v4(qg)
                    dve.tensor_tensor(qg_out, tokens(Q_A, c), v4(eR), ALU.mult).then_inc(*did("QG"))

                    def plus(step, job, g):
                        dve.wait_ge(*after("pe", job))
                        dve.tensor_tensor(Pt[g][0:n], Pt[g][0:n], psum(job)[:, 0:H], ALU.add).then_inc(*did(step))

                    def copy(step, job, dst, part=n, cols=H):
                        dve.wait_ge(*after("pe", job))
                        dve.tensor_copy(dst[0:part, 0:cols], psum(job, part)[:, 0:cols]).then_inc(*did(step))
                    if not sample:
                        for g in G:
                            dve.wait_ge(*after("dve", "M2" if g == 0 else f"mm_{g}"))
                            dve.tensor_tensor(v4(B[g], n), v4(A[g], n), bc(mask("block16")), ALU.mult)\
                                .then_inc(*did(f"B_{g}"))
                    for g in G:
                        copy(f"CT1_{g}", f"sqt1_{g}", CT[g])
                    for g in G:
                        plus(f"P1_{g}", f"x1_{g}", g)
                    for g in G:
                        plus(f"P2_{g}", f"x2_{g}", g)
                    if not sample:
                        for g in G:
                            plus(f"P3_{g}", f"x3_{g}", g)
                        for w, Tb in ((16, B), (32, CT), (64, CT)):
                            for g in G:
                                copy(f"T{w}_{g}", f"tr{w}_{g}", Tb[g])
                            for g in G:
                                plus(f"PZ{w}_{g}", f"z{w}_{g}", g)
                        if c == 0:
                            dve.wait_ge(zeroed, 2)
                        dve.tensor_tensor(v4(S0s), v4(RS), eref.rearrange("p (t i) -> p t i", t=4)
                                          .to_broadcast([P, 4, 64]), ALU.mult).then_inc(*did("S0s"))
                        dve.wait_ge(*after("pe", "ks"))
                        dve.tensor_tensor(v4(W), v4(psum("ks")), col(c, COL_BETA_GC)(P), ALU.mult).then_inc(*did("W1"))
                        dve.wait_ge(*after("dve", "W1"))
                        dve.tensor_tensor(W, VBt, W, ALU.subtract).then_inc(*did("W2"))
                        copy("RU", "ru", RU, cols=512)
                        dve.wait_ge(*after("pe", "s"))
                        last = eR.rearrange("p (h i) -> p h i", h=4)[:, :, n - 1:n].to_broadcast([P, 4, P])
                        dve.tensor_tensor(v4(S), v4(S), last, ALU.mult).then_inc(*did("S1"))
                        dve.wait_ge(*after("dve", "S1"))
                        dve.tensor_tensor(S, S, psum("s"), ALU.add).then_inc(*did("S3"))
                        dve.wait_ge(*after("pe", "rs"))
                        dve.tensor_tensor(S0s, S0s, psum("rs")[:, 0:256], ALU.add).then_inc(*did("RS1"))
                        dve.wait_ge(*after("dve", "RS1"))
                        dve.tensor_tensor(v4(RS), v4(S0s), E4[:, :, n:n + 1].to_broadcast([P, 4, 64]), ALU.mult)\
                            .then_inc(*did("RSn"))
                    else:
                        dve.wait_ge(*after("pe", "kst"))
                        dve.tensor_tensor(v4(Wd, n), v4(psum("kst"), n), col(c, COL_BETA_GC)(P), ALU.mult)\
                            .then_inc(*did("W1"))
                        dve.wait_ge(*after("dve", "W1"))
                        dve.tensor_tensor(Wd[0:n], VBt[0:n], Wd[0:n], ALU.subtract).then_inc(*did("W2"))
                        dve.wait_ge(*after("pe", "rw"))
                        dve.wait_ge(*after("act", "RWt"))
                        dve.tensor_tensor(RW[0:n], RW[0:n], psum("rw"), ALU.add).then_inc(*did("RW"))
                        ko4 = KO.rearrange("p (h a t) -> p h a t", h=4, a=2)
                        rko4 = RKO.rearrange("p (t a i) -> p t a i", t=4, a=2)
                        dve.wait_ge(*after("pe", "o"))
                        dve.tensor_tensor(tokens(Q_A, c), ko4[:, :, 1], v4(psum("o", P)[:, 0:H]), ALU.add)\
                            .then_inc(*did("O"))
                        dve.wait_ge(*after("pe", "ry"))
                        dve.tensor_tensor(htokens(NEG_KK, c), rko4[:, :, 1], v4(psum("ry", P)[:, 0:H]), ALU.add)\
                            .then_inc(*did("RY"))
                        own = k.mask("block8")[0:n, 0:n:TS]
                        dve.wait_ge(*after("act", "U"))
                        for h in range(4):
                            if h:
                                dve.wait_ge(*after("pe", f"s{h - 1}b"))
                            own_b = own[:, :, None].to_broadcast([n, NSEQ, P])
                            dve.tensor_tensor(Uw[0:n].rearrange("p (s v) -> p s v", s=NSEQ),
                                              Ud[0:n, None, h * P:(h + 1) * P].to_broadcast([n, NSEQ, P]), own_b,
                                              ALU.mult).then_inc(*did(f"Um{h}"))
                            Sh = S[:, h * 1024:(h + 1) * 1024]
                            gl = eR[:, h * n + TS - 1:(h + 1) * n:TS]
                            dve.tensor_tensor(Sh.rearrange("p (s v) -> p s v", s=NSEQ),
                                              Sh.rearrange("p (s v) -> p s v", s=NSEQ),
                                              gl[:, :, None].to_broadcast([P, NSEQ, P]), ALU.mult)\
                                .then_inc(*did(f"Sg{h}"))
                            dve.wait_ge(*after("dve", f"Sg{h}"))
                            for part in range(2):
                                x = "ab"[part]
                                dve.wait_ge(*after("pe", f"s{h}{x}"))
                                dve.tensor_tensor(Sh[:, part * 512:(part + 1) * 512], Sh[:, part * 512:(part + 1) * 512],
                                                  psum(f"s{h}{x}", P), ALU.add).then_inc(*did(f"S{h}{x}"))
                        dve.wait_ge(*after("act", "RU"))
                        dve.wait_ge(*after("pe", "s3b"))
                        for t in range(4):
                            if t:
                                dve.wait_ge(*after("pe", f"rs{t - 1}"))
                            for nm, dst, src in (("RUm", RUw, RU), ("RVm", RVw, Vt)):
                                for half in range(2):
                                    hd = 2 * t + half
                                    last = dve.tensor_tensor(
                                        dst[0:n, half * 512:(half + 1) * 512].rearrange("p (s v) -> p s v", s=NSEQ),
                                        src[0:n, None, hd * 64:(hd + 1) * 64].to_broadcast([n, NSEQ, 64]),
                                        own[:, :, None].to_broadcast([n, NSEQ, 64]), ALU.mult)
                                last.then_inc(*did(f"{nm}{t}"))
                            Rt = RS[:, t * 512:(t + 1) * 512]
                            dve.wait_ge(*after("pe", f"rs{t}"))
                            dve.tensor_tensor(Rt, Rt, psum(f"rs{t}", P), ALU.add).then_inc(*did(f"RS{t}"))
                            dve.wait_ge(*after("dve", f"RS{t}"))
                            dve.tensor_tensor(Rt.rearrange("p (s v) -> p s v", s=NSEQ),
                                              Rt.rearrange("p (s v) -> p s v", s=NSEQ),
                                              E4[:, t, :, TS:TS + 1].to_broadcast([P, NSEQ, 64]), ALU.mult)\
                                .then_inc(*did(f"RSd{t}"))


def finish_even(k):
    nc = k.nc
    big = lambda t: k.big_buf[:, t * T:(t + 1) * T]
    hb = lambda t: k.h[:, t * T:(t + 1) * T]
    sq = lambda i: k.arena[:, i * T:(i + 1) * T]
    bonus = lambda i: k.arena[:, (8 + i) * T:(9 + i) * T]
    w2 = k.arena[:, 16 * T:16 * T + 512]
    N = range(4)
    with nc.cleanup_on_exit():
        s = Phase(nc)
        q = Schedule(
            s,
            pe=[f"sum_a{i}" for i in N] + [f"mean{i}" for i in N] + [f"bonus{i}" for i in N] + [f"var{i}" for i in N]
            + [f"gate{i}" for i in N],
            act=[f"sq_a{i}" for i in N] + [f"root_a{i}" for i in N] + [f"sq_y{i}" for i in N] + [f"root_y{i}" for i in N],
            dve=[f"rk{i}" for i in N] + [f"{x}{i}" for i in N for x in ("inv_a", "norm_a", "out_a")]
            + [f"center{i}" for i in N] + [f"bonus_v{i}" for i in N]
            + [f"{x}{i}" for i in N for x in ("inv_y", "norm_y", "affine", "out_y")])
        did, after = q.did, q.after
        loaded, restored = s.sem("wg2_loaded"), s.sem("x_restored")
        halves = lambda ap: ap.rearrange("p (a t) -> p a t", a=2)
        pair = {n: k.psum_pair(i % 4) for i, n in enumerate(q.count["pe"])}
        ps = lambda nm: two_halves(pair[nm], HALF)
        with nc.Block() as block:
            @block.sync
            def _(sp):
                sp.dma_start(w2, k.io["w_g2"]).then_inc(loaded, 16)
                sp.dma_start(k.x, k.x_kept).then_inc(restored, 16)
                sp.wait_ge(loaded, 16)
                sp.wait_ge(restored, 16)

            @block.tensor
            def _(pe):
                def product(name, lhsT, rhs):
                    for a in range(2):
                        last = pe.matmul(pair[name][:, a, 0:HALF], lhsT, rhs[:, a * HALF:(a + 1) * HALF],
                                         start=True, stop=True)
                    last.then_inc(*did("pe", name))
                for i in N:
                    pe.wait_ge(*after("act", f"sq_a{i}"))
                    product(f"sum_a{i}", k.mask("ones"), sq(i))
                for i in N:
                    pe.wait_ge(*after("act", f"root_a{i}"))
                    product(f"mean{i}", k.mask("block64"), hb(NEG_KK + i))
                for i in N:
                    pe.wait_ge(*after("dve", f"rk{i}"))
                    pe.wait_ge(*after("dve", f"center{i}"))
                    product(f"bonus{i}", k.mask("block64"), bonus(i))
                for i in N:
                    pe.wait_ge(*after("act", f"sq_y{i}"))
                    pe.wait_ge(*after("dve", f"bonus_v{i}"))
                    product(f"var{i}", k.mask("block64"), sq(4 + i))
                pe.wait_ge(loaded, 16)
                for i in N:
                    pe.wait_ge(*after("act", f"root_y{i}"))
                    product(f"gate{i}", w2[:, i * P:(i + 1) * P], big(G_B))

            @block.scalar
            def _(act):
                for i in N:
                    act.activation(sq(i), big(Q_A + i), ACT.Square).then_inc(*did("act", f"sq_a{i}"))
                for i in N:
                    act.wait_ge(*after("pe", f"sum_a{i}"))
                    act.activation(halves(sq(i)), ps(f"sum_a{i}"), ACT.Sqrt, bias=k.eps[:, 0:1], scale=1.0 / P)\
                        .then_inc(*did("act", f"root_a{i}"))
                for i in N:
                    act.wait_ge(*after("dve", f"center{i}"))
                    act.activation(sq(4 + i), hb(NEG_KK + i), ACT.Square).then_inc(*did("act", f"sq_y{i}"))
                for i in N:
                    act.wait_ge(*after("pe", f"var{i}"))
                    act.activation(halves(sq(4 + i)), ps(f"var{i}"), ACT.Sqrt, bias=k.eps[:, 1:2], scale=1.0 / 64)\
                        .then_inc(*did("act", f"root_y{i}"))

            @block.vector
            def _(dve):
                stt = dve.scalar_tensor_tensor
                for i in N:
                    stt(out=bonus(i), in0=big(R_B + i), scalar=k.par("r_k")[:, i:i + 1], in1=big(K_B + i),
                        op0=ALU.mult, op1=ALU.mult).then_inc(*did("dve", f"rk{i}"))
                for i in N:
                    dve.wait_ge(*after("act", f"root_a{i}"))
                    dve.reciprocal(sq(i), sq(i)).then_inc(*did("dve", f"inv_a{i}"))
                    dve.wait_ge(*after("dve", f"inv_a{i}"))
                    stt(out=sq(i), in0=sq(i), scalar=k.par("gain_a"), in1=big(Z_A + i), op0=ALU.mult, op1=ALU.mult)\
                        .then_inc(*did("dve", f"norm_a{i}"))
                    dve.wait_ge(*after("dve", f"norm_a{i}"))
                    dve.tensor_tensor(big(Q_A + i), big(Q_A + i), sq(i), ALU.mult).then_inc(*did("dve", f"out_a{i}"))
                for i in N:
                    dve.wait_ge(*after("pe", f"mean{i}"))
                    stt(out=halves(hb(NEG_KK + i)), in0=ps(f"mean{i}"), scalar=-1.0 / 64, in1=halves(hb(NEG_KK + i)),
                        op0=ALU.mult, op1=ALU.add).then_inc(*did("dve", f"center{i}"))
                for i in N:
                    dve.wait_ge(*after("pe", f"bonus{i}"))
                    dve.tensor_tensor(halves(bonus(i)), ps(f"bonus{i}"), halves(big(V_B + i)), ALU.mult)\
                        .then_inc(*did("dve", f"bonus_v{i}"))
                for i in N:
                    y = hb(NEG_KK + i)
                    out = big(K_A + i)
                    dve.wait_ge(*after("act", f"root_y{i}"))
                    dve.reciprocal(sq(4 + i), sq(4 + i)).then_inc(*did("dve", f"inv_y{i}"))
                    dve.wait_ge(*after("dve", f"inv_y{i}"))
                    stt(out=y, in0=y, scalar=k.par("lnx_gain")[:, i:i + 1], in1=sq(4 + i), op0=ALU.mult, op1=ALU.mult)\
                        .then_inc(*did("dve", f"norm_y{i}"))
                    dve.wait_ge(*after("dve", f"norm_y{i}"))
                    stt(out=y, in0=y, scalar=k.par("lnx_bias")[:, i:i + 1], in1=bonus(i), op0=ALU.add, op1=ALU.add)\
                        .then_inc(*did("dve", f"affine{i}"))
                    dve.wait_ge(*after("dve", f"affine{i}"))
                    dve.wait_ge(*after("pe", f"gate{i}"))
                    dve.tensor_tensor(halves(out), ps(f"gate{i}"), halves(y), ALU.mult).then_inc(*did("dve", f"out_y{i}"))


def even_mixer(k, sublayer):
    normalise(k, sublayer, wide=True)
    project_even(k)
    prepare_even(k)
    even_chunks(k, sample=False)
    even_chunks(k, sample=True)
    finish_even(k)
    residual_product(k, k.io["w_out_even"], 0, lambda kt: k.big_buf[:, kt * T:(kt + 1) * T], KT, sublayer)


Q_C, K_C, V_C, Z_C, Q_D, K_D, V_D, O_D, NARROW = 0, 2, 4, 8, 12, 14, 16, 20, 24
B16, B_C = 25, 27
SCALE_64 = 64.0 ** -0.5


def project_odd(k):
    nc = k.nc
    SLOTS, TILES = 4, 25
    ROUNDS, REST = TILES // SLOTS, TILES % SLOTS
    with nc.cleanup_on_exit():
        s = Phase(nc)
        landed = [s.sem(f"in_landed{b}") for b in range(SLOTS)]
        product, evacuated = s.sem("product"), s.sem("evacuated")
        slot = [k.arena[:, b * D:(b + 1) * D] for b in range(SLOTS)]
        with nc.Block() as block:
            @block.sync
            def _(sp):
                for b in range(SLOTS):
                    sp.dma_start(slot[b], k.io["w_in_odd"][b]).then_inc(landed[b], 16)
                with sp.Fori(1, ROUNDS) as r:
                    for b in range(SLOTS):
                        sp.wait_ge(product, (r - 1) * SLOTS + b + 1)
                        sp.dma_start(slot[b], k.io["w_in_odd"][bass.ds(b + r * SLOTS, 1)]
                                     .rearrange("a p n -> (a p) n")).then_inc(landed[b], 16)
                for b in range(REST):
                    sp.wait_ge(product, (ROUNDS - 1) * SLOTS + b + 1)
                    sp.dma_start(slot[b], k.io["w_in_odd"][ROUNDS * SLOTS + b]).then_inc(landed[b], 16)

            @block.tensor
            def _(pe):
                def tile(b, wait_landed, wait_evacuated):
                    pe.wait_ge(landed[b], wait_landed)
                    if wait_evacuated is not None:
                        pe.wait_ge(evacuated, wait_evacuated)
                    for kt in range(KT):
                        for a in range(2):
                            at = kt * TX + a * HALF
                            last = pe.matmul(k.psum_pair(b)[:, a, 0:HALF], slot[b][:, kt * P:(kt + 1) * P],
                                             k.h[:, at:at + HALF], start=kt == 0, stop=kt == KT - 1)
                    last.then_inc(product, 1)
                for b in range(SLOTS):
                    tile(b, 16, None)
                with pe.Fori(1, ROUNDS) as r:
                    for b in range(SLOTS):
                        tile(b, (r + 1) * 16, (r - 1) * SLOTS + b + 1)
                for b in range(REST):
                    tile(b, (ROUNDS + 1) * 16, (ROUNDS - 1) * SLOTS + b + 1)

            @block.vector
            def _(dve):
                def tile(b, m):
                    dve.wait_ge(product, m + 1)
                    out = k.big_buf[:, bass.ds(m * T, T)].rearrange("p (a t) -> p a t", a=2)
                    dve.tensor_copy(out, two_halves(k.psum_pair(b), HALF)).then_inc(evacuated, 1)
                with dve.Fori(0, ROUNDS) as r:
                    for b in range(SLOTS):
                        tile(b, r * SLOTS + b)
                for b in range(REST):
                    m = ROUNDS * SLOTS + b
                    dve.wait_ge(product, m + 1)
                    dve.tensor_copy(k.big_buf[:, m * T:(m + 1) * T].rearrange("p (a t) -> p a t", a=2),
                                    two_halves(k.psum_pair(b), HALF)).then_inc(evacuated, 1)


def prepare_odd(k):
    nc = k.nc
    big = lambda t, n=1: k.big_buf[:, t * T:(t + n) * T]
    row = lambda i: k.arena[0:4, i * T:(i + 1) * T]
    fg, ig, lf, soft, fsum, lfm, igm, m, a_row, e_row = (row(i) for i in range(10))
    x2 = lambda i: k.arena[:, (11 + i) * T:(12 + i) * T]
    s2 = lambda i: k.arena[:, (13 + i) * T:(14 + i) * T]
    w2 = k.arena[0:16, 15 * T:15 * T + 256]
    before = k.arena[0:4, 15 * T + 256:15 * T + 256 + NCH]
    m0 = k.arena[0:4, 15 * T + 264:15 * T + 264 + NSEQ]
    bound = k.arena[0:4, 15 * T + 272:15 * T + 272 + NSEQ]
    m_last = k.arena[0:4, 15 * T + 280:15 * T + 280 + NSEQ]
    col_rows = k.arena[:, 16 * T:17 * T]
    resets16 = k.arena[:, 17 * T:18 * T]
    rfm, rw, rnm = (k.mrows[:, i * T:(i + 1) * T] for i in range(3))
    act_steps = (["silu_z", "e_o"] + ["abs_f", "exp_f", "ln_f"] + [f"{x}{i}" for i in range(2) for x in ("abs", "exp", "ln")]
                 + ["exp_e", "cols"])
    dve_steps = (["resets16", "o1", "gates", "fg", "ig", "clear", "lf0", "lf", "fsum", "lfm", "igm", "bound1", "bound2", "cut_f",
                  "cut_i", "m", "m_last", "a", "before0", "before", "fm", "w_p", "w_s", "nm", "e_p", "e_s", "a_col",
                  "o2"]
                 + [f"{x}{i}" for i in range(2) for x in ("x", "s1_", "s2_", "b", "b16_")])
    with nc.cleanup_on_exit():
        s = Phase(nc)
        q = Schedule(s, act=act_steps, dve=dve_steps, pe=["gk0", "gk1", "cols"])
        did, after = q.did, q.after
        loaded, stored, ones16 = s.sem("loaded"), s.sem("stored"), s.sem("ones16")
        with nc.Block() as block:
            @block.sync
            def _(sp):
                sp.dma_start(w2, k.io["w_gk2"]).then_inc(loaded, 16)
                sp.dma_start(m0, k.io["mm_in"]).then_inc(loaded, 16)
                sp.wait_ge(*after("dve", "m_last"))
                sp.dma_start(k.io["mm_p_out"], m[:, TP - 1:TP]).then_inc(stored, 16)
                sp.dma_start(k.io["mm_s_out"], m_last).then_inc(stored, 16)
                sp.wait_ge(stored, 32)

            @block.gpsimd
            def _(pool):
                pool.memset(resets16, 1.0).then_inc(ones16, 1)

            @block.scalar
            def _(act):
                act.activation(big(Z_C, 4), big(Z_C, 4), ACT.Silu).then_inc(*did("act", "silu_z"))
                act.activation(big(O_D, 4), big(O_D, 4), ACT.Exp, scale=-1.0).then_inc(*did("act", "e_o"))
                act.wait_ge(*after("dve", "fg"))
                act.activation(soft, fg, ACT.Abs).then_inc(*did("act", "abs_f"))
                act.wait_ge(*after("act", "abs_f"))
                act.activation(soft, soft, ACT.Exp, scale=-1.0).then_inc(*did("act", "exp_f"))
                act.wait_ge(*after("act", "exp_f"))
                act.activation(soft, soft, ACT.Ln, bias=1.0).then_inc(*did("act", "ln_f"))
                for i in range(2):
                    act.wait_ge(*after("dve", f"x{i}"))
                    act.activation(s2(i), x2(i), ACT.Abs).then_inc(*did("act", f"abs{i}"))
                    act.wait_ge(*after("act", f"abs{i}"))
                    act.activation(s2(i), s2(i), ACT.Exp, scale=-1.0).then_inc(*did("act", f"exp{i}"))
                    act.wait_ge(*after("act", f"exp{i}"))
                    act.activation(s2(i), s2(i), ACT.Ln, bias=1.0).then_inc(*did("act", f"ln{i}"))
                act.wait_ge(*after("dve", "e_s"))
                act.activation(col_rows[32:36, :], e_row, ACT.Exp).then_inc(*did("act", "exp_e"))
                act.wait_ge(*after("pe", "cols"))
                cols = k.cols.rearrange("p (c r h) -> p c r h", c=5, r=4)
                act.activation(cols[:, 0:4, 0:2], k.psum[4].rearrange("p (c r h) -> p c r h", c=4, r=4)
                               [:, :, 0:2, 0:4], ACT.Copy)
                act.activation(cols[0:64, 4, 0:2], k.psum[5][0:64, 0:P].rearrange("p (r h) -> p r h", r=4)
                               [:, 0:2, 0:4], ACT.Copy).then_inc(*did("act", "cols"))

            @block.tensor
            def _(pe):
                pe.wait_ge(loaded, 32)
                for i in range(2):
                    for a in range(2):
                        at = NARROW * T + a * HALF
                        last = pe.matmul(k.psum_pair(i)[:, a, 0:HALF], w2[:, i * P:(i + 1) * P],
                                         k.big_buf[0:16, at:at + HALF], start=True, stop=True)
                    last.then_inc(*did("pe", f"gk{i}"))
                pe.wait_ge(*after("act", "exp_e"))
                pe.wait_ge(*after("dve", "a_col"))
                for c in range(NCH):
                    pe.transpose(k.psum[4][:, c * P:(c + 1) * P], col_rows[:, c * P:(c + 1) * P], k.mask("ident"))
                pe.transpose(k.psum[5][0:64, 0:P], col_rows[:, TP:T], k.mask("ident")).then_inc(*did("pe", "cols"))

            @block.vector
            def _(dve):
                tt, ts = dve.tensor_tensor, dve.tensor_scalar
                w = lambda name: dve.wait_ge(*after("dve", name))
                chunked = lambda v: v[:, 0:TP].rearrange("p (c i) -> p c i", i=CH)
                seqs = lambda v: v[:, TP:T].rearrange("p (c i) -> p c i", i=TS)
                dve.wait_ge(ones16, 1)
                dve.memset(resets16[:, 0:TP].rearrange("p (c i) -> p c i", i=16)[:, :, 0:1], 0.0)
                dve.memset(resets16[:, TP:T].rearrange("p (c i) -> p c i", i=TS)[:, :, 0:1], 0.0)\
                    .then_inc(*did("dve", "resets16"))
                dve.wait_ge(*after("act", "e_o"))
                ts(big(O_D, 4), big(O_D, 4), 1.0, None, ALU.add).then_inc(*did("dve", "o1"))
                dve.tensor_copy(fg, k.big_buf[64:68, NARROW * T:(NARROW + 1) * T])
                dve.tensor_copy(ig, k.big_buf[32:36, NARROW * T:(NARROW + 1) * T]).then_inc(*did("dve", "gates"))
                w("gates")
                ts(fg, fg, k.par("b_f")[0:4], None, ALU.add).then_inc(*did("dve", "fg"))
                ts(ig, ig, k.par("b_i")[0:4], None, ALU.add).then_inc(*did("dve", "ig"))
                dve.memset(col_rows, 0.0).then_inc(*did("dve", "clear"))
                w("fg")
                ts(lf, fg, 0.0, None, ALU.min).then_inc(*did("dve", "lf0"))
                dve.wait_ge(*after("act", "ln_f"))
                w("lf0")
                tt(lf, lf, soft, ALU.subtract).then_inc(*did("dve", "lf"))
                w("lf")
                dve.tensor_tensor_scan(fsum, k.resets[0:4], lf, 0.0, ALU.mult, ALU.add).then_inc(*did("dve", "fsum"))
                dve.tensor_copy(lfm, lf).then_inc(*did("dve", "lfm"))
                w("ig")
                dve.tensor_copy(igm, ig).then_inc(*did("dve", "igm"))
                dve.wait_ge(loaded, 32)
                w("igm")
                tt(bound, lf[:, TP:T:TS], m0, ALU.add).then_inc(*did("dve", "bound1"))
                w("bound1")
                tt(bound, bound, igm[:, TP:T:TS], ALU.max).then_inc(*did("dve", "bound2"))
                w("bound2")
                dve.memset(lfm[:, TP:T:TS], -BIG).then_inc(*did("dve", "cut_f"))
                dve.tensor_copy(igm[:, TP:T:TS], bound).then_inc(*did("dve", "cut_i"))
                w("cut_i")
                dve.tensor_tensor_scan(m, lfm, igm, 0.0, ALU.add, ALU.max).then_inc(*did("dve", "m"))
                w("m")
                dve.tensor_copy(m_last, m[:, TP + TS - 1:T:TS]).then_inc(*did("dve", "m_last"))
                tt(a_row, ig, fsum, ALU.subtract).then_inc(*did("dve", "a"))
                dve.memset(before[:, 0:1], 0.0).then_inc(*did("dve", "before0"))
                w("m")
                dve.tensor_copy(before[:, 1:NCH], m[:, CH - 1:TP - 1:CH]).then_inc(*did("dve", "before"))
                tt(rfm, fsum, m, ALU.subtract).then_inc(*did("dve", "fm"))
                w("fm")
                tt(chunked(rw), chunked(rfm), before[:, :, None].to_broadcast([4, NCH, CH]), ALU.add)\
                    .then_inc(*did("dve", "w_p"))
                tt(seqs(rw), seqs(rfm), m0[:, :, None].to_broadcast([4, NSEQ, TS]), ALU.add)\
                    .then_inc(*did("dve", "w_s"))
                ts(rnm, m, -1.0, None, ALU.mult).then_inc(*did("dve", "nm"))
                tt(chunked(e_row), chunked(a_row), chunked(rfm)[:, :, CH - 1:CH].to_broadcast([4, NCH, CH]), ALU.add)\
                    .then_inc(*did("dve", "e_p"))
                tt(seqs(e_row), seqs(a_row), seqs(rfm)[:, :, TS - 1:TS].to_broadcast([4, NSEQ, TS]), ALU.add)\
                    .then_inc(*did("dve", "e_s"))
                w("clear")
                dve.tensor_copy(col_rows[0:4, :], a_row).then_inc(*did("dve", "a_col"))
                w("o1")
                dve.reciprocal(big(O_D, 4), big(O_D, 4)).then_inc(*did("dve", "o2"))
                for i in range(2):
                    dve.wait_ge(*after("pe", f"gk{i}"))
                    ts(x2(i).rearrange("p (a t) -> p a t", a=2), two_halves(k.psum_pair(i), HALF),
                       k.par("b_gk")[:, i:i + 1], None, ALU.add).then_inc(*did("dve", f"x{i}"))
                    dve.wait_ge(*after("act", f"ln{i}"))
                    dve.scalar_tensor_tensor(out=x2(i), in0=x2(i), scalar=0.0, in1=s2(i), op0=ALU.min,
                                             op1=ALU.subtract).then_inc(*did("dve", f"s1_{i}"))
                    w(f"s1_{i}")
                    ts(x2(i), x2(i), 1.0 / 16.0, None, ALU.mult).then_inc(*did("dve", f"s2_{i}"))
                    w(f"s2_{i}")
                    dve.tensor_tensor_scan(big(B_C + i), k.resets, x2(i), 0.0, ALU.mult, ALU.add)\
                        .then_inc(*did("dve", f"b{i}"))
                    dve.tensor_tensor_scan(big(B16 + i), resets16, x2(i), 0.0, ALU.mult, ALU.add)\
                        .then_inc(*did("dve", f"b16_{i}"))


def odd_jobs(sample):
    levels = () if sample else LEVELS
    jobs = [("r", ("dve", "log1")), ("rw", ("act", "xw")), ("nm", ("act", "xm"))]
    jobs += [(f"qk_{g}", ("dve", f"DM_{g}")) for g in range(2)]
    jobs += [("vct", ("act", "Vc")), ("vdt", ("act", "Vd")), ("kdt", ("dve", "KE"))]
    jobs += [(f"at_{g}", ("dve", f"AT_{g}")) for g in range(2)]
    jobs += [(f"at{w}_{g}", ("dve", f"L{w}_{g}")) for w in levels for g in range(2)]
    jobs += [("klt", ("act", "KL"))]
    if sample:
        jobs += [("co_s", ("act", "CO")), ("do_s", ("act", "DO")), ("dn_s", ("act", "DN"))]
    jobs += [("co", ("dve" if sample else "act", "Oc")), ("do", ("dve", "Od")), ("dn", ("dve", "den"))]
    if sample:
        for t in range(2):
            jobs += [(f"{n}{t}{x}", ("dve", f"{u}{t}{x}")) for n, u in (("sc", "SC"), ("sd", "SD")) for x in "ab"]
        jobs += [("sn", ("dve", "SN"))]
    else:
        jobs += [("sc", ("dve", "SC")), ("sd", ("dve", "SD"))]
    return jobs


def odd_chunks(k, sample):
    nc = k.nc
    n = NSEQ * TS if sample else CH
    chunks = [NCH] if sample else list(range(NCH))
    names = lambda base, c: f"{base}@{c}"
    levels = () if sample else LEVELS
    jobs = odd_jobs(sample)
    pe_steps, freed, act_steps, dve_steps = [], [], [], []
    for c in chunks:
        pe_steps += [names(j, c) for j, _ in jobs]
        freed += [(e, names(st, c)) for _, (e, st) in jobs]
        a = ["x16", "xn16", "xb", "xl"] + [x for w in levels for x in (f"abs{w}", f"F{w}")]
        a += ["xw", "xm", "xlog", "Vc", "Vd", "KL"] + (["CO", "DO", "DN"] if sample else ["Oc"]) + ["aden"]
        d = ["to_end", "Qb", "Qd", "Kd", "Kl"] + [x for w in levels for x in (f"rel{w}", f"Q{w}", f"K{w}")]
        d += ["log1", "log2", "qw", "DM_0", "DM_1", "KE", "AT_0", "AT_1"]
        d += [x for w in levels for g in range(2) for x in (f"L{w}_{g}", f"A{w}_{g}")]
        if sample:
            d += ["Nw", "Oc"]
        d += ["den", "max", "inv", "Od"] + (["Od2"] if sample else [])
        if sample:
            for t in range(2):
                for kind in ("C", "D"):
                    d += [f"V{kind}{t}", f"G{kind}{t}", f"S{kind}{t}a", f"S{kind}{t}b"]
            d += ["GN", "SN"]
        else:
            d += ["GC", "SC", "GD", "SD"]
        act_steps += [names(x, c) for x in a]
        dve_steps += [names(x, c) for x in d]
    if not sample:
        dve_steps.append("n_last")
    take = carve(k.arena[:, 0:ARENA - 3 * T])
    H, H2 = 4 * n, 2 * n
    x16, xn16, xb, xl = (take(H2) for _ in range(4))
    Qd, Kd, Qb, Kl = (take(H2) for _ in range(4))
    F = {w: take(H2) for w in levels}
    Q = {w: take(H2) for w in levels}
    K = {w: take(H2) for w in levels}
    L = {w: take(H) for w in levels}
    xw, qw = take(H2), take(H2)
    xm, lg, DM, AT, aden = (take(H) for _ in range(5))
    Vc, Vd, KE, KL = take(512), take(512), take(256), take(256)
    if sample:
        SC, SD, SN, Nw = take(2048), take(2048), take(16), take(2048)
        CO, DO, DN = take(H), take(H), take(H)
        Vw = {(kind, half): take(1024) for kind in "CD" for half in range(2)}
    else:
        n_last = take(2)
        SC, SD = take(256), take(512)
    v2 = lambda ap: ap.rearrange("p (t i) -> p t i", t=2)
    v4 = lambda ap, part=P: ap[0:part].rearrange("p (h n) -> p h n", h=4)
    par_of = lambda ap, g: ap[0:n].rearrange("p (t g i) -> p t g i", t=2, g=2)[:, :, g]
    bc = lambda m, cnt: m[:, None, :].to_broadcast([n, cnt, n])
    mask = lambda nm: k.mask(nm)[0:n, 0:n]
    sfx = "8" if sample else "16"

    with nc.cleanup_on_exit():
        ph = Phase(nc)
        sched = Schedule(ph, pe=pe_steps, act=act_steps, dve=dve_steps)
        number = {j: i for i, j in enumerate(pe_steps)}
        states_in, states_out, zeroed = ph.sem("states_in"), ph.sem("states_out"), ph.sem("zeroed")
        even_heads = ph.sem("even_heads")
        bank = lambda job, c: k.psum[number[names(job, c)] % 8]

        def tokens(t, c, count=4):
            return k.big_buf[:, t * T:(t + count) * T].rearrange("p (h t) -> p h t", t=T)[:, :, c * CH:c * CH + n]

        def col(c, r):
            v = k.cols[0:n].rearrange("p (c r h) -> p c r h", c=5, r=4)[:, c, r, :]
            return lambda w: v[:, :, None].to_broadcast([n, 4, w])

        with nc.Block() as block:
            @block.sync
            def _(sp):
                if sample:
                    sp.dma_start(SC, k.io["gla_in"]).then_inc(states_in, 16)
                    sp.dma_start(SD, k.io["mc_in"]).then_inc(states_in, 16)
                    sp.dma_start(SN, k.io["mn_in"]).then_inc(states_in, 16)
                    sp.wait_ge(*sched.after("dve", names("SN", NCH)))
                    sp.dma_start(k.io["gla_s_out"], SC).then_inc(states_out, 16)
                    sp.dma_start(k.io["mc_s_out"], SD).then_inc(states_out, 16)
                    sp.dma_start(k.io["mn_s_out"], SN).then_inc(states_out, 16)
                else:
                    sp.wait_ge(*sched.after("dve", names("SD", NCH - 1)))
                    sp.dma_start(k.io["gla_p_out"], SC).then_inc(states_out, 16)
                    sp.dma_start(k.io["mc_p_out"], SD[:, 0:256]).then_inc(states_out, 16)
                    sp.wait_ge(*sched.after("dve", "n_last"))
                    sp.dma_start(k.io["mn_p_out"], n_last).then_inc(states_out, 16)
                sp.wait_ge(states_out, 48)

            @block.gpsimd
            def _(pool):
                if not sample:
                    pool.memset(SC, 0.0).then_inc(zeroed, 1)
                    pool.memset(SD, 0.0).then_inc(zeroed, 1)

            @block.tensor
            def _(pe):
                for c in chunks:
                    after = lambda e, nm: sched.after(e, names(nm, c))

                    def claim(job):
                        i = number[names(job, c)]
                        if i >= 8:
                            pe.wait_ge(*sched.after(*freed[i - 8]))
                        return bank(job, c)

                    def done(job, ins):
                        ins.then_inc(*sched.did("pe", names(job, c)))

                    def rows(job, source, matrices):
                        b = claim(job)
                        for i, m in enumerate(matrices):
                            last = pe.matmul(b[:, i * n:(i + 1) * n], k.select(m)[0:4],
                                             source[:, c * CH:c * CH + n], start=True, stop=True)
                        done(job, last)
                    rfm, rw, rnm = (k.mrows[:, i * T:(i + 1) * T] for i in range(3))
                    rows("r", rfm, range(4))
                    rows("rw", rw, (4, 5))
                    rows("nm", rnm, range(4))
                    kd, qd = tokens(K_D, c, 2), tokens(Q_D, c, 2)

                    def pair(job, lhsT, rhs):
                        g = int(job[-1])
                        p = slice(64 * g, 64 * g + 64)
                        b = claim(job)
                        for t in range(2):
                            last = pe.matmul(b[0:n, t * n:(t + 1) * n], lhsT(p, t), rhs(p, t), start=True, stop=True)
                        done(job, last)

                    def transposes(job, source, count):
                        b = claim(job)
                        for i in range(count):
                            last = pe.transpose(b[0:n, i * P:(i + 1) * P], source(i), k.mask("ident"))
                        done(job, last)
                    for g in range(2):
                        pair(f"qk_{g}", lambda p, t: kd[p, t], lambda p, t: qd[p, t])
                    vc, vd = tokens(V_C, c), tokens(V_D, c)
                    transposes("vct", lambda i: vc[:, i], 4)
                    transposes("vdt", lambda i: vd[:, i], 4)
                    transposes("kdt", lambda i: kd[:, i], 2)
                    pe.wait_ge(*after("dve", "Kd"))
                    of = lambda buf: (lambda p, t: buf[p, t * n:(t + 1) * n])
                    for g in range(2):
                        pair(f"at_{g}", of(Kd), of(Qd))
                    for w in levels:
                        pe.wait_ge(*after("dve", f"K{w}"))
                        for g in range(2):
                            pair(f"at{w}_{g}", of(K[w]), of(Q[w]))
                    transposes("klt", lambda i: Kl[:, i * n:(i + 1) * n], 2)
                    last_a = f"A{levels[-1]}_1" if levels else "AT_1"
                    if sample:
                        pe.wait_ge(states_in, 48)
                        pe.wait_ge(*after("dve", "Nw"))
                        for turn, (job, state, right) in enumerate((
                                ("co_s", SC, Qb), ("do_s", SD, qw), ("dn_s", Nw, qw))):
                            b = claim(job)
                            for g in range(2):
                                if g:
                                    pe.wait_ge(even_heads, turn + 1)
                                for t in range(2):
                                    for q in range(NSEQ):
                                        h = 2 * t + g
                                        p = slice(64 * g, 64 * g + 64)
                                        last = pe.matmul(
                                            b[:, h * n + q * TS:h * n + (q + 1) * TS],
                                            state[p, (t * NSEQ + q) * P:(t * NSEQ + q + 1) * P],
                                            right[p, t * n + q * TS:t * n + (q + 1) * TS], start=True, stop=True)
                                if not g:
                                    last.then_inc(even_heads, 1)
                            done(job, last)
                    else:
                        if c == 0:
                            pe.wait_ge(zeroed, 2)
                        else:
                            pe.wait_ge(*sched.after("dve", names("SD", c - 1)))

                    def output(job, state, right, values, weights, ready):
                        pe.wait_ge(*ready)
                        b = claim(job)
                        for h in (0, 2, 1, 3):
                            t, g = h // 2, h % 2
                            out = b[:, h * n:(h + 1) * n]
                            if not sample and h == 1:
                                pe.wait_ge(even_heads, 3 * c + ("co", "do", "dn").index(job) + 1)
                            if not sample:
                                p = slice(64 * g, 64 * g + 64)
                                pe.matmul(out, state[p, t * P:(t + 1) * P], right[p, t * n:(t + 1) * n],
                                          start=True, stop=False)
                            last = pe.matmul(out, values(h), weights[0:n, h * n:(h + 1) * n],
                                             start=sample, stop=True)
                            if not sample and h == 2:
                                last.then_inc(even_heads, 1)
                        done(job, last)
                    pe.wait_ge(*after("act", "KL"))
                    output("co", SC, Qb, lambda h: Vc[0:n, h * P:(h + 1) * P], AT, after("dve", last_a))
                    output("do", SD, qw, lambda h: Vd[0:n, h * P:(h + 1) * P], DM, after("dve", "KE"))
                    output("dn", SD[:, 256:] if not sample else None, qw,
                           lambda h: k.mask("ones")[0:n], DM, after("dve", "KE"))
                    if not sample:
                        b = claim("sc")
                        for h in range(4):
                            t, p = h // 2, 64 * (h % 2)
                            last = pe.matmul(b[p:p + 64, t * P:(t + 1) * P], KL[:, h * 64:(h + 1) * 64],
                                             Vc[:, h * P:(h + 1) * P], start=True, stop=True)
                        done("sc", last)
                        b = claim("sd")
                        for h in range(4):
                            t, p = h // 2, 64 * (h % 2)
                            for part, values in ((0, Vd[:, h * P:(h + 1) * P]), (256, k.mask("ones"))):
                                last = pe.matmul(b[p:p + 64, part + t * P:part + (t + 1) * P],
                                                 KE[:, h * 64:(h + 1) * 64], values, start=True, stop=True)
                        done("sd", last)
                    else:
                        for t in range(2):
                            for kind, left in (("C", KL), ("D", KE)):
                                pe.wait_ge(*after("dve", f"V{kind}{t}"))
                                for part, x in enumerate("ab"):
                                    b = claim(f"s{kind.lower()}{t}{x}")
                                    for g in range(2):
                                        h = 2 * t + g
                                        last = pe.matmul(b[64 * g:64 * g + 64, :], left[0:n, h * 64:(h + 1) * 64],
                                                         Vw[kind, g][0:n, part * 512:(part + 1) * 512],
                                                         start=True, stop=True)
                                    done(f"s{kind.lower()}{t}{x}", last)
                        b = claim("sn")
                        for h in range(4):
                            t, p = h // 2, 64 * (h % 2)
                            last = pe.matmul(b[p:p + 64, t * NSEQ:(t + 1) * NSEQ], KE[0:n, h * 64:(h + 1) * 64],
                                             k.mask("block8")[0:n, 0:n:TS], start=True, stop=True)
                        done("sn", last)

            @block.scalar
            def _(act):
                for c in chunks:
                    after = lambda e, nm: sched.after(e, names(nm, c))
                    did = lambda nm: sched.did("act", names(nm, c))
                    psum = lambda job, part=n: bank(job, c)[0:part]
                    if c > chunks[0]:
                        act.wait_ge(*sched.after("dve", names("SD", c - 1)))
                        act.wait_ge(*sched.after("act", names("aden", c - 1)))
                    b16, bC = tokens(B16, c, 2), tokens(B_C, c, 2)
                    act.activation(v2(x16), b16, ACT.Exp).then_inc(*did("x16"))
                    act.activation(v2(xn16), b16, ACT.Exp, scale=-1.0).then_inc(*did("xn16"))
                    act.activation(v2(xb), bC, ACT.Exp).then_inc(*did("xb"))
                    act.wait_ge(*after("dve", "to_end"))
                    act.activation(xl, xl, ACT.Exp).then_inc(*did("xl"))
                    for w in levels:
                        act.wait_ge(*after("dve", f"rel{w}"))
                        act.activation(F[w], F[w], ACT.Abs).then_inc(*did(f"abs{w}"))
                        act.wait_ge(*after("act", f"abs{w}"))
                        act.activation(F[w], F[w], ACT.Exp, scale=-1.0).then_inc(*did(f"F{w}"))
                    act.wait_ge(*after("pe", "rw"))
                    act.activation(xw, psum("rw", P)[:, 0:H2], ACT.Exp).then_inc(*did("xw"))
                    act.wait_ge(*after("pe", "nm"))
                    act.activation(xm, psum("nm", P)[:, 0:H], ACT.Exp).then_inc(*did("xm"))
                    act.wait_ge(*after("dve", "log2"))
                    act.activation(lg[0:n], lg[0:n], ACT.Exp).then_inc(*did("xlog"))
                    for step, job, dst, cols in (("Vc", "vct", Vc, 512), ("Vd", "vdt", Vd, 512), ("KL", "klt", KL, 256)):
                        act.wait_ge(*after("pe", job))
                        act.activation(dst[0:n], psum(job)[:, 0:cols], ACT.Copy).then_inc(*did(step))
                    if sample:
                        for step, job, dst in (("CO", "co_s", CO), ("DO", "do_s", DO), ("DN", "dn_s", DN)):
                            act.wait_ge(*after("pe", job))
                            act.activation(dst, psum(job, P)[:, 0:H], ACT.Copy).then_inc(*did(step))
                        act.wait_ge(*after("dve", "den"))
                        act.activation(aden, aden, ACT.Abs).then_inc(*did("aden"))
                    else:
                        act.wait_ge(*after("pe", "co"))
                        act.activation(tokens(V_C, c), v4(psum("co", P)), ACT.Copy).then_inc(*did("Oc"))
                        act.wait_ge(*after("dve", "den"))
                        act.activation(aden, aden, ACT.Abs).then_inc(*did("aden"))

            @block.vector
            def _(dve):
                tt, ts, stt = dve.tensor_tensor, dve.tensor_scalar, dve.scalar_tensor_tensor
                for c in chunks:
                    after = lambda e, nm: sched.after(e, names(nm, c))
                    did = lambda nm: sched.did("dve", names(nm, c))
                    psum = lambda job, part=n: bank(job, c)[0:part]
                    w_ = lambda nm: dve.wait_ge(*after("dve", nm))
                    if c > chunks[0]:
                        dve.wait_ge(*sched.after("pe", names("sd", c - 1)))
                        dve.wait_ge(*sched.after("dve", names("SD", c - 1)))
                        dve.wait_ge(*sched.after("act", names("aden", c - 1)))
                    bC = tokens(B_C, c, 2)
                    if sample:
                        s8 = lambda ap: ap.rearrange("p t (s i) -> p t s i", s=NSEQ)
                        end = s8(bC)[:, :, :, TS - 1:TS].to_broadcast([P, 2, NSEQ, TS])
                        tt(s8(v2(xl)), end, s8(bC), ALU.subtract).then_inc(*did("to_end"))
                    else:
                        end = bC[:, :, n - 1:n].to_broadcast([P, 2, n])
                        tt(v2(xl), end, bC, ALU.subtract).then_inc(*did("to_end"))
                    q, kk = tokens(Q_C, c, 2), tokens(K_C, c, 2)
                    dve.wait_ge(*after("act", "xl"))
                    stt(out=v2(Qb), in0=q, scalar=SCALE_64, in1=v2(xb), op0=ALU.mult, op1=ALU.mult).then_inc(*did("Qb"))
                    stt(out=v2(Qd), in0=q, scalar=SCALE_64, in1=v2(x16), op0=ALU.mult, op1=ALU.mult)\
                        .then_inc(*did("Qd"))
                    tt(v2(Kd), kk, v2(xn16), ALU.mult).then_inc(*did("Kd"))
                    tt(v2(Kl), kk, v2(xl), ALU.mult).then_inc(*did("Kl"))
                    for w in levels:
                        blocks = n // (2 * w)
                        b4 = lambda ap: ap.rearrange("p t (b i) -> p t b i", b=blocks)
                        tt(b4(v2(F[w])), b4(bC), b4(bC)[:, :, :, w - 1:w].to_broadcast([P, 2, blocks, 2 * w]),
                           ALU.subtract).then_inc(*did(f"rel{w}"))
                        dve.wait_ge(*after("act", f"F{w}"))
                        stt(out=v2(Q[w]), in0=q, scalar=SCALE_64, in1=v2(F[w]), op0=ALU.mult, op1=ALU.mult)\
                            .then_inc(*did(f"Q{w}"))
                        tt(v2(K[w]), kk, v2(F[w]), ALU.mult).then_inc(*did(f"K{w}"))
                    dve.wait_ge(*after("pe", "r"))
                    nb = k.big("not_above_eq" + ("8" if sample else ""))[0:n, 0:n][:, None, :].to_broadcast([n, 4, n])
                    tt(v4(lg, n), v4(psum("r")[:, 0:H], n), nb, ALU.subtract).then_inc(*did("log1"))
                    w_("log1")
                    tt(v4(lg, n), v4(lg, n), col(c, 0)(n), ALU.add).then_inc(*did("log2"))
                    dve.wait_ge(*after("act", "xw"))
                    tt(v2(qw), tokens(Q_D, c, 2), v2(xw), ALU.mult).then_inc(*did("qw"))
                    dve.wait_ge(*after("act", "xlog"))
                    for g in range(2):
                        dve.wait_ge(*after("pe", f"qk_{g}"))
                        stt(out=par_of(DM, g), in0=v2(psum(f"qk_{g}")[:, 0:H2]), scalar=SCALE_64, in1=par_of(lg, g),
                            op0=ALU.mult, op1=ALU.mult).then_inc(*did(f"DM_{g}"))
                    dve.wait_ge(*after("pe", "kdt"))
                    stt(out=v4(KE, n), in0=v4(psum("kdt")[:, 0:256], n), scalar=SCALE_64, in1=col(c, 1)(64),
                        op0=ALU.mult, op1=ALU.mult).then_inc(*did("KE"))
                    for g in range(2):
                        dve.wait_ge(*after("pe", f"at_{g}"))
                        tt(par_of(AT, g), v2(psum(f"at_{g}")[:, 0:H2]), bc(mask("above_eq" + sfx), 2), ALU.mult)\
                            .then_inc(*did(f"AT_{g}"))
                    before = "AT"
                    for w in levels:
                        for g in range(2):
                            dve.wait_ge(*after("pe", f"at{w}_{g}"))
                            tt(par_of(L[w], g), v2(psum(f"at{w}_{g}")[:, 0:H2]), bc(mask(f"above_level{w}"), 2), ALU.mult)\
                                .then_inc(*did(f"L{w}_{g}"))
                            w_(f"L{w}_{g}")
                            tt(par_of(AT, g), par_of(AT, g), par_of(L[w], g), ALU.add).then_inc(*did(f"A{w}_{g}"))
                    if sample:
                        dve.wait_ge(states_in, 48)
                        dve.tensor_copy(Nw.rearrange("p (s v) -> p s v", v=P), SN[:, :, None].to_broadcast([P, 16, P]))\
                            .then_inc(*did("Nw"))
                        dve.wait_ge(*after("pe", "co"))
                        dve.wait_ge(*after("act", "CO"))
                        tt(tokens(V_C, c), v4(psum("co", P)[:, 0:H]), v4(CO), ALU.add).then_inc(*did("Oc"))
                        dve.wait_ge(*after("pe", "dn"))
                        dve.wait_ge(*after("act", "DN"))
                        tt(aden, psum("dn", P)[:, 0:H], DN, ALU.add).then_inc(*did("den"))
                    else:
                        dve.wait_ge(*after("pe", "dn"))
                        dve.tensor_copy(aden, psum("dn", P)[:, 0:H]).then_inc(*did("den"))
                    dve.wait_ge(*after("act", "aden"))
                    tt(aden, aden, xm, ALU.max).then_inc(*did("max"))
                    w_("max")
                    dve.reciprocal(aden, aden).then_inc(*did("inv"))
                    w_("inv")
                    if sample:
                        dve.wait_ge(*after("act", "DO"))
                        tt(DO, psum("do", P)[:, 0:H], DO, ALU.add).then_inc(*did("Od"))
                        w_("Od")
                        tt(tokens(V_D, c), v4(DO), v4(aden), ALU.mult).then_inc(*did("Od2"))
                        own = mask("block8")[:, 0:n:TS]
                        own_b = own[:, :, None].to_broadcast([n, NSEQ, P])
                        for t in range(2):
                            for kind, values, state in (("C", Vc, SC), ("D", Vd, SD)):
                                if t:
                                    dve.wait_ge(*after("pe", f"s{kind.lower()}{t - 1}b"))
                                for g in range(2):
                                    h = 2 * t + g
                                    last = tt(Vw[kind, g][0:n].rearrange("p (s v) -> p s v", s=NSEQ),
                                              values[0:n, None, h * P:(h + 1) * P].to_broadcast([n, NSEQ, P]),
                                              own_b, ALU.mult)
                                last.then_inc(*did(f"V{kind}{t}"))
                                St = state[:, t * 1024:(t + 1) * 1024]
                                ends = (xb if kind == "C" else xw)[:, t * n + TS - 1:(t + 1) * n:TS]
                                tt(St.rearrange("p (s v) -> p s v", s=NSEQ), St.rearrange("p (s v) -> p s v", s=NSEQ),
                                   ends[:, :, None].to_broadcast([P, NSEQ, P]), ALU.mult).then_inc(*did(f"G{kind}{t}"))
                                w_(f"G{kind}{t}")
                                for part, x in enumerate("ab"):
                                    dve.wait_ge(*after("pe", f"s{kind.lower()}{t}{x}"))
                                    cs = slice(part * 512, (part + 1) * 512)
                                    tt(St[:, cs], St[:, cs], psum(f"s{kind.lower()}{t}{x}", P), ALU.add)\
                                        .then_inc(*did(f"S{kind}{t}{x}"))
                        ends = xw.rearrange("p (t s i) -> p t s i", t=2, s=NSEQ)[:, :, :, TS - 1]
                        sn = SN.rearrange("p (t s) -> p t s", t=2)
                        tt(sn, sn, ends, ALU.mult).then_inc(*did("GN"))
                        w_("GN")
                        dve.wait_ge(*after("pe", "sn"))
                        tt(SN, SN, psum("sn", P)[:, 0:16], ALU.add).then_inc(*did("SN"))
                    else:
                        tt(tokens(V_D, c), v4(psum("do", P)), v4(aden), ALU.mult).then_inc(*did("Od"))
                        if c == 0:
                            dve.wait_ge(zeroed, 2)
                        dve.wait_ge(*after("pe", "sc"))
                        tt(v2(SC), v2(SC), v2(xb)[:, :, n - 1:n].to_broadcast([P, 2, P]), ALU.mult).then_inc(*did("GC"))
                        w_("GC")
                        tt(SC, SC, psum("sc", P)[:, 0:256], ALU.add).then_inc(*did("SC"))
                        dve.wait_ge(*after("pe", "sd"))
                        ends = v2(xw)[:, :, n - 1:n]
                        d4 = SD.rearrange("p (a t v) -> p a t v", a=2, t=2)
                        tt(d4, d4, ends[:, None].to_broadcast([P, 2, 2, P]), ALU.mult).then_inc(*did("GD"))
                        w_("GD")
                        tt(SD, SD, psum("sd", P), ALU.add).then_inc(*did("SD"))
                        if c == chunks[-1]:
                            w_("SD")
                            dve.tensor_copy(n_last, SD[:, 256:512:P]).then_inc(*sched.did("dve", "n_last"))


def finish_odd(k):
    nc = k.nc
    big = lambda t: k.big_buf[:, t * T:(t + 1) * T]
    sq = lambda i: k.arena[:, i * T:(i + 1) * T]
    N = range(8)
    src = lambda i: big(V_C + i) if i < 4 else big(V_D + i - 4)
    gate = lambda i: big(Z_C + i) if i < 4 else big(O_D + i - 4)
    with nc.cleanup_on_exit():
        s = Phase(nc)
        q = Schedule(s, pe=[f"sum{i}" for i in N], act=[f"{x}{i}" for x in ("sq", "root") for i in N],
                     dve=[f"{x}{i}" for i in N for x in ("inv", "gated", "out")])
        did, after = q.did, q.after
        with nc.Block() as block:
            @block.tensor
            def _(pe):
                for i in N:
                    pe.wait_ge(*after("act", f"sq{i}"))
                    if i >= 4:
                        pe.wait_ge(*after("act", f"root{i - 4}"))
                    for a in range(2):
                        last = pe.matmul(k.psum_pair(i % 4)[:, a, 0:HALF], k.mask("ones"),
                                         sq(i)[:, a * HALF:(a + 1) * HALF], start=True, stop=True)
                    last.then_inc(*did("pe", f"sum{i}"))

            @block.scalar
            def _(act):
                for i in N:
                    act.activation(sq(i), src(i), ACT.Square).then_inc(*did("act", f"sq{i}"))
                for i in N:
                    act.wait_ge(*after("pe", f"sum{i}"))
                    act.activation(sq(i).rearrange("p (a t) -> p a t", a=2), two_halves(k.psum_pair(i % 4), HALF),
                                   ACT.Sqrt, bias=k.eps[:, 0:1], scale=1.0 / P).then_inc(*did("act", f"root{i}"))

            @block.vector
            def _(dve):
                for i in N:
                    dve.wait_ge(*after("act", f"root{i}"))
                    dve.reciprocal(sq(i), sq(i)).then_inc(*did("dve", f"inv{i}"))
                    dve.wait_ge(*after("dve", f"inv{i}"))
                    gain = k.par("gain_c") if i < 4 else k.par("gain_d")
                    dve.scalar_tensor_tensor(out=sq(i), in0=sq(i), scalar=gain, in1=gate(i), op0=ALU.mult,
                                             op1=ALU.mult).then_inc(*did("dve", f"gated{i}"))
                    dve.wait_ge(*after("dve", f"gated{i}"))
                    dve.tensor_tensor(src(i), src(i), sq(i), ALU.mult).then_inc(*did("dve", f"out{i}"))


def odd_mixer(k, sublayer):
    normalise(k, sublayer)
    project_odd(k)
    prepare_odd(k)
    odd_chunks(k, sample=False)
    odd_chunks(k, sample=True)
    finish_odd(k)
    tile = lambda kt: V_C + kt if kt < 4 else V_D + kt - 4
    residual_product(k, k.io["w_out_odd"], 0, lambda kt: k.big_buf[:, tile(kt) * T:(tile(kt) + 1) * T], KT, sublayer)


class Kernel:

    def __init__(self, nc, io):
        def sb(name, cols):
            return nc.alloc_sbuf_tensor(name, [P, cols], F32)[:]
        self.nc = nc
        self.io = io
        self.masks = sb("masks", N_MASK * P)
        self.bigs = sb("bigs", len(BIGS) * P)
        self.params = sb("params", N_PARAM)
        self.selection = sb("selection", 6 * P)
        self.work = sb("work", WORK)
        self.x = self.work[:, 0:KT * T]
        self.arena = self.work[:, KT * T:]
        self.x_kept = nc.dram_tensor("x_kept", (P, KT * T), F32, kind="Internal").ap()
        self.h = sb("h", KT * TX)
        self.big_buf = sb("big_buf", 30 * T)
        self.mods = [sb(f"mod{i}", MT * NC) for i in range(2)]
        self.cs = sb("cs", KT * NC)
        self.gated = sb("gated", 4 * (T - TP))
        self.resets = sb("resets", T)
        self.eps = sb("eps", 4)
        self.rows = sb("rows", T)
        self.cols = sb("cols", 5 * 16)
        self.pairs = [nc.alloc_psum_tensor(f"banks{b}", [P, 2, 512], F32)[:] for b in range(4)]
        self.psum = [self.pairs[b // 2][:, b % 2, :] for b in range(8)]
        self.cs_tmp = self.arena[:, 0:KT * NC]
        self.lc = self.arena[:, ARENA - 4 * T:]
        self.rows_b = self.arena[:, ARENA - 5 * T:ARENA - 4 * T]
        self.mrows = self.arena[0:4, ARENA - 3 * T:]

    def psum_pair(self, b):
        return self.pairs[b]

    def mask(self, name):
        at = MASKS.index(name) * P
        return self.masks[:, at:at + P]

    def big(self, name):
        at = BIGS.index(name) * P
        return self.bigs[:, at:at + P]

    def par(self, name):
        at, width = PARAM[name]
        return self.params[:, at:at + width]

    def select(self, h):
        return self.selection[:, h * P:(h + 1) * P]


def build(nc, io):
    k = Kernel(nc, io)
    setup(k)
    first_modulation(k)
    for layer in range(DEPTH):
        normalise(k, 3 * layer)
        feed_forward(k, 3 * layer)
        if layer % 2 == 0:
            even_mixer(k, 3 * layer + 1)
        else:
            odd_mixer(k, 3 * layer + 1)
        normalise(k, 3 * layer + 2)
        feed_forward(k, 3 * layer + 2)
    normalise(k, 3 * DEPTH, final=True)


def tile_weights(w):
    c, m = w.shape
    return w.reshape(c // P, P, m // P, P).transpose(2, 1, 0, 3).reshape(m // P, P, c)


def by_feature(v):
    n, f = v.shape
    return v.reshape(n, f // P, P).transpose(2, 0, 1).reshape(P, n * (f // P))


def pack(i):
    import numpy as np
    i = {n: np.asarray(v) for n, v in i.items()}
    cat = np.concatenate

    def column(v):
        out = np.zeros((P, 1), np.float32)
        out[:v.size, 0] = v.ravel()
        return out

    def padded(w, pieces):
        out = np.zeros((w.shape[0], P), np.float32)
        for at, lo, n in pieces:
            out[:, at:at + n] = w[:, lo:lo + n]
        return out

    x = cat([i["x_prompt"].reshape(TP, D), i["x_sample"].reshape(NSEQ * TS, D)])
    c = cat([i["c_prompt"], i["c_sample"]])
    we, wo = i["w_in_even"][0], i["w_in_odd"][0]
    a_end = 3 * 512
    b0 = 3 * 512 + 8 + 512
    even = cat([we[:, 0:a_end], we[:, b0:b0 + 1792], we[:, a_end + 8:b0], padded(we, [(0, a_end, 4), (32, a_end + 4, 4)])],
               axis=1)
    c_lr, c_z, d0 = 1024, 1040, 1552
    odd = cat([wo[:, 0:c_lr], wo[:, c_z:d0], wo[:, d0:d0 + 1024], wo[:, d0 + 1032:],
               padded(wo, [(0, c_lr, 16), (32, d0 + 1024, 4), (64, d0 + 1028, 4)])], axis=1)
    params = {
        "b_mod": by_feature(i["b_mod"].reshape(DEPTH * 9, D)),
        "norm_gain": by_feature(i["norm_gain"].reshape(DEPTH * 3, D)),
        "final_gain": by_feature(i["final_gain"][None]),
        "conv_w": i["conv_w"][0].reshape(CONV_W, 12, P).transpose(2, 1, 0).reshape(P, 48),
        "mu": by_feature(i["mu_b"]), "w0": by_feature(i["w0_b"]), "a0": by_feature(i["a0_b"]),
        "k_k": by_feature(i["k_k"]), "k_a": by_feature(i["k_a"]), "r_k": by_feature(i["r_k"].reshape(1, 512)),
        "lnx_gain": by_feature(i["lnx_gain"]), "lnx_bias": by_feature(i["lnx_bias"]),
        "gain_a": i["gain_a"].T, "a_log": column(i["a_log"]), "dt_bias": column(i["dt_bias"]),
        "b_gk": by_feature(i["b_gk"]), "gain_c": i["gain_c"].T, "gain_d": i["gain_d"].T,
        "b_i": column(i["b_i"]), "b_f": column(i["b_f"]),
    }
    selection = np.zeros((P, 6, P), np.float32)
    for h in range(4):
        selection[h, h] = 1.0
        selection[h, 4 + h // 2, 64 * (h % 2):64 * (h % 2) + 64] = 1.0
    ff = cat([tile_weights(i[n][l, s])[:, :, None] for l in range(DEPTH) for s in range(2) for n in ("w_ffn_gate",)])
    fu = cat([tile_weights(i["w_ffn_up"][l, s])[:, :, None] for l in range(DEPTH) for s in range(2)])
    pair_state = lambda v: v[0].reshape(NSEQ, -1, 2, v.shape[-2], v.shape[-1]).transpose(2, 3, 1, 0, 4)
    arrays = {
        "x_in": x.reshape(T, KT, P).transpose(2, 1, 0).reshape(P, KT * T),
        "c_in": c.reshape(NC, KT, P).transpose(2, 1, 0).reshape(P, KT * NC),
        "params_in": cat([params[n] for n, _ in PARAM_WIDTHS], axis=1),
        "selection_in": selection.reshape(P, 6 * P),
        "w_mod": i["w_mod"].reshape(DEPTH, KT, P, 3, 2, MOD_W).transpose(0, 3, 1, 4, 2, 5).reshape(-1, P, MOD_W),
        "w_ff": cat([ff, fu], axis=2).reshape(-1, P, 2 * D),
        "w_down": cat([tile_weights(i["w_ffn_down"][l, s]) for l in range(DEPTH) for s in range(2)]),
        "w_in_even": tile_weights(even), "w_out_even": tile_weights(i["w_out_even"][0]),
        "w_in_odd": tile_weights(odd), "w_out_odd": tile_weights(i["w_out_odd"][0]),
        "w_wa2": cat([i["w_w2"][0], i["w_a2"][0]]), "w_g2": i["w_g2"][0], "w_gk2": i["w_gk2"][0],
        "xbuf_in": i["state_xbuf_even"][0].reshape(NSEQ, PAD, KT, P).transpose(3, 2, 0, 1),
        "delta_in": i["state_delta"][0].transpose(2, 1, 0, 3).reshape(P, 32 * P),
        "rwkv_in": pair_state(i["state_rwkv"].swapaxes(-1, -2)).reshape(P, 4 * NSEQ * 64),
        "gla_in": pair_state(i["state_gla"]).reshape(P, 2 * NSEQ * P),
        "mc_in": pair_state(i["state_mlstm_c"]).reshape(P, 2 * NSEQ * P),
        "mn_in": pair_state(i["state_mlstm_n"][..., None]).reshape(P, 2 * NSEQ),
        "mm_in": i["state_mlstm_m"][0].T,
    }
    return {n: np.ascontiguousarray(a, dtype=np.float32) for n, a in arrays.items()}


OUTPUTS = {
    "y_out": (P, KT, T), "xbuf_p_out": (P, KT, PAD), "xbuf_s_out": (P, KT, NSEQ, PAD),
    "delta_p_out": (P, 512), "delta_s_out": (P, 32 * P), "rwkv_p_out": (P, 256), "rwkv_s_out": (P, 2048),
    "gla_p_out": (P, 256), "gla_s_out": (P, 2048), "mc_p_out": (P, 256), "mc_s_out": (P, 2048),
    "mn_p_out": (P, 2), "mn_s_out": (P, 16), "mm_p_out": (4, 1), "mm_s_out": (4, NSEQ),
}


def unpack(o):
    import numpy as np
    y = o["y_out"].transpose(2, 1, 0).reshape(T, D)

    def pair_state(v, seqs, rows, cols):
        v = v.reshape(2, rows, -1, seqs, cols).transpose(3, 2, 0, 1, 4)
        return v.reshape(1, seqs, -1, rows, cols)
    out = (
        y[:TP].reshape(1, TP, D), y[TP:].reshape(NSEQ, TS, D),
        o["xbuf_p_out"].transpose(2, 1, 0).reshape(1, 1, PAD, D),
        o["xbuf_s_out"].transpose(2, 3, 1, 0).reshape(1, NSEQ, PAD, D),
        o["delta_p_out"].reshape(P, 4, 1, P).transpose(2, 1, 0, 3)[None],
        o["delta_s_out"].reshape(P, 4, NSEQ, P).transpose(2, 1, 0, 3)[None],
        pair_state(o["rwkv_p_out"], 1, 64, 64).swapaxes(-1, -2),
        pair_state(o["rwkv_s_out"], NSEQ, 64, 64).swapaxes(-1, -2),
        pair_state(o["gla_p_out"], 1, 64, P), pair_state(o["gla_s_out"], NSEQ, 64, P),
        pair_state(o["mc_p_out"], 1, 64, P), pair_state(o["mc_s_out"], NSEQ, 64, P),
        pair_state(o["mn_p_out"], 1, 64, 1)[..., 0], pair_state(o["mn_s_out"], NSEQ, 64, 1)[..., 0],
        o["mm_p_out"].T[None], o["mm_s_out"].T[None],
    )
    return tuple(np.ascontiguousarray(v) for v in out)


def kernel(**inputs):
    import concourse.bacc as bacc
    from concourse.bass_utils import run_bass_kernel_spmd
    arrays = pack(inputs)
    nc = bacc.Bacc("TRN2", target_bir_lowering=False, num_devices=1)
    io = {n: nc.dram_tensor(n + "_dram", a.shape, F32, kind="ExternalInput").ap() for n, a in arrays.items()}
    io |= {n: nc.dram_tensor(n + "_dram", s, F32, kind="ExternalOutput").ap() for n, s in OUTPUTS.items()}
    build(nc, io)
    r = run_bass_kernel_spmd(nc, [{n + "_dram": a for n, a in arrays.items()}], core_ids=[0])
    return unpack({n: r.results[0][n + "_dram"] for n in OUTPUTS})
```

```python
import concourse.bass as bass
from concourse import mybir

F32 = mybir.dt.float32
F32R = mybir.dt.float32r
ACT = mybir.ActivationFunctionType
ALU = mybir.AluOpType

P = 128
D = 1024
KT = D // P
TP = 512
NSEQ = 8
TS = 8
T = TP + NSEQ * TS
NC = 1 + NSEQ
CONV_W = 4
PAD = CONV_W - 1
TX = TP + NSEQ * (TS + PAD)
HALF = T // 2
HALFX = TX // 2
DFF = 2816
FT = DFF // P
DEPTH = 2
MT = 3 * KT
EPS = 1e-6
GN_EPS = 64e-5
BIG = 1e30
CH = 128
NCH = TP // CH
NEG_E_HALF = -0.6065306597126334

PARAM_WIDTHS = [
    ("b_mod", DEPTH * 9 * KT), ("norm_gain", DEPTH * 3 * KT), ("final_gain", KT),
    ("conv_w", 12 * CONV_W), ("mu", 14), ("w0", 4), ("a0", 4), ("k_k", 4), ("k_a", 4), ("r_k", 4),
    ("lnx_gain", 4), ("lnx_bias", 4), ("gain_a", 1), ("a_log", 1), ("dt_bias", 1),
    ("b_gk", 2), ("gain_c", 1), ("gain_d", 1), ("b_i", 1), ("b_f", 1),
]
PARAM = {}
_at = 0
for _n, _w in PARAM_WIDTHS:
    PARAM[_n] = (_at, _w)
    _at += _w
N_PARAM = _at

WORK = 24744
ARENA = WORK - KT * T
RAW_SLOTS, SPLIT_SLOTS = 4, 2
H_LOW = (RAW_SLOTS + 2 * SPLIT_SLOTS) * D
PROJECTION_END = H_LOW + KT * TX
LOW = ARENA - FT * T


def two_halves(bank_pair, width):
    return bank_pair[:, :, 0:width]


class Phase:

    def __init__(self, nc):
        self.nc, self.sems = nc, {}

    def sem(self, name):
        if name not in self.sems:
            self.sems[name] = self.nc.alloc_semaphore(f"{name}_{self.nc.next_id()}")
        return self.sems[name]


def setup(k):
    nc = k.nc
    with nc.cleanup_on_exit():
        s = Phase(nc)
        loaded, ones_ready, base_ready, masks_ready, sig_ready, cs_ready = (
            s.sem(n) for n in ("loaded", "ones_ready", "base_ready", "masks_ready", "sig_ready", "cs_ready"))
        with nc.Block() as block:
            @block.sync
            def _(sp):
                sp.dma_start(k.cs, k.io["c_in"]).then_inc(loaded, 16)
                sp.dma_start(k.x, k.io["x_in"]).then_inc(loaded, 16)
                sp.dma_start(k.params, k.io["params_in"]).then_inc(loaded, 16)
                sp.dma_start(k.selection, k.io["selection_in"]).then_inc(loaded, 16)
                sp.wait_ge(loaded, 64)

            @block.gpsimd
            def _(pool):
                m = k.masks
                pool.memset(k.eps[:, 0:1], EPS)
                pool.memset(k.eps[:, 1:2], GN_EPS)
                pool.memset(k.eps[:, 2:3], 1.0)
                pool.memset(m[:, 0:N_MASK * P], 1.0).then_inc(ones_ready, 1)
                pool.memset(k.resets, 1.0).then_inc(ones_ready, 1)
                pool.memset(k.bigs, 0.0).then_inc(ones_ready, 1)
                pool.wait_ge(ones_ready, 3)

                def keep(name, op, base, cm, step, fill=0.0, view=None):
                    v = view if view is not None else k.mask(name)
                    return pool.affine_select(out=v, in_=v, compare_op=op, fill=fill, base=base,
                                              pattern=[[step, P]], channel_multiplier=cm)
                keep("ident", ALU.is_equal, 0, 1, -1)
                keep("below", ALU.is_gt, 0, 1, -1)
                keep("above", ALU.is_gt, 0, -1, 1)
                keep("above_eq", ALU.is_ge, 0, -1, 1)
                keep(None, ALU.is_gt, 0, 1, -1, fill=BIG, view=k.big("not_below"))
                keep(None, ALU.is_ge, 0, -1, 1, fill=BIG, view=k.big("not_above_eq"))
                for w in (8, 16, 32, 64):
                    v = k.mask(f"block{w}").rearrange("p (b i) -> p b i", i=w)
                    pool.affine_select(out=v, in_=v, compare_op=ALU.is_ge, fill=0.0, base=0,
                                       pattern=[[-w, P // w], [0, w]], channel_multiplier=1)
                last = pool.memset(k.resets[:, 0:TP].rearrange("p (c i) -> p c i", i=CH)[:, :, 0:1], 0.0)
                last = pool.memset(k.resets[:, TP:T].rearrange("p (c i) -> p c i", i=TS)[:, :, 0:1], 0.0)
                last.then_inc(base_ready, 1)
                pool.wait_ge(base_ready, 1)
                for w in (8, 16, 32, 64):
                    v = k.mask(f"block{w}").rearrange("p (b i) -> p b i", i=w)
                    last = pool.affine_select(out=v, in_=v, compare_op=ALU.is_ge, fill=0.0, base=w - 1,
                                              pattern=[[w, P // w], [0, w]], channel_multiplier=-1)
                last.then_inc(base_ready, 1)
                pool.wait_ge(base_ready, 2)
                for w in (16, 32, 64):
                    outer = k.mask("ones") if w == 64 else k.mask(f"block{2 * w}")
                    pool.tensor_tensor(k.mask(f"level{w}"), outer, k.mask(f"block{w}"), ALU.subtract)
                pool.tensor_tensor(k.mask("below8"), k.mask("below"), k.mask("block8"), ALU.mult)
                pool.tensor_tensor(k.mask("above8"), k.mask("above"), k.mask("block8"), ALU.mult)
                pool.tensor_tensor(k.mask("above_eq8"), k.mask("above_eq"), k.mask("block8"), ALU.mult)
                pool.tensor_tensor(k.mask("above_eq16"), k.mask("above_eq"), k.mask("block16"), ALU.mult)
                pool.tensor_tensor(k.mask("above16"), k.mask("above"), k.mask("block16"), ALU.mult)
                pool.tensor_scalar(k.big("outside8"), k.mask("block8"), -BIG, BIG, ALU.mult, ALU.add)\
                    .then_inc(base_ready, 1)
                pool.wait_ge(base_ready, 3)
                for w in (16, 32, 64):
                    pool.tensor_tensor(k.mask(f"above_level{w}"), k.mask("above"), k.mask(f"level{w}"), ALU.mult)
                for a, b in (("not_below8", "not_below"), ("not_above_eq8", "not_above_eq")):
                    last = pool.tensor_tensor(k.big(a), k.big("outside8"), k.big(b), ALU.add)
                last.then_inc(masks_ready, 1)

            @block.scalar
            def _(act):
                act.wait_ge(loaded, 64)
                act.activation(k.cs_tmp, k.cs, ACT.Sigmoid).then_inc(sig_ready, 1)

            @block.vector
            def _(dve):
                dve.wait_ge(sig_ready, 1)
                dve.tensor_tensor(k.cs, k.cs, k.cs_tmp, ALU.mult).then_inc(cs_ready, 1)


MASKS = ("ident ones below above above_eq block8 block16 block32 block64 level16 level32 level64 "
         "below8 above8 above_eq8 above16 above_eq16 above_level16 above_level32 above_level64").split()
N_MASK = len(MASKS)
BIGS = "not_below not_above_eq outside8 not_below8 not_above_eq8".split()


MOD_W = MT * P // 2
MOD_G = MOD_W // 4
MOD_STEPS = 2 * KT


class Modulation:

    def __init__(self, k, s, sublayer, slots, room):
        self.k, self.sublayer, self.slots = k, sublayer, slots
        self.landed = [s.sem(f"mod_landed{b}") for b in range(slots)]
        self.done, self.cleared, self.copied, self.turned, self.biased, self.finished = (
            s.sem(n) for n in ("mod_done", "mod_cleared", "mod_copied", "mod_turned", "mod_biased",
                               "mod_finished"))
        self.slot = [room[:, b * MOD_W:(b + 1) * MOD_W] for b in range(slots)]
        at = slots * MOD_W
        self.by_vector = room[:, at:at + 2 * MOD_G]
        self.row0 = sublayer * MOD_STEPS

    def load(self, sp, slot, step):
        at = self.row0 + step
        src = self.k.io["w_mod"][at] if isinstance(step, int) else \
            self.k.io["w_mod"][bass.ds(at, 1)].rearrange("a p n -> (a p) n")
        sp.dma_start(self.slot[slot], src).then_inc(self.landed[slot], 16)

    def clear(self, pool):
        pool.memset(self.by_vector, 0.0).then_inc(self.cleared, 1)

    def products(self, pe, kt, slot, half, wait_landed):
        k = self.k
        pe.wait_ge(self.landed[slot], wait_landed)
        for j in range(4):
            last = pe.matmul(k.psum[6 + half][32 * j:32 * j + NC, 0:MOD_G], k.cs[:, kt * NC:(kt + 1) * NC],
                             self.slot[slot][:, j * MOD_G:(j + 1) * MOD_G], start=kt == 0, stop=kt == KT - 1)
        last.then_inc(self.done, 1)

    def copy(self, act):
        act.wait_ge(self.cleared, 1)
        act.wait_ge(self.done, MOD_STEPS)
        for j in range(4):
            at = slice(32 * j, 32 * j + NC)
            last = act.activation(self.by_vector[at].rearrange("p (a n) -> p a n", a=2),
                                  self.k.psum_pair(3)[at, :, 0:MOD_G], ACT.Copy)
        last.then_inc(self.copied, 1)

    def turn(self, pe):
        pe.wait_ge(self.copied, 1)
        for half in range(2):
            for b in range(3):
                at = half * MOD_G + b * P
                last = pe.transpose(self.k.psum[4 + half][:, b * P:(b + 1) * P], self.by_vector[:, at:at + P],
                                    self.k.mask("ident"))
        last.then_inc(self.turned, 1)

    def finish(self, dve):
        k, mod = self.k, self.k.mods[self.sublayer % 2]
        bias = k.par("b_mod")[:, self.sublayer * MT:(self.sublayer + 1) * MT]
        dve.wait_ge(self.turned, 1)
        for half in range(2):
            tiles = slice(half * MT // 2, (half + 1) * MT // 2)
            dve.tensor_tensor(
                mod[:, tiles.start * NC:tiles.stop * NC].rearrange("p (j b s) -> p j b s", j=4, s=NC),
                k.psum[4 + half][:, 0:3 * P].rearrange("p (b j i) -> p j b i", b=3, i=32)[:, :, :, 0:NC],
                bias[:, tiles].rearrange("p (j b) -> p j b", j=4)[:, :, :, None].to_broadcast([P, 4, 3, NC]),
                ALU.add).then_inc(self.biased, 1)
        dve.wait_ge(self.biased, 2)
        mod = mod.rearrange("p (m s) -> p m s", s=NC)
        gain = k.par("norm_gain")[:, self.sublayer * KT:(self.sublayer + 1) * KT, None].to_broadcast([P, KT, NC])
        dve.scalar_tensor_tensor(out=mod[:, KT:2 * KT], in0=mod[:, KT:2 * KT], scalar=1.0, in1=gain,
                                 op0=ALU.add, op1=ALU.mult).then_inc(self.finished, 1)
        weight = 1.0 if self.sublayer % 3 == 1 else 0.5
        dve.tensor_scalar(mod[:, 2 * KT:3 * KT], mod[:, 2 * KT:3 * KT], 1.0, weight, ALU.add, ALU.mult)\
            .then_inc(self.finished, 1)


def first_modulation(k):
    nc = k.nc
    SLOTS = 8
    with nc.cleanup_on_exit():
        s = Phase(nc)
        mod = Modulation(k, s, 0, SLOTS, k.arena)
        with nc.Block() as block:
            @block.sync
            def _(sp):
                for i in range(SLOTS):
                    mod.load(sp, i, i)
                with sp.Fori(1, MOD_STEPS // SLOTS) as r:
                    for b in range(SLOTS):
                        sp.wait_ge(mod.done, (r - 1) * SLOTS + b + 1)
                        mod.load(sp, b, r * SLOTS + b)

            @block.gpsimd
            def _(pool):
                mod.clear(pool)

            @block.tensor
            def _(pe):
                for i in range(MOD_STEPS):
                    mod.products(pe, i // 2, i % SLOTS, i % 2, (i // SLOTS + 1) * 16)
                mod.turn(pe)

            @block.scalar
            def _(act):
                mod.copy(act)

            @block.vector
            def _(dve):
                mod.finish(dve)


def split_high(act, raw, high):
    return act.activation(high, raw, ACT.Copy)


def split_low(engine, raw, high, low):
    return engine.tensor_tensor(low, raw, high.bitcast(F32), ALU.subtract)


def split_products(pe, pair, width, w_high, w_low, tokens, first, last):
    x = [tokens(a) for a in range(2)]
    for a in range(2):
        pe.matmul(pair[:, a, 0:width], w_low, x[a][0], start=first, stop=False)
    for a in range(2):
        pe.matmul(pair[:, a, 0:width], w_high, x[a][1], start=False, stop=False)
    for a in range(2):
        done = pe.matmul(pair[:, a, 0:width], w_high, x[a][0], start=False, stop=last)
    return done


def tokens_of(high, low, stride_high, stride_low, width):
    return lambda kt: lambda a: (high[:, kt * stride_high + a * width:kt * stride_high + (a + 1) * width],
                                 low[:, kt * stride_low + a * width:kt * stride_low + (a + 1) * width])


def normalise(k, sublayer, h_low=None, final=False, wide=False):
    nc = k.nc
    with nc.cleanup_on_exit():
        s = Phase(nc)
        squared, summed, rooted, inverse, scaled, shifted, stored, loaded, high_done, low_done = (
            s.sem(n) for n in ("squared", "summed", "rooted", "inverse", "scaled", "shifted", "stored", "loaded",
                               "high_done", "low_done"))
        x = k.x.rearrange("p (k t) -> p k t", t=T)
        sq = k.big_buf[:, KT * TX:KT * TX + KT * T].rearrange("p (k t) -> p k t", t=T)
        rstd = k.arena[:, 0:T]
        root = k.arena[:, T:2 * T]
        last_rows = k.arena[:, 2 * T:2 * T + KT * PAD].rearrange("p (k t) -> p k t", t=PAD)
        h = k.big_buf[:, 0:KT * TX].rearrange("p (k t) -> p k t", t=TX)
        high = k.h_r.rearrange("p (k t) -> p k t", t=TX)
        END = TX if wide else T
        low = None if final else h_low.rearrange("p (k t) -> p k t", k=KT)
        hs = h[:, :, TP:TX].rearrange("p k (s t) -> p k s t", s=NSEQ)[:, :, :, PAD:] if wide else \
            h[:, :, TP:T].rearrange("p k (s t) -> p k s t", s=NSEQ)
        mod = k.mods[sublayer % 2].rearrange("p (m s) -> p m s", s=NC)
        pair = k.psum_pair(0)
        SAMPLE = KT + 3
        with nc.Block() as block:
            @block.scalar
            def _(act):
                for kt in range(KT):
                    act.activation(sq[:, kt], x[:, kt], ACT.Square).then_inc(squared, 1)
                act.wait_ge(summed, 1)
                act.activation(root.rearrange("p (a t) -> p a t", a=2), two_halves(pair, HALF), ACT.Sqrt,
                               bias=k.eps[:, 0:1], scale=1.0 / D).then_inc(rooted, 1)
                if not final:
                    for kt in range(KT):
                        act.wait_ge(scaled, kt + 1)
                        act.activation(high[:, kt, 0:TP], h[:, kt, 0:TP], ACT.Identity,
                                       bias=mod[:, kt, 0:1]).then_inc(high_done, 1)
                    act.wait_ge(scaled, SAMPLE)
                    if wide:
                        act.wait_ge(loaded, 16 * KT)
                    act.activation(high[:, :, TP:END], h[:, :, TP:END], ACT.Copy).then_inc(high_done, 1)

            @block.tensor
            def _(pe):
                for kt in range(KT):
                    pe.wait_ge(squared, kt + 1)
                    for a in range(2):
                        last = pe.matmul(pair[:, a, 0:HALF], k.mask("ones"), sq[:, kt, a * HALF:(a + 1) * HALF],
                                         start=kt == 0, stop=kt == KT - 1)
                last.then_inc(summed, 1)

            def low_part(engine, kt):
                engine.wait_ge(high_done, kt + 1)
                engine.scalar_tensor_tensor(out=low[:, kt, 0:TP], in0=h[:, kt, 0:TP],
                                            scalar=mod[:, kt, 0:1], in1=high[:, kt, 0:TP].bitcast(F32), op0=ALU.add,
                                            op1=ALU.subtract).then_inc(low_done, 1)

            @block.vector
            def _(dve):
                dve.wait_ge(rooted, 1)
                dve.reciprocal(rstd, root).then_inc(inverse, 1)
                dve.wait_ge(inverse, 1)
                rs = rstd[:, None, TP:T].to_broadcast([P, KT, T - TP]).rearrange("p k (s t) -> p k s t", s=NSEQ)
                for kt in range(KT):
                    gain = k.par("final_gain")[:, kt:kt + 1] if final else mod[:, KT + kt, 0:1]
                    dve.scalar_tensor_tensor(out=h[:, kt, 0:TP], in0=x[:, kt, 0:TP], scalar=gain,
                                             in1=rstd[:, 0:TP], op0=ALU.mult, op1=ALU.mult).then_inc(scaled, 1)
                dve.tensor_tensor(hs, x[:, :, TP:T].rearrange("p k (s t) -> p k s t", s=NSEQ), rs, ALU.mult)\
                    .then_inc(scaled, 1)
                if final:
                    g = k.par("final_gain")[:, :, None, None].to_broadcast([P, KT, NSEQ, TS])
                else:
                    g = mod[:, KT:2 * KT, 1:NC, None].to_broadcast([P, KT, NSEQ, TS])
                dve.wait_ge(scaled, KT + 1)
                dve.tensor_tensor(hs, hs, g, ALU.mult).then_inc(scaled, 1)
                if not final:
                    dve.wait_ge(scaled, KT + 2)
                    dve.tensor_tensor(hs, hs, mod[:, 0:KT, 1:NC, None].to_broadcast([P, KT, NSEQ, TS]), ALU.add)\
                        .then_inc(scaled, 1)
                    if wide:
                        dve.tensor_tensor(last_rows, h[:, :, TP - PAD:TP], mod[:, 0:KT, 0:1].to_broadcast([P, KT, PAD]),
                                          ALU.add).then_inc(shifted, 1)
                    for kt in range(KT):
                        low_part(dve, kt)
                    dve.wait_ge(high_done, KT + 1)
                    split_low(dve, h[:, :, TP:END], high[:, :, TP:END], low[:, :, TP:END]).then_inc(low_done, 1)

            @block.sync
            def _(sp):
                if final:
                    sp.wait_ge(scaled, KT + 2)
                    sp.dma_start(k.io["y_out"], h[:, :, 0:T]).then_inc(stored, 16)
                    sp.wait_ge(stored, 16)
                if wide:
                    for kt in range(KT):
                        sp.dma_start(h[:, kt, TP:TX].rearrange("p (s t) -> p s t", s=NSEQ)[:, :, 0:PAD],
                                     k.io["xbuf_in"][:, kt]).then_inc(loaded, 16)
                    sp.wait_ge(loaded, 16 * KT)
                    sp.wait_ge(shifted, 1)
                    sp.dma_start(k.io["xbuf_p_out"], last_rows).then_inc(stored, 16)
                    sp.wait_ge(scaled, SAMPLE)
                    for kt in range(KT):
                        sp.dma_start(k.io["xbuf_s_out"][:, kt], h[:, kt, TP:TX].rearrange("p (s t) -> p s t", s=NSEQ)
                                     [:, :, TS:]).then_inc(stored, 16)
                    sp.wait_ge(stored, 16 + 16 * KT)


def add_gated(dve, k, product, gate, m, scratch, prompt_done, sample_done):
    x = k.x[:, bass.ds(m * T, T)]
    g = gate[:, bass.ds(m * NC, NC)]
    dve.scalar_tensor_tensor(out=x[:, 0:HALF], in0=product[:, 0, 0:HALF], scalar=g[:, 0:1],
                             in1=x[:, 0:HALF], op0=ALU.mult, op1=ALU.add)
    dve.scalar_tensor_tensor(out=x[:, HALF:TP], in0=product[:, 1, 0:TP - HALF], scalar=g[:, 0:1],
                             in1=x[:, HALF:TP], op0=ALU.mult, op1=ALU.add).then_inc(prompt_done, 1)
    per_token = g[:, 1:NC, None].to_broadcast([P, NSEQ, TS])
    dve.tensor_tensor(scratch.rearrange("p (s t) -> p s t", s=NSEQ),
                      product[:, 1, TP - HALF:HALF].rearrange("p (s t) -> p s t", s=NSEQ),
                      per_token, ALU.mult).then_inc(sample_done, 1)


def residual_product(k, weights, row0, n_in, sublayer, tokens, raw, split, source=None):
    nc = k.nc
    W = raw[0].shape[1]
    PIECES = n_in * P // W
    DEEP = W // P
    RAW, SPLIT = len(raw), len(split)
    with nc.cleanup_on_exit():
        s = Phase(nc)
        landed = [s.sem(f"out_landed{b}") for b in range(RAW)]
        high_done, low_done, source_high, source_low, piece_done, product, prompt_done, sample_done, taken = (
            s.sem(n) for n in ("high_done", "low_done", "source_high", "source_low", "piece_done", "product",
                               "prompt_done", "sample_done", "taken"))
        gate = k.mods[sublayer % 2][:, 2 * KT * NC:3 * KT * NC]
        mod = Modulation(k, s, sublayer + 1, 2, k.h) if sublayer + 1 < DEPTH * 3 else None
        with nc.Block() as block:
            @block.sync
            def _(sp):
                for m in range(KT):
                    for piece in range(m * PIECES, (m + 1) * PIECES):
                        if piece >= RAW:
                            sp.wait_ge(low_done, piece - RAW + 1)
                        at = piece % PIECES * W
                        sp.dma_start(raw[piece % RAW], weights[row0 + m][:, at:at + W]).then_inc(landed[piece % RAW], 16)
                    if mod:
                        for half in range(2):
                            if m > 0:
                                sp.wait_ge(mod.done, 2 * (m - 1) + half + 1)
                            mod.load(sp, half, 2 * m + half)

            @block.gpsimd
            def _(pool):
                if mod:
                    mod.clear(pool)

            @block.tensor
            def _(pe):
                for m in range(KT):
                    if m >= 2:
                        pe.wait_ge(taken, m - 1)
                    for piece in range(m * PIECES, (m + 1) * PIECES):
                        pe.wait_ge(low_done, piece + 1)
                        high, low = split[piece % SPLIT]
                        for i in range(DEEP):
                            kt = piece % PIECES * DEEP + i
                            if source and m == 0:
                                pe.wait_ge(source_low, kt + 1)
                            last = split_products(pe, k.psum_pair(m % 2), HALF, high[:, i * P:(i + 1) * P],
                                                  low[:, i * P:(i + 1) * P], tokens(kt), kt == 0, kt == n_in - 1)
                        last.then_inc(piece_done, 1)
                    if mod:
                        for half in range(2):
                            mod.products(pe, m, half, half, (m + 1) * 16)
                if mod:
                    mod.turn(pe)

            @block.scalar
            def _(act):
                def high_part(piece):
                    act.wait_ge(landed[piece % RAW], (piece // RAW + 1) * 16)
                    if piece >= SPLIT:
                        act.wait_ge(piece_done, piece - SPLIT + 1)
                    split_high(act, raw[piece % RAW], split[piece % SPLIT][0]).then_inc(high_done, 1)
                high_part(0)
                if source:
                    for kt in range(n_in):
                        high = [part[0] for part in (tokens(kt)(0), tokens(kt)(1))]
                        for a in range(2):
                            done = split_high(act, source(kt)[:, a * HALF:(a + 1) * HALF], high[a])
                        done.then_inc(source_high, 1)
                for piece in range(1, KT * PIECES):
                    high_part(piece)
                if mod:
                    mod.copy(act)

            @block.vector
            def _(dve):
                def low_part(piece):
                    dve.wait_ge(high_done, piece + 1)
                    split_low(dve, raw[piece % RAW], *split[piece % SPLIT]).then_inc(low_done, 1)

                def add(m):
                    dve.wait_ge(piece_done, (m + 1) * PIECES)
                    scratch = k.gated[:, m % 4 * (T - TP):(m % 4 + 1) * (T - TP)]
                    add_gated(dve, k, k.psum_pair(m % 2), gate, m, scratch, prompt_done, sample_done)
                    dve.wait_ge(sample_done, m + 1)
                    xs = k.x[:, m * T + TP:(m + 1) * T]
                    dve.tensor_tensor(xs, xs, scratch, ALU.add).then_inc(taken, 1)
                low_part(0)
                if source:
                    for kt in range(n_in):
                        dve.wait_ge(source_high, kt + 1)
                        for a in range(2):
                            done = split_low(dve, source(kt)[:, a * HALF:(a + 1) * HALF], *tokens(kt)(a))
                        done.then_inc(source_low, 1)
                for piece in range(1, KT * PIECES):
                    low_part(piece)
                    if piece >= SPLIT and (piece - SPLIT) % PIECES == PIECES - 1:
                        add((piece - SPLIT) // PIECES)
                for m in range((KT * PIECES - SPLIT) // PIECES, KT):
                    add(m)
                if mod:
                    mod.finish(dve)


def feed_forward(k, sublayer):
    nc = k.nc
    which = sublayer // 3 * 2 + sublayer % 3 // 2
    row0 = which * FT
    act_low = k.low_r
    raw = [k.arena[:, g * D:(g + 1) * D] for g in range(2)]
    split = [[k.weights_r[:, (2 + 2 * g + part) * D:(3 + 2 * g + part) * D] for part in range(2)] for g in range(2)]
    silu = [k.arena[:, 6 * D + b * T:6 * D + (b + 1) * T] for b in range(2)]
    assert 6 * D + 2 * T <= LOW
    with nc.cleanup_on_exit():
        s = Phase(nc)
        landed = [s.sem(f"ff_landed{g}") for g in range(2)]
        high_done, low_done, product, silu_done, act_done, act_high_done, act_low_done = (
            s.sem(n) for n in ("high_done", "low_done", "product", "silu_done", "act_done", "act_high_done",
                               "act_low_done"))
        tokens = tokens_of(k.h_r, k.h_low_ff, TX, T, HALF)
        pairs = FT // 2
        with nc.Block() as block:
            @block.sync
            def _(sp):
                for g in range(2):
                    sp.dma_start(raw[g], k.io["w_ff"][row0][:, g * D:(g + 1) * D]).then_inc(landed[g], 16)
                with sp.Fori(1, FT) as m:
                    for g in range(2):
                        sp.wait_ge(low_done, 2 * m + g - 1)
                        sp.dma_start(raw[g], k.io["w_ff"][bass.ds(row0 + m, 1)].rearrange("a p n -> (a p) n")
                                     [:, g * D:(g + 1) * D]).then_inc(landed[g], 16)

            @block.tensor
            def _(pe):
                def tile(b, m, first):
                    if not first:
                        pe.wait_ge(act_done, m - 1)
                    for g in range(2):
                        pe.wait_ge(low_done, 2 * m + g + 1)
                        high, low = split[g]
                        for kt in range(KT):
                            last = split_products(pe, k.psum_pair(2 * b + g), HALF, high[:, kt * P:(kt + 1) * P],
                                                  low[:, kt * P:(kt + 1) * P], tokens(kt), kt == 0, kt == KT - 1)
                        last.then_inc(product, 1)
                for b in range(2):
                    tile(b, b, True)
                with pe.Fori(1, pairs) as r:
                    for b in range(2):
                        tile(b, 2 * r + b, False)

            def halves(v):
                return v.rearrange("p (a t) -> p a t", a=2)

            @block.scalar
            def _(act):
                def high_parts(m, first=False):
                    for g in range(2):
                        act.wait_ge(landed[g], (m + 1) * 16)
                        if not first:
                            act.wait_ge(product, 2 * m + g - 1)
                        split_high(act, raw[g], split[g][0]).then_inc(high_done, 1)

                def activation(b, m, first):
                    act.wait_ge(product, 2 * m + 2)
                    if not first:
                        act.wait_ge(act_low_done, m - 1)
                    act.activation(halves(silu[b]), two_halves(k.psum_pair(2 * b), HALF), ACT.Silu)\
                        .then_inc(silu_done, 1)
                    act.wait_ge(act_done, m + 1)
                    split_high(act, silu[b], k.big_r[:, bass.ds(m * T, T)]).then_inc(act_high_done, 1)
                high_parts(0, True)
                high_parts(1)
                activation(0, 0, True)
                high_parts(2)
                activation(1, 1, True)
                with act.Fori(1, pairs - 1) as r:
                    for b in range(2):
                        high_parts(2 * r + b + 1)
                        activation(b, 2 * r + b, False)
                high_parts(FT - 1)
                activation(0, FT - 2, False)
                activation(1, FT - 1, False)

            @block.vector
            def _(dve):
                def low_parts(m):
                    for g in range(2):
                        dve.wait_ge(high_done, 2 * m + g + 1)
                        split_low(dve, raw[g], *split[g]).then_inc(low_done, 1)

                def activation(b, m):
                    dve.wait_ge(silu_done, m + 1)
                    dve.tensor_tensor(halves(silu[b]), halves(silu[b]), two_halves(k.psum_pair(2 * b + 1), HALF),
                                      ALU.mult).then_inc(act_done, 1)
                    dve.wait_ge(act_high_done, m + 1)
                    at = bass.ds(m * T, T)
                    split_low(dve, silu[b], k.big_r[:, at], act_low[:, at]).then_inc(act_low_done, 1)
                low_parts(0)
                with dve.Fori(0, pairs - 1) as r:
                    for b in range(2):
                        low_parts(2 * r + b + 1)
                        activation(b, 2 * r + b)
                low_parts(FT - 1)
                activation(0, FT - 2)
                activation(1, FT - 1)
    W = FT * P // 2
    room = k.big_buf[:, FT * T:]
    residual_product(k, k.io["w_down"], which * KT, FT, sublayer, tokens_of(k.big_r, act_low, T, T, HALF),
                     raw=[room[:, i * W:(i + 1) * W] for i in range(3)],
                     split=[[k.weights_r[:, (2 * i + part) * W:(2 * i + part + 1) * W] for part in range(2)]
                            for i in range(2)])


def mixer_output(k, weights, source, sublayer):
    at = 2 * KT * T
    split = k.low_r[:, at + 4 * D - LOW:]
    residual_product(k, weights, 0, KT, sublayer, tokens_of(k.mixed_r, k.mixed_r[:, KT * T:], T, T, HALF),
                     raw=[k.arena[:, at + i * D:at + (i + 1) * D] for i in range(4)],
                     split=[[split[:, (2 * i + part) * D:(2 * i + part + 1) * D] for part in range(2)] for i in range(2)],
                     source=source)


class Schedule:

    def __init__(self, phase, **steps):
        self.count = {e: {n: i + 1 for i, n in enumerate(names)} for e, names in steps.items()}
        for e, names in steps.items():
            assert len(set(names)) == len(names), (e, [n for n in names if names.count(n) > 1])
        self.sems = {e: phase.sem(f"{e}_steps") for e in steps}
        self.said = {e: 0 for e in steps}

    def did(self, engine, name):
        self.said[engine] += 1
        assert self.count[engine][name] == self.said[engine], (engine, name)
        return self.sems[engine], 1

    def after(self, engine, name):
        return self.sems[engine], self.count[engine][name]


class SplitWeights:

    def __init__(self, k, s, weights, tiles):
        self.k, self.weights, self.tiles = k, weights, tiles
        self.landed = [s.sem(f"in_landed{b}") for b in range(RAW_SLOTS)]
        self.high_done, self.low_done, self.product = (s.sem(n) for n in ("high_done", "low_done", "product"))
        at = lambda room, i: room[:, i * D:(i + 1) * D]
        self.raw = [at(k.arena, b) for b in range(RAW_SLOTS)]
        self.split = [[at(k.weights_r, RAW_SLOTS + 2 * b + part) for part in range(2)] for b in range(SPLIT_SLOTS)]

    def load(self, sp):
        rounds = self.tiles // RAW_SLOTS
        for b in range(RAW_SLOTS):
            sp.dma_start(self.raw[b], self.weights[b]).then_inc(self.landed[b], 16)
        with sp.Fori(1, rounds) as r:
            for b in range(RAW_SLOTS):
                sp.wait_ge(self.low_done, (r - 1) * RAW_SLOTS + b + 1)
                sp.dma_start(self.raw[b], self.weights[bass.ds(b + r * RAW_SLOTS, 1)]
                             .rearrange("a p n -> (a p) n")).then_inc(self.landed[b], 16)
        for b in range(self.tiles % RAW_SLOTS):
            sp.wait_ge(self.low_done, (rounds - 1) * RAW_SLOTS + b + 1)
            sp.dma_start(self.raw[b], self.weights[rounds * RAW_SLOTS + b]).then_inc(self.landed[b], 16)

    def high(self, act, raw_slot, split_slot, m, first=False):
        act.wait_ge(self.landed[raw_slot], (m - raw_slot) * (16 // RAW_SLOTS) + 16)
        if not first:
            act.wait_ge(self.product, m - 1)
        split_high(act, self.raw[raw_slot], self.split[split_slot][0]).then_inc(self.high_done, 1)

    def low(self, dve, raw_slot, split_slot, m):
        dve.wait_ge(self.high_done, m + 1)
        split_low(dve, self.raw[raw_slot], *self.split[split_slot]).then_inc(self.low_done, 1)

    def products(self, pe, tokens, width, evacuated):
        def tile(b, m, first=False):
            pe.wait_ge(self.low_done, m + 1)
            if not first:
                pe.wait_ge(evacuated, m - 3)
            high, low = self.split[b % SPLIT_SLOTS]
            for kt in range(KT):
                last = split_products(pe, self.k.psum_pair(b), width, high[:, kt * P:(kt + 1) * P],
                                      low[:, kt * P:(kt + 1) * P], tokens(kt), kt == 0, kt == KT - 1)
            last.then_inc(self.product, 1)
        for b in range(4):
            tile(b, b, first=True)
        with pe.Fori(1, self.tiles // 4) as r:
            for b in range(4):
                tile(b, 4 * r + b)
        for b in range(self.tiles % 4):
            tile(b, self.tiles // 4 * 4 + b)


def project_even(k):
    nc = k.nc
    NCONV, NMIX, NZ = 12, 14, 4
    TILES = NCONV + NMIX + NZ + 1
    with nc.cleanup_on_exit():
        s = Phase(nc)
        w = SplitWeights(k, s, k.io["w_in_even"], TILES)
        product, cleared, staged, tile_done, chain = w.product, *(
            s.sem(n) for n in ("cleared", "staged", "tile_done", "chain"))
        SW = PAD + TX + 5
        stage = [k.arena[:, PROJECTION_END + b * SW:PROJECTION_END + (b + 1) * SW] for b in range(2)]
        delta = k.arena[:, PROJECTION_END + 2 * SW:PROJECTION_END + 2 * SW + T]
        rows = k.rows
        with nc.Block() as block:
            @block.sync
            def _(sp):
                w.load(sp)

            @block.tensor
            def _(pe):
                w.products(pe, tokens_of(k.h_r, k.low_r[:, H_LOW - LOW:], TX, TX, HALFX), HALFX, staged)

            @block.scalar
            def _(act):
                def to_stage(b, pair, m, wait_free):
                    act.wait_ge(product, m + 1)
                    if wait_free is not None:
                        act.wait_ge(tile_done, wait_free)
                    act.activation(stage[b][:, PAD:PAD + TX].rearrange("p (a t) -> p a t", a=2),
                                   two_halves(k.psum_pair(pair), HALFX), ACT.Copy).then_inc(staged, 1)

                def compact(out, pair, rows_out):
                    ps = k.psum_pair(pair)[0:rows_out]
                    act.activation(out[0:rows_out, 0:HALFX], ps[:, 0, 0:HALFX], ACT.Copy)
                    act.activation(out[0:rows_out, HALFX:TP], ps[:, 1, 0:TP - HALFX], ACT.Copy)
                    return act.activation(
                        out[0:rows_out, TP:T].rearrange("p (s t) -> p s t", s=NSEQ),
                        ps[:, 1, TP - HALFX:HALFX].rearrange("p (s t) -> p s t", s=NSEQ)[:, :, PAD:], ACT.Copy)
                def high(b, m, first=False):
                    w.high(act, b % RAW_SLOTS, b % SPLIT_SLOTS, m, first)
                high(0, 0, True)
                high(1, 1, True)
                act.wait_ge(cleared, 2)
                for m in range(4):
                    high(m + 2, m + 2)
                    to_stage(m % 2, m, m, None if m < 2 else m - 1)
                with act.Fori(1, (NCONV + NMIX) // 4) as r:
                    for b in range(4):
                        high(b + 2, 4 * r + b + 2)
                        to_stage(b % 2, b, 4 * r + b, 4 * r + b - 1)
                for m in range((NCONV + NMIX) // 4 * 4, NCONV + NMIX):
                    high(m + 2, m + 2)
                    to_stage(m % 2, m % 4, m, m - 1)
                for i in range(NZ):
                    m = NCONV + NMIX + i
                    if m + 2 < TILES:
                        high(m + 2, m + 2)
                    act.wait_ge(product, m + 1)
                    compact(k.big_buf[:, (NCONV + i) * T:(NCONV + i + 1) * T], m % 4, P).then_inc(staged, 1)
                act.wait_ge(product, TILES)
                compact(rows, (TILES - 1) % 4, 64).then_inc(staged, 1)

            @block.vector
            def _(dve):
                for b in range(2):
                    dve.memset(stage[b][:, 0:PAD], 0.0).then_inc(cleared, 1)

                def views(b, shift):
                    return (stage[b][:, shift:shift + TP],
                            stage[b][:, PAD + TP:PAD + TX].rearrange("p (s t) -> p s t", s=NSEQ)
                            [:, :, shift:shift + TS])

                def conv(b, m):
                    dve.wait_ge(staged, m + 1)
                    out = k.big_buf[:, bass.ds(m * T, T)]
                    out_s = out[:, TP:T].rearrange("p (s t) -> p s t", s=NSEQ)
                    w = k.par("conv_w")[:, bass.ds(m * CONV_W, CONV_W)]
                    for j in range(CONV_W):
                        in_p, in_s = views(b, j)
                        if j == 0:
                            dve.tensor_scalar(out[:, 0:TP], in_p, w[:, 0:1], None, ALU.mult)
                            last = dve.tensor_scalar(out_s, in_s, w[:, 0:1], None, ALU.mult)
                        else:
                            dve.wait_ge(chain, m * (CONV_W - 1) + j)
                            dve.scalar_tensor_tensor(out=out[:, 0:TP], in0=in_p, scalar=w[:, j:j + 1],
                                                     in1=out[:, 0:TP], op0=ALU.mult, op1=ALU.add)
                            last = dve.scalar_tensor_tensor(out=out_s, in0=in_s, scalar=w[:, j:j + 1],
                                                            in1=out_s, op0=ALU.mult, op1=ALU.add)
                        if j < CONV_W - 1:
                            last.then_inc(chain, 1)
                        else:
                            last.then_inc(tile_done, 1)

                def mix(b, i):
                    dve.wait_ge(staged, NCONV + i + 1)
                    cur_p, cur_s = views(b, PAD)
                    prev_p, prev_s = views(b, PAD - 1)
                    out = k.big_buf[:, bass.ds((i + NCONV + NZ) * T, T)]
                    d_s = delta[:, TP:T].rearrange("p (s t) -> p s t", s=NSEQ)
                    dve.wait_ge(tile_done, NCONV + i)
                    dve.tensor_tensor(delta[:, 0:TP], prev_p, cur_p, ALU.subtract)
                    dve.tensor_tensor(d_s, prev_s, cur_s, ALU.subtract).then_inc(chain, 1)
                    dve.wait_ge(chain, NCONV * (CONV_W - 1) + i + 1)
                    mu = k.par("mu")[:, bass.ds(i, 1)]
                    dve.scalar_tensor_tensor(out=out[:, 0:TP], in0=delta[:, 0:TP], scalar=mu, in1=cur_p,
                                             op0=ALU.mult, op1=ALU.add)
                    dve.scalar_tensor_tensor(out=out[:, TP:T].rearrange("p (s t) -> p s t", s=NSEQ), in0=d_s,
                                             scalar=mu, in1=cur_s, op0=ALU.mult, op1=ALU.add)\
                        .then_inc(tile_done, 1)

                def low(b, m):
                    w.low(dve, b % RAW_SLOTS, b % SPLIT_SLOTS, m)
                low(0, 0)
                low(1, 1)
                with dve.Fori(0, NCONV // 4) as r:
                    for b in range(4):
                        low(b + 2, 4 * r + b + 2)
                        conv(b % 2, 4 * r + b)
                with dve.Fori(0, NMIX // 4) as r:
                    for b in range(4):
                        low(b + 2, NCONV + 4 * r + b + 2)
                        mix(b % 2, 4 * r + b)
                for i in range(NMIX // 4 * 4, NMIX):
                    low(NCONV + i + 2, NCONV + i + 2)
                    mix(i % 2, i)
                for m in range(NCONV + NMIX + 2, TILES):
                    low(m, m)


Q_A, K_A, V_A, Z_A, R_B, K_B, V_B, LR_B, G_B = 0, 4, 8, 12, 16, 20, 24, 28, 29
NEG_KK, KK_A = 0, 4
ROW_GC, ROW_BETA, ROW_TO_END, COL_BETA_GC = 0, 1, 2, 3


def prepare_even(k):
    nc = k.nc
    big = lambda t, n=1: k.big_buf[:, t * T:(t + n) * T]
    hb = lambda t, n=1: k.h[:, t * T:(t + n) * T]
    sq = lambda i: k.arena[:, i * T:(i + 1) * T]
    rate = lambda i: k.arena[:, (12 + i) * T:(13 + i) * T]
    spare = lambda i: k.arena[:, (16 + i) * T:(17 + i) * T]
    w2 = k.arena[:, 20 * T:20 * T + 512]
    neg = k.arena[:, 20 * T + 512:20 * T + 520]
    ea = k.arena[:, 20 * T + 520:20 * T + 521]
    softp = k.arena[0:4, 21 * T:22 * T]
    rows = k.rows
    N = range(12)
    act_steps = ([f"silu{i}" for i in range(4)] + ["tanh"] + [f"square{i}" for i in N]
                 + ["abs", "exp", "ln", "exp_a_log", "exp_b", "exp_g"]
                 + [f"exp_w{i}" for i in range(4)] + [f"exp_r{i}" for i in range(4)] + ["exp_to_end", "cols", "exp_gc"]
                 + [f"root{i}" for i in N])
    dve_steps = (["neg_w0", "neg_a0", "rows_b", "rows_clear"] + [f"kk_raw{i}" for i in range(4)]
                 + ["relu", "softplus", "g", "gc", "to_end_p", "to_end_s", "beta1", "beta", "sig1", "sig"]
                 + [f"{n}{i}" for i in range(4) for n in ("w1_", "w2_", "w3_", "lc")]
                 + [f"{n}{i}" for i in range(4) for n in ("r1_", "r2_", "t1_", "k")]
                 + ["beta_gc"]
                 + [f"{n}{i}" for i in N for n in ("inv", "unit")] + [f"kka{i}" for i in range(4)])
    with nc.cleanup_on_exit():
        s = Phase(nc)
        q = Schedule(s, act=act_steps, dve=dve_steps,
                     pe=[f"w{i}" for i in range(4)] + [f"r{i}" for i in range(4)] + ["cols"] + [f"sum{i}" for i in N])
        did, after = q.did, q.after
        loaded, kept = s.sem("w2_loaded"), s.sem("x_kept")
        with nc.Block() as block:
            @block.sync
            def _(sp):
                sp.dma_start(w2, k.io["w_wa2"]).then_inc(loaded, 16)
                sp.dma_start(k.x_kept, k.x).then_inc(kept, 16)
                sp.wait_ge(loaded, 16)
                sp.wait_ge(kept, 16)

            @block.scalar
            def _(act):
                for i in range(4):
                    act.activation(big(4 * i, 4), big(4 * i, 4), ACT.Silu).then_inc(*did("act", f"silu{i}"))
                act.activation(k.big_buf[0:64, LR_B * T:(LR_B + 1) * T], k.big_buf[0:64, LR_B * T:(LR_B + 1) * T],
                               ACT.Tanh).then_inc(*did("act", "tanh"))
                act.wait_ge(*after("act", "silu1"))
                for i in range(8):
                    act.activation(sq(i), big(Q_A + i), ACT.Square).then_inc(*did("act", f"square{i}"))
                for i in range(4):
                    act.wait_ge(*after("dve", f"kk_raw{i}"))
                    act.activation(sq(8 + i), hb(NEG_KK + i), ACT.Square).then_inc(*did("act", f"square{8 + i}"))
                act.wait_ge(*after("dve", "rows_b"))
                act.activation(softp, rows[0:4, :], ACT.Abs, bias=k.par("dt_bias")[0:4, :]).then_inc(*did("act", "abs"))
                act.wait_ge(*after("act", "abs"))
                act.activation(softp, softp, ACT.Exp, scale=-1.0).then_inc(*did("act", "exp"))
                act.wait_ge(*after("act", "exp"))
                act.activation(softp, softp, ACT.Ln, bias=1.0).then_inc(*did("act", "ln"))
                act.activation(ea[0:4, :], k.par("a_log")[0:4, :], ACT.Exp).then_inc(*did("act", "exp_a_log"))
                act.activation(k.rows_b[0:4, :], k.rows_b[0:4, :], ACT.Exp, scale=-1.0).then_inc(*did("act", "exp_b"))
                act.activation(big(G_B), big(G_B), ACT.Exp, scale=-1.0).then_inc(*did("act", "exp_g"))
                for n, first, sem_name in (("w", 0, "exp_w"), ("r", 4, "exp_r")):
                    for i in range(4):
                        act.wait_ge(*after("pe", f"{n}{i}"))
                        dst = spare(i) if n == "w" else rate(i)
                        act.activation(dst.rearrange("p (a t) -> p a t", a=2), two_halves(k.psum_pair(i), HALF),
                                       ACT.Exp, scale=-1.0, bias=neg[:, first + i:first + i + 1])\
                            .then_inc(*did("act", f"{sem_name}{i}"))
                act.wait_ge(*after("dve", "to_end_s"))
                act.activation(rows[64:68, :], rows[64:68, :], ACT.Exp).then_inc(*did("act", "exp_to_end"))
                act.wait_ge(*after("pe", "cols"))
                cols = k.cols.rearrange("p (c r h) -> p c r h", c=5, r=4)
                act.activation(cols[:, 0:4, 0:3], k.psum[0].rearrange("p (c r h) -> p c r h", c=4, r=4)
                               [:, :, 0:3, 0:4], ACT.Copy)
                act.activation(cols[0:64, 4, 0:3], k.psum[1][0:64, 0:128].rearrange("p (r h) -> p r h", r=4)
                               [:, 0:3, 0:4], ACT.Copy).then_inc(*did("act", "cols"))
                act.wait_ge(*after("act", "cols"))
                act.activation(cols[:, 0:4, 3], cols[:, 0:4, 0], ACT.Exp)
                act.activation(cols[0:64, 4, 3], cols[0:64, 4, 0], ACT.Exp).then_inc(*did("act", "exp_gc"))
                for i in N:
                    act.wait_ge(*after("pe", f"sum{i}"))
                    act.activation(sq(i).rearrange("p (a t) -> p a t", a=2), two_halves(k.psum_pair(1 + i % 3), HALF),
                                   ACT.Sqrt, bias=k.eps[:, 0:1]).then_inc(*did("act", f"root{i}"))

            @block.tensor
            def _(pe):
                pe.wait_ge(loaded, 16)
                pe.wait_ge(*after("act", "tanh"))
                for n, lo in (("w", 0), ("r", 64)):
                    for i in range(4):
                        if n == "r":
                            pe.wait_ge(*after("act", f"exp_w{i}"))
                        for a in range(2):
                            at = LR_B * T + a * HALF
                            last = pe.matmul(k.psum_pair(i)[:, a, 0:HALF], w2[lo:lo + 64, i * P:(i + 1) * P],
                                             k.big_buf[lo:lo + 64, at:at + HALF], start=True, stop=True)
                        last.then_inc(*did("pe", f"{n}{i}"))
                pe.wait_ge(*after("act", "exp_to_end"))
                pe.wait_ge(*after("dve", "beta"))
                pe.wait_ge(*after("act", "exp_r3"))
                for c in range(NCH):
                    pe.transpose(k.psum[0][:, c * P:(c + 1) * P], rows[:, c * P:(c + 1) * P], k.mask("ident"))
                pe.transpose(k.psum[1][0:64, 0:P], rows[:, TP:T], k.mask("ident")).then_inc(*did("pe", "cols"))
                for i in N:
                    pe.wait_ge(*after("act", f"square{i}"))
                    if i >= 3:
                        pe.wait_ge(*after("act", f"root{i - 3}"))
                    ones = k.mask("ones") if i < 8 else k.mask("block64")
                    for a in range(2):
                        last = pe.matmul(k.psum_pair(1 + i % 3)[:, a, 0:HALF], ones, sq(i)[:, a * HALF:(a + 1) * HALF],
                                         start=True, stop=True)
                    last.then_inc(*did("pe", f"sum{i}"))

            @block.vector
            def _(dve):
                dve.tensor_scalar(neg[:, 0:4], k.par("w0"), -1.0, None, ALU.mult).then_inc(*did("dve", "neg_w0"))
                dve.tensor_scalar(neg[:, 4:8], k.par("a0"), -1.0, None, ALU.mult).then_inc(*did("dve", "neg_a0"))
                dve.tensor_copy(k.rows_b[0:4, :], rows[32:36, :]).then_inc(*did("dve", "rows_b"))
                dve.wait_ge(*after("dve", "rows_b"))
                dve.memset(rows[32:64, :], 0.0)
                dve.memset(rows[64:128, :], 0.0).then_inc(*did("dve", "rows_clear"))
                for i in range(4):
                    dve.tensor_scalar(hb(NEG_KK + i), big(K_B + i), k.par("k_k")[:, i:i + 1], None, ALU.mult)\
                        .then_inc(*did("dve", f"kk_raw{i}"))
                dve.wait_ge(*after("act", "abs"))
                dve.tensor_scalar(rows[0:4, :], rows[0:4, :], k.par("dt_bias")[0:4, :], 0.0, ALU.add, ALU.max)\
                    .then_inc(*did("dve", "relu"))
                dve.wait_ge(*after("act", "exp_a_log"))
                dve.wait_ge(*after("dve", "relu"))
                dve.tensor_tensor(softp, rows[0:4, :], softp, ALU.add).then_inc(*did("dve", "softplus"))
                dve.wait_ge(*after("dve", "softplus"))
                dve.tensor_scalar(softp, softp, ea[0:4, :], -1.0, ALU.mult, ALU.mult).then_inc(*did("dve", "g"))
                dve.wait_ge(*after("dve", "g"))
                dve.tensor_tensor_scan(rows[0:4, :], k.resets[0:4, :], softp, 0.0, ALU.mult, ALU.add)\
                    .then_inc(*did("dve", "gc"))
                dve.wait_ge(*after("dve", "gc"))
                dve.wait_ge(*after("dve", "rows_clear"))
                for name, lo, hi, w in (("to_end_p", 0, TP, CH), ("to_end_s", TP, T, TS)):
                    v = rows[0:4, lo:hi].rearrange("p (c i) -> p c i", i=w)
                    dve.tensor_tensor(rows[64:68, lo:hi].rearrange("p (c i) -> p c i", i=w),
                                      v[:, :, w - 1:w].to_broadcast([4, (hi - lo) // w, w]), v, ALU.subtract)\
                        .then_inc(*did("dve", name))
                dve.wait_ge(*after("act", "exp_b"))
                dve.tensor_scalar(k.rows_b[0:4, :], k.rows_b[0:4, :], 1.0, None, ALU.add)\
                    .then_inc(*did("dve", "beta1"))
                dve.wait_ge(*after("dve", "beta1"))
                dve.reciprocal(rows[32:36, :], k.rows_b[0:4, :]).then_inc(*did("dve", "beta"))
                dve.wait_ge(*after("act", "exp_g"))
                dve.tensor_scalar(big(G_B), big(G_B), 1.0, None, ALU.add).then_inc(*did("dve", "sig1"))
                dve.wait_ge(*after("dve", "sig1"))
                dve.reciprocal(big(G_B), big(G_B)).then_inc(*did("dve", "sig"))
                for i in range(4):
                    w = spare(i)
                    dve.wait_ge(*after("act", f"exp_w{i}"))
                    dve.tensor_scalar(w, w, 1.0, None, ALU.add).then_inc(*did("dve", f"w1_{i}"))
                    dve.wait_ge(*after("dve", f"w1_{i}"))
                    dve.reciprocal(w, w).then_inc(*did("dve", f"w2_{i}"))
                    dve.wait_ge(*after("dve", f"w2_{i}"))
                    dve.tensor_scalar(w, w, NEG_E_HALF, None, ALU.mult).then_inc(*did("dve", f"w3_{i}"))
                    dve.wait_ge(*after("dve", f"w3_{i}"))
                    dve.tensor_tensor_scan(k.lc[:, i * T:(i + 1) * T], k.resets, w, 0.0, ALU.mult, ALU.add)\
                        .then_inc(*did("dve", f"lc{i}"))
                for i in range(4):
                    a = rate(i)
                    dve.wait_ge(*after("act", f"exp_r{i}"))
                    dve.tensor_scalar(a, a, 1.0, None, ALU.add).then_inc(*did("dve", f"r1_{i}"))
                    dve.wait_ge(*after("dve", f"r1_{i}"))
                    dve.reciprocal(a, a).then_inc(*did("dve", f"r2_{i}"))
                    dve.wait_ge(*after("dve", f"r2_{i}"))
                    dve.tensor_scalar(spare(i), a, 1.0, k.par("k_a")[:, i:i + 1], ALU.subtract, ALU.mult)\
                        .then_inc(*did("dve", f"t1_{i}"))
                    dve.wait_ge(*after("dve", f"t1_{i}"))
                    dve.scalar_tensor_tensor(out=big(K_B + i), in0=spare(i), scalar=1.0, in1=big(K_B + i),
                                             op0=ALU.add, op1=ALU.mult).then_inc(*did("dve", f"k{i}"))
                dve.wait_ge(*after("act", "exp_gc"))
                cols = k.cols.rearrange("p (c r h) -> p c r h", c=5, r=4)
                dve.tensor_tensor(cols[:, 0:4, 3], cols[:, 0:4, 3], cols[:, 0:4, 1], ALU.mult)
                dve.tensor_tensor(cols[0:64, 4, 3], cols[0:64, 4, 3], cols[0:64, 4, 1], ALU.mult)\
                    .then_inc(*did("dve", "beta_gc"))
                for i in N:
                    dve.wait_ge(*after("act", f"root{i}"))
                    dve.reciprocal(sq(i), sq(i)).then_inc(*did("dve", f"inv{i}"))
                    dve.wait_ge(*after("dve", f"inv{i}"))
                    x, scale = (big(Q_A + i), 128.0 ** -0.5 if i < 4 else 1.0) if i < 8 else (hb(NEG_KK + i - 8), -1.0)
                    dve.scalar_tensor_tensor(out=x, in0=x, scalar=scale, in1=sq(i), op0=ALU.mult, op1=ALU.mult)\
                        .then_inc(*did("dve", f"unit{i}"))
                for i in range(4):
                    dve.wait_ge(*after("dve", f"unit{8 + i}"))
                    dve.scalar_tensor_tensor(out=hb(KK_A + i), in0=hb(NEG_KK + i), scalar=-1.0, in1=rate(i),
                                             op0=ALU.mult, op1=ALU.mult).then_inc(*did("dve", f"kka{i}"))


def carve(region, at=0):
    def take(n):
        nonlocal at
        at += n
        assert at <= region.shape[-1], (at, region.shape)
        return region[:, at - n:at]
    return take


def heads4(ap, n):
    return ap.rearrange("p (h n) -> p h n", n=n)


STREAMS = 3
LEVELS = (16, 32, 64)


def inverse_jobs(sample):
    jobs = []
    G = range(STREAMS)
    for g in G:
        jobs += [(f"sq1_{g}", ("act", f"C1_{g}")), (f"sqt1_{g}", ("dve", f"CT1_{g}"))]
    for g in G:
        jobs += [(f"x1_{g}", ("dve", f"P1_{g}")), (f"sq2_{g}", ("act", f"B2_{g}"))]
        if not sample:
            jobs += [(f"sqt2_{g}", ("act", f"BT2_{g}"))]
    for g in G:
        jobs += [(f"x2_{g}", ("dve", f"P2_{g}"))]
        if not sample:
            jobs += [(f"sq3_{g}", ("act", f"C3_{g}"))]
    if sample:
        return jobs
    for g in G:
        jobs += [(f"x3_{g}", ("dve", f"P3_{g}"))]
    for w in LEVELS:
        for g in G:
            jobs += [(f"y{w}_{g}", ("act", f"Y{w}_{g}")), (f"tr{w}_{g}", ("dve", f"T{w}_{g}"))]
        for g in G:
            jobs += [(f"z{w}_{g}", ("dve", f"PZ{w}_{g}"))]
    return jobs


def even_jobs(sample):
    rw = [(f"{n}_{g}", ("dve", f"{n}m_{g}")) for g in (1, 2) for n in ("m", "mt", "rb", "ka", "kr")]
    jobs = [("R", ("act", "eR")), ("kk", ("dve", "M0")), ("kq", ("dve", "KQD")), ("mt_0", ("dve", "mtm_0"))] + rw + [
        ("vt", ("dve", "VB")), ("kt", ("dve", "KD")), ("rvt", ("act", "RVt")), ("rbt", ("act", "RBt")),
        ("rkt", ("act", "RKt"))]
    jobs += inverse_jobs(sample)
    if not sample:
        jobs += [("ks", ("dve", "W1")), ("rw_1", ("act", "RW_1")), ("rw_2", ("act", "RW_2")), ("u", ("act", "U")),
                 ("ru", ("dve", "RU")), ("o", ("act", "O")), ("s", ("dve", "S3")), ("ry", ("act", "RY")), ("rs", ("dve", "RS1"))]
    else:
        jobs += [("ko", ("act", "KO")), ("rko", ("act", "RKO")), ("kst", ("dve", "W1")), ("rwt", ("act", "RWt")),
                 ("rw", ("dve", "RW")), ("u", ("act", "U")), ("ru", ("act", "RU")), ("o", ("dve", "O")),
                 ("ry", ("dve", "RY"))]
        for h in range(4):
            jobs += [(f"s{h}a", ("dve", f"S{h}a")), (f"s{h}b", ("dve", f"S{h}b"))]
        jobs += [(f"rs{t}", ("dve", f"RS{t}")) for t in range(4)]
    return jobs


def even_chunks(k, sample):
    nc = k.nc
    n = NSEQ * TS if sample else CH
    chunks = [NCH] if sample else list(range(NCH))
    G = range(STREAMS)
    jobs1 = even_jobs(sample)
    names = lambda base, c: f"{base}@{c}"
    pe_steps, bank_freed_by = [], []
    act_steps, dve_steps = [], []
    inv_act = lambda: [f"C1_{g}" for g in G] + [x for g in G for x in ([f"B2_{g}"] if sample else [f"B2_{g}", f"BT2_{g}"])]
    for c in chunks:
        pe_steps += [names(j, c) for j, _ in jobs1]
        bank_freed_by += [(e, names(st, c)) for _, (e, st) in jobs1]
        a = ["eR", "DT", "D", "E"] + ([] if sample else ["exp_ref"]) + ["exp_E", "RVt", "RBt", "RKt"] + inv_act()
        d = ["d", "dU", "dL", "Et", "Eref", "Aq", "Rq", "Bq", "Kq"] + (["k_copy"] if sample else []) \
            + ["M0", "M1", "M2", "KQD"]
        d += ["mtm_0", "P0_0"]
        d += [f"{x}_{g}" for g in (1, 2) for x in ("mm", "mtm", "rbm", "kam", "krm", "P0")]
        d += ["VB", "KD", "QG"]
        if sample:
            a += ["KO", "RKO", "RWt", "U", "RU"]
            d += [f"CT1_{g}" for g in G] + [f"P1_{g}" for g in G] + [f"P2_{g}" for g in G]
            d += ["W1", "W2", "RW"] + ["O", "RY"]
            for h in range(4):
                d += [f"Um{h}", f"Sg{h}", f"S{h}a", f"S{h}b"]
            for t in range(4):
                d += [f"RUm{t}", f"RVm{t}", f"RS{t}", f"RSd{t}"]
        else:
            a += [f"C3_{g}" for g in G] + [f"Y{w}_{g}" for w in LEVELS for g in G] + ["RW_1", "RW_2", "U", "O", "RY"]
            d += [f"B_{g}" for g in G] + [f"CT1_{g}" for g in G] + [f"P1_{g}" for g in G] + [f"P2_{g}" for g in G] \
                + [f"P3_{g}" for g in G]
            for w in LEVELS:
                d += [f"T{w}_{g}" for g in G] + [f"PZ{w}_{g}" for g in G]
            d += ["S0s", "W1", "W2", "RU", "S1", "S3", "RS1", "RSn"]
        act_steps += [names(x, c) for x in a]
        dve_steps += [names(x, c) for x in d]
    pool_steps = [] if sample else [names(f"Ms{w}_{g}", c) for c in chunks for w in LEVELS for g in G]

    take = carve(k.work[:, 0:WORK - 4 * T])
    H = 4 * n
    new = lambda cols=H: take(cols)
    eR, KQD = new(), new()
    qg, KD, W, U = (None,) * 4 if sample else (new() for _ in range(4))
    Em = take(4 * (n + 1) if not sample else 4 * NSEQ * (TS + 1))
    AR, BK = take(2 * H), take(2 * H)
    Vt, Bt, Kt = take(512), take(512), take(512)
    if sample:
        Wd, Ud = take(512), take(512)
        KDt, VBt = take(512), take(512)
    else:
        Wd, Ud, KDt, VBt = W, U, KD, take(512)
    RW, RU = take(512), take(512)
    KA, KR, RB = ([None, new(), new()] for _ in range(3))
    A, B, BT, C, CT, Pt = ([new() for _ in G] for _ in range(6))
    Dm, DT, En = C[0], CT[0], C[1]
    if sample:
        S = take(32 * P)
        RS = take(4 * NSEQ * 64)
        KQg = take(2 * H)
        KO, RKO = take(2 * H), take(2 * H)
        RUw, RVw = take(1024), take(1024)
        Uw = RUw
    else:
        S, RS, S0s = take(512), take(256), take(256)
        eref = take(4)
    mask = lambda nm, part=n: k.mask(nm)[0:part, 0:n]
    bc = lambda m: m[:, None, :].to_broadcast([n, 4, n])
    v4 = lambda ap, part=P: ap[0:part].rearrange("p (h n) -> p h n", h=4)
    sfx = "8" if sample else ""

    with nc.cleanup_on_exit():
        ph = Phase(nc)
        sched = Schedule(ph, pe=pe_steps, act=act_steps, dve=dve_steps, pool=pool_steps)
        job_number = {j: i for i, j in enumerate(pe_steps)}
        states_in, states_out, zeroed = ph.sem("states_in"), ph.sem("states_out"), ph.sem("zeroed")

        def bank(job, c):
            return k.psum[job_number[names(job, c)] % 8]

        def tokens(t, c, count=4):
            return k.big_buf[:, t * T:(t + count) * T].rearrange("p (h t) -> p h t", t=T)[:, :, c * CH:c * CH + n]

        def htokens(t, c, count=4):
            return k.h[:, t * T:(t + count) * T].rearrange("p (h t) -> p h t", t=T)[:, :, c * CH:c * CH + n]

        def col(c, r):
            v = k.cols[0:n].rearrange("p (c r h) -> p c r h", c=5, r=4)[:, c, r, :]
            return lambda w: v[:, :, None].to_broadcast([n, 4, w])

        with nc.Block() as block:
            @block.sync
            def _(sp):
                if sample:
                    sp.dma_start(S, k.io["delta_in"]).then_inc(states_in, 16)
                    sp.dma_start(RS, k.io["rwkv_in"]).then_inc(states_in, 16)
                    sp.wait_ge(*sched.after("dve", names("S3b", NCH)))
                    sp.dma_start(k.io["delta_s_out"], S).then_inc(states_out, 16)
                    sp.wait_ge(*sched.after("dve", names("RSd3", NCH)))
                    sp.dma_start(k.io["rwkv_s_out"], RS).then_inc(states_out, 16)
                else:
                    sp.wait_ge(*sched.after("dve", names("S3", NCH - 1)))
                    sp.dma_start(k.io["delta_p_out"], S).then_inc(states_out, 16)
                    sp.wait_ge(*sched.after("dve", names("RSn", NCH - 1)))
                    sp.dma_start(k.io["rwkv_p_out"], RS).then_inc(states_out, 16)
                sp.wait_ge(states_out, 32)

            @block.gpsimd
            def _(pool):
                if not sample:
                    pool.memset(S, 0.0).then_inc(zeroed, 1)
                    pool.memset(RS, 0.0).then_inc(zeroed, 1)
                    for c in chunks:
                        after = lambda e, nm: sched.after(e, names(nm, c))
                        for w, dst, free in ((16, CT, "sqt2"), (32, BT, "sq3"), (64, B, None)):
                            for g in G:
                                if free:
                                    pool.wait_ge(*after("pe", f"{free}_{g}"))
                                else:
                                    pool.wait_ge(*after("pe", f"z16_{g}"))
                                pool.tensor_tensor(v4(dst[g]), v4(A[g]), bc(k.mask(f"level{w}")), ALU.mult)\
                                    .then_inc(*sched.did("pool", names(f"Ms{w}_{g}", c)))

            @block.tensor
            def _(pe):
                for c in chunks:
                    after = lambda e, nm: sched.after(e, names(nm, c))

                    def claim(job):
                        i = job_number[names(job, c)]
                        if i >= 8:
                            pe.wait_ge(*sched.after(*bank_freed_by[i - 8]))
                        return bank(job, c)

                    def done(job, ins):
                        ins.then_inc(*sched.did("pe", names(job, c)))

                    def four(job, lhsT, rhs, out_part=n, width=n):
                        b = claim(job)
                        for h in range(4):
                            last = pe.matmul(b[0:out_part, h * width:(h + 1) * width], lhsT(h), rhs(h),
                                             start=True, stop=True)
                        done(job, last)

                    def four_transposes(job, source, cols=P):
                        b = claim(job)
                        for h in range(4):
                            src = source(h)
                            last = pe.transpose(b[0:src.shape[1], h * cols:(h + 1) * cols], src,
                                                k.mask("ident")[0:src.shape[0], 0:src.shape[0]])
                        done(job, last)

                    def of(buf, w=n, part=n):
                        return lambda h: buf[0:part, h * w:(h + 1) * w]

                    kc, qc, vc = (tokens(t, c) for t in (K_A, Q_A, V_A))
                    def place(g, h):
                        return h, 64 * (g - 1)

                    def ar(g, h, which):
                        t, p = place(g, h)
                        return AR[p:p + 64, (2 * t + which) * n:(2 * t + which + 1) * n]

                    def bk(g, h, which):
                        t, p = place(g, h)
                        return BK[p:p + 64, (2 * t + which) * n:(2 * t + which + 1) * n]

                    b = claim("R")
                    for h in range(4):
                        last = pe.matmul(b[:, h * n:(h + 1) * n], k.select(h)[0:4],
                                         k.rows[0:4, c * CH:c * CH + n], start=True, stop=True)
                    done("R", last)
                    four("kk", lambda h: kc[:, h], lambda h: kc[:, h])
                    four("kq", lambda h: kc[:, h], lambda h: qc[:, h])
                    pe.wait_ge(*after("dve", "M2"))
                    four_transposes("mt_0", lambda h: A[0][0:n, h * n:(h + 1) * n], n)
                    pe.wait_ge(*after("dve", "Kq"))
                    for g in (1, 2):
                        four(f"m_{g}", lambda h: ar(g, h, 0), lambda h: bk(g, h, 0))
                        four(f"mt_{g}", lambda h: bk(g, h, 0), lambda h: ar(g, h, 0))
                        four(f"rb_{g}", lambda h: bk(g, h, 0), lambda h: ar(g, h, 1))
                        four(f"ka_{g}", lambda h: bk(g, h, 1), lambda h: ar(g, h, 0))
                        four(f"kr_{g}", lambda h: bk(g, h, 1), lambda h: ar(g, h, 1))
                    four_transposes("vt", lambda h: vc[:, h])
                    four_transposes("kt", lambda h: kc[:, h])
                    rv = tokens(V_B, c)
                    four_transposes("rvt", lambda h: rv[:, h])
                    four_transposes("rbt", lambda h: BK[:, 2 * h * n:(2 * h + 1) * n])
                    four_transposes("rkt", lambda h: BK[:, (2 * h + 1) * n:(2 * h + 2) * n])

                    Bs = A if sample else B
                    for g in G:
                        pe.wait_ge(*after("dve", f"P0_{g}"))
                        if not sample:
                            pe.wait_ge(*after("dve", f"B_{g}"))
                        four(f"sq1_{g}", of(BT[g]), of(Bs[g]))
                        four(f"sqt1_{g}", of(Bs[g]), of(BT[g]))
                    for g in G:
                        pe.wait_ge(*after("act", f"C1_{g}"))
                        pe.wait_ge(*after("dve", f"CT1_{g}"))
                        four(f"x1_{g}", of(C[g]), of(Pt[g]))
                        four(f"sq2_{g}", of(CT[g]), of(C[g]))
                        if not sample:
                            four(f"sqt2_{g}", of(C[g]), of(CT[g]))
                    for g in G:
                        pe.wait_ge(*after("dve", f"P1_{g}"))
                        pe.wait_ge(*after("act", f"B2_{g}" if sample else f"BT2_{g}"))
                        four(f"x2_{g}", of(B[g]), of(Pt[g]))
                        if not sample:
                            four(f"sq3_{g}", of(BT[g]), of(B[g]))
                    if not sample:
                        for g in G:
                            pe.wait_ge(*after("act", f"C3_{g}"))
                            pe.wait_ge(*after("dve", f"P2_{g}"))
                            four(f"x3_{g}", of(C[g]), of(Pt[g]))
                        before = "P3"
                        for w, Ms, Tb in ((16, CT, B), (32, BT, CT), (64, B, CT)):
                            for g in G:
                                pe.wait_ge(*after("pool", f"Ms{w}_{g}"))
                                pe.wait_ge(*after("dve", f"{before}_{g}"))
                                four(f"y{w}_{g}", of(Ms[g]), of(Pt[g]))
                                four_transposes(f"tr{w}_{g}", of(Pt[g]), n)
                            for g in G:
                                pe.wait_ge(*after("act", f"Y{w}_{g}"))
                                pe.wait_ge(*after("dve", f"T{w}_{g}"))
                                four(f"z{w}_{g}", of(Tb[g]), of(C[g]))
                            before = f"PZ{w}"

                    last_p = "P2" if sample else "PZ64"

                    def rwkv_u():
                        for g in (1, 2):
                            pe.wait_ge(*after("dve", f"{last_p}_{g}"))
                        b = claim("ru")
                        for g in (1, 2):
                            for h in range(4):
                                hd = 2 * h + g - 1
                                last = pe.matmul(b[0:n, hd * 64:(hd + 1) * 64], Pt[g][0:n, h * n:(h + 1) * n],
                                                 RW[0:n, hd * 64:(hd + 1) * 64], start=True, stop=True)
                        done("ru", last)

                    def head_place(hd):
                        return hd // 2, 64 * (hd % 2), hd % 2 + 1, hd // 2

                    if not sample:
                        if c == 0:
                            pe.wait_ge(zeroed, 2)
                        else:
                            pe.wait_ge(*sched.after("dve", names("S3", c - 1)))
                        four("ks", lambda h: kc[:, h], lambda h: S[:, h * P:(h + 1) * P])
                        pe.wait_ge(*after("dve", "S0s"))
                        pe.wait_ge(*after("act", "RVt"))
                        for g in (1, 2):
                            b = claim(f"rw_{g}")
                            for h in range(4):
                                out = b[:, h * 64:(h + 1) * 64]
                                t, p = place(g, h)
                                hd = 2 * h + g - 1
                                pe.matmul(out, ar(g, h, 0), S0s[p:p + 64, t * 64:(t + 1) * 64],
                                          start=True, stop=False)
                                last = pe.matmul(out, KA[g][:, h * n:(h + 1) * n], Vt[:, hd * 64:(hd + 1) * 64],
                                                 start=False, stop=True)
                            done(f"rw_{g}", last)
                        pe.wait_ge(*after("dve", "W2"))
                        four("u", of(Pt[0]), lambda h: W[:, h * P:(h + 1) * P], width=P)
                        pe.wait_ge(*after("act", "RW_2"))
                        rwkv_u()
                        pe.wait_ge(*after("act", "U"))
                        pe.wait_ge(*after("dve", "QG"))
                        b = claim("o")
                        for h in range(4):
                            out = b[:, h * n:(h + 1) * n]
                            pe.matmul(out, S[:, h * P:(h + 1) * P], qg[:, h * n:(h + 1) * n], start=True, stop=False)
                            last = pe.matmul(out, U[:, h * P:(h + 1) * P], KQD[:, h * n:(h + 1) * n],
                                             start=False, stop=True)
                        done("o", last)
                        four("s", lambda h: KD[:, h * P:(h + 1) * P], lambda h: U[:, h * P:(h + 1) * P],
                             out_part=P, width=P)
                        pe.wait_ge(*after("dve", "RU"))
                        b = claim("ry")
                        for hd in range(8):
                            t, p, g, h = head_place(hd)
                            out = b[p:p + 64, t * n:(t + 1) * n]
                            hc = slice(hd * 64, (hd + 1) * 64)
                            pe.matmul(out, RU[:, hc], RB[g][:, h * n:(h + 1) * n], start=True, stop=False)
                            pe.matmul(out, Vt[:, hc], KR[g][:, h * n:(h + 1) * n], start=False, stop=False)
                            last = pe.matmul(out, S0s[p:p + 64, t * 64:(t + 1) * 64], ar(g, h, 1),
                                             start=False, stop=True)
                        done("ry", last)
                        b = claim("rs")
                        for hd in range(8):
                            t, p, g, h = head_place(hd)
                            out = b[p:p + 64, t * 64:(t + 1) * 64]
                            hc = slice(hd * 64, (hd + 1) * 64)
                            pe.matmul(out, Bt[:, hc], RU[:, hc], start=True, stop=False)
                            last = pe.matmul(out, Kt[:, hc], Vt[:, hc], start=False, stop=True)
                        done("rs", last)
                    else:
                        pe.wait_ge(states_in, 32)
                        pe.wait_ge(*after("dve", "QG"))
                        b = claim("ko")
                        out4 = b.rearrange("p (h a t) -> p h a t", h=4, a=2)
                        in4 = KQg.rearrange("p (h a t) -> p h a t", h=4, a=2)
                        S4 = S.rearrange("p (h s v) -> p h s v", h=4, s=NSEQ)
                        for h in range(4):
                            for q in range(NSEQ):
                                last = pe.matmul(out4[:, h, :, q * TS:(q + 1) * TS], S4[:, h, q],
                                                 in4[:, h, :, q * TS:(q + 1) * TS], start=True, stop=True)
                        done("ko", last)
                        b = claim("rko")
                        out4 = b.rearrange("p (t a i) -> p t a i", t=4, a=2)
                        in4 = AR.rearrange("p (t a i) -> p t a i", t=4, a=2)
                        S4 = RS.rearrange("p (t s v) -> p t s v", t=4, s=NSEQ)
                        for hd in range(8):
                            t, p, g, h = head_place(hd)
                            for q in range(NSEQ):
                                last = pe.matmul(out4[p:p + 64, t, :, q * TS:(q + 1) * TS], S4[p:p + 64, t, q],
                                                 in4[p:p + 64, t, :, q * TS:(q + 1) * TS], start=True, stop=True)
                        done("rko", last)
                        pe.wait_ge(*after("act", "RKO"))
                        ko4 = KO.rearrange("p (h a t) -> p h a t", h=4, a=2)
                        rko4 = RKO.rearrange("p (t a i) -> p t a i", t=4, a=2)
                        four_transposes("kst", lambda h: ko4[:, h, 0])
                        four_transposes("rwt", lambda h: rko4[:, h, 0])
                        b = claim("rw")
                        for hd in range(8):
                            t, p, g, h = head_place(hd)
                            last = pe.matmul(b[0:n, hd * 64:(hd + 1) * 64], KA[g][0:n, h * n:(h + 1) * n],
                                             Vt[0:n, hd * 64:(hd + 1) * 64], start=True, stop=True)
                        done("rw", last)
                        pe.wait_ge(*after("dve", "W2"))
                        four("u", of(Pt[0]), lambda h: Wd[0:n, h * P:(h + 1) * P], width=P)
                        pe.wait_ge(*after("dve", "RW"))
                        rwkv_u()
                        pe.wait_ge(*after("act", "U"))
                        four("o", lambda h: Ud[0:n, h * P:(h + 1) * P], lambda h: KQD[0:n, h * n:(h + 1) * n], out_part=P)
                        pe.wait_ge(*after("act", "RU"))
                        b = claim("ry")
                        for hd in range(8):
                            t, p, g, h = head_place(hd)
                            out = b[p:p + 64, t * n:(t + 1) * n]
                            hc = slice(hd * 64, (hd + 1) * 64)
                            pe.matmul(out, RU[0:n, hc], RB[g][0:n, h * n:(h + 1) * n], start=True, stop=False)
                            last = pe.matmul(out, Vt[0:n, hc], KR[g][0:n, h * n:(h + 1) * n], start=False, stop=True)
                        done("ry", last)
                        for h in range(4):
                            pe.wait_ge(*after("dve", f"Um{h}"))
                            for part in range(2):
                                b = claim(f"s{h}{'ab'[part]}")
                                done(f"s{h}{'ab'[part]}",
                                     pe.matmul(b[:, :], KDt[0:n, h * P:(h + 1) * P],
                                               Uw[0:n, part * 512:(part + 1) * 512], start=True, stop=True))
                        for t in range(4):
                            pe.wait_ge(*after("dve", f"RVm{t}"))
                            b = claim(f"rs{t}")
                            for half in range(2):
                                hc = slice((2 * t + half) * 64, (2 * t + half + 1) * 64)
                                out = b[half * 64:half * 64 + 64, :]
                                pe.matmul(out, Bt[0:n, hc], RUw[0:n, half * 512:(half + 1) * 512],
                                          start=True, stop=False)
                                last = pe.matmul(out, Kt[0:n, hc], RVw[0:n, half * 512:(half + 1) * 512],
                                                 start=False, stop=True)
                            done(f"rs{t}", last)

            @block.scalar
            def _(act):
                for c in chunks:
                    after = lambda e, nm: sched.after(e, names(nm, c))
                    did = lambda nm: sched.did("act", names(nm, c))
                    prev = lambda e, nm: sched.after(e, names(nm, c - 1))
                    psum = lambda job, part=n: bank(job, c)[0:part]

                    def copy(step, job, dst, part=n, cols=H):
                        act.wait_ge(*after("pe", job))
                        act.activation(dst[0:part, 0:cols], psum(job, part)[:, 0:cols], ACT.Copy).then_inc(*did(step))

                    act.wait_ge(*after("pe", "R"))
                    act.wait_ge(*after("dve", "d"))
                    act.activation(eR[:, 0:H], psum("R", P)[:, 0:H], ACT.Exp).then_inc(*did("eR"))
                    act.wait_ge(*after("dve", "dU"))
                    act.activation(DT[0:n], DT[0:n], ACT.Exp).then_inc(*did("DT"))
                    act.wait_ge(*after("dve", "dL"))
                    act.activation(Dm[0:n], Dm[0:n], ACT.Exp, scale=-1.0).then_inc(*did("D"))
                    act.wait_ge(*after("dve", "Eref"))
                    if sample:
                        e = Em.rearrange("p (b i) -> p b i", i=TS + 1)
                        act.activation(En.rearrange("p (b i) -> p b i", i=TS), e[:, :, 1:], ACT.Exp, scale=-1.0)\
                            .then_inc(*did("E"))
                    else:
                        e = Em.rearrange("p (t i) -> p t i", t=4)
                        act.activation(v4(En), e[:, :, 1:], ACT.Exp, scale=-1.0).then_inc(*did("E"))
                        act.activation(eref.rearrange("p (t i) -> p t i", t=4), e[:, :, 0:1], ACT.Exp, scale=-1.0)\
                            .then_inc(*did("exp_ref"))
                    act.wait_ge(*after("act", "E" if sample else "exp_ref"))
                    act.activation(Em, Em, ACT.Exp).then_inc(*did("exp_E"))
                    copy("RVt", "rvt", Vt, cols=512)
                    copy("RBt", "rbt", Bt, cols=512)
                    copy("RKt", "rkt", Kt, cols=512)
                    for g in G:
                        if g == 0:
                            act.wait_ge(*after("dve", "KQD"))
                            act.wait_ge(*after("dve", "M0"))
                        if g == 1:
                            act.wait_ge(*after("dve", "Kq"))
                        copy(f"C1_{g}", f"sq1_{g}", C[g])
                    for g in G:
                        copy(f"B2_{g}", f"sq2_{g}", B[g])
                        if not sample:
                            copy(f"BT2_{g}", f"sqt2_{g}", BT[g])
                    if not sample:
                        for g in G:
                            copy(f"C3_{g}", f"sq3_{g}", C[g])
                        for w in LEVELS:
                            for g in G:
                                copy(f"Y{w}_{g}", f"y{w}_{g}", C[g])
                        for g in (1, 2):
                            act.wait_ge(*after("pe", f"rw_{g}"))
                            act.activation(RW.rearrange("p (h g v) -> p h g v", h=4, g=2)[:, :, g - 1],
                                           v4(psum(f"rw_{g}")[:, 0:256]), ACT.Copy).then_inc(*did(f"RW_{g}"))
                        copy("U", "u", U, cols=512)
                        act.wait_ge(*after("pe", "o"))
                        act.activation(tokens(Q_A, c), v4(psum("o", P)), ACT.Copy).then_inc(*did("O"))
                        act.wait_ge(*after("pe", "ry"))
                        act.activation(htokens(NEG_KK, c), v4(psum("ry", P)), ACT.Copy).then_inc(*did("RY"))
                    else:
                        copy("KO", "ko", KO, part=P, cols=512)
                        copy("RKO", "rko", RKO, part=P, cols=512)
                        copy("RWt", "rwt", RW, cols=512)
                        copy("U", "u", Ud, cols=512)
                        copy("RU", "ru", RU, cols=512)

            @block.vector
            def _(dve):
                for c in chunks:
                    after = lambda e, nm: sched.after(e, names(nm, c))
                    did = lambda nm: sched.did("dve", names(nm, c))
                    psum = lambda job, part=n: bank(job, c)[0:part]
                    if c > chunks[0]:
                        dve.wait_ge(*sched.after("pe", names("rs", c - 1)))
                        dve.wait_ge(*sched.after("act", names("RY", c - 1)))
                        dve.wait_ge(*sched.after("dve", names("RSn", c - 1)))
                    dve.wait_ge(*after("pe", "R"))
                    dve.tensor_tensor(v4(Dm, n), v4(psum("R")[:, 0:H], n), col(c, ROW_GC)(n), ALU.subtract)\
                        .then_inc(*did("d"))
                    dve.wait_ge(*after("dve", "d"))
                    big = lambda nm: k.big(nm)[0:n, 0:n][:, None, :].to_broadcast([n, 4, n])
                    dve.tensor_tensor(v4(DT, n), v4(Dm, n), big("not_above_eq" + sfx), ALU.subtract)\
                        .then_inc(*did("dU"))
                    dve.wait_ge(*after("dve", "dU"))
                    dve.tensor_tensor(v4(Dm, n), v4(Dm, n), big("not_below" + sfx), ALU.add).then_inc(*did("dL"))
                    if sample:
                        lcs = k.lc.rearrange("p (t i) -> p t i", t=4)[:, :, TP:T].rearrange("p t (s i) -> p t s i", s=NSEQ)
                        E4 = Em.rearrange("p (t s i) -> p t s i", t=4, s=NSEQ)
                        dve.memset(Em, 0.0).then_inc(*did("Et"))
                        dve.wait_ge(*after("dve", "Et"))
                        dve.tensor_copy(E4[:, :, :, 1:], lcs).then_inc(*did("Eref"))
                        E0, E1 = E4[:, :, :, 0:TS], E4[:, :, :, 1:]
                        v = lambda ap: ap.rearrange("p t (s i) -> p t s i", s=NSEQ)
                    else:
                        lcc = k.lc.rearrange("p (t i) -> p t i", t=4)[:, :, c * CH:(c + 1) * CH]
                        mid = lcc[:, :, CH // 2 - 1:CH // 2]
                        E4 = Em.rearrange("p (t i) -> p t i", t=4)
                        dve.tensor_tensor(E4[:, :, 1:], lcc, mid.to_broadcast([P, 4, CH]), ALU.subtract)\
                            .then_inc(*did("Et"))
                        dve.tensor_scalar(E4[:, :, 0:1], mid, -1.0, None, ALU.mult).then_inc(*did("Eref"))
                        E0, E1 = E4[:, :, 0:n], E4[:, :, 1:]
                        v = lambda ap: ap
                    dve.wait_ge(*after("act", "exp_E"))
                    ar4 = AR.rearrange("p (t a i) -> p t a i", t=4, a=2)
                    bk4 = BK.rearrange("p (t a i) -> p t a i", t=4, a=2)
                    dve.tensor_tensor(v(ar4[:, :, 0]), v(htokens(NEG_KK, c)), E0, ALU.mult).then_inc(*did("Aq"))
                    dve.tensor_tensor(v(ar4[:, :, 1]), v(tokens(R_B, c)), E1, ALU.mult).then_inc(*did("Rq"))
                    dve.tensor_tensor(bk4[:, :, 0], htokens(KK_A, c), v4(En), ALU.mult).then_inc(*did("Bq"))
                    dve.tensor_tensor(bk4[:, :, 1], tokens(K_B, c), v4(En), ALU.mult).then_inc(*did("Kq"))
                    if sample:
                        kq4 = KQg.rearrange("p (h a t) -> p h a t", h=4, a=2)
                        dve.tensor_copy(kq4[:, :, 0], tokens(K_A, c)).then_inc(*did("k_copy"))
                    dve.wait_ge(*after("pe", "kk"))
                    dve.wait_ge(*after("act", "D"))
                    dve.tensor_tensor(v4(A[0], n), v4(psum("kk")[:, 0:H], n), v4(Dm, n), ALU.mult).then_inc(*did("M0"))
                    dve.wait_ge(*after("dve", "M0"))
                    dve.tensor_tensor(v4(A[0], n), v4(A[0], n), col(c, ROW_BETA)(n), ALU.mult).then_inc(*did("M1"))
                    dve.wait_ge(*after("dve", "M1"))
                    dve.tensor_scalar(A[0][0:n], A[0][0:n], -1.0, None, ALU.mult).then_inc(*did("M2"))
                    dve.wait_ge(*after("pe", "kq"))
                    dve.tensor_tensor(v4(KQD, n), v4(psum("kq")[:, 0:H], n), v4(DT, n), ALU.mult).then_inc(*did("KQD"))

                    def masked(step, job, dst, mask_name):
                        dve.wait_ge(*after("pe", job))
                        dve.tensor_tensor(v4(dst, n), v4(psum(job)[:, 0:H], n), bc(mask(mask_name)), ALU.mult)\
                            .then_inc(*did(step))

                    def start_inverse(g):
                        dve.wait_ge(*after("dve", f"mtm_{g}"))
                        dve.tensor_tensor(v4(Pt[g], n), v4(BT[g], n), bc(mask("ident")), ALU.add).then_inc(*did(f"P0_{g}"))
                    masked("mtm_0", "mt_0", BT[0], "block8" if sample else "block16")
                    start_inverse(0)
                    for g in (1, 2):
                        masked(f"mm_{g}", f"m_{g}", A[g], "below" + sfx)
                        masked(f"mtm_{g}", f"mt_{g}", BT[g], "above8" if sample else "above16")
                        masked(f"rbm_{g}", f"rb_{g}", RB[g], "above_eq" + sfx)
                        masked(f"kam_{g}", f"ka_{g}", KA[g], "above" + sfx)
                        masked(f"krm_{g}", f"kr_{g}", KR[g], "above_eq" + sfx)
                        start_inverse(g)
                    dve.wait_ge(*after("pe", "vt"))
                    dve.tensor_tensor(v4(VBt, n), v4(psum("vt"), n), col(c, ROW_BETA)(P), ALU.mult).then_inc(*did("VB"))
                    dve.wait_ge(*after("pe", "kt"))
                    dve.tensor_tensor(v4(KDt, n), v4(psum("kt"), n), col(c, ROW_TO_END)(P), ALU.mult).then_inc(*did("KD"))
                    dve.wait_ge(*after("act", "eR"))
                    qg_out = KQg.rearrange("p (h a t) -> p h a t", h=4, a=2)[:, :, 1] if sample else v4(qg)
                    dve.tensor_tensor(qg_out, tokens(Q_A, c), v4(eR), ALU.mult).then_inc(*did("QG"))

                    def plus(step, job, g):
                        dve.wait_ge(*after("pe", job))
                        dve.tensor_tensor(Pt[g][0:n], Pt[g][0:n], psum(job)[:, 0:H], ALU.add).then_inc(*did(step))

                    def copy(step, job, dst, part=n, cols=H):
                        dve.wait_ge(*after("pe", job))
                        dve.tensor_copy(dst[0:part, 0:cols], psum(job, part)[:, 0:cols]).then_inc(*did(step))
                    if not sample:
                        for g in G:
                            dve.wait_ge(*after("dve", "M2" if g == 0 else f"mm_{g}"))
                            dve.tensor_tensor(v4(B[g], n), v4(A[g], n), bc(mask("block16")), ALU.mult)\
                                .then_inc(*did(f"B_{g}"))
                    for g in G:
                        copy(f"CT1_{g}", f"sqt1_{g}", CT[g])
                    for g in G:
                        plus(f"P1_{g}", f"x1_{g}", g)
                    for g in G:
                        plus(f"P2_{g}", f"x2_{g}", g)
                    if not sample:
                        for g in G:
                            plus(f"P3_{g}", f"x3_{g}", g)
                        for w, Tb in ((16, B), (32, CT), (64, CT)):
                            for g in G:
                                copy(f"T{w}_{g}", f"tr{w}_{g}", Tb[g])
                            for g in G:
                                plus(f"PZ{w}_{g}", f"z{w}_{g}", g)
                        if c == 0:
                            dve.wait_ge(zeroed, 2)
                        dve.tensor_tensor(v4(S0s), v4(RS), eref.rearrange("p (t i) -> p t i", t=4)
                                          .to_broadcast([P, 4, 64]), ALU.mult).then_inc(*did("S0s"))
                        dve.wait_ge(*after("pe", "ks"))
                        dve.tensor_tensor(v4(W), v4(psum("ks")), col(c, COL_BETA_GC)(P), ALU.mult).then_inc(*did("W1"))
                        dve.wait_ge(*after("dve", "W1"))
                        dve.tensor_tensor(W, VBt, W, ALU.subtract).then_inc(*did("W2"))
                        copy("RU", "ru", RU, cols=512)
                        dve.wait_ge(*after("pe", "s"))
                        last = eR.rearrange("p (h i) -> p h i", h=4)[:, :, n - 1:n].to_broadcast([P, 4, P])
                        dve.tensor_tensor(v4(S), v4(S), last, ALU.mult).then_inc(*did("S1"))
                        dve.wait_ge(*after("dve", "S1"))
                        dve.tensor_tensor(S, S, psum("s"), ALU.add).then_inc(*did("S3"))
                        dve.wait_ge(*after("pe", "rs"))
                        dve.tensor_tensor(S0s, S0s, psum("rs")[:, 0:256], ALU.add).then_inc(*did("RS1"))
                        dve.wait_ge(*after("dve", "RS1"))
                        dve.tensor_tensor(v4(RS), v4(S0s), E4[:, :, n:n + 1].to_broadcast([P, 4, 64]), ALU.mult)\
                            .then_inc(*did("RSn"))
                    else:
                        dve.wait_ge(*after("pe", "kst"))
                        dve.tensor_tensor(v4(Wd, n), v4(psum("kst"), n), col(c, COL_BETA_GC)(P), ALU.mult)\
                            .then_inc(*did("W1"))
                        dve.wait_ge(*after("dve", "W1"))
                        dve.tensor_tensor(Wd[0:n], VBt[0:n], Wd[0:n], ALU.subtract).then_inc(*did("W2"))
                        dve.wait_ge(*after("pe", "rw"))
                        dve.wait_ge(*after("act", "RWt"))
                        dve.tensor_tensor(RW[0:n], RW[0:n], psum("rw"), ALU.add).then_inc(*did("RW"))
                        ko4 = KO.rearrange("p (h a t) -> p h a t", h=4, a=2)
                        rko4 = RKO.rearrange("p (t a i) -> p t a i", t=4, a=2)
                        dve.wait_ge(*after("pe", "o"))
                        dve.tensor_tensor(tokens(Q_A, c), ko4[:, :, 1], v4(psum("o", P)[:, 0:H]), ALU.add)\
                            .then_inc(*did("O"))
                        dve.wait_ge(*after("pe", "ry"))
                        dve.tensor_tensor(htokens(NEG_KK, c), rko4[:, :, 1], v4(psum("ry", P)[:, 0:H]), ALU.add)\
                            .then_inc(*did("RY"))
                        own = k.mask("block8")[0:n, 0:n:TS]
                        dve.wait_ge(*after("act", "U"))
                        for h in range(4):
                            if h:
                                dve.wait_ge(*after("pe", f"s{h - 1}b"))
                            own_b = own[:, :, None].to_broadcast([n, NSEQ, P])
                            dve.tensor_tensor(Uw[0:n].rearrange("p (s v) -> p s v", s=NSEQ),
                                              Ud[0:n, None, h * P:(h + 1) * P].to_broadcast([n, NSEQ, P]), own_b,
                                              ALU.mult).then_inc(*did(f"Um{h}"))
                            Sh = S[:, h * 1024:(h + 1) * 1024]
                            gl = eR[:, h * n + TS - 1:(h + 1) * n:TS]
                            dve.tensor_tensor(Sh.rearrange("p (s v) -> p s v", s=NSEQ),
                                              Sh.rearrange("p (s v) -> p s v", s=NSEQ),
                                              gl[:, :, None].to_broadcast([P, NSEQ, P]), ALU.mult)\
                                .then_inc(*did(f"Sg{h}"))
                            dve.wait_ge(*after("dve", f"Sg{h}"))
                            for part in range(2):
                                x = "ab"[part]
                                dve.wait_ge(*after("pe", f"s{h}{x}"))
                                dve.tensor_tensor(Sh[:, part * 512:(part + 1) * 512], Sh[:, part * 512:(part + 1) * 512],
                                                  psum(f"s{h}{x}", P), ALU.add).then_inc(*did(f"S{h}{x}"))
                        dve.wait_ge(*after("act", "RU"))
                        dve.wait_ge(*after("pe", "s3b"))
                        for t in range(4):
                            if t:
                                dve.wait_ge(*after("pe", f"rs{t - 1}"))
                            for nm, dst, src in (("RUm", RUw, RU), ("RVm", RVw, Vt)):
                                for half in range(2):
                                    hd = 2 * t + half
                                    last = dve.tensor_tensor(
                                        dst[0:n, half * 512:(half + 1) * 512].rearrange("p (s v) -> p s v", s=NSEQ),
                                        src[0:n, None, hd * 64:(hd + 1) * 64].to_broadcast([n, NSEQ, 64]),
                                        own[:, :, None].to_broadcast([n, NSEQ, 64]), ALU.mult)
                                last.then_inc(*did(f"{nm}{t}"))
                            Rt = RS[:, t * 512:(t + 1) * 512]
                            dve.wait_ge(*after("pe", f"rs{t}"))
                            dve.tensor_tensor(Rt, Rt, psum(f"rs{t}", P), ALU.add).then_inc(*did(f"RS{t}"))
                            dve.wait_ge(*after("dve", f"RS{t}"))
                            dve.tensor_tensor(Rt.rearrange("p (s v) -> p s v", s=NSEQ),
                                              Rt.rearrange("p (s v) -> p s v", s=NSEQ),
                                              E4[:, t, :, TS:TS + 1].to_broadcast([P, NSEQ, 64]), ALU.mult)\
                                .then_inc(*did(f"RSd{t}"))


def finish_even(k):
    nc = k.nc
    big = lambda t: k.big_buf[:, t * T:(t + 1) * T]
    hb = lambda t: k.h[:, t * T:(t + 1) * T]
    sq = lambda i: k.arena[:, i * T:(i + 1) * T]
    bonus = lambda i: k.arena[:, (8 + i) * T:(9 + i) * T]
    w2 = k.arena[:, 16 * T:16 * T + 512]
    N = range(4)
    with nc.cleanup_on_exit():
        s = Phase(nc)
        q = Schedule(
            s,
            pe=[f"sum_a{i}" for i in N] + [f"mean{i}" for i in N] + [f"bonus{i}" for i in N] + [f"var{i}" for i in N]
            + [f"gate{i}" for i in N],
            act=[f"sq_a{i}" for i in N] + [f"root_a{i}" for i in N] + [f"sq_y{i}" for i in N] + [f"root_y{i}" for i in N],
            dve=[f"rk{i}" for i in N] + [f"{x}{i}" for i in N for x in ("inv_a", "norm_a", "out_a")]
            + [f"center{i}" for i in N] + [f"bonus_v{i}" for i in N]
            + [f"{x}{i}" for i in N for x in ("inv_y", "norm_y", "affine", "out_y")])
        did, after = q.did, q.after
        loaded, restored = s.sem("wg2_loaded"), s.sem("x_restored")
        halves = lambda ap: ap.rearrange("p (a t) -> p a t", a=2)
        pair = {n: k.psum_pair(i % 4) for i, n in enumerate(q.count["pe"])}
        ps = lambda nm: two_halves(pair[nm], HALF)
        with nc.Block() as block:
            @block.sync
            def _(sp):
                sp.dma_start(w2, k.io["w_g2"]).then_inc(loaded, 16)
                sp.dma_start(k.x, k.x_kept).then_inc(restored, 16)
                sp.wait_ge(loaded, 16)
                sp.wait_ge(restored, 16)

            @block.tensor
            def _(pe):
                def product(name, lhsT, rhs):
                    for a in range(2):
                        last = pe.matmul(pair[name][:, a, 0:HALF], lhsT, rhs[:, a * HALF:(a + 1) * HALF],
                                         start=True, stop=True)
                    last.then_inc(*did("pe", name))
                for i in N:
                    pe.wait_ge(*after("act", f"sq_a{i}"))
                    product(f"sum_a{i}", k.mask("ones"), sq(i))
                for i in N:
                    pe.wait_ge(*after("act", f"root_a{i}"))
                    product(f"mean{i}", k.mask("block64"), hb(NEG_KK + i))
                for i in N:
                    pe.wait_ge(*after("dve", f"rk{i}"))
                    pe.wait_ge(*after("dve", f"center{i}"))
                    product(f"bonus{i}", k.mask("block64"), bonus(i))
                for i in N:
                    pe.wait_ge(*after("act", f"sq_y{i}"))
                    pe.wait_ge(*after("dve", f"bonus_v{i}"))
                    product(f"var{i}", k.mask("block64"), sq(4 + i))
                pe.wait_ge(loaded, 16)
                for i in N:
                    pe.wait_ge(*after("act", f"root_y{i}"))
                    product(f"gate{i}", w2[:, i * P:(i + 1) * P], big(G_B))

            @block.scalar
            def _(act):
                for i in N:
                    act.activation(sq(i), big(Q_A + i), ACT.Square).then_inc(*did("act", f"sq_a{i}"))
                for i in N:
                    act.wait_ge(*after("pe", f"sum_a{i}"))
                    act.activation(halves(sq(i)), ps(f"sum_a{i}"), ACT.Sqrt, bias=k.eps[:, 0:1], scale=1.0 / P)\
                        .then_inc(*did("act", f"root_a{i}"))
                for i in N:
                    act.wait_ge(*after("dve", f"center{i}"))
                    act.activation(sq(4 + i), hb(NEG_KK + i), ACT.Square).then_inc(*did("act", f"sq_y{i}"))
                for i in N:
                    act.wait_ge(*after("pe", f"var{i}"))
                    act.activation(halves(sq(4 + i)), ps(f"var{i}"), ACT.Sqrt, bias=k.eps[:, 1:2], scale=1.0 / 64)\
                        .then_inc(*did("act", f"root_y{i}"))

            @block.vector
            def _(dve):
                stt = dve.scalar_tensor_tensor
                for i in N:
                    stt(out=bonus(i), in0=big(R_B + i), scalar=k.par("r_k")[:, i:i + 1], in1=big(K_B + i),
                        op0=ALU.mult, op1=ALU.mult).then_inc(*did("dve", f"rk{i}"))
                for i in N:
                    dve.wait_ge(*after("act", f"root_a{i}"))
                    dve.reciprocal(sq(i), sq(i)).then_inc(*did("dve", f"inv_a{i}"))
                    dve.wait_ge(*after("dve", f"inv_a{i}"))
                    stt(out=sq(i), in0=sq(i), scalar=k.par("gain_a"), in1=big(Z_A + i), op0=ALU.mult, op1=ALU.mult)\
                        .then_inc(*did("dve", f"norm_a{i}"))
                    dve.wait_ge(*after("dve", f"norm_a{i}"))
                    dve.tensor_tensor(big(Q_A + i), big(Q_A + i), sq(i), ALU.mult).then_inc(*did("dve", f"out_a{i}"))
                for i in N:
                    dve.wait_ge(*after("pe", f"mean{i}"))
                    stt(out=halves(hb(NEG_KK + i)), in0=ps(f"mean{i}"), scalar=-1.0 / 64, in1=halves(hb(NEG_KK + i)),
                        op0=ALU.mult, op1=ALU.add).then_inc(*did("dve", f"center{i}"))
                for i in N:
                    dve.wait_ge(*after("pe", f"bonus{i}"))
                    dve.tensor_tensor(halves(bonus(i)), ps(f"bonus{i}"), halves(big(V_B + i)), ALU.mult)\
                        .then_inc(*did("dve", f"bonus_v{i}"))
                for i in N:
                    y = hb(NEG_KK + i)
                    out = big(K_A + i)
                    dve.wait_ge(*after("act", f"root_y{i}"))
                    dve.reciprocal(sq(4 + i), sq(4 + i)).then_inc(*did("dve", f"inv_y{i}"))
                    dve.wait_ge(*after("dve", f"inv_y{i}"))
                    stt(out=y, in0=y, scalar=k.par("lnx_gain")[:, i:i + 1], in1=sq(4 + i), op0=ALU.mult, op1=ALU.mult)\
                        .then_inc(*did("dve", f"norm_y{i}"))
                    dve.wait_ge(*after("dve", f"norm_y{i}"))
                    stt(out=y, in0=y, scalar=k.par("lnx_bias")[:, i:i + 1], in1=bonus(i), op0=ALU.add, op1=ALU.add)\
                        .then_inc(*did("dve", f"affine{i}"))
                    dve.wait_ge(*after("dve", f"affine{i}"))
                    dve.wait_ge(*after("pe", f"gate{i}"))
                    dve.tensor_tensor(halves(out), ps(f"gate{i}"), halves(y), ALU.mult).then_inc(*did("dve", f"out_y{i}"))


def even_mixer(k, sublayer):
    normalise(k, sublayer, k.low_r[:, H_LOW - LOW:PROJECTION_END - LOW], wide=True)
    project_even(k)
    prepare_even(k)
    even_chunks(k, sample=False)
    even_chunks(k, sample=True)
    finish_even(k)
    mixer_output(k, k.io["w_out_even"], lambda kt: k.big_buf[:, kt * T:(kt + 1) * T], sublayer)


Q_C, K_C, V_C, Z_C, Q_D, K_D, V_D, O_D, NARROW = 0, 2, 4, 8, 12, 14, 16, 20, 24
B16, B_C = 25, 27
SCALE_64 = 64.0 ** -0.5


def project_odd(k):
    nc = k.nc
    TILES = 25
    with nc.cleanup_on_exit():
        s = Phase(nc)
        w = SplitWeights(k, s, k.io["w_in_odd"], TILES)
        evacuated = s.sem("evacuated")
        tokens = tokens_of(k.h_r, k.low_r[:, H_LOW - LOW:], TX, TX, HALF)
        with nc.Block() as block:
            @block.sync
            def _(sp):
                w.load(sp)

            @block.tensor
            def _(pe):
                w.products(pe, tokens, HALF, evacuated)

            @block.scalar
            def _(act):
                for m in range(2):
                    w.high(act, m % RAW_SLOTS, m % SPLIT_SLOTS, m, first=True)
                w.high(act, 2, 0, 2)
                w.high(act, 3, 1, 3)
                with act.Fori(1, TILES // 4) as r:
                    for b in range(4):
                        w.high(act, b, b % 2, 4 * r + b)
                w.high(act, 0, 0, TILES - 1)

            @block.vector
            def _(dve):
                def tile(b, m):
                    dve.wait_ge(w.product, m + 1)
                    out = k.big_buf[:, bass.ds(m * T, T)].rearrange("p (a t) -> p a t", a=2)
                    dve.tensor_copy(out, two_halves(k.psum_pair(b), HALF)).then_inc(evacuated, 1)
                w.low(dve, 0, 0, 0)
                w.low(dve, 1, 1, 1)
                with dve.Fori(0, TILES // 4 - 1) as r:
                    for b in range(4):
                        w.low(dve, (b + 2) % 4, b % 2, 4 * r + b + 2)
                        tile(b, 4 * r + b)
                for m in range(TILES - 5, TILES):
                    if m + 2 < TILES:
                        w.low(dve, (m + 2) % 4, m % 2, m + 2)
                    tile(m % 4, m)


def prepare_odd(k):
    nc = k.nc
    big = lambda t, n=1: k.big_buf[:, t * T:(t + n) * T]
    row = lambda i: k.arena[0:4, i * T:(i + 1) * T]
    fg, ig, lf, soft, fsum, lfm, igm, m, a_row, e_row = (row(i) for i in range(10))
    x2 = lambda i: k.arena[:, (11 + i) * T:(12 + i) * T]
    s2 = lambda i: k.arena[:, (13 + i) * T:(14 + i) * T]
    w2 = k.arena[0:16, 15 * T:15 * T + 256]
    before = k.arena[0:4, 15 * T + 256:15 * T + 256 + NCH]
    m0 = k.arena[0:4, 15 * T + 264:15 * T + 264 + NSEQ]
    bound = k.arena[0:4, 15 * T + 272:15 * T + 272 + NSEQ]
    m_last = k.arena[0:4, 15 * T + 280:15 * T + 280 + NSEQ]
    col_rows = k.arena[:, 16 * T:17 * T]
    resets16 = k.arena[:, 17 * T:18 * T]
    rfm, rw, rnm = (k.mrows[:, i * T:(i + 1) * T] for i in range(3))
    act_steps = (["silu_z", "e_o"] + ["abs_f", "exp_f", "ln_f"] + [f"{x}{i}" for i in range(2) for x in ("abs", "exp", "ln")]
                 + ["exp_e", "cols"])
    dve_steps = (["resets16", "o1", "gates", "fg", "ig", "clear", "lf0", "lf", "fsum", "lfm", "igm", "bound1", "bound2", "cut_f",
                  "cut_i", "m", "m_last", "a", "before0", "before", "fm", "w_p", "w_s", "nm", "e_p", "e_s", "a_col",
                  "o2"]
                 + [f"{x}{i}" for i in range(2) for x in ("x", "s1_", "s2_", "b", "b16_")])
    with nc.cleanup_on_exit():
        s = Phase(nc)
        q = Schedule(s, act=act_steps, dve=dve_steps, pe=["gk0", "gk1", "cols"])
        did, after = q.did, q.after
        loaded, stored, ones16 = s.sem("loaded"), s.sem("stored"), s.sem("ones16")
        with nc.Block() as block:
            @block.sync
            def _(sp):
                sp.dma_start(w2, k.io["w_gk2"]).then_inc(loaded, 16)
                sp.dma_start(m0, k.io["mm_in"]).then_inc(loaded, 16)
                sp.wait_ge(*after("dve", "m_last"))
                sp.dma_start(k.io["mm_p_out"], m[:, TP - 1:TP]).then_inc(stored, 16)
                sp.dma_start(k.io["mm_s_out"], m_last).then_inc(stored, 16)
                sp.wait_ge(stored, 32)

            @block.gpsimd
            def _(pool):
                pool.memset(resets16, 1.0).then_inc(ones16, 1)

            @block.scalar
            def _(act):
                act.activation(big(Z_C, 4), big(Z_C, 4), ACT.Silu).then_inc(*did("act", "silu_z"))
                act.activation(big(O_D, 4), big(O_D, 4), ACT.Exp, scale=-1.0).then_inc(*did("act", "e_o"))
                act.wait_ge(*after("dve", "fg"))
                act.activation(soft, fg, ACT.Abs).then_inc(*did("act", "abs_f"))
                act.wait_ge(*after("act", "abs_f"))
                act.activation(soft, soft, ACT.Exp, scale=-1.0).then_inc(*did("act", "exp_f"))
                act.wait_ge(*after("act", "exp_f"))
                act.activation(soft, soft, ACT.Ln, bias=1.0).then_inc(*did("act", "ln_f"))
                for i in range(2):
                    act.wait_ge(*after("dve", f"x{i}"))
                    act.activation(s2(i), x2(i), ACT.Abs).then_inc(*did("act", f"abs{i}"))
                    act.wait_ge(*after("act", f"abs{i}"))
                    act.activation(s2(i), s2(i), ACT.Exp, scale=-1.0).then_inc(*did("act", f"exp{i}"))
                    act.wait_ge(*after("act", f"exp{i}"))
                    act.activation(s2(i), s2(i), ACT.Ln, bias=1.0).then_inc(*did("act", f"ln{i}"))
                act.wait_ge(*after("dve", "e_s"))
                act.activation(col_rows[32:36, :], e_row, ACT.Exp).then_inc(*did("act", "exp_e"))
                act.wait_ge(*after("pe", "cols"))
                cols = k.cols.rearrange("p (c r h) -> p c r h", c=5, r=4)
                act.activation(cols[:, 0:4, 0:2], k.psum[4].rearrange("p (c r h) -> p c r h", c=4, r=4)
                               [:, :, 0:2, 0:4], ACT.Copy)
                act.activation(cols[0:64, 4, 0:2], k.psum[5][0:64, 0:P].rearrange("p (r h) -> p r h", r=4)
                               [:, 0:2, 0:4], ACT.Copy).then_inc(*did("act", "cols"))

            @block.tensor
            def _(pe):
                pe.wait_ge(loaded, 32)
                for i in range(2):
                    for a in range(2):
                        at = NARROW * T + a * HALF
                        last = pe.matmul(k.psum_pair(i)[:, a, 0:HALF], w2[:, i * P:(i + 1) * P],
                                         k.big_buf[0:16, at:at + HALF], start=True, stop=True)
                    last.then_inc(*did("pe", f"gk{i}"))
                pe.wait_ge(*after("act", "exp_e"))
                pe.wait_ge(*after("dve", "a_col"))
                for c in range(NCH):
                    pe.transpose(k.psum[4][:, c * P:(c + 1) * P], col_rows[:, c * P:(c + 1) * P], k.mask("ident"))
                pe.transpose(k.psum[5][0:64, 0:P], col_rows[:, TP:T], k.mask("ident")).then_inc(*did("pe", "cols"))

            @block.vector
            def _(dve):
                tt, ts = dve.tensor_tensor, dve.tensor_scalar
                w = lambda name: dve.wait_ge(*after("dve", name))
                chunked = lambda v: v[:, 0:TP].rearrange("p (c i) -> p c i", i=CH)
                seqs = lambda v: v[:, TP:T].rearrange("p (c i) -> p c i", i=TS)
                dve.wait_ge(ones16, 1)
                dve.memset(resets16[:, 0:TP].rearrange("p (c i) -> p c i", i=16)[:, :, 0:1], 0.0)
                dve.memset(resets16[:, TP:T].rearrange("p (c i) -> p c i", i=TS)[:, :, 0:1], 0.0)\
                    .then_inc(*did("dve", "resets16"))
                dve.wait_ge(*after("act", "e_o"))
                ts(big(O_D, 4), big(O_D, 4), 1.0, None, ALU.add).then_inc(*did("dve", "o1"))
                dve.tensor_copy(fg, k.big_buf[64:68, NARROW * T:(NARROW + 1) * T])
                dve.tensor_copy(ig, k.big_buf[32:36, NARROW * T:(NARROW + 1) * T]).then_inc(*did("dve", "gates"))
                w("gates")
                ts(fg, fg, k.par("b_f")[0:4], None, ALU.add).then_inc(*did("dve", "fg"))
                ts(ig, ig, k.par("b_i")[0:4], None, ALU.add).then_inc(*did("dve", "ig"))
                dve.memset(col_rows, 0.0).then_inc(*did("dve", "clear"))
                w("fg")
                ts(lf, fg, 0.0, None, ALU.min).then_inc(*did("dve", "lf0"))
                dve.wait_ge(*after("act", "ln_f"))
                w("lf0")
                tt(lf, lf, soft, ALU.subtract).then_inc(*did("dve", "lf"))
                w("lf")
                dve.tensor_tensor_scan(fsum, k.resets[0:4], lf, 0.0, ALU.mult, ALU.add).then_inc(*did("dve", "fsum"))
                dve.tensor_copy(lfm, lf).then_inc(*did("dve", "lfm"))
                w("ig")
                dve.tensor_copy(igm, ig).then_inc(*did("dve", "igm"))
                dve.wait_ge(loaded, 32)
                w("igm")
                tt(bound, lf[:, TP:T:TS], m0, ALU.add).then_inc(*did("dve", "bound1"))
                w("bound1")
                tt(bound, bound, igm[:, TP:T:TS], ALU.max).then_inc(*did("dve", "bound2"))
                w("bound2")
                dve.memset(lfm[:, TP:T:TS], -BIG).then_inc(*did("dve", "cut_f"))
                dve.tensor_copy(igm[:, TP:T:TS], bound).then_inc(*did("dve", "cut_i"))
                w("cut_i")
                dve.tensor_tensor_scan(m, lfm, igm, 0.0, ALU.add, ALU.max).then_inc(*did("dve", "m"))
                w("m")
                dve.tensor_copy(m_last, m[:, TP + TS - 1:T:TS]).then_inc(*did("dve", "m_last"))
                tt(a_row, ig, fsum, ALU.subtract).then_inc(*did("dve", "a"))
                dve.memset(before[:, 0:1], 0.0).then_inc(*did("dve", "before0"))
                w("m")
                dve.tensor_copy(before[:, 1:NCH], m[:, CH - 1:TP - 1:CH]).then_inc(*did("dve", "before"))
                tt(rfm, fsum, m, ALU.subtract).then_inc(*did("dve", "fm"))
                w("fm")
                tt(chunked(rw), chunked(rfm), before[:, :, None].to_broadcast([4, NCH, CH]), ALU.add)\
                    .then_inc(*did("dve", "w_p"))
                tt(seqs(rw), seqs(rfm), m0[:, :, None].to_broadcast([4, NSEQ, TS]), ALU.add)\
                    .then_inc(*did("dve", "w_s"))
                ts(rnm, m, -1.0, None, ALU.mult).then_inc(*did("dve", "nm"))
                tt(chunked(e_row), chunked(a_row), chunked(rfm)[:, :, CH - 1:CH].to_broadcast([4, NCH, CH]), ALU.add)\
                    .then_inc(*did("dve", "e_p"))
                tt(seqs(e_row), seqs(a_row), seqs(rfm)[:, :, TS - 1:TS].to_broadcast([4, NSEQ, TS]), ALU.add)\
                    .then_inc(*did("dve", "e_s"))
                w("clear")
                dve.tensor_copy(col_rows[0:4, :], a_row).then_inc(*did("dve", "a_col"))
                w("o1")
                dve.reciprocal(big(O_D, 4), big(O_D, 4)).then_inc(*did("dve", "o2"))
                for i in range(2):
                    dve.wait_ge(*after("pe", f"gk{i}"))
                    ts(x2(i).rearrange("p (a t) -> p a t", a=2), two_halves(k.psum_pair(i), HALF),
                       k.par("b_gk")[:, i:i + 1], None, ALU.add).then_inc(*did("dve", f"x{i}"))
                    dve.wait_ge(*after("act", f"ln{i}"))
                    dve.scalar_tensor_tensor(out=x2(i), in0=x2(i), scalar=0.0, in1=s2(i), op0=ALU.min,
                                             op1=ALU.subtract).then_inc(*did("dve", f"s1_{i}"))
                    w(f"s1_{i}")
                    ts(x2(i), x2(i), 1.0 / 16.0, None, ALU.mult).then_inc(*did("dve", f"s2_{i}"))
                    w(f"s2_{i}")
                    dve.tensor_tensor_scan(big(B_C + i), k.resets, x2(i), 0.0, ALU.mult, ALU.add)\
                        .then_inc(*did("dve", f"b{i}"))
                    dve.tensor_tensor_scan(big(B16 + i), resets16, x2(i), 0.0, ALU.mult, ALU.add)\
                        .then_inc(*did("dve", f"b16_{i}"))


def odd_jobs(sample):
    levels = () if sample else LEVELS
    jobs = [("r", ("dve", "log1")), ("rw", ("act", "xw")), ("nm", ("act", "xm"))]
    jobs += [(f"qk_{g}", ("dve", f"DM_{g}")) for g in range(2)]
    jobs += [("vct", ("act", "Vc")), ("vdt", ("act", "Vd")), ("kdt", ("dve", "KE"))]
    jobs += [(f"at_{g}", ("dve", f"AT_{g}")) for g in range(2)]
    jobs += [(f"at{w}_{g}", ("dve", f"L{w}_{g}")) for w in levels for g in range(2)]
    jobs += [("klt", ("act", "KL"))]
    if sample:
        jobs += [("co_s", ("act", "CO")), ("do_s", ("act", "DO")), ("dn_s", ("act", "DN"))]
    jobs += [("co", ("dve" if sample else "act", "Oc")), ("do", ("dve", "Od")), ("dn", ("dve", "den"))]
    if sample:
        for t in range(2):
            jobs += [(f"{n}{t}{x}", ("dve", f"{u}{t}{x}")) for n, u in (("sc", "SC"), ("sd", "SD")) for x in "ab"]
        jobs += [("sn", ("dve", "SN"))]
    else:
        jobs += [("sc", ("dve", "SC")), ("sd", ("dve", "SD"))]
    return jobs


def odd_chunks(k, sample):
    nc = k.nc
    n = NSEQ * TS if sample else CH
    chunks = [NCH] if sample else list(range(NCH))
    names = lambda base, c: f"{base}@{c}"
    levels = () if sample else LEVELS
    jobs = odd_jobs(sample)
    pe_steps, freed, act_steps, dve_steps = [], [], [], []
    for c in chunks:
        pe_steps += [names(j, c) for j, _ in jobs]
        freed += [(e, names(st, c)) for _, (e, st) in jobs]
        a = ["x16", "xn16", "xb", "xl"] + [x for w in levels for x in (f"abs{w}", f"F{w}")]
        a += ["xw", "xm", "xlog", "Vc", "Vd", "KL"] + (["CO", "DO", "DN"] if sample else ["Oc"]) + ["aden"]
        d = ["to_end", "Qb", "Qd", "Kd", "Kl"] + [x for w in levels for x in (f"rel{w}", f"Q{w}", f"K{w}")]
        d += ["log1", "log2", "qw", "DM_0", "DM_1", "KE", "AT_0", "AT_1"]
        d += [x for w in levels for g in range(2) for x in (f"L{w}_{g}", f"A{w}_{g}")]
        if sample:
            d += ["Nw", "Oc"]
        d += ["den", "max", "inv", "Od"] + (["Od2"] if sample else [])
        if sample:
            for t in range(2):
                for kind in ("C", "D"):
                    d += [f"V{kind}{t}", f"G{kind}{t}", f"S{kind}{t}a", f"S{kind}{t}b"]
            d += ["GN", "SN"]
        else:
            d += ["GC", "SC", "GD", "SD"]
        act_steps += [names(x, c) for x in a]
        dve_steps += [names(x, c) for x in d]
    if not sample:
        dve_steps.append("n_last")
    take = carve(k.arena[:, 0:ARENA - 3 * T])
    H, H2 = 4 * n, 2 * n
    x16, xn16, xb, xl = (take(H2) for _ in range(4))
    Qd, Kd, Qb, Kl = (take(H2) for _ in range(4))
    F = {w: take(H2) for w in levels}
    Q = {w: take(H2) for w in levels}
    K = {w: take(H2) for w in levels}
    L = {w: take(H) for w in levels}
    xw, qw = take(H2), take(H2)
    xm, lg, DM, AT, aden = (take(H) for _ in range(5))
    Vc, Vd, KE, KL = take(512), take(512), take(256), take(256)
    if sample:
        SC, SD, SN, Nw = take(2048), take(2048), take(16), take(2048)
        CO, DO, DN = take(H), take(H), take(H)
        Vw = {(kind, half): take(1024) for kind in "CD" for half in range(2)}
    else:
        n_last = take(2)
        SC, SD = take(256), take(512)
    v2 = lambda ap: ap.rearrange("p (t i) -> p t i", t=2)
    v4 = lambda ap, part=P: ap[0:part].rearrange("p (h n) -> p h n", h=4)
    par_of = lambda ap, g: ap[0:n].rearrange("p (t g i) -> p t g i", t=2, g=2)[:, :, g]
    bc = lambda m, cnt: m[:, None, :].to_broadcast([n, cnt, n])
    mask = lambda nm: k.mask(nm)[0:n, 0:n]
    sfx = "8" if sample else "16"

    with nc.cleanup_on_exit():
        ph = Phase(nc)
        sched = Schedule(ph, pe=pe_steps, act=act_steps, dve=dve_steps)
        number = {j: i for i, j in enumerate(pe_steps)}
        states_in, states_out, zeroed = ph.sem("states_in"), ph.sem("states_out"), ph.sem("zeroed")
        even_heads = ph.sem("even_heads")
        bank = lambda job, c: k.psum[number[names(job, c)] % 8]

        def tokens(t, c, count=4):
            return k.big_buf[:, t * T:(t + count) * T].rearrange("p (h t) -> p h t", t=T)[:, :, c * CH:c * CH + n]

        def col(c, r):
            v = k.cols[0:n].rearrange("p (c r h) -> p c r h", c=5, r=4)[:, c, r, :]
            return lambda w: v[:, :, None].to_broadcast([n, 4, w])

        with nc.Block() as block:
            @block.sync
            def _(sp):
                if sample:
                    sp.dma_start(SC, k.io["gla_in"]).then_inc(states_in, 16)
                    sp.dma_start(SD, k.io["mc_in"]).then_inc(states_in, 16)
                    sp.dma_start(SN, k.io["mn_in"]).then_inc(states_in, 16)
                    sp.wait_ge(*sched.after("dve", names("SN", NCH)))
                    sp.dma_start(k.io["gla_s_out"], SC).then_inc(states_out, 16)
                    sp.dma_start(k.io["mc_s_out"], SD).then_inc(states_out, 16)
                    sp.dma_start(k.io["mn_s_out"], SN).then_inc(states_out, 16)
                else:
                    sp.wait_ge(*sched.after("dve", names("SD", NCH - 1)))
                    sp.dma_start(k.io["gla_p_out"], SC).then_inc(states_out, 16)
                    sp.dma_start(k.io["mc_p_out"], SD[:, 0:256]).then_inc(states_out, 16)
                    sp.wait_ge(*sched.after("dve", "n_last"))
                    sp.dma_start(k.io["mn_p_out"], n_last).then_inc(states_out, 16)
                sp.wait_ge(states_out, 48)

            @block.gpsimd
            def _(pool):
                if not sample:
                    pool.memset(SC, 0.0).then_inc(zeroed, 1)
                    pool.memset(SD, 0.0).then_inc(zeroed, 1)

            @block.tensor
            def _(pe):
                for c in chunks:
                    after = lambda e, nm: sched.after(e, names(nm, c))

                    def claim(job):
                        i = number[names(job, c)]
                        if i >= 8:
                            pe.wait_ge(*sched.after(*freed[i - 8]))
                        return bank(job, c)

                    def done(job, ins):
                        ins.then_inc(*sched.did("pe", names(job, c)))

                    def rows(job, source, matrices):
                        b = claim(job)
                        for i, m in enumerate(matrices):
                            last = pe.matmul(b[:, i * n:(i + 1) * n], k.select(m)[0:4],
                                             source[:, c * CH:c * CH + n], start=True, stop=True)
                        done(job, last)
                    rfm, rw, rnm = (k.mrows[:, i * T:(i + 1) * T] for i in range(3))
                    rows("r", rfm, range(4))
                    rows("rw", rw, (4, 5))
                    rows("nm", rnm, range(4))
                    kd, qd = tokens(K_D, c, 2), tokens(Q_D, c, 2)

                    def pair(job, lhsT, rhs):
                        g = int(job[-1])
                        p = slice(64 * g, 64 * g + 64)
                        b = claim(job)
                        for t in range(2):
                            last = pe.matmul(b[0:n, t * n:(t + 1) * n], lhsT(p, t), rhs(p, t), start=True, stop=True)
                        done(job, last)

                    def transposes(job, source, count):
                        b = claim(job)
                        for i in range(count):
                            last = pe.transpose(b[0:n, i * P:(i + 1) * P], source(i), k.mask("ident"))
                        done(job, last)
                    for g in range(2):
                        pair(f"qk_{g}", lambda p, t: kd[p, t], lambda p, t: qd[p, t])
                    vc, vd = tokens(V_C, c), tokens(V_D, c)
                    transposes("vct", lambda i: vc[:, i], 4)
                    transposes("vdt", lambda i: vd[:, i], 4)
                    transposes("kdt", lambda i: kd[:, i], 2)
                    pe.wait_ge(*after("dve", "Kd"))
                    of = lambda buf: (lambda p, t: buf[p, t * n:(t + 1) * n])
                    for g in range(2):
                        pair(f"at_{g}", of(Kd), of(Qd))
                    for w in levels:
                        pe.wait_ge(*after("dve", f"K{w}"))
                        for g in range(2):
                            pair(f"at{w}_{g}", of(K[w]), of(Q[w]))
                    transposes("klt", lambda i: Kl[:, i * n:(i + 1) * n], 2)
                    last_a = f"A{levels[-1]}_1" if levels else "AT_1"
                    if sample:
                        pe.wait_ge(states_in, 48)
                        pe.wait_ge(*after("dve", "Nw"))
                        for turn, (job, state, right) in enumerate((
                                ("co_s", SC, Qb), ("do_s", SD, qw), ("dn_s", Nw, qw))):
                            b = claim(job)
                            for g in range(2):
                                if g:
                                    pe.wait_ge(even_heads, turn + 1)
                                for t in range(2):
                                    for q in range(NSEQ):
                                        h = 2 * t + g
                                        p = slice(64 * g, 64 * g + 64)
                                        last = pe.matmul(
                                            b[:, h * n + q * TS:h * n + (q + 1) * TS],
                                            state[p, (t * NSEQ + q) * P:(t * NSEQ + q + 1) * P],
                                            right[p, t * n + q * TS:t * n + (q + 1) * TS], start=True, stop=True)
                                if not g:
                                    last.then_inc(even_heads, 1)
                            done(job, last)
                    else:
                        if c == 0:
                            pe.wait_ge(zeroed, 2)
                        else:
                            pe.wait_ge(*sched.after("dve", names("SD", c - 1)))

                    def output(job, state, right, values, weights, ready):
                        pe.wait_ge(*ready)
                        b = claim(job)
                        for h in (0, 2, 1, 3):
                            t, g = h // 2, h % 2
                            out = b[:, h * n:(h + 1) * n]
                            if not sample and h == 1:
                                pe.wait_ge(even_heads, 3 * c + ("co", "do", "dn").index(job) + 1)
                            if not sample:
                                p = slice(64 * g, 64 * g + 64)
                                pe.matmul(out, state[p, t * P:(t + 1) * P], right[p, t * n:(t + 1) * n],
                                          start=True, stop=False)
                            last = pe.matmul(out, values(h), weights[0:n, h * n:(h + 1) * n],
                                             start=sample, stop=True)
                            if not sample and h == 2:
                                last.then_inc(even_heads, 1)
                        done(job, last)
                    pe.wait_ge(*after("act", "KL"))
                    output("co", SC, Qb, lambda h: Vc[0:n, h * P:(h + 1) * P], AT, after("dve", last_a))
                    output("do", SD, qw, lambda h: Vd[0:n, h * P:(h + 1) * P], DM, after("dve", "KE"))
                    output("dn", SD[:, 256:] if not sample else None, qw,
                           lambda h: k.mask("ones")[0:n], DM, after("dve", "KE"))
                    if not sample:
                        b = claim("sc")
                        for h in range(4):
                            t, p = h // 2, 64 * (h % 2)
                            last = pe.matmul(b[p:p + 64, t * P:(t + 1) * P], KL[:, h * 64:(h + 1) * 64],
                                             Vc[:, h * P:(h + 1) * P], start=True, stop=True)
                        done("sc", last)
                        b = claim("sd")
                        for h in range(4):
                            t, p = h // 2, 64 * (h % 2)
                            for part, values in ((0, Vd[:, h * P:(h + 1) * P]), (256, k.mask("ones"))):
                                last = pe.matmul(b[p:p + 64, part + t * P:part + (t + 1) * P],
                                                 KE[:, h * 64:(h + 1) * 64], values, start=True, stop=True)
                        done("sd", last)
                    else:
                        for t in range(2):
                            for kind, left in (("C", KL), ("D", KE)):
                                pe.wait_ge(*after("dve", f"V{kind}{t}"))
                                for part, x in enumerate("ab"):
                                    b = claim(f"s{kind.lower()}{t}{x}")
                                    for g in range(2):
                                        h = 2 * t + g
                                        last = pe.matmul(b[64 * g:64 * g + 64, :], left[0:n, h * 64:(h + 1) * 64],
                                                         Vw[kind, g][0:n, part * 512:(part + 1) * 512],
                                                         start=True, stop=True)
                                    done(f"s{kind.lower()}{t}{x}", last)
                        b = claim("sn")
                        for h in range(4):
                            t, p = h // 2, 64 * (h % 2)
                            last = pe.matmul(b[p:p + 64, t * NSEQ:(t + 1) * NSEQ], KE[0:n, h * 64:(h + 1) * 64],
                                             k.mask("block8")[0:n, 0:n:TS], start=True, stop=True)
                        done("sn", last)

            @block.scalar
            def _(act):
                for c in chunks:
                    after = lambda e, nm: sched.after(e, names(nm, c))
                    did = lambda nm: sched.did("act", names(nm, c))
                    psum = lambda job, part=n: bank(job, c)[0:part]
                    if c > chunks[0]:
                        act.wait_ge(*sched.after("dve", names("SD", c - 1)))
                        act.wait_ge(*sched.after("act", names("aden", c - 1)))
                    b16, bC = tokens(B16, c, 2), tokens(B_C, c, 2)
                    act.activation(v2(x16), b16, ACT.Exp).then_inc(*did("x16"))
                    act.activation(v2(xn16), b16, ACT.Exp, scale=-1.0).then_inc(*did("xn16"))
                    act.activation(v2(xb), bC, ACT.Exp).then_inc(*did("xb"))
                    act.wait_ge(*after("dve", "to_end"))
                    act.activation(xl, xl, ACT.Exp).then_inc(*did("xl"))
                    for w in levels:
                        act.wait_ge(*after("dve", f"rel{w}"))
                        act.activation(F[w], F[w], ACT.Abs).then_inc(*did(f"abs{w}"))
                        act.wait_ge(*after("act", f"abs{w}"))
                        act.activation(F[w], F[w], ACT.Exp, scale=-1.0).then_inc(*did(f"F{w}"))
                    act.wait_ge(*after("pe", "rw"))
                    act.activation(xw, psum("rw", P)[:, 0:H2], ACT.Exp).then_inc(*did("xw"))
                    act.wait_ge(*after("pe", "nm"))
                    act.activation(xm, psum("nm", P)[:, 0:H], ACT.Exp).then_inc(*did("xm"))
                    act.wait_ge(*after("dve", "log2"))
                    act.activation(lg[0:n], lg[0:n], ACT.Exp).then_inc(*did("xlog"))
                    for step, job, dst, cols in (("Vc", "vct", Vc, 512), ("Vd", "vdt", Vd, 512), ("KL", "klt", KL, 256)):
                        act.wait_ge(*after("pe", job))
                        act.activation(dst[0:n], psum(job)[:, 0:cols], ACT.Copy).then_inc(*did(step))
                    if sample:
                        for step, job, dst in (("CO", "co_s", CO), ("DO", "do_s", DO), ("DN", "dn_s", DN)):
                            act.wait_ge(*after("pe", job))
                            act.activation(dst, psum(job, P)[:, 0:H], ACT.Copy).then_inc(*did(step))
                        act.wait_ge(*after("dve", "den"))
                        act.activation(aden, aden, ACT.Abs).then_inc(*did("aden"))
                    else:
                        act.wait_ge(*after("pe", "co"))
                        act.activation(tokens(V_C, c), v4(psum("co", P)), ACT.Copy).then_inc(*did("Oc"))
                        act.wait_ge(*after("dve", "den"))
                        act.activation(aden, aden, ACT.Abs).then_inc(*did("aden"))

            @block.vector
            def _(dve):
                tt, ts, stt = dve.tensor_tensor, dve.tensor_scalar, dve.scalar_tensor_tensor
                for c in chunks:
                    after = lambda e, nm: sched.after(e, names(nm, c))
                    did = lambda nm: sched.did("dve", names(nm, c))
                    psum = lambda job, part=n: bank(job, c)[0:part]
                    w_ = lambda nm: dve.wait_ge(*after("dve", nm))
                    if c > chunks[0]:
                        dve.wait_ge(*sched.after("pe", names("sd", c - 1)))
                        dve.wait_ge(*sched.after("dve", names("SD", c - 1)))
                        dve.wait_ge(*sched.after("act", names("aden", c - 1)))
                    bC = tokens(B_C, c, 2)
                    if sample:
                        s8 = lambda ap: ap.rearrange("p t (s i) -> p t s i", s=NSEQ)
                        end = s8(bC)[:, :, :, TS - 1:TS].to_broadcast([P, 2, NSEQ, TS])
                        tt(s8(v2(xl)), end, s8(bC), ALU.subtract).then_inc(*did("to_end"))
                    else:
                        end = bC[:, :, n - 1:n].to_broadcast([P, 2, n])
                        tt(v2(xl), end, bC, ALU.subtract).then_inc(*did("to_end"))
                    q, kk = tokens(Q_C, c, 2), tokens(K_C, c, 2)
                    dve.wait_ge(*after("act", "xl"))
                    stt(out=v2(Qb), in0=q, scalar=SCALE_64, in1=v2(xb), op0=ALU.mult, op1=ALU.mult).then_inc(*did("Qb"))
                    stt(out=v2(Qd), in0=q, scalar=SCALE_64, in1=v2(x16), op0=ALU.mult, op1=ALU.mult)\
                        .then_inc(*did("Qd"))
                    tt(v2(Kd), kk, v2(xn16), ALU.mult).then_inc(*did("Kd"))
                    tt(v2(Kl), kk, v2(xl), ALU.mult).then_inc(*did("Kl"))
                    for w in levels:
                        blocks = n // (2 * w)
                        b4 = lambda ap: ap.rearrange("p t (b i) -> p t b i", b=blocks)
                        tt(b4(v2(F[w])), b4(bC), b4(bC)[:, :, :, w - 1:w].to_broadcast([P, 2, blocks, 2 * w]),
                           ALU.subtract).then_inc(*did(f"rel{w}"))
                        dve.wait_ge(*after("act", f"F{w}"))
                        stt(out=v2(Q[w]), in0=q, scalar=SCALE_64, in1=v2(F[w]), op0=ALU.mult, op1=ALU.mult)\
                            .then_inc(*did(f"Q{w}"))
                        tt(v2(K[w]), kk, v2(F[w]), ALU.mult).then_inc(*did(f"K{w}"))
                    dve.wait_ge(*after("pe", "r"))
                    nb = k.big("not_above_eq" + ("8" if sample else ""))[0:n, 0:n][:, None, :].to_broadcast([n, 4, n])
                    tt(v4(lg, n), v4(psum("r")[:, 0:H], n), nb, ALU.subtract).then_inc(*did("log1"))
                    w_("log1")
                    tt(v4(lg, n), v4(lg, n), col(c, 0)(n), ALU.add).then_inc(*did("log2"))
                    dve.wait_ge(*after("act", "xw"))
                    tt(v2(qw), tokens(Q_D, c, 2), v2(xw), ALU.mult).then_inc(*did("qw"))
                    dve.wait_ge(*after("act", "xlog"))
                    for g in range(2):
                        dve.wait_ge(*after("pe", f"qk_{g}"))
                        stt(out=par_of(DM, g), in0=v2(psum(f"qk_{g}")[:, 0:H2]), scalar=SCALE_64, in1=par_of(lg, g),
                            op0=ALU.mult, op1=ALU.mult).then_inc(*did(f"DM_{g}"))
                    dve.wait_ge(*after("pe", "kdt"))
                    stt(out=v4(KE, n), in0=v4(psum("kdt")[:, 0:256], n), scalar=SCALE_64, in1=col(c, 1)(64),
                        op0=ALU.mult, op1=ALU.mult).then_inc(*did("KE"))
                    for g in range(2):
                        dve.wait_ge(*after("pe", f"at_{g}"))
                        tt(par_of(AT, g), v2(psum(f"at_{g}")[:, 0:H2]), bc(mask("above_eq" + sfx), 2), ALU.mult)\
                            .then_inc(*did(f"AT_{g}"))
                    before = "AT"
                    for w in levels:
                        for g in range(2):
                            dve.wait_ge(*after("pe", f"at{w}_{g}"))
                            tt(par_of(L[w], g), v2(psum(f"at{w}_{g}")[:, 0:H2]), bc(mask(f"above_level{w}"), 2), ALU.mult)\
                                .then_inc(*did(f"L{w}_{g}"))
                            w_(f"L{w}_{g}")
                            tt(par_of(AT, g), par_of(AT, g), par_of(L[w], g), ALU.add).then_inc(*did(f"A{w}_{g}"))
                    if sample:
                        dve.wait_ge(states_in, 48)
                        dve.tensor_copy(Nw.rearrange("p (s v) -> p s v", v=P), SN[:, :, None].to_broadcast([P, 16, P]))\
                            .then_inc(*did("Nw"))
                        dve.wait_ge(*after("pe", "co"))
                        dve.wait_ge(*after("act", "CO"))
                        tt(tokens(V_C, c), v4(psum("co", P)[:, 0:H]), v4(CO), ALU.add).then_inc(*did("Oc"))
                        dve.wait_ge(*after("pe", "dn"))
                        dve.wait_ge(*after("act", "DN"))
                        tt(aden, psum("dn", P)[:, 0:H], DN, ALU.add).then_inc(*did("den"))
                    else:
                        dve.wait_ge(*after("pe", "dn"))
                        dve.tensor_copy(aden, psum("dn", P)[:, 0:H]).then_inc(*did("den"))
                    dve.wait_ge(*after("act", "aden"))
                    tt(aden, aden, xm, ALU.max).then_inc(*did("max"))
                    w_("max")
                    dve.reciprocal(aden, aden).then_inc(*did("inv"))
                    w_("inv")
                    if sample:
                        dve.wait_ge(*after("act", "DO"))
                        tt(DO, psum("do", P)[:, 0:H], DO, ALU.add).then_inc(*did("Od"))
                        w_("Od")
                        tt(tokens(V_D, c), v4(DO), v4(aden), ALU.mult).then_inc(*did("Od2"))
                        own = mask("block8")[:, 0:n:TS]
                        own_b = own[:, :, None].to_broadcast([n, NSEQ, P])
                        for t in range(2):
                            for kind, values, state in (("C", Vc, SC), ("D", Vd, SD)):
                                if t:
                                    dve.wait_ge(*after("pe", f"s{kind.lower()}{t - 1}b"))
                                for g in range(2):
                                    h = 2 * t + g
                                    last = tt(Vw[kind, g][0:n].rearrange("p (s v) -> p s v", s=NSEQ),
                                              values[0:n, None, h * P:(h + 1) * P].to_broadcast([n, NSEQ, P]),
                                              own_b, ALU.mult)
                                last.then_inc(*did(f"V{kind}{t}"))
                                St = state[:, t * 1024:(t + 1) * 1024]
                                ends = (xb if kind == "C" else xw)[:, t * n + TS - 1:(t + 1) * n:TS]
                                tt(St.rearrange("p (s v) -> p s v", s=NSEQ), St.rearrange("p (s v) -> p s v", s=NSEQ),
                                   ends[:, :, None].to_broadcast([P, NSEQ, P]), ALU.mult).then_inc(*did(f"G{kind}{t}"))
                                w_(f"G{kind}{t}")
                                for part, x in enumerate("ab"):
                                    dve.wait_ge(*after("pe", f"s{kind.lower()}{t}{x}"))
                                    cs = slice(part * 512, (part + 1) * 512)
                                    tt(St[:, cs], St[:, cs], psum(f"s{kind.lower()}{t}{x}", P), ALU.add)\
                                        .then_inc(*did(f"S{kind}{t}{x}"))
                        ends = xw.rearrange("p (t s i) -> p t s i", t=2, s=NSEQ)[:, :, :, TS - 1]
                        sn = SN.rearrange("p (t s) -> p t s", t=2)
                        tt(sn, sn, ends, ALU.mult).then_inc(*did("GN"))
                        w_("GN")
                        dve.wait_ge(*after("pe", "sn"))
                        tt(SN, SN, psum("sn", P)[:, 0:16], ALU.add).then_inc(*did("SN"))
                    else:
                        tt(tokens(V_D, c), v4(psum("do", P)), v4(aden), ALU.mult).then_inc(*did("Od"))
                        if c == 0:
                            dve.wait_ge(zeroed, 2)
                        dve.wait_ge(*after("pe", "sc"))
                        tt(v2(SC), v2(SC), v2(xb)[:, :, n - 1:n].to_broadcast([P, 2, P]), ALU.mult).then_inc(*did("GC"))
                        w_("GC")
                        tt(SC, SC, psum("sc", P)[:, 0:256], ALU.add).then_inc(*did("SC"))
                        dve.wait_ge(*after("pe", "sd"))
                        ends = v2(xw)[:, :, n - 1:n]
                        d4 = SD.rearrange("p (a t v) -> p a t v", a=2, t=2)
                        tt(d4, d4, ends[:, None].to_broadcast([P, 2, 2, P]), ALU.mult).then_inc(*did("GD"))
                        w_("GD")
                        tt(SD, SD, psum("sd", P), ALU.add).then_inc(*did("SD"))
                        if c == chunks[-1]:
                            w_("SD")
                            dve.tensor_copy(n_last, SD[:, 256:512:P]).then_inc(*sched.did("dve", "n_last"))


def finish_odd(k):
    nc = k.nc
    big = lambda t: k.big_buf[:, t * T:(t + 1) * T]
    sq = lambda i: k.arena[:, i * T:(i + 1) * T]
    N = range(8)
    src = lambda i: big(V_C + i) if i < 4 else big(V_D + i - 4)
    gate = lambda i: big(Z_C + i) if i < 4 else big(O_D + i - 4)
    with nc.cleanup_on_exit():
        s = Phase(nc)
        q = Schedule(s, pe=[f"sum{i}" for i in N], act=[f"{x}{i}" for x in ("sq", "root") for i in N],
                     dve=[f"{x}{i}" for i in N for x in ("inv", "gated", "out")])
        did, after = q.did, q.after
        with nc.Block() as block:
            @block.tensor
            def _(pe):
                for i in N:
                    pe.wait_ge(*after("act", f"sq{i}"))
                    if i >= 4:
                        pe.wait_ge(*after("act", f"root{i - 4}"))
                    for a in range(2):
                        last = pe.matmul(k.psum_pair(i % 4)[:, a, 0:HALF], k.mask("ones"),
                                         sq(i)[:, a * HALF:(a + 1) * HALF], start=True, stop=True)
                    last.then_inc(*did("pe", f"sum{i}"))

            @block.scalar
            def _(act):
                for i in N:
                    act.activation(sq(i), src(i), ACT.Square).then_inc(*did("act", f"sq{i}"))
                for i in N:
                    act.wait_ge(*after("pe", f"sum{i}"))
                    act.activation(sq(i).rearrange("p (a t) -> p a t", a=2), two_halves(k.psum_pair(i % 4), HALF),
                                   ACT.Sqrt, bias=k.eps[:, 0:1], scale=1.0 / P).then_inc(*did("act", f"root{i}"))

            @block.vector
            def _(dve):
                for i in N:
                    dve.wait_ge(*after("act", f"root{i}"))
                    dve.reciprocal(sq(i), sq(i)).then_inc(*did("dve", f"inv{i}"))
                    dve.wait_ge(*after("dve", f"inv{i}"))
                    gain = k.par("gain_c") if i < 4 else k.par("gain_d")
                    dve.scalar_tensor_tensor(out=sq(i), in0=sq(i), scalar=gain, in1=gate(i), op0=ALU.mult,
                                             op1=ALU.mult).then_inc(*did("dve", f"gated{i}"))
                    dve.wait_ge(*after("dve", f"gated{i}"))
                    dve.tensor_tensor(src(i), src(i), sq(i), ALU.mult).then_inc(*did("dve", f"out{i}"))


def odd_mixer(k, sublayer):
    normalise(k, sublayer, k.low_r[:, H_LOW - LOW:PROJECTION_END - LOW])
    project_odd(k)
    prepare_odd(k)
    odd_chunks(k, sample=False)
    odd_chunks(k, sample=True)
    finish_odd(k)
    tile = lambda kt: V_C + kt if kt < 4 else V_D + kt - 4
    mixer_output(k, k.io["w_out_odd"], lambda kt: k.big_buf[:, tile(kt) * T:(tile(kt) + 1) * T], sublayer)


class Kernel:

    def __init__(self, nc, io):
        def sb(name, cols):
            return nc.alloc_sbuf_tensor(name, [P, cols], F32)[:]

        def rounded(name, cols, at=0):
            return nc.alloc_sbuf_tensor_at(name, [P, cols], F32R, offset=start + at * 4)[:]
        self.nc = nc
        self.io = io
        self.masks = sb("masks", N_MASK * P)
        self.bigs = sb("bigs", len(BIGS) * P)
        self.params = sb("params", N_PARAM)
        self.selection = sb("selection", 6 * P)
        self.work = sb("work", WORK)
        start = nc.sbuf_base - (WORK - KT * T) * 4
        self.weights_r = rounded("weights_r", H_LOW)
        self.low_r = rounded("low_r", ARENA - LOW, at=LOW)
        self.mixed_r = rounded("mixed_r", 2 * KT * T)
        self.x = self.work[:, 0:KT * T]
        self.arena = self.work[:, KT * T:]
        self.x_kept = nc.dram_tensor("x_kept", (P, KT * T), F32, kind="Internal").ap()
        self.h = sb("h", KT * TX)
        start = nc.sbuf_base - KT * TX * 4
        self.h_r = rounded("h_r", KT * TX)
        self.big_buf = sb("big_buf", 30 * T)
        start = nc.sbuf_base - 30 * T * 4
        self.big_r = rounded("big_r", 30 * T)
        self.h_low_ff = self.big_r[:, FT * T:]
        self.mods = [sb(f"mod{i}", MT * NC) for i in range(2)]
        self.cs = sb("cs", KT * NC)
        self.gated = sb("gated", 4 * (T - TP))
        self.resets = sb("resets", T)
        self.eps = sb("eps", 4)
        self.rows = sb("rows", T)
        self.cols = sb("cols", 5 * 16)
        self.pairs = [nc.alloc_psum_tensor(f"banks{b}", [P, 2, 512], F32)[:] for b in range(4)]
        self.psum = [self.pairs[b // 2][:, b % 2, :] for b in range(8)]
        self.cs_tmp = self.arena[:, 0:KT * NC]
        self.lc = self.arena[:, ARENA - 4 * T:]
        self.rows_b = self.arena[:, ARENA - 5 * T:ARENA - 4 * T]
        self.mrows = self.arena[0:4, ARENA - 3 * T:]

    def psum_pair(self, b):
        return self.pairs[b]

    def mask(self, name):
        at = MASKS.index(name) * P
        return self.masks[:, at:at + P]

    def big(self, name):
        at = BIGS.index(name) * P
        return self.bigs[:, at:at + P]

    def par(self, name):
        at, width = PARAM[name]
        return self.params[:, at:at + width]

    def select(self, h):
        return self.selection[:, h * P:(h + 1) * P]


def build(nc, io):
    k = Kernel(nc, io)
    setup(k)
    first_modulation(k)
    for layer in range(DEPTH):
        normalise(k, 3 * layer, k.h_low_ff)
        feed_forward(k, 3 * layer)
        if layer % 2 == 0:
            even_mixer(k, 3 * layer + 1)
        else:
            odd_mixer(k, 3 * layer + 1)
        normalise(k, 3 * layer + 2, k.h_low_ff)
        feed_forward(k, 3 * layer + 2)
    normalise(k, 3 * DEPTH, final=True)


def tile_weights(w):
    c, m = w.shape
    return w.reshape(c // P, P, m // P, P).transpose(2, 1, 0, 3).reshape(m // P, P, c)


def by_feature(v):
    n, f = v.shape
    return v.reshape(n, f // P, P).transpose(2, 0, 1).reshape(P, n * (f // P))


def pack(i):
    import numpy as np
    i = {n: np.asarray(v) for n, v in i.items()}
    cat = np.concatenate

    def column(v):
        out = np.zeros((P, 1), np.float32)
        out[:v.size, 0] = v.ravel()
        return out

    def padded(w, pieces):
        out = np.zeros((w.shape[0], P), np.float32)
        for at, lo, n in pieces:
            out[:, at:at + n] = w[:, lo:lo + n]
        return out

    x = cat([i["x_prompt"].reshape(TP, D), i["x_sample"].reshape(NSEQ * TS, D)])
    c = cat([i["c_prompt"], i["c_sample"]])
    we, wo = i["w_in_even"][0], i["w_in_odd"][0]
    a_end = 3 * 512
    b0 = 3 * 512 + 8 + 512
    even = cat([we[:, 0:a_end], we[:, b0:b0 + 1792], we[:, a_end + 8:b0], padded(we, [(0, a_end, 4), (32, a_end + 4, 4)])],
               axis=1)
    c_lr, c_z, d0 = 1024, 1040, 1552
    odd = cat([wo[:, 0:c_lr], wo[:, c_z:d0], wo[:, d0:d0 + 1024], wo[:, d0 + 1032:],
               padded(wo, [(0, c_lr, 16), (32, d0 + 1024, 4), (64, d0 + 1028, 4)])], axis=1)
    params = {
        "b_mod": by_feature(i["b_mod"].reshape(DEPTH * 9, D)),
        "norm_gain": by_feature(i["norm_gain"].reshape(DEPTH * 3, D)),
        "final_gain": by_feature(i["final_gain"][None]),
        "conv_w": i["conv_w"][0].reshape(CONV_W, 12, P).transpose(2, 1, 0).reshape(P, 48),
        "mu": by_feature(i["mu_b"]), "w0": by_feature(i["w0_b"]), "a0": by_feature(i["a0_b"]),
        "k_k": by_feature(i["k_k"]), "k_a": by_feature(i["k_a"]), "r_k": by_feature(i["r_k"].reshape(1, 512)),
        "lnx_gain": by_feature(i["lnx_gain"]), "lnx_bias": by_feature(i["lnx_bias"]),
        "gain_a": i["gain_a"].T, "a_log": column(i["a_log"]), "dt_bias": column(i["dt_bias"]),
        "b_gk": by_feature(i["b_gk"]), "gain_c": i["gain_c"].T, "gain_d": i["gain_d"].T,
        "b_i": column(i["b_i"]), "b_f": column(i["b_f"]),
    }
    selection = np.zeros((P, 6, P), np.float32)
    for h in range(4):
        selection[h, h] = 1.0
        selection[h, 4 + h // 2, 64 * (h % 2):64 * (h % 2) + 64] = 1.0
    ff = cat([tile_weights(i[n][l, s])[:, :, None] for l in range(DEPTH) for s in range(2) for n in ("w_ffn_gate",)])
    fu = cat([tile_weights(i["w_ffn_up"][l, s])[:, :, None] for l in range(DEPTH) for s in range(2)])
    pair_state = lambda v: v[0].reshape(NSEQ, -1, 2, v.shape[-2], v.shape[-1]).transpose(2, 3, 1, 0, 4)
    arrays = {
        "x_in": x.reshape(T, KT, P).transpose(2, 1, 0).reshape(P, KT * T),
        "c_in": c.reshape(NC, KT, P).transpose(2, 1, 0).reshape(P, KT * NC),
        "params_in": cat([params[n] for n, _ in PARAM_WIDTHS], axis=1),
        "selection_in": selection.reshape(P, 6 * P),
        "w_mod": i["w_mod"].reshape(DEPTH, KT, P, 3, 2, MOD_W).transpose(0, 3, 1, 4, 2, 5).reshape(-1, P, MOD_W),
        "w_ff": cat([ff, fu], axis=2).reshape(-1, P, 2 * D),
        "w_down": cat([tile_weights(i["w_ffn_down"][l, s]) for l in range(DEPTH) for s in range(2)]),
        "w_in_even": tile_weights(even), "w_out_even": tile_weights(i["w_out_even"][0]),
        "w_in_odd": tile_weights(odd), "w_out_odd": tile_weights(i["w_out_odd"][0]),
        "w_wa2": cat([i["w_w2"][0], i["w_a2"][0]]), "w_g2": i["w_g2"][0], "w_gk2": i["w_gk2"][0],
        "xbuf_in": i["state_xbuf_even"][0].reshape(NSEQ, PAD, KT, P).transpose(3, 2, 0, 1),
        "delta_in": i["state_delta"][0].transpose(2, 1, 0, 3).reshape(P, 32 * P),
        "rwkv_in": pair_state(i["state_rwkv"].swapaxes(-1, -2)).reshape(P, 4 * NSEQ * 64),
        "gla_in": pair_state(i["state_gla"]).reshape(P, 2 * NSEQ * P),
        "mc_in": pair_state(i["state_mlstm_c"]).reshape(P, 2 * NSEQ * P),
        "mn_in": pair_state(i["state_mlstm_n"][..., None]).reshape(P, 2 * NSEQ),
        "mm_in": i["state_mlstm_m"][0].T,
    }
    return {n: np.ascontiguousarray(a, dtype=np.float32) for n, a in arrays.items()}


OUTPUTS = {
    "y_out": (P, KT, T), "xbuf_p_out": (P, KT, PAD), "xbuf_s_out": (P, KT, NSEQ, PAD),
    "delta_p_out": (P, 512), "delta_s_out": (P, 32 * P), "rwkv_p_out": (P, 256), "rwkv_s_out": (P, 2048),
    "gla_p_out": (P, 256), "gla_s_out": (P, 2048), "mc_p_out": (P, 256), "mc_s_out": (P, 2048),
    "mn_p_out": (P, 2), "mn_s_out": (P, 16), "mm_p_out": (4, 1), "mm_s_out": (4, NSEQ),
}


def unpack(o):
    import numpy as np
    y = o["y_out"].transpose(2, 1, 0).reshape(T, D)

    def pair_state(v, seqs, rows, cols):
        v = v.reshape(2, rows, -1, seqs, cols).transpose(3, 2, 0, 1, 4)
        return v.reshape(1, seqs, -1, rows, cols)
    out = (
        y[:TP].reshape(1, TP, D), y[TP:].reshape(NSEQ, TS, D),
        o["xbuf_p_out"].transpose(2, 1, 0).reshape(1, 1, PAD, D),
        o["xbuf_s_out"].transpose(2, 3, 1, 0).reshape(1, NSEQ, PAD, D),
        o["delta_p_out"].reshape(P, 4, 1, P).transpose(2, 1, 0, 3)[None],
        o["delta_s_out"].reshape(P, 4, NSEQ, P).transpose(2, 1, 0, 3)[None],
        pair_state(o["rwkv_p_out"], 1, 64, 64).swapaxes(-1, -2),
        pair_state(o["rwkv_s_out"], NSEQ, 64, 64).swapaxes(-1, -2),
        pair_state(o["gla_p_out"], 1, 64, P), pair_state(o["gla_s_out"], NSEQ, 64, P),
        pair_state(o["mc_p_out"], 1, 64, P), pair_state(o["mc_s_out"], NSEQ, 64, P),
        pair_state(o["mn_p_out"], 1, 64, 1)[..., 0], pair_state(o["mn_s_out"], NSEQ, 64, 1)[..., 0],
        o["mm_p_out"].T[None], o["mm_s_out"].T[None],
    )
    return tuple(np.ascontiguousarray(v) for v in out)


def kernel(**inputs):
    import concourse.bacc as bacc
    from concourse.bass_utils import run_bass_kernel_spmd
    arrays = pack(inputs)
    nc = bacc.Bacc("TRN2", target_bir_lowering=False, num_devices=1)
    io = {n: nc.dram_tensor(n + "_dram", a.shape, F32, kind="ExternalInput").ap() for n, a in arrays.items()}
    io |= {n: nc.dram_tensor(n + "_dram", s, F32, kind="ExternalOutput").ap() for n, s in OUTPUTS.items()}
    build(nc, io)
    r = run_bass_kernel_spmd(nc, [{n + "_dram": a for n, a in arrays.items()}], core_ids=[0])
    return unpack({n: r.results[0][n + "_dram"] for n in OUTPUTS})
```

```python
import concourse.bass as bass
from concourse import mybir

F32 = mybir.dt.float32
F32R = mybir.dt.float32r
ACT = mybir.ActivationFunctionType
ALU = mybir.AluOpType

P = 128
D = 1024
KT = D // P
TP = 512
NSEQ = 8
TS = 8
T = TP + NSEQ * TS
NC = 1 + NSEQ
CONV_W = 4
PAD = CONV_W - 1
TX = TP + NSEQ * (TS + PAD)
HALF = T // 2
HALFX = TX // 2
DFF = 2816
FT = DFF // P
DEPTH = 2
MT = 3 * KT
EPS = 1e-6
GN_EPS = 64e-5
BIG = 1e30
CH = 128
NCH = TP // CH
NEG_E_HALF = -0.6065306597126334

PARAM_WIDTHS = [
    ("b_mod", DEPTH * 9 * KT), ("norm_gain", DEPTH * 3 * KT), ("final_gain", KT),
    ("conv_w", 12 * CONV_W), ("mu", 14), ("w0", 4), ("a0", 4), ("k_k", 4), ("k_a", 4), ("r_k", 4),
    ("lnx_gain", 4), ("lnx_bias", 4), ("gain_a", 1), ("a_log", 1), ("dt_bias", 1),
    ("b_gk", 2), ("gain_c", 1), ("gain_d", 1), ("b_i", 1), ("b_f", 1),
]
PARAM = {}
_at = 0
for _n, _w in PARAM_WIDTHS:
    PARAM[_n] = (_at, _w)
    _at += _w
N_PARAM = _at

WORK = 24744
ARENA = WORK - KT * T
RAW_SLOTS, SPLIT_SLOTS = 4, 2
H_LOW = (RAW_SLOTS + 2 * SPLIT_SLOTS) * D
PROJECTION_END = H_LOW + KT * TX
LOW = ARENA - FT * T


def two_halves(bank_pair, width):
    return bank_pair[:, :, 0:width]


class Phase:

    def __init__(self, nc):
        self.nc, self.sems = nc, {}

    def sem(self, name):
        if name not in self.sems:
            self.sems[name] = self.nc.alloc_semaphore(f"{name}_{self.nc.next_id()}")
        return self.sems[name]


MASKS = ("ident ones below above above_eq block8 block16 block32 block64 level16 level32 level64 "
         "below8 above8 above_eq8 above16 above_eq16 above_level16 above_level32 above_level64").split()
N_MASK = len(MASKS)
BIGS = "not_below not_above_eq outside8 not_below8 not_above_eq8".split()


MOD_W = MT * P // 2
MOD_G = MOD_W // 4
MOD_STEPS = 2 * KT
MOD_ROOM = 2 * MOD_W + 2 * MOD_G


class Modulation:

    def __init__(self, k, s, sublayer, slots):
        self.k, self.sublayer, self.slot, slots = k, sublayer, slots, len(slots)
        self.landed = [s.sem(f"mod_landed{b}") for b in range(slots)]
        self.done, self.cleared, self.copied, self.turned, self.biased, self.finished = (
            s.sem(n) for n in ("mod_done", "mod_cleared", "mod_copied", "mod_turned", "mod_biased",
                               "mod_finished"))
        self.by_vector = k.h[:, 2 * MOD_W:MOD_ROOM]
        self.row0 = sublayer * MOD_STEPS

    def load(self, sp, slot, step):
        at = self.row0 + step
        src = self.k.io["w_mod"][at] if isinstance(step, int) else \
            self.k.io["w_mod"][bass.ds(at, 1)].rearrange("a p n -> (a p) n")
        sp.dma_start(self.slot[slot], src).then_inc(self.landed[slot], 16)

    def clear(self, pool):
        pool.memset(self.by_vector, 0.0).then_inc(self.cleared, 1)

    def products(self, pe, kt, slot, half, wait_landed):
        k = self.k
        pe.wait_ge(self.landed[slot], wait_landed)
        for j in range(4):
            last = pe.matmul(k.psum[6 + half][32 * j:32 * j + NC, 0:MOD_G], k.cs[:, kt * NC:(kt + 1) * NC],
                             self.slot[slot][:, j * MOD_G:(j + 1) * MOD_G], start=kt == 0, stop=kt == KT - 1)
        last.then_inc(self.done, 1)

    def copy(self, act):
        act.wait_ge(self.cleared, 1)
        act.wait_ge(self.done, MOD_STEPS)
        for j in range(4):
            at = slice(32 * j, 32 * j + NC)
            last = act.activation(self.by_vector[at].rearrange("p (a n) -> p a n", a=2),
                                  self.k.psum_pair(3)[at, :, 0:MOD_G], ACT.Copy)
        last.then_inc(self.copied, 1)

    def turn(self, pe):
        pe.wait_ge(self.copied, 1)
        for half in range(2):
            for b in range(3):
                at = half * MOD_G + b * P
                last = pe.transpose(self.k.psum[4 + half][:, b * P:(b + 1) * P], self.by_vector[:, at:at + P],
                                    self.k.mask("ident"))
        last.then_inc(self.turned, 1)

    def finish(self, dve):
        k, mod = self.k, self.k.mods[self.sublayer % 2]
        bias = k.par("b_mod")[:, self.sublayer * MT:(self.sublayer + 1) * MT]
        dve.wait_ge(self.turned, 1)
        for half in range(2):
            tiles = slice(half * MT // 2, (half + 1) * MT // 2)
            dve.tensor_tensor(
                mod[:, tiles.start * NC:tiles.stop * NC].rearrange("p (j b s) -> p j b s", j=4, s=NC),
                k.psum[4 + half][:, 0:3 * P].rearrange("p (b j i) -> p j b i", b=3, i=32)[:, :, :, 0:NC],
                bias[:, tiles].rearrange("p (j b) -> p j b", j=4)[:, :, :, None].to_broadcast([P, 4, 3, NC]),
                ALU.add).then_inc(self.biased, 1)
        dve.wait_ge(self.biased, 2)
        mod = mod.rearrange("p (m s) -> p m s", s=NC)
        gain = k.par("norm_gain")[:, self.sublayer * KT:(self.sublayer + 1) * KT, None].to_broadcast([P, KT, NC])
        dve.scalar_tensor_tensor(out=mod[:, KT:2 * KT], in0=mod[:, KT:2 * KT], scalar=1.0, in1=gain,
                                 op0=ALU.add, op1=ALU.mult).then_inc(self.finished, 1)
        weight = 1.0 if self.sublayer % 3 == 1 else 0.5
        dve.tensor_scalar(mod[:, 2 * KT:3 * KT], mod[:, 2 * KT:3 * KT], 1.0, weight, ALU.add, ALU.mult)\
            .then_inc(self.finished, 1)


def setup(k):
    nc = k.nc
    SLOTS = 8
    with nc.cleanup_on_exit():
        s = Phase(nc)
        mod = Modulation(k, s, 0, [k.arena[:, b * MOD_W:(b + 1) * MOD_W] for b in range(SLOTS)])
        stats = Statistics(k, s)
        loaded, ones_ready, base_ready, masks_ready, sig_ready, cs_ready = (
            s.sem(n) for n in ("loaded", "ones_ready", "base_ready", "masks_ready", "sig_ready", "cs_ready"))
        with nc.Block() as block:
            @block.sync
            def _(sp):
                sp.dma_start(k.cs, k.io["c_in"]).then_inc(loaded, 16)
                sp.dma_start(k.x, k.io["x_in"]).then_inc(loaded, 16)
                sp.dma_start(k.params, k.io["params_in"]).then_inc(loaded, 16)
                sp.dma_start(k.selection, k.io["selection_in"]).then_inc(loaded, 16)
                for i in range(SLOTS):
                    mod.load(sp, i, i)
                with sp.Fori(1, MOD_STEPS // SLOTS) as r:
                    for b in range(SLOTS):
                        sp.wait_ge(mod.done, (r - 1) * SLOTS + b + 1)
                        mod.load(sp, b, r * SLOTS + b)

            @block.gpsimd
            def _(pool):
                m = k.masks
                pool.memset(k.eps[:, 0:1], EPS)
                pool.memset(k.eps[:, 1:2], GN_EPS)
                pool.memset(k.eps[:, 2:3], 1.0)
                pool.memset(m[:, 0:N_MASK * P], 1.0).then_inc(ones_ready, 1)
                pool.memset(k.resets, 1.0).then_inc(ones_ready, 1)
                pool.memset(k.bigs, 0.0).then_inc(ones_ready, 1)
                pool.wait_ge(ones_ready, 3)

                def keep(name, op, base, cm, step, fill=0.0, view=None):
                    v = view if view is not None else k.mask(name)
                    return pool.affine_select(out=v, in_=v, compare_op=op, fill=fill, base=base,
                                              pattern=[[step, P]], channel_multiplier=cm)
                keep("ident", ALU.is_equal, 0, 1, -1)
                keep("below", ALU.is_gt, 0, 1, -1)
                keep("above", ALU.is_gt, 0, -1, 1)
                keep("above_eq", ALU.is_ge, 0, -1, 1)
                keep(None, ALU.is_gt, 0, 1, -1, fill=BIG, view=k.big("not_below"))
                keep(None, ALU.is_ge, 0, -1, 1, fill=BIG, view=k.big("not_above_eq"))
                for w in (8, 16, 32, 64):
                    v = k.mask(f"block{w}").rearrange("p (b i) -> p b i", i=w)
                    pool.affine_select(out=v, in_=v, compare_op=ALU.is_ge, fill=0.0, base=0,
                                       pattern=[[-w, P // w], [0, w]], channel_multiplier=1)
                last = pool.memset(k.resets[:, 0:TP].rearrange("p (c i) -> p c i", i=CH)[:, :, 0:1], 0.0)
                last = pool.memset(k.resets[:, TP:T].rearrange("p (c i) -> p c i", i=TS)[:, :, 0:1], 0.0)
                last.then_inc(base_ready, 1)
                pool.wait_ge(base_ready, 1)
                for w in (8, 16, 32, 64):
                    v = k.mask(f"block{w}").rearrange("p (b i) -> p b i", i=w)
                    last = pool.affine_select(out=v, in_=v, compare_op=ALU.is_ge, fill=0.0, base=w - 1,
                                              pattern=[[w, P // w], [0, w]], channel_multiplier=-1)
                last.then_inc(base_ready, 1)
                pool.wait_ge(base_ready, 2)
                for w in (16, 32, 64):
                    outer = k.mask("ones") if w == 64 else k.mask(f"block{2 * w}")
                    pool.tensor_tensor(k.mask(f"level{w}"), outer, k.mask(f"block{w}"), ALU.subtract)
                pool.tensor_tensor(k.mask("below8"), k.mask("below"), k.mask("block8"), ALU.mult)
                pool.tensor_tensor(k.mask("above8"), k.mask("above"), k.mask("block8"), ALU.mult)
                pool.tensor_tensor(k.mask("above_eq8"), k.mask("above_eq"), k.mask("block8"), ALU.mult)
                pool.tensor_tensor(k.mask("above_eq16"), k.mask("above_eq"), k.mask("block16"), ALU.mult)
                pool.tensor_tensor(k.mask("above16"), k.mask("above"), k.mask("block16"), ALU.mult)
                pool.tensor_scalar(k.big("outside8"), k.mask("block8"), -BIG, BIG, ALU.mult, ALU.add)\
                    .then_inc(base_ready, 1)
                pool.wait_ge(base_ready, 3)
                for w in (16, 32, 64):
                    pool.tensor_tensor(k.mask(f"above_level{w}"), k.mask("above"), k.mask(f"level{w}"), ALU.mult)
                for a, b in (("not_below8", "not_below"), ("not_above_eq8", "not_above_eq")):
                    last = pool.tensor_tensor(k.big(a), k.big("outside8"), k.big(b), ALU.add)
                last.then_inc(masks_ready, 1)
                mod.clear(pool)
                stats.add_tiles(pool)

            @block.tensor
            def _(pe):
                pe.wait_ge(cs_ready, 1)
                for i in range(MOD_STEPS):
                    mod.products(pe, i // 2, i % SLOTS, i % 2, (i // SLOTS + 1) * 16)
                pe.wait_ge(masks_ready, 1)
                stats.sum_features(pe)
                mod.turn(pe)

            @block.scalar
            def _(act):
                act.wait_ge(loaded, 64)
                act.activation(k.cs_tmp, k.cs, ACT.Sigmoid).then_inc(sig_ready, 1)
                for m in range(KT):
                    stats.square_tile(act, m)
                stats.root(act)
                mod.copy(act)

            @block.vector
            def _(dve):
                dve.wait_ge(sig_ready, 1)
                dve.tensor_tensor(k.cs, k.cs, k.cs_tmp, ALU.mult).then_inc(cs_ready, 1)
                stats.invert(dve)
                dve.wait_ge(loaded, 64)
                mod.finish(dve)


def split_high(act, raw, high):
    return act.activation(high, raw, ACT.Copy)


def split_low(engine, raw, high, low):
    return engine.tensor_tensor(low, raw, high.bitcast(F32), ALU.subtract)


def split_products(pe, pair, width, w_high, w_low, tokens, first, last):
    x = [tokens(a) for a in range(2)]
    for a in range(2):
        pe.matmul(pair[:, a, 0:width], w_low, x[a][0], start=first, stop=False)
    for a in range(2):
        pe.matmul(pair[:, a, 0:width], w_high, x[a][1], start=False, stop=False)
    for a in range(2):
        done = pe.matmul(pair[:, a, 0:width], w_high, x[a][0], start=False, stop=last)
    return done


def tokens_of(high, low, stride_high, stride_low, width):
    return lambda kt: lambda a: (high[:, kt * stride_high + a * width:kt * stride_high + (a + 1) * width],
                                 low[:, kt * stride_low + a * width:kt * stride_low + (a + 1) * width])


class Statistics:

    def __init__(self, k, s):
        self.k = k
        self.squared, self.added, self.summed, self.rooted, self.inverse = (
            s.sem(n) for n in ("squared", "added", "summed", "rooted", "inverse"))
        self.square = k.h[:, MOD_ROOM:MOD_ROOM + T]

    def square_tile(self, act, m):
        if m >= 2:
            act.wait_ge(self.added, m - 1)
        act.activation(self.k.rows if m == 0 else self.square, self.k.x[:, m * T:(m + 1) * T], ACT.Square)\
            .then_inc(self.squared, 1)

    def add_tiles(self, pool):
        for m in range(1, KT):
            pool.wait_ge(self.squared, m + 1)
            if m >= 2:
                pool.wait_ge(self.added, m - 1)
            pool.tensor_tensor(self.k.rows, self.k.rows, self.square, ALU.add).then_inc(self.added, 1)

    def sum_features(self, pe):
        pe.wait_ge(self.added, KT - 1)
        for a in range(2):
            last = pe.matmul(self.k.psum_pair(0)[:, a, 0:HALF], self.k.mask("ones"),
                             self.k.rows[:, a * HALF:(a + 1) * HALF], start=True, stop=True)
        last.then_inc(self.summed, 1)

    def root(self, act):
        act.wait_ge(self.summed, 1)
        act.activation(self.square.rearrange("p (a t) -> p a t", a=2), two_halves(self.k.psum_pair(0), HALF),
                       ACT.Sqrt, bias=self.k.eps[:, 0:1], scale=1.0 / D).then_inc(self.rooted, 1)

    def invert(self, dve):
        dve.wait_ge(self.rooted, 1)
        dve.reciprocal(self.k.rows, self.square).then_inc(self.inverse, 1)


class Normalised:

    def __init__(self, k, s, sublayer, h_low, wide=False):
        self.k, self.wide = k, wide
        self.scaled, self.shifted, self.high_done, self.low_done, self.loaded, self.stored = (
            s.sem(n) for n in ("h_scaled", "rows_shifted", "h_high_done", "h_low_done", "buffered_loaded",
                               "buffered_stored"))
        self.last_rows = k.arena[:, ARENA - KT * PAD:].rearrange("p (k t) -> p k t", t=PAD)
        self.h = k.big_buf[:, 0:KT * TX].rearrange("p (k t) -> p k t", t=TX)
        self.high = k.h_r.rearrange("p (k t) -> p k t", t=TX)
        self.low = h_low.rearrange("p (k t) -> p k t", k=KT)
        self.end = TX if wide else T
        samples = self.h[:, :, TP:self.end].rearrange("p k (s t) -> p k s t", s=NSEQ)
        self.samples = samples[:, :, :, PAD:] if wide else samples
        self.mod = k.mods[sublayer % 2].rearrange("p (m s) -> p m s", s=NC)

    def load(self, sp):
        for kt in range(KT):
            sp.dma_start(self.h[:, kt, TP:TX].rearrange("p (s t) -> p s t", s=NSEQ)[:, :, 0:PAD],
                         self.k.io["xbuf_in"][:, kt]).then_inc(self.loaded, 16)

    def store(self, sp):
        sp.wait_ge(self.scaled, 3)
        for kt in range(KT):
            sp.dma_start(self.k.io["xbuf_s_out"][:, kt], self.h[:, kt, TP:TX].rearrange("p (s t) -> p s t", s=NSEQ)
                         [:, :, TS:]).then_inc(self.stored, 16)
        sp.wait_ge(self.shifted, 1)
        sp.dma_start(self.k.io["xbuf_p_out"], self.last_rows).then_inc(self.stored, 16)
        sp.wait_ge(self.stored, 16 + 16 * KT)

    def scale_samples(self, dve):
        k = self.k
        rs = k.rows[:, None, TP:T].to_broadcast([P, KT, T - TP]).rearrange("p k (s t) -> p k s t", s=NSEQ)
        x = k.x.rearrange("p (k t) -> p k t", t=T)[:, :, TP:T].rearrange("p k (s t) -> p k s t", s=NSEQ)
        shape = [P, KT, NSEQ, TS]
        dve.tensor_tensor(self.samples, x, rs, ALU.mult).then_inc(self.scaled, 1)
        dve.wait_ge(self.scaled, 1)
        dve.tensor_tensor(self.samples, self.samples, self.mod[:, KT:2 * KT, 1:NC, None].to_broadcast(shape),
                          ALU.mult).then_inc(self.scaled, 1)
        dve.wait_ge(self.scaled, 2)
        dve.tensor_tensor(self.samples, self.samples, self.mod[:, 0:KT, 1:NC, None].to_broadcast(shape), ALU.add)\
            .then_inc(self.scaled, 1)

    def scale_and_low(self, dve, first, last):
        k = self.k
        for kt in range(first, last):
            if kt < KT:
                dve.scalar_tensor_tensor(out=self.h[:, kt, 0:TP], in0=k.x[:, kt * T:kt * T + TP],
                                         scalar=self.mod[:, KT + kt, 0:1], in1=k.rows[:, 0:TP], op0=ALU.mult,
                                         op1=ALU.mult).then_inc(self.scaled, 1)
            if kt == 0:
                dve.wait_ge(self.high_done, 1)
                split_low(dve, self.h[:, :, TP:self.end], self.high[:, :, TP:self.end], self.low[:, :, TP:self.end])\
                    .then_inc(self.low_done, 1)
            else:
                dve.wait_ge(self.high_done, kt + 1)
                dve.scalar_tensor_tensor(out=self.low[:, kt - 1, 0:TP], in0=self.h[:, kt - 1, 0:TP],
                                         scalar=self.mod[:, kt - 1, 0:1], in1=self.high[:, kt - 1, 0:TP].bitcast(F32),
                                         op0=ALU.add, op1=ALU.subtract).then_inc(self.low_done, 1)
        if self.wide and last > KT:
            dve.tensor_tensor(self.last_rows, self.h[:, :, TP - PAD:TP], self.mod[:, 0:KT, 0:1]
                              .to_broadcast([P, KT, PAD]), ALU.add).then_inc(self.shifted, 1)

    def high_samples(self, act):
        act.wait_ge(self.scaled, 3)
        if self.wide:
            act.wait_ge(self.loaded, 16 * KT)
        split_high(act, self.h[:, :, TP:self.end], self.high[:, :, TP:self.end]).then_inc(self.high_done, 1)

    def high_tiles(self, act, first, last):
        for kt in range(first, last):
            act.wait_ge(self.scaled, kt + 4)
            act.activation(self.high[:, kt, 0:TP], self.h[:, kt, 0:TP], ACT.Identity, bias=self.mod[:, kt, 0:1])\
                .then_inc(self.high_done, 1)


def final_norm(k):
    nc = k.nc
    with nc.cleanup_on_exit():
        s = Phase(nc)
        scaled, stored = s.sem("scaled"), s.sem("stored")
        with nc.Block() as block:
            @block.vector
            def _(dve):
                for kt in range(KT):
                    dve.scalar_tensor_tensor(out=k.big_buf[:, kt * T:(kt + 1) * T], in0=k.x[:, kt * T:(kt + 1) * T],
                                             scalar=k.par("final_gain")[:, kt:kt + 1], in1=k.rows, op0=ALU.mult,
                                             op1=ALU.mult).then_inc(scaled, 1)

            @block.sync
            def _(sp):
                for kt in range(KT):
                    sp.wait_ge(scaled, kt + 1)
                    sp.dma_start(k.io["y_out"][:, kt], k.big_buf[:, kt * T:(kt + 1) * T]).then_inc(stored, 16)
                sp.wait_ge(stored, 16 * KT)


def add_gated(dve, k, product, gate, m, scratch, prompt_done, sample_done):
    x = k.x[:, bass.ds(m * T, T)]
    g = gate[:, bass.ds(m * NC, NC)]
    dve.scalar_tensor_tensor(out=x[:, 0:HALF], in0=product[:, 0, 0:HALF], scalar=g[:, 0:1],
                             in1=x[:, 0:HALF], op0=ALU.mult, op1=ALU.add)
    dve.scalar_tensor_tensor(out=x[:, HALF:TP], in0=product[:, 1, 0:TP - HALF], scalar=g[:, 0:1],
                             in1=x[:, HALF:TP], op0=ALU.mult, op1=ALU.add).then_inc(prompt_done, 1)
    per_token = g[:, 1:NC, None].to_broadcast([P, NSEQ, TS])
    dve.tensor_tensor(scratch.rearrange("p (s t) -> p s t", s=NSEQ),
                      product[:, 1, TP - HALF:HALF].rearrange("p (s t) -> p s t", s=NSEQ),
                      per_token, ALU.mult).then_inc(sample_done, 1)


def residual_product(k, weights, row0, n_in, sublayer, tokens, raw, split, mod_slots, source=None,
                     source_parts=None):
    nc = k.nc
    W = raw[0].shape[1]
    PIECES = n_in * P // W
    DEEP = W // P
    RAW, SPLIT = len(raw), len(split)
    with nc.cleanup_on_exit():
        s = Phase(nc)
        landed = [s.sem(f"out_landed{b}") for b in range(RAW)]
        high_done, low_done, source_high, source_low, piece_done, prompt_done, sample_done, taken = (
            s.sem(n) for n in ("high_done", "low_done", "source_high", "source_low", "piece_done", "prompt_done",
                                "sample_done", "taken"))
        gate = k.mods[sublayer % 2][:, 2 * KT * NC:3 * KT * NC]
        mod = Modulation(k, s, sublayer + 1, mod_slots) if sublayer + 1 < DEPTH * 3 else None
        MOD_SLOTS = len(mod_slots)
        stats = Statistics(k, s)
        with nc.Block() as block:
            @block.sync
            def _(sp):
                for m in range(KT):
                    for piece in range(m * PIECES, (m + 1) * PIECES):
                        if piece >= RAW:
                            sp.wait_ge(low_done, piece - RAW + 1)
                        at = piece % PIECES * W
                        sp.dma_start(raw[piece % RAW], weights[row0 + m][:, at:at + W]).then_inc(landed[piece % RAW], 16)
                    if mod:
                        for step in (2 * m, 2 * m + 1):
                            if step >= MOD_SLOTS:
                                sp.wait_ge(mod.done, step - MOD_SLOTS + 1)
                            mod.load(sp, step % MOD_SLOTS, step)

            @block.gpsimd
            def _(pool):
                if mod:
                    mod.clear(pool)
                stats.add_tiles(pool)

            @block.tensor
            def _(pe):
                for m in range(KT):
                    if m >= 2:
                        pe.wait_ge(taken, m - 1)
                    for piece in range(m * PIECES, (m + 1) * PIECES):
                        pe.wait_ge(low_done, piece + 1)
                        high, low = split[piece % SPLIT]
                        for i in range(DEEP):
                            kt = piece % PIECES * DEEP + i
                            if source and m == 0:
                                pe.wait_ge(source_low, kt + 1)
                            last = split_products(pe, k.psum_pair(m % 2), HALF, high[:, i * P:(i + 1) * P],
                                                  low[:, i * P:(i + 1) * P], tokens(kt), kt == 0, kt == n_in - 1)
                        last.then_inc(piece_done, 1)
                    if mod:
                        for step in (2 * m, 2 * m + 1):
                            mod.products(pe, m, step % MOD_SLOTS, step % 2, (step // MOD_SLOTS + 1) * 16)
                if mod:
                    mod.turn(pe)
                stats.sum_features(pe)

            @block.scalar
            def _(act):
                def high_part(piece):
                    act.wait_ge(landed[piece % RAW], (piece // RAW + 1) * 16)
                    if piece >= SPLIT:
                        act.wait_ge(piece_done, piece - SPLIT + 1)
                    split_high(act, raw[piece % RAW], split[piece % SPLIT][0]).then_inc(high_done, 1)
                high_part(0)
                if source:
                    for kt in range(n_in):
                        split_high(act, source(kt), source_parts(kt)[0]).then_inc(source_high, 1)
                squares = 0
                for piece in range(1, KT * PIECES):
                    high_part(piece)
                    while (squares + 1) * PIECES + SPLIT <= piece:
                        act.wait_ge(taken, squares + 1)
                        stats.square_tile(act, squares)
                        squares += 1
                if mod:
                    mod.copy(act)
                for m in range(squares, KT):
                    act.wait_ge(taken, m + 1)
                    stats.square_tile(act, m)
                stats.root(act)

            @block.vector
            def _(dve):
                def low_part(piece):
                    dve.wait_ge(high_done, piece + 1)
                    split_low(dve, raw[piece % RAW], *split[piece % SPLIT]).then_inc(low_done, 1)

                def add(m):
                    dve.wait_ge(piece_done, (m + 1) * PIECES)
                    scratch = k.gated[:, m % 4 * (T - TP):(m % 4 + 1) * (T - TP)]
                    add_gated(dve, k, k.psum_pair(m % 2), gate, m, scratch, prompt_done, sample_done)
                    dve.wait_ge(sample_done, m + 1)
                    xs = k.x[:, m * T + TP:(m + 1) * T]
                    dve.tensor_tensor(xs, xs, scratch, ALU.add).then_inc(taken, 1)
                low_part(0)
                if source:
                    for kt in range(n_in):
                        dve.wait_ge(source_high, kt + 1)
                        split_low(dve, source(kt), *source_parts(kt)).then_inc(source_low, 1)
                for piece in range(1, KT * PIECES):
                    low_part(piece)
                    if piece >= SPLIT and (piece - SPLIT) % PIECES == PIECES - 1:
                        add((piece - SPLIT) // PIECES)
                for m in range((KT * PIECES - SPLIT) // PIECES, KT):
                    add(m)
                if mod:
                    mod.finish(dve)
                stats.invert(dve)


def feed_forward(k, sublayer):
    nc = k.nc
    which = sublayer // 3 * 2 + sublayer % 3 // 2
    row0 = which * FT
    act_low = k.low_r
    raw = [k.arena[:, g * D:(g + 1) * D] for g in range(2)]
    split = [[k.weights_r[:, (2 + 2 * g + part) * D:(3 + 2 * g + part) * D] for part in range(2)] for g in range(2)]
    silu = [k.arena[:, 6 * D + b * T:6 * D + (b + 1) * T] for b in range(2)]
    assert 6 * D + 2 * T <= LOW
    with nc.cleanup_on_exit():
        s = Phase(nc)
        landed = [s.sem(f"ff_landed{g}") for g in range(2)]
        high_done, low_done, product, silu_done, act_done, act_high_done, act_low_done = (
            s.sem(n) for n in ("high_done", "low_done", "product", "silu_done", "act_done", "act_high_done",
                               "act_low_done"))
        tokens = tokens_of(k.h_r, k.h_low_ff, TX, T, HALF)
        norm = Normalised(k, s, sublayer, k.h_low_ff)
        pairs = FT // 2
        with nc.Block() as block:
            @block.sync
            def _(sp):
                for g in range(2):
                    sp.dma_start(raw[g], k.io["w_ff"][row0][:, g * D:(g + 1) * D]).then_inc(landed[g], 16)
                with sp.Fori(1, FT) as m:
                    for g in range(2):
                        sp.wait_ge(low_done, 2 * m + g - 1)
                        sp.dma_start(raw[g], k.io["w_ff"][bass.ds(row0 + m, 1)].rearrange("a p n -> (a p) n")
                                     [:, g * D:(g + 1) * D]).then_inc(landed[g], 16)

            @block.tensor
            def _(pe):
                def tile(b, m, first):
                    if not first:
                        pe.wait_ge(act_done, m - 1)
                    for g in range(2):
                        pe.wait_ge(low_done, 2 * m + g + 1)
                        high, low = split[g]
                        for kt in range(KT):
                            if first and b == 0 and g == 0:
                                pe.wait_ge(norm.low_done, kt + 2)
                            last = split_products(pe, k.psum_pair(2 * b + g), HALF, high[:, kt * P:(kt + 1) * P],
                                                  low[:, kt * P:(kt + 1) * P], tokens(kt), kt == 0, kt == KT - 1)
                        last.then_inc(product, 1)
                for b in range(2):
                    tile(b, b, True)
                with pe.Fori(1, pairs) as r:
                    for b in range(2):
                        tile(b, 2 * r + b, False)

            def halves(v):
                return v.rearrange("p (a t) -> p a t", a=2)

            @block.scalar
            def _(act):
                def high_parts(m, first=False):
                    for g in range(2):
                        act.wait_ge(landed[g], (m + 1) * 16)
                        if not first:
                            act.wait_ge(product, 2 * m + g - 1)
                        split_high(act, raw[g], split[g][0]).then_inc(high_done, 1)

                def activation(b, m, first):
                    act.wait_ge(product, 2 * m + 2)
                    if not first:
                        act.wait_ge(act_low_done, m - 1)
                    act.activation(halves(silu[b]), two_halves(k.psum_pair(2 * b), HALF), ACT.Silu)\
                        .then_inc(silu_done, 1)
                    act.wait_ge(act_done, m + 1)
                    split_high(act, silu[b], k.big_r[:, bass.ds(m * T, T)]).then_inc(act_high_done, 1)
                norm.high_samples(act)
                norm.high_tiles(act, 0, 2)
                high_parts(0, True)
                norm.high_tiles(act, 2, KT)
                high_parts(1)
                activation(0, 0, True)
                high_parts(2)
                activation(1, 1, True)
                with act.Fori(1, pairs - 1) as r:
                    for b in range(2):
                        high_parts(2 * r + b + 1)
                        activation(b, 2 * r + b, False)
                high_parts(FT - 1)
                activation(0, FT - 2, False)
                activation(1, FT - 1, False)

            @block.vector
            def _(dve):
                def low_parts(m):
                    for g in range(2):
                        dve.wait_ge(high_done, 2 * m + g + 1)
                        split_low(dve, raw[g], *split[g]).then_inc(low_done, 1)

                def activation(b, m):
                    dve.wait_ge(silu_done, m + 1)
                    dve.tensor_tensor(halves(silu[b]), halves(silu[b]), two_halves(k.psum_pair(2 * b + 1), HALF),
                                      ALU.mult).then_inc(act_done, 1)
                    dve.wait_ge(act_high_done, m + 1)
                    at = bass.ds(m * T, T)
                    split_low(dve, silu[b], k.big_r[:, at], act_low[:, at]).then_inc(act_low_done, 1)
                norm.scale_samples(dve)
                norm.scale_and_low(dve, 0, 2)
                low_parts(0)
                norm.scale_and_low(dve, 2, KT + 1)
                with dve.Fori(0, pairs - 1) as r:
                    for b in range(2):
                        low_parts(2 * r + b + 1)
                        activation(b, 2 * r + b)
                low_parts(FT - 1)
                activation(0, FT - 2)
                activation(1, FT - 1)
    W = FT * P // 2
    room = k.big_buf[:, FT * T:]
    residual_product(k, k.io["w_down"], which * KT, FT, sublayer, tokens_of(k.big_r, act_low, T, T, HALF),
                     raw=[room[:, i * W:(i + 1) * W] for i in range(3)],
                     split=[[k.weights_r[:, (2 * i + part) * W:(2 * i + part + 1) * W] for part in range(2)]
                            for i in range(2)],
                     mod_slots=[k.h[:, b * MOD_W:(b + 1) * MOD_W] for b in range(2)])


def mixer_output(k, weights, source, sublayer):
    at = 2 * KT * T
    split = k.low_r[:, at + 4 * D - LOW:]
    residual_product(k, weights, 0, KT, sublayer, tokens_of(k.mixed_r, k.mixed_r[:, KT * T:], T, T, HALF),
                     raw=[k.arena[:, at + i * D:at + (i + 1) * D] for i in range(4)],
                     split=[[split[:, (2 * i + part) * D:(2 * i + part + 1) * D] for part in range(2)] for i in range(2)],
                     mod_slots=[k.h[:, b * MOD_W:(b + 1) * MOD_W] for b in range(2)]
                     + [k.big_buf[:, 20 * T + b * MOD_W:20 * T + (b + 1) * MOD_W] for b in range(2)],
                     source=source,
                     source_parts=lambda kt: [k.mixed_r[:, (part * KT + kt) * T:(part * KT + kt + 1) * T]
                                              for part in range(2)])


class Schedule:

    def __init__(self, phase, **steps):
        self.count = {e: {n: i + 1 for i, n in enumerate(names)} for e, names in steps.items()}
        for e, names in steps.items():
            assert len(set(names)) == len(names), (e, [n for n in names if names.count(n) > 1])
        self.sems = {e: phase.sem(f"{e}_steps") for e in steps}
        self.said = {e: 0 for e in steps}

    def did(self, engine, name):
        self.said[engine] += 1
        assert self.count[engine][name] == self.said[engine], (engine, name)
        return self.sems[engine], 1

    def after(self, engine, name):
        return self.sems[engine], self.count[engine][name]


class SplitWeights:

    def __init__(self, k, s, weights, tiles):
        self.k, self.weights, self.tiles = k, weights, tiles
        self.landed = [s.sem(f"in_landed{b}") for b in range(RAW_SLOTS)]
        self.high_done, self.low_done, self.product = (s.sem(n) for n in ("high_done", "low_done", "product"))
        at = lambda room, i: room[:, i * D:(i + 1) * D]
        self.raw = [at(k.arena, b) for b in range(RAW_SLOTS)]
        self.split = [[at(k.weights_r, RAW_SLOTS + 2 * b + part) for part in range(2)] for b in range(SPLIT_SLOTS)]

    def load_first(self, sp):
        for b in range(RAW_SLOTS):
            sp.dma_start(self.raw[b], self.weights[b]).then_inc(self.landed[b], 16)

    def load_rest(self, sp):
        rounds = self.tiles // RAW_SLOTS
        with sp.Fori(1, rounds) as r:
            for b in range(RAW_SLOTS):
                sp.wait_ge(self.low_done, (r - 1) * RAW_SLOTS + b + 1)
                sp.dma_start(self.raw[b], self.weights[bass.ds(b + r * RAW_SLOTS, 1)]
                             .rearrange("a p n -> (a p) n")).then_inc(self.landed[b], 16)
        for b in range(self.tiles % RAW_SLOTS):
            sp.wait_ge(self.low_done, (rounds - 1) * RAW_SLOTS + b + 1)
            sp.dma_start(self.raw[b], self.weights[rounds * RAW_SLOTS + b]).then_inc(self.landed[b], 16)

    def high(self, act, raw_slot, split_slot, m, first=False):
        act.wait_ge(self.landed[raw_slot], (m - raw_slot) * (16 // RAW_SLOTS) + 16)
        if not first:
            act.wait_ge(self.product, m - 1)
        split_high(act, self.raw[raw_slot], self.split[split_slot][0]).then_inc(self.high_done, 1)

    def low(self, dve, raw_slot, split_slot, m):
        dve.wait_ge(self.high_done, m + 1)
        split_low(dve, self.raw[raw_slot], *self.split[split_slot]).then_inc(self.low_done, 1)

    def products(self, pe, tokens, width, evacuated, norm):
        def tile(b, m, first=False):
            pe.wait_ge(self.low_done, m + 1)
            if not first:
                pe.wait_ge(evacuated, m - 3)
            high, low = self.split[b % SPLIT_SLOTS]
            for kt in range(KT):
                if first and b == 0:
                    pe.wait_ge(norm.low_done, kt + 2)
                last = split_products(pe, self.k.psum_pair(b), width, high[:, kt * P:(kt + 1) * P],
                                      low[:, kt * P:(kt + 1) * P], tokens(kt), kt == 0, kt == KT - 1)
            last.then_inc(self.product, 1)
        for b in range(4):
            tile(b, b, first=True)
        with pe.Fori(1, self.tiles // 4) as r:
            for b in range(4):
                tile(b, 4 * r + b)
        for b in range(self.tiles % 4):
            tile(b, self.tiles // 4 * 4 + b)


class InverseRoots:

    def __init__(self, k, s, name, n, width, room):
        self.k, self.n, self.width = k, n, width
        self.per_tile = P // width
        self.units = n * self.per_tile
        self.pack, self.spread = room[:, 0:64], room[0:self.units, 64:64 + n * P]
        at = 64 + n * P
        self.roots, self.inverses = room[0:self.units, at:at + T], room[0:self.units, at + T:at + 2 * T]
        self.filled, self.ready = s.sem(f"{name}_filled"), s.sem(f"{name}_ready")

    @staticmethod
    def room(n):
        return 64 + n * P + 2 * T

    def constants(self, pool):
        pool.memset(self.pack, 0.0).then_inc(self.filled, 1)
        pool.memset(self.spread, 1.0).then_inc(self.filled, 1)
        pool.wait_ge(self.filled, 2)
        for i in range(self.per_tile):
            at = 32 - self.per_tile + i
            pool.memset(self.pack[i * self.width:(i + 1) * self.width, at:at + 1], 1.0)
        v = self.spread.rearrange("p (u i) -> p u i", i=self.width)
        pool.affine_select(out=v, in_=v, compare_op=ALU.is_equal, fill=0.0, base=0,
                           pattern=[[-1, self.units], [0, self.width]], channel_multiplier=1).then_inc(self.ready, 1)

    def sum_tile(self, pe, i, pair, squares):
        at = 32 - self.per_tile * (i + 1)
        if i == 0:
            pe.wait_ge(self.ready, 1)
        for a in range(2):
            last = pe.matmul(pair[0:self.units, a, 0:HALF], self.pack[:, at:at + self.units],
                             squares[:, a * HALF:(a + 1) * HALF], start=i == 0, stop=i == self.n - 1)
        return last

    def root(self, act, pair, eps, scale):
        return act.activation(self.roots.rearrange("p (a t) -> p a t", a=2), pair[0:self.units, :, 0:HALF], ACT.Sqrt,
                              bias=eps[0:self.units], scale=scale)

    def invert(self, dve):
        return dve.reciprocal(self.inverses, self.roots)

    def spread_tile(self, pe, i, pair):
        for a in range(2):
            last = pe.matmul(pair[:, a, 0:HALF], self.spread[:, i * P:(i + 1) * P],
                             self.inverses[:, a * HALF:(a + 1) * HALF], start=True, stop=True)
        return last


def project_even(k, sublayer):
    nc = k.nc
    NCONV, NMIX, NZ = 12, 14, 4
    TILES = NCONV + NMIX + NZ + 1
    with nc.cleanup_on_exit():
        s = Phase(nc)
        w = SplitWeights(k, s, k.io["w_in_even"], TILES)
        norm = Normalised(k, s, sublayer, k.low_r[:, H_LOW - LOW:PROJECTION_END - LOW], wide=True)
        product, cleared, staged, tile_done, chain = w.product, *(
            s.sem(n) for n in ("cleared", "staged", "tile_done", "chain"))
        SW = PAD + TX + 5
        stage = [k.arena[:, PROJECTION_END + b * SW:PROJECTION_END + (b + 1) * SW] for b in range(2)]
        delta = k.arena[:, PROJECTION_END + 2 * SW:PROJECTION_END + 2 * SW + T]
        rows = k.rows
        with nc.Block() as block:
            @block.sync
            def _(sp):
                norm.load(sp)
                w.load_first(sp)
                norm.store(sp)
                w.load_rest(sp)

            @block.tensor
            def _(pe):
                w.products(pe, tokens_of(k.h_r, k.low_r[:, H_LOW - LOW:], TX, TX, HALFX), HALFX, staged, norm)

            @block.scalar
            def _(act):
                def to_stage(b, pair, m, wait_free):
                    act.wait_ge(product, m + 1)
                    if wait_free is not None:
                        act.wait_ge(tile_done, wait_free)
                    act.activation(stage[b][:, PAD:PAD + TX].rearrange("p (a t) -> p a t", a=2),
                                   two_halves(k.psum_pair(pair), HALFX), ACT.Copy).then_inc(staged, 1)

                def compact(out, pair, rows_out):
                    ps = k.psum_pair(pair)[0:rows_out]
                    act.activation(out[0:rows_out, 0:HALFX], ps[:, 0, 0:HALFX], ACT.Copy)
                    act.activation(out[0:rows_out, HALFX:TP], ps[:, 1, 0:TP - HALFX], ACT.Copy)
                    return act.activation(
                        out[0:rows_out, TP:T].rearrange("p (s t) -> p s t", s=NSEQ),
                        ps[:, 1, TP - HALFX:HALFX].rearrange("p (s t) -> p s t", s=NSEQ)[:, :, PAD:], ACT.Copy)
                def high(b, m, first=False):
                    w.high(act, b % RAW_SLOTS, b % SPLIT_SLOTS, m, first)
                norm.high_samples(act)
                norm.high_tiles(act, 0, 2)
                high(0, 0, True)
                norm.high_tiles(act, 2, KT)
                high(1, 1, True)
                act.wait_ge(cleared, 2)
                for m in range(4):
                    high(m + 2, m + 2)
                    to_stage(m % 2, m, m, None if m < 2 else m - 1)
                with act.Fori(1, (NCONV + NMIX) // 4) as r:
                    for b in range(4):
                        high(b + 2, 4 * r + b + 2)
                        to_stage(b % 2, b, 4 * r + b, 4 * r + b - 1)
                for m in range((NCONV + NMIX) // 4 * 4, NCONV + NMIX):
                    high(m + 2, m + 2)
                    to_stage(m % 2, m % 4, m, m - 1)
                for i in range(NZ):
                    m = NCONV + NMIX + i
                    if m + 2 < TILES:
                        high(m + 2, m + 2)
                    act.wait_ge(product, m + 1)
                    compact(k.big_buf[:, (NCONV + i) * T:(NCONV + i + 1) * T], m % 4, P).then_inc(staged, 1)
                act.wait_ge(product, TILES)
                compact(rows, (TILES - 1) % 4, 64).then_inc(staged, 1)

            @block.vector
            def _(dve):
                for b in range(2):
                    dve.memset(stage[b][:, 0:PAD], 0.0).then_inc(cleared, 1)

                def views(b, shift):
                    return (stage[b][:, shift:shift + TP],
                            stage[b][:, PAD + TP:PAD + TX].rearrange("p (s t) -> p s t", s=NSEQ)
                            [:, :, shift:shift + TS])

                def conv(b, m):
                    dve.wait_ge(staged, m + 1)
                    out = k.big_buf[:, bass.ds(m * T, T)]
                    out_s = out[:, TP:T].rearrange("p (s t) -> p s t", s=NSEQ)
                    w = k.par("conv_w")[:, bass.ds(m * CONV_W, CONV_W)]
                    for j in range(CONV_W):
                        in_p, in_s = views(b, j)
                        if j == 0:
                            dve.tensor_scalar(out[:, 0:TP], in_p, w[:, 0:1], None, ALU.mult)
                            last = dve.tensor_scalar(out_s, in_s, w[:, 0:1], None, ALU.mult)
                        else:
                            dve.wait_ge(chain, m * (CONV_W - 1) + j)
                            dve.scalar_tensor_tensor(out=out[:, 0:TP], in0=in_p, scalar=w[:, j:j + 1],
                                                     in1=out[:, 0:TP], op0=ALU.mult, op1=ALU.add)
                            last = dve.scalar_tensor_tensor(out=out_s, in0=in_s, scalar=w[:, j:j + 1],
                                                            in1=out_s, op0=ALU.mult, op1=ALU.add)
                        if j < CONV_W - 1:
                            last.then_inc(chain, 1)
                        else:
                            last.then_inc(tile_done, 1)

                def mix(b, i):
                    dve.wait_ge(staged, NCONV + i + 1)
                    cur_p, cur_s = views(b, PAD)
                    prev_p, prev_s = views(b, PAD - 1)
                    out = k.big_buf[:, bass.ds((i + NCONV + NZ) * T, T)]
                    d_s = delta[:, TP:T].rearrange("p (s t) -> p s t", s=NSEQ)
                    dve.wait_ge(tile_done, NCONV + i)
                    dve.tensor_tensor(delta[:, 0:TP], prev_p, cur_p, ALU.subtract)
                    dve.tensor_tensor(d_s, prev_s, cur_s, ALU.subtract).then_inc(chain, 1)
                    dve.wait_ge(chain, NCONV * (CONV_W - 1) + i + 1)
                    mu = k.par("mu")[:, bass.ds(i, 1)]
                    dve.scalar_tensor_tensor(out=out[:, 0:TP], in0=delta[:, 0:TP], scalar=mu, in1=cur_p,
                                             op0=ALU.mult, op1=ALU.add)
                    dve.scalar_tensor_tensor(out=out[:, TP:T].rearrange("p (s t) -> p s t", s=NSEQ), in0=d_s,
                                             scalar=mu, in1=cur_s, op0=ALU.mult, op1=ALU.add)\
                        .then_inc(tile_done, 1)

                def low(b, m):
                    w.low(dve, b % RAW_SLOTS, b % SPLIT_SLOTS, m)
                norm.scale_samples(dve)
                norm.scale_and_low(dve, 0, 2)
                low(0, 0)
                norm.scale_and_low(dve, 2, KT + 1)
                low(1, 1)
                dve.wait_ge(norm.stored, 16 + 16 * KT)
                with dve.Fori(0, NCONV // 4) as r:
                    for b in range(4):
                        low(b + 2, 4 * r + b + 2)
                        conv(b % 2, 4 * r + b)
                with dve.Fori(0, NMIX // 4) as r:
                    for b in range(4):
                        low(b + 2, NCONV + 4 * r + b + 2)
                        mix(b % 2, 4 * r + b)
                for i in range(NMIX // 4 * 4, NMIX):
                    low(NCONV + i + 2, NCONV + i + 2)
                    mix(i % 2, i)
                for m in range(NCONV + NMIX + 2, TILES):
                    low(m, m)


Q_A, K_A, V_A, Z_A, R_B, K_B, V_B, LR_B, G_B = 0, 4, 8, 12, 16, 20, 24, 28, 29
NEG_KK, KK_A = 0, 4
ROW_GC, ROW_BETA, ROW_TO_END, COL_BETA_GC = 0, 1, 2, 3


def prepare_even(k):
    nc = k.nc
    big = lambda t, n=1: k.big_buf[:, t * T:(t + n) * T]
    hb = lambda t, n=1: k.h[:, t * T:(t + n) * T]
    sq = lambda i: k.arena[:, i * T:(i + 1) * T]
    rate = lambda i: k.arena[:, (12 + i) * T:(13 + i) * T]
    spare = lambda i: k.arena[:, (16 + i) * T:(17 + i) * T]
    w2 = k.arena[:, 20 * T:20 * T + 512]
    ea = k.arena[:, 20 * T + 520:20 * T + 521]
    softp = k.arena[0:4, 21 * T:22 * T]
    rows = k.rows
    N = range(12)
    act_steps = ([f"silu{i}" for i in range(4)] + ["tanh"] + [f"square{i}" for i in N]
                 + ["abs", "exp", "ln", "exp_a_log", "beta", "sig_g"]
                 + [f"sig_w{i}" for i in range(4)] + [f"sig_r{i}" for i in range(4)] + ["exp_to_end", "cols", "exp_gc"]
                 + ["root_qk", "root_kk"])
    dve_steps = (["rows_b", "rows_clear"] + [f"kk_raw{i}" for i in range(4)]
                 + ["relu", "softplus", "g", "gc", "to_end_p", "to_end_s"]
                 + [f"{n}{i}" for i in range(4) for n in ("w", "lc")]
                 + [f"{n}{i}" for i in range(4) for n in ("t", "k")]
                 + ["beta_gc"]
                 + ["inv_qk", "inv_kk"] + [f"unit{i}" for i in N] + [f"kka{i}" for i in range(4)])
    halves = lambda ap: ap.rearrange("p (a t) -> p a t", a=2)
    with nc.cleanup_on_exit():
        s = Phase(nc)
        q = Schedule(s, act=act_steps, dve=dve_steps,
                     pe=[f"w{i}" for i in range(4)] + [f"r{i}" for i in range(4)] + ["cols"]
                     + [f"sum{i}" for i in N] + [f"spread{i}" for i in N])
        at = 22 * T
        norm_qk = InverseRoots(k, s, "norm_qk", 8, P, k.arena[:, at:])
        norm_kk = InverseRoots(k, s, "norm_kk", 4, 64, k.arena[:, at + InverseRoots.room(8):])
        spread_pair = lambda i: k.psum_pair((3, 0, 1, 2)[i % 4])
        did, after = q.did, q.after
        loaded, kept = s.sem("w2_loaded"), s.sem("x_kept")
        with nc.Block() as block:
            @block.sync
            def _(sp):
                sp.dma_start(w2, k.io["w_wa2"]).then_inc(loaded, 16)
                sp.dma_start(k.x_kept, k.x).then_inc(kept, 16)
                sp.wait_ge(loaded, 16)
                sp.wait_ge(kept, 16)

            @block.gpsimd
            def _(pool):
                norm_qk.constants(pool)
                norm_kk.constants(pool)

            @block.scalar
            def _(act):
                for i in range(4):
                    act.activation(big(4 * i, 4), big(4 * i, 4), ACT.Silu).then_inc(*did("act", f"silu{i}"))
                act.activation(k.big_buf[0:64, LR_B * T:(LR_B + 1) * T], k.big_buf[0:64, LR_B * T:(LR_B + 1) * T],
                               ACT.Tanh).then_inc(*did("act", "tanh"))
                act.wait_ge(*after("act", "silu1"))
                for i in range(8):
                    act.activation(sq(i), big(Q_A + i), ACT.Square).then_inc(*did("act", f"square{i}"))
                for i in range(4):
                    act.wait_ge(*after("dve", f"kk_raw{i}"))
                    act.activation(sq(8 + i), hb(NEG_KK + i), ACT.Square).then_inc(*did("act", f"square{8 + i}"))
                act.wait_ge(*after("dve", "rows_b"))
                act.activation(softp, rows[0:4, :], ACT.Abs, bias=k.par("dt_bias")[0:4, :]).then_inc(*did("act", "abs"))
                act.wait_ge(*after("act", "abs"))
                act.activation(softp, softp, ACT.Exp, scale=-1.0).then_inc(*did("act", "exp"))
                act.wait_ge(*after("act", "exp"))
                act.activation(softp, softp, ACT.Ln, bias=1.0).then_inc(*did("act", "ln"))
                act.activation(ea[0:4, :], k.par("a_log")[0:4, :], ACT.Exp).then_inc(*did("act", "exp_a_log"))
                act.wait_ge(*after("dve", "rows_clear"))
                act.activation(rows[32:36, :], k.rows_b[0:4, :], ACT.Sigmoid).then_inc(*did("act", "beta"))
                act.activation(big(G_B), big(G_B), ACT.Sigmoid).then_inc(*did("act", "sig_g"))
                for n, bias in (("w", "w0"), ("r", "a0")):
                    for i in range(4):
                        act.wait_ge(*after("pe", f"{n}{i}"))
                        dst = spare(i) if n == "w" else rate(i)
                        act.activation(dst.rearrange("p (a t) -> p a t", a=2), two_halves(k.psum_pair(i), HALF),
                                       ACT.Sigmoid, bias=k.par(bias)[:, i:i + 1])\
                            .then_inc(*did("act", f"sig_{n}{i}"))
                act.wait_ge(*after("dve", "to_end_s"))
                act.activation(rows[64:68, :], rows[64:68, :], ACT.Exp).then_inc(*did("act", "exp_to_end"))
                act.wait_ge(*after("pe", "cols"))
                cols = k.cols.rearrange("p (c r h) -> p c r h", c=5, r=4)
                act.activation(cols[:, 0:4, 0:3], k.psum[0].rearrange("p (c r h) -> p c r h", c=4, r=4)
                               [:, :, 0:3, 0:4], ACT.Copy)
                act.activation(cols[0:64, 4, 0:3], k.psum[1][0:64, 0:128].rearrange("p (r h) -> p r h", r=4)
                               [:, 0:3, 0:4], ACT.Copy).then_inc(*did("act", "cols"))
                act.wait_ge(*after("act", "cols"))
                act.activation(cols[:, 0:4, 3], cols[:, 0:4, 0], ACT.Exp)
                act.activation(cols[0:64, 4, 3], cols[0:64, 4, 0], ACT.Exp).then_inc(*did("act", "exp_gc"))
                act.wait_ge(*after("pe", "sum7"))
                norm_qk.root(act, k.psum_pair(1), k.eps[:, 0:1], 1.0).then_inc(*did("act", "root_qk"))
                act.wait_ge(*after("pe", "sum11"))
                norm_kk.root(act, k.psum_pair(2), k.eps[:, 0:1], 1.0).then_inc(*did("act", "root_kk"))

            @block.tensor
            def _(pe):
                pe.wait_ge(loaded, 16)
                pe.wait_ge(*after("act", "tanh"))
                for n, lo in (("w", 0), ("r", 64)):
                    for i in range(4):
                        if n == "r":
                            pe.wait_ge(*after("act", f"sig_w{i}"))
                        for a in range(2):
                            at = LR_B * T + a * HALF
                            last = pe.matmul(k.psum_pair(i)[:, a, 0:HALF], w2[lo:lo + 64, i * P:(i + 1) * P],
                                             k.big_buf[lo:lo + 64, at:at + HALF], start=True, stop=True)
                        last.then_inc(*did("pe", f"{n}{i}"))
                pe.wait_ge(*after("act", "exp_to_end"))
                pe.wait_ge(*after("act", "sig_r3"))
                for c in range(NCH):
                    pe.transpose(k.psum[0][:, c * P:(c + 1) * P], rows[:, c * P:(c + 1) * P], k.mask("ident"))
                pe.transpose(k.psum[1][0:64, 0:P], rows[:, TP:T], k.mask("ident")).then_inc(*did("pe", "cols"))
                for i in N:
                    pe.wait_ge(*after("act", f"square{i}"))
                    norm, j, pair = (norm_qk, i, 1) if i < 8 else (norm_kk, i - 8, 2)
                    norm.sum_tile(pe, j, k.psum_pair(pair), sq(i)).then_inc(*did("pe", f"sum{i}"))
                for i in N:
                    norm, j, inverse = (norm_qk, i, "inv_qk") if i < 8 else (norm_kk, i - 8, "inv_kk")
                    pe.wait_ge(*after("dve", inverse))
                    if i == 1:
                        pe.wait_ge(*after("act", "cols"))
                    if i == 3:
                        pe.wait_ge(*after("act", "root_kk"))
                    if i >= 4:
                        pe.wait_ge(*after("dve", f"unit{i - 4}"))
                    norm.spread_tile(pe, j, spread_pair(i)).then_inc(*did("pe", f"spread{i}"))

            @block.vector
            def _(dve):
                dve.tensor_copy(k.rows_b[0:4, :], rows[32:36, :]).then_inc(*did("dve", "rows_b"))
                dve.wait_ge(*after("dve", "rows_b"))
                dve.memset(rows[32:64, :], 0.0)
                dve.memset(rows[64:128, :], 0.0).then_inc(*did("dve", "rows_clear"))
                for i in range(4):
                    dve.tensor_scalar(hb(NEG_KK + i), big(K_B + i), k.par("k_k")[:, i:i + 1], None, ALU.mult)\
                        .then_inc(*did("dve", f"kk_raw{i}"))
                dve.wait_ge(*after("act", "abs"))
                dve.tensor_scalar(rows[0:4, :], rows[0:4, :], k.par("dt_bias")[0:4, :], 0.0, ALU.add, ALU.max)\
                    .then_inc(*did("dve", "relu"))
                dve.wait_ge(*after("act", "exp_a_log"))
                dve.wait_ge(*after("dve", "relu"))
                dve.tensor_tensor(softp, rows[0:4, :], softp, ALU.add).then_inc(*did("dve", "softplus"))
                dve.wait_ge(*after("dve", "softplus"))
                dve.tensor_scalar(softp, softp, ea[0:4, :], -1.0, ALU.mult, ALU.mult).then_inc(*did("dve", "g"))
                dve.wait_ge(*after("dve", "g"))
                dve.tensor_tensor_scan(rows[0:4, :], k.resets[0:4, :], softp, 0.0, ALU.mult, ALU.add)\
                    .then_inc(*did("dve", "gc"))
                dve.wait_ge(*after("dve", "gc"))
                dve.wait_ge(*after("dve", "rows_clear"))
                for name, lo, hi, w in (("to_end_p", 0, TP, CH), ("to_end_s", TP, T, TS)):
                    v = rows[0:4, lo:hi].rearrange("p (c i) -> p c i", i=w)
                    dve.tensor_tensor(rows[64:68, lo:hi].rearrange("p (c i) -> p c i", i=w),
                                      v[:, :, w - 1:w].to_broadcast([4, (hi - lo) // w, w]), v, ALU.subtract)\
                        .then_inc(*did("dve", name))
                for i in range(4):
                    w = spare(i)
                    dve.wait_ge(*after("act", f"sig_w{i}"))
                    dve.tensor_scalar(w, w, NEG_E_HALF, None, ALU.mult).then_inc(*did("dve", f"w{i}"))
                    dve.wait_ge(*after("dve", f"w{i}"))
                    dve.tensor_tensor_scan(k.lc[:, i * T:(i + 1) * T], k.resets, w, 0.0, ALU.mult, ALU.add)\
                        .then_inc(*did("dve", f"lc{i}"))
                for i in range(4):
                    a = rate(i)
                    dve.wait_ge(*after("act", f"sig_r{i}"))
                    dve.tensor_scalar(spare(i), a, 1.0, k.par("k_a")[:, i:i + 1], ALU.subtract, ALU.mult)\
                        .then_inc(*did("dve", f"t{i}"))
                    dve.wait_ge(*after("dve", f"t{i}"))
                    dve.scalar_tensor_tensor(out=big(K_B + i), in0=spare(i), scalar=1.0, in1=big(K_B + i),
                                             op0=ALU.add, op1=ALU.mult).then_inc(*did("dve", f"k{i}"))
                dve.wait_ge(*after("act", "exp_gc"))
                cols = k.cols.rearrange("p (c r h) -> p c r h", c=5, r=4)
                dve.tensor_tensor(cols[:, 0:4, 3], cols[:, 0:4, 3], cols[:, 0:4, 1], ALU.mult)
                dve.tensor_tensor(cols[0:64, 4, 3], cols[0:64, 4, 3], cols[0:64, 4, 1], ALU.mult)\
                    .then_inc(*did("dve", "beta_gc"))
                dve.wait_ge(*after("act", "root_qk"))
                norm_qk.invert(dve).then_inc(*did("dve", "inv_qk"))
                dve.wait_ge(*after("act", "root_kk"))
                norm_kk.invert(dve).then_inc(*did("dve", "inv_kk"))
                for i in N:
                    dve.wait_ge(*after("pe", f"spread{i}"))
                    x, scale = (big(Q_A + i), 128.0 ** -0.5 if i < 4 else 1.0) if i < 8 else (hb(NEG_KK + i - 8), -1.0)
                    dve.scalar_tensor_tensor(out=halves(x), in0=halves(x), scalar=scale,
                                             in1=two_halves(spread_pair(i), HALF), op0=ALU.mult, op1=ALU.mult)\
                        .then_inc(*did("dve", f"unit{i}"))
                for i in range(4):
                    dve.wait_ge(*after("dve", f"unit{8 + i}"))
                    dve.scalar_tensor_tensor(out=hb(KK_A + i), in0=hb(NEG_KK + i), scalar=-1.0, in1=rate(i),
                                             op0=ALU.mult, op1=ALU.mult).then_inc(*did("dve", f"kka{i}"))


def carve(region, at=0):
    def take(n):
        nonlocal at
        at += n
        assert at <= region.shape[-1], (at, region.shape)
        return region[:, at - n:at]
    return take


STREAMS = 3
LEVELS = (16, 32, 64)


def inverse_jobs(sample):
    jobs = []
    G = range(STREAMS)
    for g in G:
        jobs += [(f"sq1_{g}", ("act", f"C1_{g}")), (f"sqt1_{g}", ("dve", f"CT1_{g}"))]
    for g in G:
        jobs += [(f"x1_{g}", ("dve", f"P1_{g}")), (f"sq2_{g}", ("act", f"B2_{g}"))]
        if not sample:
            jobs += [(f"sqt2_{g}", ("act", f"BT2_{g}"))]
    for g in G:
        jobs += [(f"x2_{g}", ("dve", f"P2_{g}"))]
        if not sample:
            jobs += [(f"sq3_{g}", ("act", f"C3_{g}"))]
    if sample:
        return jobs
    for g in G:
        jobs += [(f"x3_{g}", ("dve", f"P3_{g}"))]
    for w in LEVELS:
        for g in G:
            jobs += [(f"y{w}_{g}", ("act", f"Y{w}_{g}")), (f"tr{w}_{g}", ("dve", f"T{w}_{g}"))]
        for g in G:
            jobs += [(f"z{w}_{g}", ("dve", f"PZ{w}_{g}"))]
    return jobs


def even_jobs(sample):
    rw = [(f"{n}_{g}", ("dve", f"{n}m_{g}")) for g in (1, 2) for n in ("m", "mt", "rb", "ka", "kr")]
    jobs = [("R", ("act", "eR")), ("kk", ("dve", "M0")), ("kq", ("dve", "KQD")), ("mt_0", ("dve", "mtm_0"))] + rw + [
        ("vt", ("dve", "VB")), ("kt", ("dve", "KD")), ("rvt", ("act", "RVt")), ("rbt", ("act", "RBt")),
        ("rkt", ("act", "RKt"))]
    jobs += inverse_jobs(sample)
    if not sample:
        jobs += [("ks", ("dve", "W1")), ("rw_1", ("act", "RW_1")), ("rw_2", ("act", "RW_2")), ("u", ("act", "U")),
                 ("ru", ("dve", "RU")), ("o", ("act", "O")), ("s", ("dve", "S3")), ("ry", ("act", "RY")),
                 ("rs", ("dve", "RS1"))]
    else:
        jobs += [("ko", ("act", "KO")), ("rko", ("act", "RKO")), ("kst", ("dve", "W1")), ("rwt", ("act", "RWt")),
                 ("rw", ("dve", "RW")), ("u", ("act", "U")), ("ru", ("act", "RU")), ("o", ("dve", "O")),
                 ("ry", ("dve", "RY"))]
        for h in range(4):
            jobs += [(f"s{h}a", ("dve", f"S{h}a")), (f"s{h}b", ("dve", f"S{h}b"))]
        jobs += [(f"rs{t}", ("dve", f"RS{t}")) for t in range(4)]
    return jobs


def even_chunks(k, sample):
    nc = k.nc
    n = NSEQ * TS if sample else CH
    chunks = [NCH] if sample else list(range(NCH))
    G = range(STREAMS)
    jobs1 = even_jobs(sample)
    names = lambda base, c: f"{base}@{c}"
    pe_steps, bank_freed_by = [], []
    act_steps, dve_steps = [], []
    inv_act = lambda: [f"C1_{g}" for g in G] + [x for g in G for x in ([f"B2_{g}"] if sample else [f"B2_{g}", f"BT2_{g}"])]
    for c in chunks:
        pe_steps += [names(j, c) for j, _ in jobs1]
        bank_freed_by += [(e, names(st, c)) for _, (e, st) in jobs1]
        a = ["eR", "DT", "D", "E"] + ([] if sample else ["exp_ref"]) + ["exp_E", "RVt", "RBt", "RKt"] + inv_act()
        d = ["d", "dU", "dL", "Et", "Eref", "Aq", "Rq", "Bq", "Kq"] + (["k_copy"] if sample else []) \
            + ["M0", "M1", "M2", "KQD"]
        d += ["mtm_0", "P0_0"]
        d += [f"{x}_{g}" for g in (1, 2) for x in ("mm", "mtm", "rbm", "kam", "krm", "P0")]
        d += ["VB", "KD", "QG"]
        if sample:
            a += ["KO", "RKO", "RWt", "U", "RU"]
            d += [f"CT1_{g}" for g in G] + [f"P1_{g}" for g in G] + [f"P2_{g}" for g in G]
            d += ["W1", "W2", "RW"] + ["O", "RY"]
            for h in range(4):
                d += [f"Um{h}", f"Sg{h}", f"S{h}a", f"S{h}b"]
            for t in range(4):
                d += [f"RUm{t}", f"RVm{t}", f"RS{t}", f"RSd{t}"]
        else:
            a += [f"C3_{g}" for g in G] + [f"Y{w}_{g}" for w in LEVELS for g in G] + ["RW_1", "RW_2", "U", "O", "RY"]
            d += [f"B_{g}" for g in G] + [f"CT1_{g}" for g in G] + [f"P1_{g}" for g in G] + [f"P2_{g}" for g in G] \
                + [f"P3_{g}" for g in G]
            for w in LEVELS:
                d += [f"T{w}_{g}" for g in G] + [f"PZ{w}_{g}" for g in G]
            d += ["S0s", "W1", "W2", "RU", "S1", "S3", "RS1", "RSn"]
        act_steps += [names(x, c) for x in a]
        dve_steps += [names(x, c) for x in d]
    pool_steps = [] if sample else [names(f"Ms{w}_{g}", c) for c in chunks for w in LEVELS for g in G]

    take = carve(k.work[:, 0:WORK - 4 * T])
    H = 4 * n
    new = lambda cols=H: take(cols)
    eR, KQD = new(), new()
    qg, KD, W, U = (None,) * 4 if sample else (new() for _ in range(4))
    Em = take(4 * (n + 1) if not sample else 4 * NSEQ * (TS + 1))
    AR, BK = take(2 * H), take(2 * H)
    Vt, Bt, Kt = take(512), take(512), take(512)
    if sample:
        Wd, Ud = take(512), take(512)
        KDt, VBt = take(512), take(512)
    else:
        Wd, Ud, KDt, VBt = W, U, KD, take(512)
    RW, RU = take(512), take(512)
    KA, KR, RB = ([None, new(), new()] for _ in range(3))
    A, B, BT, C, CT, Pt = ([new() for _ in G] for _ in range(6))
    Dm, DT, En = C[0], CT[0], C[1]
    if sample:
        S = take(32 * P)
        RS = take(4 * NSEQ * 64)
        KQg = take(2 * H)
        KO, RKO = take(2 * H), take(2 * H)
        RUw, RVw = take(1024), take(1024)
        Uw = RUw
    else:
        S, RS, S0s = take(512), take(256), take(256)
        eref = take(4)
    mask = lambda nm, part=n: k.mask(nm)[0:part, 0:n]
    bc = lambda m: m[:, None, :].to_broadcast([n, 4, n])
    v4 = lambda ap, part=P: ap[0:part].rearrange("p (h n) -> p h n", h=4)
    sfx = "8" if sample else ""

    with nc.cleanup_on_exit():
        ph = Phase(nc)
        sched = Schedule(ph, pe=pe_steps, act=act_steps, dve=dve_steps, pool=pool_steps)
        job_number = {j: i for i, j in enumerate(pe_steps)}
        states_in, states_out, zeroed = ph.sem("states_in"), ph.sem("states_out"), ph.sem("zeroed")

        def bank(job, c):
            return k.psum[job_number[names(job, c)] % 8]

        def tokens(t, c, count=4):
            return k.big_buf[:, t * T:(t + count) * T].rearrange("p (h t) -> p h t", t=T)[:, :, c * CH:c * CH + n]

        def htokens(t, c, count=4):
            return k.h[:, t * T:(t + count) * T].rearrange("p (h t) -> p h t", t=T)[:, :, c * CH:c * CH + n]

        def col(c, r):
            v = k.cols[0:n].rearrange("p (c r h) -> p c r h", c=5, r=4)[:, c, r, :]
            return lambda w: v[:, :, None].to_broadcast([n, 4, w])

        with nc.Block() as block:
            @block.sync
            def _(sp):
                if sample:
                    sp.dma_start(S, k.io["delta_in"]).then_inc(states_in, 16)
                    sp.dma_start(RS, k.io["rwkv_in"]).then_inc(states_in, 16)
                    sp.wait_ge(*sched.after("dve", names("S3b", NCH)))
                    sp.dma_start(k.io["delta_s_out"], S).then_inc(states_out, 16)
                    sp.wait_ge(*sched.after("dve", names("RSd3", NCH)))
                    sp.dma_start(k.io["rwkv_s_out"], RS).then_inc(states_out, 16)
                else:
                    sp.wait_ge(*sched.after("dve", names("S3", NCH - 1)))
                    sp.dma_start(k.io["delta_p_out"], S).then_inc(states_out, 16)
                    sp.wait_ge(*sched.after("dve", names("RSn", NCH - 1)))
                    sp.dma_start(k.io["rwkv_p_out"], RS).then_inc(states_out, 16)
                sp.wait_ge(states_out, 32)

            @block.gpsimd
            def _(pool):
                if not sample:
                    pool.memset(S, 0.0).then_inc(zeroed, 1)
                    pool.memset(RS, 0.0).then_inc(zeroed, 1)
                    for c in chunks:
                        after = lambda e, nm: sched.after(e, names(nm, c))
                        for w, dst, free in ((16, CT, "sqt2"), (32, BT, "sq3"), (64, B, None)):
                            for g in G:
                                if free:
                                    pool.wait_ge(*after("pe", f"{free}_{g}"))
                                else:
                                    pool.wait_ge(*after("pe", f"z16_{g}"))
                                pool.tensor_tensor(v4(dst[g]), v4(A[g]), bc(k.mask(f"level{w}")), ALU.mult)\
                                    .then_inc(*sched.did("pool", names(f"Ms{w}_{g}", c)))

            @block.tensor
            def _(pe):
                for c in chunks:
                    after = lambda e, nm: sched.after(e, names(nm, c))

                    def claim(job):
                        i = job_number[names(job, c)]
                        if i >= 8:
                            pe.wait_ge(*sched.after(*bank_freed_by[i - 8]))
                        return bank(job, c)

                    def done(job, ins):
                        ins.then_inc(*sched.did("pe", names(job, c)))

                    def four(job, lhsT, rhs, out_part=n, width=n):
                        b = claim(job)
                        for h in range(4):
                            last = pe.matmul(b[0:out_part, h * width:(h + 1) * width], lhsT(h), rhs(h),
                                             start=True, stop=True)
                        done(job, last)

                    def four_transposes(job, source, cols=P):
                        b = claim(job)
                        for h in range(4):
                            src = source(h)
                            last = pe.transpose(b[0:src.shape[1], h * cols:(h + 1) * cols], src,
                                                k.mask("ident")[0:src.shape[0], 0:src.shape[0]])
                        done(job, last)

                    def of(buf, w=n, part=n):
                        return lambda h: buf[0:part, h * w:(h + 1) * w]

                    kc, qc, vc = (tokens(t, c) for t in (K_A, Q_A, V_A))
                    def place(g, h):
                        return h, 64 * (g - 1)

                    def ar(g, h, which):
                        t, p = place(g, h)
                        return AR[p:p + 64, (2 * t + which) * n:(2 * t + which + 1) * n]

                    def bk(g, h, which):
                        t, p = place(g, h)
                        return BK[p:p + 64, (2 * t + which) * n:(2 * t + which + 1) * n]

                    b = claim("R")
                    for h in range(4):
                        last = pe.matmul(b[:, h * n:(h + 1) * n], k.select(h)[0:4],
                                         k.rows[0:4, c * CH:c * CH + n], start=True, stop=True)
                    done("R", last)
                    four("kk", lambda h: kc[:, h], lambda h: kc[:, h])
                    four("kq", lambda h: kc[:, h], lambda h: qc[:, h])
                    pe.wait_ge(*after("dve", "M2"))
                    four_transposes("mt_0", lambda h: A[0][0:n, h * n:(h + 1) * n], n)
                    pe.wait_ge(*after("dve", "Kq"))
                    for g in (1, 2):
                        four(f"m_{g}", lambda h: ar(g, h, 0), lambda h: bk(g, h, 0))
                        four(f"mt_{g}", lambda h: bk(g, h, 0), lambda h: ar(g, h, 0))
                        four(f"rb_{g}", lambda h: bk(g, h, 0), lambda h: ar(g, h, 1))
                        four(f"ka_{g}", lambda h: bk(g, h, 1), lambda h: ar(g, h, 0))
                        four(f"kr_{g}", lambda h: bk(g, h, 1), lambda h: ar(g, h, 1))
                    four_transposes("vt", lambda h: vc[:, h])
                    four_transposes("kt", lambda h: kc[:, h])
                    rv = tokens(V_B, c)
                    four_transposes("rvt", lambda h: rv[:, h])
                    four_transposes("rbt", lambda h: BK[:, 2 * h * n:(2 * h + 1) * n])
                    four_transposes("rkt", lambda h: BK[:, (2 * h + 1) * n:(2 * h + 2) * n])

                    Bs = A if sample else B
                    for g in G:
                        pe.wait_ge(*after("dve", f"P0_{g}"))
                        if not sample:
                            pe.wait_ge(*after("dve", f"B_{g}"))
                        four(f"sq1_{g}", of(BT[g]), of(Bs[g]))
                        four(f"sqt1_{g}", of(Bs[g]), of(BT[g]))
                    for g in G:
                        pe.wait_ge(*after("act", f"C1_{g}"))
                        pe.wait_ge(*after("dve", f"CT1_{g}"))
                        four(f"x1_{g}", of(C[g]), of(Pt[g]))
                        four(f"sq2_{g}", of(CT[g]), of(C[g]))
                        if not sample:
                            four(f"sqt2_{g}", of(C[g]), of(CT[g]))
                    for g in G:
                        pe.wait_ge(*after("dve", f"P1_{g}"))
                        pe.wait_ge(*after("act", f"B2_{g}" if sample else f"BT2_{g}"))
                        four(f"x2_{g}", of(B[g]), of(Pt[g]))
                        if not sample:
                            four(f"sq3_{g}", of(BT[g]), of(B[g]))
                    if not sample:
                        for g in G:
                            pe.wait_ge(*after("act", f"C3_{g}"))
                            pe.wait_ge(*after("dve", f"P2_{g}"))
                            four(f"x3_{g}", of(C[g]), of(Pt[g]))
                        before = "P3"
                        for w, Ms, Tb in ((16, CT, B), (32, BT, CT), (64, B, CT)):
                            for g in G:
                                pe.wait_ge(*after("pool", f"Ms{w}_{g}"))
                                pe.wait_ge(*after("dve", f"{before}_{g}"))
                                four(f"y{w}_{g}", of(Ms[g]), of(Pt[g]))
                                four_transposes(f"tr{w}_{g}", of(Pt[g]), n)
                            for g in G:
                                pe.wait_ge(*after("act", f"Y{w}_{g}"))
                                pe.wait_ge(*after("dve", f"T{w}_{g}"))
                                four(f"z{w}_{g}", of(Tb[g]), of(C[g]))
                            before = f"PZ{w}"

                    last_p = "P2" if sample else "PZ64"

                    def rwkv_u():
                        for g in (1, 2):
                            pe.wait_ge(*after("dve", f"{last_p}_{g}"))
                        b = claim("ru")
                        for g in (1, 2):
                            for h in range(4):
                                hd = 2 * h + g - 1
                                last = pe.matmul(b[0:n, hd * 64:(hd + 1) * 64], Pt[g][0:n, h * n:(h + 1) * n],
                                                 RW[0:n, hd * 64:(hd + 1) * 64], start=True, stop=True)
                        done("ru", last)

                    def head_place(hd):
                        return hd // 2, 64 * (hd % 2), hd % 2 + 1, hd // 2

                    if not sample:
                        if c == 0:
                            pe.wait_ge(zeroed, 2)
                        else:
                            pe.wait_ge(*sched.after("dve", names("S3", c - 1)))
                        four("ks", lambda h: kc[:, h], lambda h: S[:, h * P:(h + 1) * P])
                        pe.wait_ge(*after("dve", "S0s"))
                        pe.wait_ge(*after("act", "RVt"))
                        for g in (1, 2):
                            b = claim(f"rw_{g}")
                            for h in range(4):
                                out = b[:, h * 64:(h + 1) * 64]
                                t, p = place(g, h)
                                hd = 2 * h + g - 1
                                pe.matmul(out, ar(g, h, 0), S0s[p:p + 64, t * 64:(t + 1) * 64],
                                          start=True, stop=False)
                                last = pe.matmul(out, KA[g][:, h * n:(h + 1) * n], Vt[:, hd * 64:(hd + 1) * 64],
                                                 start=False, stop=True)
                            done(f"rw_{g}", last)
                        pe.wait_ge(*after("dve", "W2"))
                        four("u", of(Pt[0]), lambda h: W[:, h * P:(h + 1) * P], width=P)
                        pe.wait_ge(*after("act", "RW_2"))
                        rwkv_u()
                        pe.wait_ge(*after("act", "U"))
                        pe.wait_ge(*after("dve", "QG"))
                        b = claim("o")
                        for h in range(4):
                            out = b[:, h * n:(h + 1) * n]
                            pe.matmul(out, S[:, h * P:(h + 1) * P], qg[:, h * n:(h + 1) * n], start=True, stop=False)
                            last = pe.matmul(out, U[:, h * P:(h + 1) * P], KQD[:, h * n:(h + 1) * n],
                                             start=False, stop=True)
                        done("o", last)
                        four("s", lambda h: KD[:, h * P:(h + 1) * P], lambda h: U[:, h * P:(h + 1) * P],
                             out_part=P, width=P)
                        pe.wait_ge(*after("dve", "RU"))
                        b = claim("ry")
                        for hd in range(8):
                            t, p, g, h = head_place(hd)
                            out = b[p:p + 64, t * n:(t + 1) * n]
                            hc = slice(hd * 64, (hd + 1) * 64)
                            pe.matmul(out, RU[:, hc], RB[g][:, h * n:(h + 1) * n], start=True, stop=False)
                            pe.matmul(out, Vt[:, hc], KR[g][:, h * n:(h + 1) * n], start=False, stop=False)
                            last = pe.matmul(out, S0s[p:p + 64, t * 64:(t + 1) * 64], ar(g, h, 1),
                                             start=False, stop=True)
                        done("ry", last)
                        b = claim("rs")
                        for hd in range(8):
                            t, p, g, h = head_place(hd)
                            out = b[p:p + 64, t * 64:(t + 1) * 64]
                            hc = slice(hd * 64, (hd + 1) * 64)
                            pe.matmul(out, Bt[:, hc], RU[:, hc], start=True, stop=False)
                            last = pe.matmul(out, Kt[:, hc], Vt[:, hc], start=False, stop=True)
                        done("rs", last)
                    else:
                        pe.wait_ge(states_in, 32)
                        pe.wait_ge(*after("dve", "QG"))
                        b = claim("ko")
                        out4 = b.rearrange("p (h a t) -> p h a t", h=4, a=2)
                        in4 = KQg.rearrange("p (h a t) -> p h a t", h=4, a=2)
                        S4 = S.rearrange("p (h s v) -> p h s v", h=4, s=NSEQ)
                        for h in range(4):
                            for q in range(NSEQ):
                                last = pe.matmul(out4[:, h, :, q * TS:(q + 1) * TS], S4[:, h, q],
                                                 in4[:, h, :, q * TS:(q + 1) * TS], start=True, stop=True)
                        done("ko", last)
                        b = claim("rko")
                        out4 = b.rearrange("p (t a i) -> p t a i", t=4, a=2)
                        in4 = AR.rearrange("p (t a i) -> p t a i", t=4, a=2)
                        S4 = RS.rearrange("p (t s v) -> p t s v", t=4, s=NSEQ)
                        for hd in range(8):
                            t, p, g, h = head_place(hd)
                            for q in range(NSEQ):
                                last = pe.matmul(out4[p:p + 64, t, :, q * TS:(q + 1) * TS], S4[p:p + 64, t, q],
                                                 in4[p:p + 64, t, :, q * TS:(q + 1) * TS], start=True, stop=True)
                        done("rko", last)
                        pe.wait_ge(*after("act", "RKO"))
                        ko4 = KO.rearrange("p (h a t) -> p h a t", h=4, a=2)
                        rko4 = RKO.rearrange("p (t a i) -> p t a i", t=4, a=2)
                        four_transposes("kst", lambda h: ko4[:, h, 0])
                        four_transposes("rwt", lambda h: rko4[:, h, 0])
                        b = claim("rw")
                        for hd in range(8):
                            t, p, g, h = head_place(hd)
                            last = pe.matmul(b[0:n, hd * 64:(hd + 1) * 64], KA[g][0:n, h * n:(h + 1) * n],
                                             Vt[0:n, hd * 64:(hd + 1) * 64], start=True, stop=True)
                        done("rw", last)
                        pe.wait_ge(*after("dve", "W2"))
                        four("u", of(Pt[0]), lambda h: Wd[0:n, h * P:(h + 1) * P], width=P)
                        pe.wait_ge(*after("dve", "RW"))
                        rwkv_u()
                        pe.wait_ge(*after("act", "U"))
                        four("o", lambda h: Ud[0:n, h * P:(h + 1) * P], lambda h: KQD[0:n, h * n:(h + 1) * n], out_part=P)
                        pe.wait_ge(*after("act", "RU"))
                        b = claim("ry")
                        for hd in range(8):
                            t, p, g, h = head_place(hd)
                            out = b[p:p + 64, t * n:(t + 1) * n]
                            hc = slice(hd * 64, (hd + 1) * 64)
                            pe.matmul(out, RU[0:n, hc], RB[g][0:n, h * n:(h + 1) * n], start=True, stop=False)
                            last = pe.matmul(out, Vt[0:n, hc], KR[g][0:n, h * n:(h + 1) * n], start=False, stop=True)
                        done("ry", last)
                        for h in range(4):
                            pe.wait_ge(*after("dve", f"Um{h}"))
                            for part in range(2):
                                b = claim(f"s{h}{'ab'[part]}")
                                done(f"s{h}{'ab'[part]}",
                                     pe.matmul(b[:, :], KDt[0:n, h * P:(h + 1) * P],
                                               Uw[0:n, part * 512:(part + 1) * 512], start=True, stop=True))
                        for t in range(4):
                            pe.wait_ge(*after("dve", f"RVm{t}"))
                            b = claim(f"rs{t}")
                            for half in range(2):
                                hc = slice((2 * t + half) * 64, (2 * t + half + 1) * 64)
                                out = b[half * 64:half * 64 + 64, :]
                                pe.matmul(out, Bt[0:n, hc], RUw[0:n, half * 512:(half + 1) * 512],
                                          start=True, stop=False)
                                last = pe.matmul(out, Kt[0:n, hc], RVw[0:n, half * 512:(half + 1) * 512],
                                                 start=False, stop=True)
                            done(f"rs{t}", last)

            @block.scalar
            def _(act):
                for c in chunks:
                    after = lambda e, nm: sched.after(e, names(nm, c))
                    did = lambda nm: sched.did("act", names(nm, c))
                    psum = lambda job, part=n: bank(job, c)[0:part]

                    def copy(step, job, dst, part=n, cols=H):
                        act.wait_ge(*after("pe", job))
                        act.activation(dst[0:part, 0:cols], psum(job, part)[:, 0:cols], ACT.Copy).then_inc(*did(step))

                    act.wait_ge(*after("pe", "R"))
                    act.wait_ge(*after("dve", "d"))
                    act.activation(eR[:, 0:H], psum("R", P)[:, 0:H], ACT.Exp).then_inc(*did("eR"))
                    act.wait_ge(*after("dve", "dU"))
                    act.activation(DT[0:n], DT[0:n], ACT.Exp).then_inc(*did("DT"))
                    act.wait_ge(*after("dve", "dL"))
                    act.activation(Dm[0:n], Dm[0:n], ACT.Exp, scale=-1.0).then_inc(*did("D"))
                    act.wait_ge(*after("dve", "Eref"))
                    if sample:
                        e = Em.rearrange("p (b i) -> p b i", i=TS + 1)
                        act.activation(En.rearrange("p (b i) -> p b i", i=TS), e[:, :, 1:], ACT.Exp, scale=-1.0)\
                            .then_inc(*did("E"))
                    else:
                        e = Em.rearrange("p (t i) -> p t i", t=4)
                        act.activation(v4(En), e[:, :, 1:], ACT.Exp, scale=-1.0).then_inc(*did("E"))
                        act.activation(eref.rearrange("p (t i) -> p t i", t=4), e[:, :, 0:1], ACT.Exp, scale=-1.0)\
                            .then_inc(*did("exp_ref"))
                    act.wait_ge(*after("act", "E" if sample else "exp_ref"))
                    act.activation(Em, Em, ACT.Exp).then_inc(*did("exp_E"))
                    copy("RVt", "rvt", Vt, cols=512)
                    copy("RBt", "rbt", Bt, cols=512)
                    copy("RKt", "rkt", Kt, cols=512)
                    for g in G:
                        if g == 0:
                            act.wait_ge(*after("dve", "KQD"))
                            act.wait_ge(*after("dve", "M0"))
                        if g == 1:
                            act.wait_ge(*after("dve", "Kq"))
                        copy(f"C1_{g}", f"sq1_{g}", C[g])
                    for g in G:
                        copy(f"B2_{g}", f"sq2_{g}", B[g])
                        if not sample:
                            copy(f"BT2_{g}", f"sqt2_{g}", BT[g])
                    if not sample:
                        for g in G:
                            copy(f"C3_{g}", f"sq3_{g}", C[g])
                        for w in LEVELS:
                            for g in G:
                                copy(f"Y{w}_{g}", f"y{w}_{g}", C[g])
                        for g in (1, 2):
                            act.wait_ge(*after("pe", f"rw_{g}"))
                            act.activation(RW.rearrange("p (h g v) -> p h g v", h=4, g=2)[:, :, g - 1],
                                           v4(psum(f"rw_{g}")[:, 0:256]), ACT.Copy).then_inc(*did(f"RW_{g}"))
                        copy("U", "u", U, cols=512)
                        act.wait_ge(*after("pe", "o"))
                        act.activation(tokens(Q_A, c), v4(psum("o", P)), ACT.Copy).then_inc(*did("O"))
                        act.wait_ge(*after("pe", "ry"))
                        act.activation(htokens(NEG_KK, c), v4(psum("ry", P)), ACT.Copy).then_inc(*did("RY"))
                    else:
                        copy("KO", "ko", KO, part=P, cols=512)
                        copy("RKO", "rko", RKO, part=P, cols=512)
                        copy("RWt", "rwt", RW, cols=512)
                        copy("U", "u", Ud, cols=512)
                        copy("RU", "ru", RU, cols=512)

            @block.vector
            def _(dve):
                for c in chunks:
                    after = lambda e, nm: sched.after(e, names(nm, c))
                    did = lambda nm: sched.did("dve", names(nm, c))
                    psum = lambda job, part=n: bank(job, c)[0:part]
                    if c > chunks[0]:
                        dve.wait_ge(*sched.after("pe", names("rs", c - 1)))
                        dve.wait_ge(*sched.after("act", names("RY", c - 1)))
                        dve.wait_ge(*sched.after("dve", names("RSn", c - 1)))
                    dve.wait_ge(*after("pe", "R"))
                    dve.tensor_tensor(v4(Dm, n), v4(psum("R")[:, 0:H], n), col(c, ROW_GC)(n), ALU.subtract)\
                        .then_inc(*did("d"))
                    dve.wait_ge(*after("dve", "d"))
                    big = lambda nm: k.big(nm)[0:n, 0:n][:, None, :].to_broadcast([n, 4, n])
                    dve.tensor_tensor(v4(DT, n), v4(Dm, n), big("not_above_eq" + sfx), ALU.subtract)\
                        .then_inc(*did("dU"))
                    dve.wait_ge(*after("dve", "dU"))
                    dve.tensor_tensor(v4(Dm, n), v4(Dm, n), big("not_below" + sfx), ALU.add).then_inc(*did("dL"))
                    if sample:
                        lcs = k.lc.rearrange("p (t i) -> p t i", t=4)[:, :, TP:T].rearrange("p t (s i) -> p t s i", s=NSEQ)
                        E4 = Em.rearrange("p (t s i) -> p t s i", t=4, s=NSEQ)
                        dve.memset(Em, 0.0).then_inc(*did("Et"))
                        dve.wait_ge(*after("dve", "Et"))
                        dve.tensor_copy(E4[:, :, :, 1:], lcs).then_inc(*did("Eref"))
                        E0, E1 = E4[:, :, :, 0:TS], E4[:, :, :, 1:]
                        v = lambda ap: ap.rearrange("p t (s i) -> p t s i", s=NSEQ)
                    else:
                        lcc = k.lc.rearrange("p (t i) -> p t i", t=4)[:, :, c * CH:(c + 1) * CH]
                        mid = lcc[:, :, CH // 2 - 1:CH // 2]
                        E4 = Em.rearrange("p (t i) -> p t i", t=4)
                        dve.tensor_tensor(E4[:, :, 1:], lcc, mid.to_broadcast([P, 4, CH]), ALU.subtract)\
                            .then_inc(*did("Et"))
                        dve.tensor_scalar(E4[:, :, 0:1], mid, -1.0, None, ALU.mult).then_inc(*did("Eref"))
                        E0, E1 = E4[:, :, 0:n], E4[:, :, 1:]
                        v = lambda ap: ap
                    dve.wait_ge(*after("act", "exp_E"))
                    ar4 = AR.rearrange("p (t a i) -> p t a i", t=4, a=2)
                    bk4 = BK.rearrange("p (t a i) -> p t a i", t=4, a=2)
                    dve.tensor_tensor(v(ar4[:, :, 0]), v(htokens(NEG_KK, c)), E0, ALU.mult).then_inc(*did("Aq"))
                    dve.tensor_tensor(v(ar4[:, :, 1]), v(tokens(R_B, c)), E1, ALU.mult).then_inc(*did("Rq"))
                    dve.tensor_tensor(bk4[:, :, 0], htokens(KK_A, c), v4(En), ALU.mult).then_inc(*did("Bq"))
                    dve.tensor_tensor(bk4[:, :, 1], tokens(K_B, c), v4(En), ALU.mult).then_inc(*did("Kq"))
                    if sample:
                        kq4 = KQg.rearrange("p (h a t) -> p h a t", h=4, a=2)
                        dve.tensor_copy(kq4[:, :, 0], tokens(K_A, c)).then_inc(*did("k_copy"))
                    dve.wait_ge(*after("pe", "kk"))
                    dve.wait_ge(*after("act", "D"))
                    dve.tensor_tensor(v4(A[0], n), v4(psum("kk")[:, 0:H], n), v4(Dm, n), ALU.mult).then_inc(*did("M0"))
                    dve.wait_ge(*after("dve", "M0"))
                    dve.tensor_tensor(v4(A[0], n), v4(A[0], n), col(c, ROW_BETA)(n), ALU.mult).then_inc(*did("M1"))
                    dve.wait_ge(*after("dve", "M1"))
                    dve.tensor_scalar(A[0][0:n], A[0][0:n], -1.0, None, ALU.mult).then_inc(*did("M2"))
                    dve.wait_ge(*after("pe", "kq"))
                    dve.tensor_tensor(v4(KQD, n), v4(psum("kq")[:, 0:H], n), v4(DT, n), ALU.mult).then_inc(*did("KQD"))

                    def masked(step, job, dst, mask_name):
                        dve.wait_ge(*after("pe", job))
                        dve.tensor_tensor(v4(dst, n), v4(psum(job)[:, 0:H], n), bc(mask(mask_name)), ALU.mult)\
                            .then_inc(*did(step))

                    def start_inverse(g):
                        dve.wait_ge(*after("dve", f"mtm_{g}"))
                        dve.tensor_tensor(v4(Pt[g], n), v4(BT[g], n), bc(mask("ident")), ALU.add).then_inc(*did(f"P0_{g}"))
                    masked("mtm_0", "mt_0", BT[0], "block8" if sample else "block16")
                    start_inverse(0)
                    for g in (1, 2):
                        masked(f"mm_{g}", f"m_{g}", A[g], "below" + sfx)
                        masked(f"mtm_{g}", f"mt_{g}", BT[g], "above8" if sample else "above16")
                        masked(f"rbm_{g}", f"rb_{g}", RB[g], "above_eq" + sfx)
                        masked(f"kam_{g}", f"ka_{g}", KA[g], "above" + sfx)
                        masked(f"krm_{g}", f"kr_{g}", KR[g], "above_eq" + sfx)
                        start_inverse(g)
                    dve.wait_ge(*after("pe", "vt"))
                    dve.tensor_tensor(v4(VBt, n), v4(psum("vt"), n), col(c, ROW_BETA)(P), ALU.mult).then_inc(*did("VB"))
                    dve.wait_ge(*after("pe", "kt"))
                    dve.tensor_tensor(v4(KDt, n), v4(psum("kt"), n), col(c, ROW_TO_END)(P), ALU.mult).then_inc(*did("KD"))
                    dve.wait_ge(*after("act", "eR"))
                    qg_out = KQg.rearrange("p (h a t) -> p h a t", h=4, a=2)[:, :, 1] if sample else v4(qg)
                    dve.tensor_tensor(qg_out, tokens(Q_A, c), v4(eR), ALU.mult).then_inc(*did("QG"))

                    def plus(step, job, g):
                        dve.wait_ge(*after("pe", job))
                        dve.tensor_tensor(Pt[g][0:n], Pt[g][0:n], psum(job)[:, 0:H], ALU.add).then_inc(*did(step))

                    def copy(step, job, dst, part=n, cols=H):
                        dve.wait_ge(*after("pe", job))
                        dve.tensor_copy(dst[0:part, 0:cols], psum(job, part)[:, 0:cols]).then_inc(*did(step))
                    if not sample:
                        for g in G:
                            dve.wait_ge(*after("dve", "M2" if g == 0 else f"mm_{g}"))
                            dve.tensor_tensor(v4(B[g], n), v4(A[g], n), bc(mask("block16")), ALU.mult)\
                                .then_inc(*did(f"B_{g}"))
                    for g in G:
                        copy(f"CT1_{g}", f"sqt1_{g}", CT[g])
                    for g in G:
                        plus(f"P1_{g}", f"x1_{g}", g)
                    for g in G:
                        plus(f"P2_{g}", f"x2_{g}", g)
                    if not sample:
                        for g in G:
                            plus(f"P3_{g}", f"x3_{g}", g)
                        for w, Tb in ((16, B), (32, CT), (64, CT)):
                            for g in G:
                                copy(f"T{w}_{g}", f"tr{w}_{g}", Tb[g])
                            for g in G:
                                plus(f"PZ{w}_{g}", f"z{w}_{g}", g)
                        if c == 0:
                            dve.wait_ge(zeroed, 2)
                        dve.tensor_tensor(v4(S0s), v4(RS), eref.rearrange("p (t i) -> p t i", t=4)
                                          .to_broadcast([P, 4, 64]), ALU.mult).then_inc(*did("S0s"))
                        dve.wait_ge(*after("pe", "ks"))
                        dve.tensor_tensor(v4(W), v4(psum("ks")), col(c, COL_BETA_GC)(P), ALU.mult).then_inc(*did("W1"))
                        dve.wait_ge(*after("dve", "W1"))
                        dve.tensor_tensor(W, VBt, W, ALU.subtract).then_inc(*did("W2"))
                        copy("RU", "ru", RU, cols=512)
                        dve.wait_ge(*after("pe", "s"))
                        last = eR.rearrange("p (h i) -> p h i", h=4)[:, :, n - 1:n].to_broadcast([P, 4, P])
                        dve.tensor_tensor(v4(S), v4(S), last, ALU.mult).then_inc(*did("S1"))
                        dve.wait_ge(*after("dve", "S1"))
                        dve.tensor_tensor(S, S, psum("s"), ALU.add).then_inc(*did("S3"))
                        dve.wait_ge(*after("pe", "rs"))
                        dve.tensor_tensor(S0s, S0s, psum("rs")[:, 0:256], ALU.add).then_inc(*did("RS1"))
                        dve.wait_ge(*after("dve", "RS1"))
                        dve.tensor_tensor(v4(RS), v4(S0s), E4[:, :, n:n + 1].to_broadcast([P, 4, 64]), ALU.mult)\
                            .then_inc(*did("RSn"))
                    else:
                        dve.wait_ge(*after("pe", "kst"))
                        dve.tensor_tensor(v4(Wd, n), v4(psum("kst"), n), col(c, COL_BETA_GC)(P), ALU.mult)\
                            .then_inc(*did("W1"))
                        dve.wait_ge(*after("dve", "W1"))
                        dve.tensor_tensor(Wd[0:n], VBt[0:n], Wd[0:n], ALU.subtract).then_inc(*did("W2"))
                        dve.wait_ge(*after("pe", "rw"))
                        dve.wait_ge(*after("act", "RWt"))
                        dve.tensor_tensor(RW[0:n], RW[0:n], psum("rw"), ALU.add).then_inc(*did("RW"))
                        ko4 = KO.rearrange("p (h a t) -> p h a t", h=4, a=2)
                        rko4 = RKO.rearrange("p (t a i) -> p t a i", t=4, a=2)
                        dve.wait_ge(*after("pe", "o"))
                        dve.tensor_tensor(tokens(Q_A, c), ko4[:, :, 1], v4(psum("o", P)[:, 0:H]), ALU.add)\
                            .then_inc(*did("O"))
                        dve.wait_ge(*after("pe", "ry"))
                        dve.tensor_tensor(htokens(NEG_KK, c), rko4[:, :, 1], v4(psum("ry", P)[:, 0:H]), ALU.add)\
                            .then_inc(*did("RY"))
                        own = k.mask("block8")[0:n, 0:n:TS]
                        dve.wait_ge(*after("act", "U"))
                        for h in range(4):
                            if h:
                                dve.wait_ge(*after("pe", f"s{h - 1}b"))
                            own_b = own[:, :, None].to_broadcast([n, NSEQ, P])
                            dve.tensor_tensor(Uw[0:n].rearrange("p (s v) -> p s v", s=NSEQ),
                                              Ud[0:n, None, h * P:(h + 1) * P].to_broadcast([n, NSEQ, P]), own_b,
                                              ALU.mult).then_inc(*did(f"Um{h}"))
                            Sh = S[:, h * 1024:(h + 1) * 1024]
                            gl = eR[:, h * n + TS - 1:(h + 1) * n:TS]
                            dve.tensor_tensor(Sh.rearrange("p (s v) -> p s v", s=NSEQ),
                                              Sh.rearrange("p (s v) -> p s v", s=NSEQ),
                                              gl[:, :, None].to_broadcast([P, NSEQ, P]), ALU.mult)\
                                .then_inc(*did(f"Sg{h}"))
                            dve.wait_ge(*after("dve", f"Sg{h}"))
                            for part in range(2):
                                x = "ab"[part]
                                dve.wait_ge(*after("pe", f"s{h}{x}"))
                                dve.tensor_tensor(Sh[:, part * 512:(part + 1) * 512], Sh[:, part * 512:(part + 1) * 512],
                                                  psum(f"s{h}{x}", P), ALU.add).then_inc(*did(f"S{h}{x}"))
                        dve.wait_ge(*after("act", "RU"))
                        dve.wait_ge(*after("pe", "s3b"))
                        for t in range(4):
                            if t:
                                dve.wait_ge(*after("pe", f"rs{t - 1}"))
                            for nm, dst, src in (("RUm", RUw, RU), ("RVm", RVw, Vt)):
                                for half in range(2):
                                    hd = 2 * t + half
                                    last = dve.tensor_tensor(
                                        dst[0:n, half * 512:(half + 1) * 512].rearrange("p (s v) -> p s v", s=NSEQ),
                                        src[0:n, None, hd * 64:(hd + 1) * 64].to_broadcast([n, NSEQ, 64]),
                                        own[:, :, None].to_broadcast([n, NSEQ, 64]), ALU.mult)
                                last.then_inc(*did(f"{nm}{t}"))
                            Rt = RS[:, t * 512:(t + 1) * 512]
                            dve.wait_ge(*after("pe", f"rs{t}"))
                            dve.tensor_tensor(Rt, Rt, psum(f"rs{t}", P), ALU.add).then_inc(*did(f"RS{t}"))
                            dve.wait_ge(*after("dve", f"RS{t}"))
                            dve.tensor_tensor(Rt.rearrange("p (s v) -> p s v", s=NSEQ),
                                              Rt.rearrange("p (s v) -> p s v", s=NSEQ),
                                              E4[:, t, :, TS:TS + 1].to_broadcast([P, NSEQ, 64]), ALU.mult)\
                                .then_inc(*did(f"RSd{t}"))


def finish_even(k):
    nc = k.nc
    big = lambda t: k.big_buf[:, t * T:(t + 1) * T]
    hb = lambda t: k.h[:, t * T:(t + 1) * T]
    sq = lambda i: k.arena[:, i * T:(i + 1) * T]
    bonus = lambda i: k.arena[:, (8 + i) * T:(9 + i) * T]
    w2 = k.arena[:, 16 * T:16 * T + 512]
    N = range(4)
    with nc.cleanup_on_exit():
        s = Phase(nc)
        jobs = ([("sum_a", ("act", "root_a"))] + [(f"mean{i}", ("dve", f"center{i}")) for i in N]
                + [(f"spread_a{i}", ("dve", f"norm_a{i}")) for i in N]
                + [(f"bonus{i}", ("dve", f"bonus_v{i}")) for i in N] + [("var", ("act", "root_y"))]
                + [(f"spread_y{i}", ("dve", f"norm_y{i}")) for i in N] + [(f"gate{i}", ("dve", f"out_y{i}")) for i in N])
        q = Schedule(
            s, pe=[n for n, _ in jobs],
            act=[f"sq_a{i}" for i in N] + ["root_a"] + [f"sq_y{i}" for i in N] + ["root_y"],
            dve=[f"rk{i}" for i in N] + [f"center{i}" for i in N] + ["inv_a"]
            + [f"{x}{i}" for i in N for x in ("norm_a", "out_a")] + [f"bonus_v{i}" for i in N] + ["inv_y"]
            + [f"{x}{i}" for i in N for x in ("norm_y", "affine", "out_y")])
        did, after = q.did, q.after
        loaded, restored = s.sem("wg2_loaded"), s.sem("x_restored")
        halves = lambda ap: ap.rearrange("p (a t) -> p a t", a=2)
        norm_a = InverseRoots(k, s, "norm_a", 4, P, k.arena[:, 12 * T:])
        norm_y = InverseRoots(k, s, "norm_y", 4, 64, k.arena[:, 17 * T:])
        pair = {n: k.psum_pair(i % 4) for i, (n, _) in enumerate(jobs)}
        ps = lambda nm: two_halves(pair[nm], HALF)
        with nc.Block() as block:
            @block.sync
            def _(sp):
                sp.dma_start(w2, k.io["w_g2"]).then_inc(loaded, 16)
                sp.dma_start(k.x, k.x_kept).then_inc(restored, 16)
                sp.wait_ge(loaded, 16)
                sp.wait_ge(restored, 16)

            @block.gpsimd
            def _(pool):
                norm_a.constants(pool)
                norm_y.constants(pool)

            @block.tensor
            def _(pe):
                at = {n: i for i, (n, _) in enumerate(jobs)}

                def pair_free(name):
                    if at[name] >= 4:
                        pe.wait_ge(*after(*jobs[at[name] - 4][1]))

                def product(name, lhsT, rhs):
                    pair_free(name)
                    for a in range(2):
                        last = pe.matmul(pair[name][:, a, 0:HALF], lhsT, rhs[:, a * HALF:(a + 1) * HALF],
                                         start=True, stop=True)
                    last.then_inc(*did("pe", name))
                for i in N:
                    pe.wait_ge(*after("act", f"sq_a{i}"))
                    last = norm_a.sum_tile(pe, i, pair["sum_a"], sq(i))
                last.then_inc(*did("pe", "sum_a"))
                for i in N:
                    product(f"mean{i}", k.mask("block64"), hb(NEG_KK + i))
                pe.wait_ge(*after("dve", "inv_a"))
                for i in N:
                    pair_free(f"spread_a{i}")
                    norm_a.spread_tile(pe, i, pair[f"spread_a{i}"]).then_inc(*did("pe", f"spread_a{i}"))
                for i in N:
                    pe.wait_ge(*after("dve", f"rk{i}"))
                    product(f"bonus{i}", k.mask("block64"), bonus(i))
                pair_free("var")
                for i in N:
                    pe.wait_ge(*after("act", f"sq_y{i}"))
                    last = norm_y.sum_tile(pe, i, pair["var"], sq(4 + i))
                last.then_inc(*did("pe", "var"))
                pe.wait_ge(*after("dve", "inv_y"))
                for i in N:
                    pair_free(f"spread_y{i}")
                    norm_y.spread_tile(pe, i, pair[f"spread_y{i}"]).then_inc(*did("pe", f"spread_y{i}"))
                pe.wait_ge(loaded, 16)
                for i in N:
                    product(f"gate{i}", w2[:, i * P:(i + 1) * P], big(G_B))

            @block.scalar
            def _(act):
                for i in N:
                    act.activation(sq(i), big(Q_A + i), ACT.Square).then_inc(*did("act", f"sq_a{i}"))
                act.wait_ge(*after("pe", "sum_a"))
                norm_a.root(act, pair["sum_a"], k.eps[:, 0:1], 1.0 / P).then_inc(*did("act", "root_a"))
                for i in N:
                    act.wait_ge(*after("dve", f"center{i}"))
                    act.activation(sq(4 + i), hb(NEG_KK + i), ACT.Square).then_inc(*did("act", f"sq_y{i}"))
                act.wait_ge(*after("pe", "var"))
                norm_y.root(act, pair["var"], k.eps[:, 1:2], 1.0 / 64).then_inc(*did("act", "root_y"))

            @block.vector
            def _(dve):
                stt = dve.scalar_tensor_tensor
                for i in N:
                    stt(out=bonus(i), in0=big(R_B + i), scalar=k.par("r_k")[:, i:i + 1], in1=big(K_B + i),
                        op0=ALU.mult, op1=ALU.mult).then_inc(*did("dve", f"rk{i}"))
                for i in N:
                    dve.wait_ge(*after("pe", f"mean{i}"))
                    stt(out=halves(hb(NEG_KK + i)), in0=ps(f"mean{i}"), scalar=-1.0 / 64, in1=halves(hb(NEG_KK + i)),
                        op0=ALU.mult, op1=ALU.add).then_inc(*did("dve", f"center{i}"))
                dve.wait_ge(*after("act", "root_a"))
                norm_a.invert(dve).then_inc(*did("dve", "inv_a"))
                for i in N:
                    dve.wait_ge(*after("pe", f"spread_a{i}"))
                    stt(out=halves(sq(i)), in0=ps(f"spread_a{i}"), scalar=k.par("gain_a"), in1=halves(big(Z_A + i)),
                        op0=ALU.mult, op1=ALU.mult).then_inc(*did("dve", f"norm_a{i}"))
                    dve.wait_ge(*after("dve", f"norm_a{i}"))
                    dve.tensor_tensor(big(Q_A + i), big(Q_A + i), sq(i), ALU.mult).then_inc(*did("dve", f"out_a{i}"))
                for i in N:
                    dve.wait_ge(*after("pe", f"bonus{i}"))
                    dve.tensor_tensor(halves(bonus(i)), ps(f"bonus{i}"), halves(big(V_B + i)), ALU.mult)\
                        .then_inc(*did("dve", f"bonus_v{i}"))
                dve.wait_ge(*after("act", "root_y"))
                norm_y.invert(dve).then_inc(*did("dve", "inv_y"))
                for i in N:
                    y = hb(NEG_KK + i)
                    out = big(K_A + i)
                    dve.wait_ge(*after("pe", f"spread_y{i}"))
                    stt(out=halves(y), in0=halves(y), scalar=k.par("lnx_gain")[:, i:i + 1], in1=ps(f"spread_y{i}"),
                        op0=ALU.mult, op1=ALU.mult).then_inc(*did("dve", f"norm_y{i}"))
                    dve.wait_ge(*after("dve", f"norm_y{i}"))
                    stt(out=y, in0=y, scalar=k.par("lnx_bias")[:, i:i + 1], in1=bonus(i), op0=ALU.add, op1=ALU.add)\
                        .then_inc(*did("dve", f"affine{i}"))
                    dve.wait_ge(*after("dve", f"affine{i}"))
                    dve.wait_ge(*after("pe", f"gate{i}"))
                    dve.tensor_tensor(halves(out), ps(f"gate{i}"), halves(y), ALU.mult).then_inc(*did("dve", f"out_y{i}"))


def even_mixer(k, sublayer):
    project_even(k, sublayer)
    prepare_even(k)
    even_chunks(k, sample=False)
    even_chunks(k, sample=True)
    finish_even(k)
    mixer_output(k, k.io["w_out_even"], lambda kt: k.big_buf[:, kt * T:(kt + 1) * T], sublayer)


Q_C, K_C, V_C, Z_C, Q_D, K_D, V_D, O_D, NARROW = 0, 2, 4, 8, 12, 14, 16, 20, 24
B16, B_C = 25, 27
SCALE_64 = 64.0 ** -0.5


def project_odd(k, sublayer):
    nc = k.nc
    TILES = 25
    with nc.cleanup_on_exit():
        s = Phase(nc)
        w = SplitWeights(k, s, k.io["w_in_odd"], TILES)
        norm = Normalised(k, s, sublayer, k.low_r[:, H_LOW - LOW:PROJECTION_END - LOW])
        evacuated = s.sem("evacuated")
        tokens = tokens_of(k.h_r, k.low_r[:, H_LOW - LOW:], TX, TX, HALF)
        with nc.Block() as block:
            @block.sync
            def _(sp):
                w.load_first(sp)
                w.load_rest(sp)

            @block.tensor
            def _(pe):
                w.products(pe, tokens, HALF, evacuated, norm)

            @block.scalar
            def _(act):
                norm.high_samples(act)
                norm.high_tiles(act, 0, 2)
                w.high(act, 0, 0, 0, first=True)
                norm.high_tiles(act, 2, KT)
                w.high(act, 1, 1, 1, first=True)
                w.high(act, 2, 0, 2)
                w.high(act, 3, 1, 3)
                with act.Fori(1, TILES // 4) as r:
                    for b in range(4):
                        w.high(act, b, b % 2, 4 * r + b)
                w.high(act, 0, 0, TILES - 1)

            @block.vector
            def _(dve):
                def tile(b, m):
                    dve.wait_ge(w.product, m + 1)
                    out = k.big_buf[:, bass.ds(m * T, T)].rearrange("p (a t) -> p a t", a=2)
                    dve.tensor_copy(out, two_halves(k.psum_pair(b), HALF)).then_inc(evacuated, 1)
                norm.scale_samples(dve)
                norm.scale_and_low(dve, 0, 2)
                w.low(dve, 0, 0, 0)
                norm.scale_and_low(dve, 2, KT + 1)
                w.low(dve, 1, 1, 1)
                with dve.Fori(0, TILES // 4 - 1) as r:
                    for b in range(4):
                        w.low(dve, (b + 2) % 4, b % 2, 4 * r + b + 2)
                        tile(b, 4 * r + b)
                for m in range(TILES - 5, TILES):
                    if m + 2 < TILES:
                        w.low(dve, (m + 2) % 4, m % 2, m + 2)
                    tile(m % 4, m)


def prepare_odd(k):
    nc = k.nc
    big = lambda t, n=1: k.big_buf[:, t * T:(t + n) * T]
    row = lambda i: k.arena[0:4, i * T:(i + 1) * T]
    fg, ig, lf, soft, fsum, lfm, igm, m, a_row, e_row = (row(i) for i in range(10))
    x2 = lambda i: k.arena[:, (11 + i) * T:(12 + i) * T]
    s2 = lambda i: k.arena[:, (13 + i) * T:(14 + i) * T]
    w2 = k.arena[0:16, 15 * T:15 * T + 256]
    before = k.arena[0:4, 15 * T + 256:15 * T + 256 + NCH]
    m0 = k.arena[0:4, 15 * T + 264:15 * T + 264 + NSEQ]
    bound = k.arena[0:4, 15 * T + 272:15 * T + 272 + NSEQ]
    m_last = k.arena[0:4, 15 * T + 280:15 * T + 280 + NSEQ]
    col_rows = k.arena[:, 16 * T:17 * T]
    resets16 = k.arena[:, 17 * T:18 * T]
    rfm, rw, rnm = (k.mrows[:, i * T:(i + 1) * T] for i in range(3))
    act_steps = (["silu_z", "sig_o"] + ["abs_f", "exp_f", "ln_f"]
                 + [f"{x}{i}" for i in range(2) for x in ("abs", "exp", "ln")] + ["exp_e", "cols"])
    dve_steps = (["resets16", "gates", "fg", "ig", "clear", "lf0", "lf", "fsum", "lfm", "igm", "bound1", "bound2", "cut_f",
                  "cut_i", "m", "m_last", "a", "before0", "before", "fm", "w_p", "w_s", "nm", "e_p", "e_s", "a_col"]
                 + [f"{x}{i}" for i in range(2) for x in ("x", "s1_", "s2_", "b", "b16_")])
    with nc.cleanup_on_exit():
        s = Phase(nc)
        q = Schedule(s, act=act_steps, dve=dve_steps, pe=["gk0", "gk1", "cols"])
        did, after = q.did, q.after
        loaded, stored, ones16 = s.sem("loaded"), s.sem("stored"), s.sem("ones16")
        with nc.Block() as block:
            @block.sync
            def _(sp):
                sp.dma_start(w2, k.io["w_gk2"]).then_inc(loaded, 16)
                sp.dma_start(m0, k.io["mm_in"]).then_inc(loaded, 16)
                sp.wait_ge(*after("dve", "m_last"))
                sp.dma_start(k.io["mm_p_out"], m[:, TP - 1:TP]).then_inc(stored, 16)
                sp.dma_start(k.io["mm_s_out"], m_last).then_inc(stored, 16)
                sp.wait_ge(stored, 32)

            @block.gpsimd
            def _(pool):
                pool.memset(resets16, 1.0).then_inc(ones16, 1)

            @block.scalar
            def _(act):
                act.activation(big(Z_C, 4), big(Z_C, 4), ACT.Silu).then_inc(*did("act", "silu_z"))
                act.activation(big(O_D, 4), big(O_D, 4), ACT.Sigmoid).then_inc(*did("act", "sig_o"))
                act.wait_ge(*after("dve", "fg"))
                act.activation(soft, fg, ACT.Abs).then_inc(*did("act", "abs_f"))
                act.wait_ge(*after("act", "abs_f"))
                act.activation(soft, soft, ACT.Exp, scale=-1.0).then_inc(*did("act", "exp_f"))
                act.wait_ge(*after("act", "exp_f"))
                act.activation(soft, soft, ACT.Ln, bias=1.0).then_inc(*did("act", "ln_f"))
                for i in range(2):
                    act.wait_ge(*after("dve", f"x{i}"))
                    act.activation(s2(i), x2(i), ACT.Abs).then_inc(*did("act", f"abs{i}"))
                    act.wait_ge(*after("act", f"abs{i}"))
                    act.activation(s2(i), s2(i), ACT.Exp, scale=-1.0).then_inc(*did("act", f"exp{i}"))
                    act.wait_ge(*after("act", f"exp{i}"))
                    act.activation(s2(i), s2(i), ACT.Ln, bias=1.0).then_inc(*did("act", f"ln{i}"))
                act.wait_ge(*after("dve", "e_s"))
                act.activation(col_rows[32:36, :], e_row, ACT.Exp).then_inc(*did("act", "exp_e"))
                act.wait_ge(*after("pe", "cols"))
                cols = k.cols.rearrange("p (c r h) -> p c r h", c=5, r=4)
                act.activation(cols[:, 0:4, 0:2], k.psum[4].rearrange("p (c r h) -> p c r h", c=4, r=4)
                               [:, :, 0:2, 0:4], ACT.Copy)
                act.activation(cols[0:64, 4, 0:2], k.psum[5][0:64, 0:P].rearrange("p (r h) -> p r h", r=4)
                               [:, 0:2, 0:4], ACT.Copy).then_inc(*did("act", "cols"))

            @block.tensor
            def _(pe):
                pe.wait_ge(loaded, 32)
                for i in range(2):
                    for a in range(2):
                        at = NARROW * T + a * HALF
                        last = pe.matmul(k.psum_pair(i)[:, a, 0:HALF], w2[:, i * P:(i + 1) * P],
                                         k.big_buf[0:16, at:at + HALF], start=True, stop=True)
                    last.then_inc(*did("pe", f"gk{i}"))
                pe.wait_ge(*after("act", "exp_e"))
                pe.wait_ge(*after("dve", "a_col"))
                for c in range(NCH):
                    pe.transpose(k.psum[4][:, c * P:(c + 1) * P], col_rows[:, c * P:(c + 1) * P], k.mask("ident"))
                pe.transpose(k.psum[5][0:64, 0:P], col_rows[:, TP:T], k.mask("ident")).then_inc(*did("pe", "cols"))

            @block.vector
            def _(dve):
                tt, ts = dve.tensor_tensor, dve.tensor_scalar
                w = lambda name: dve.wait_ge(*after("dve", name))
                chunked = lambda v: v[:, 0:TP].rearrange("p (c i) -> p c i", i=CH)
                seqs = lambda v: v[:, TP:T].rearrange("p (c i) -> p c i", i=TS)
                dve.wait_ge(ones16, 1)
                dve.memset(resets16[:, 0:TP].rearrange("p (c i) -> p c i", i=16)[:, :, 0:1], 0.0)
                dve.memset(resets16[:, TP:T].rearrange("p (c i) -> p c i", i=TS)[:, :, 0:1], 0.0)\
                    .then_inc(*did("dve", "resets16"))
                dve.tensor_copy(fg, k.big_buf[64:68, NARROW * T:(NARROW + 1) * T])
                dve.tensor_copy(ig, k.big_buf[32:36, NARROW * T:(NARROW + 1) * T]).then_inc(*did("dve", "gates"))
                w("gates")
                ts(fg, fg, k.par("b_f")[0:4], None, ALU.add).then_inc(*did("dve", "fg"))
                ts(ig, ig, k.par("b_i")[0:4], None, ALU.add).then_inc(*did("dve", "ig"))
                dve.memset(col_rows, 0.0).then_inc(*did("dve", "clear"))
                w("fg")
                ts(lf, fg, 0.0, None, ALU.min).then_inc(*did("dve", "lf0"))
                dve.wait_ge(*after("act", "ln_f"))
                w("lf0")
                tt(lf, lf, soft, ALU.subtract).then_inc(*did("dve", "lf"))
                w("lf")
                dve.tensor_tensor_scan(fsum, k.resets[0:4], lf, 0.0, ALU.mult, ALU.add).then_inc(*did("dve", "fsum"))
                dve.tensor_copy(lfm, lf).then_inc(*did("dve", "lfm"))
                w("ig")
                dve.tensor_copy(igm, ig).then_inc(*did("dve", "igm"))
                dve.wait_ge(loaded, 32)
                w("igm")
                tt(bound, lf[:, TP:T:TS], m0, ALU.add).then_inc(*did("dve", "bound1"))
                w("bound1")
                tt(bound, bound, igm[:, TP:T:TS], ALU.max).then_inc(*did("dve", "bound2"))
                w("bound2")
                dve.memset(lfm[:, TP:T:TS], -BIG).then_inc(*did("dve", "cut_f"))
                dve.tensor_copy(igm[:, TP:T:TS], bound).then_inc(*did("dve", "cut_i"))
                w("cut_i")
                dve.tensor_tensor_scan(m, lfm, igm, 0.0, ALU.add, ALU.max).then_inc(*did("dve", "m"))
                w("m")
                dve.tensor_copy(m_last, m[:, TP + TS - 1:T:TS]).then_inc(*did("dve", "m_last"))
                tt(a_row, ig, fsum, ALU.subtract).then_inc(*did("dve", "a"))
                dve.memset(before[:, 0:1], 0.0).then_inc(*did("dve", "before0"))
                w("m")
                dve.tensor_copy(before[:, 1:NCH], m[:, CH - 1:TP - 1:CH]).then_inc(*did("dve", "before"))
                tt(rfm, fsum, m, ALU.subtract).then_inc(*did("dve", "fm"))
                w("fm")
                tt(chunked(rw), chunked(rfm), before[:, :, None].to_broadcast([4, NCH, CH]), ALU.add)\
                    .then_inc(*did("dve", "w_p"))
                tt(seqs(rw), seqs(rfm), m0[:, :, None].to_broadcast([4, NSEQ, TS]), ALU.add)\
                    .then_inc(*did("dve", "w_s"))
                ts(rnm, m, -1.0, None, ALU.mult).then_inc(*did("dve", "nm"))
                tt(chunked(e_row), chunked(a_row), chunked(rfm)[:, :, CH - 1:CH].to_broadcast([4, NCH, CH]), ALU.add)\
                    .then_inc(*did("dve", "e_p"))
                tt(seqs(e_row), seqs(a_row), seqs(rfm)[:, :, TS - 1:TS].to_broadcast([4, NSEQ, TS]), ALU.add)\
                    .then_inc(*did("dve", "e_s"))
                w("clear")
                dve.tensor_copy(col_rows[0:4, :], a_row).then_inc(*did("dve", "a_col"))
                for i in range(2):
                    dve.wait_ge(*after("pe", f"gk{i}"))
                    ts(x2(i).rearrange("p (a t) -> p a t", a=2), two_halves(k.psum_pair(i), HALF),
                       k.par("b_gk")[:, i:i + 1], None, ALU.add).then_inc(*did("dve", f"x{i}"))
                    dve.wait_ge(*after("act", f"ln{i}"))
                    dve.scalar_tensor_tensor(out=x2(i), in0=x2(i), scalar=0.0, in1=s2(i), op0=ALU.min,
                                             op1=ALU.subtract).then_inc(*did("dve", f"s1_{i}"))
                    w(f"s1_{i}")
                    ts(x2(i), x2(i), 1.0 / 16.0, None, ALU.mult).then_inc(*did("dve", f"s2_{i}"))
                    w(f"s2_{i}")
                    dve.tensor_tensor_scan(big(B_C + i), k.resets, x2(i), 0.0, ALU.mult, ALU.add)\
                        .then_inc(*did("dve", f"b{i}"))
                    dve.tensor_tensor_scan(big(B16 + i), resets16, x2(i), 0.0, ALU.mult, ALU.add)\
                        .then_inc(*did("dve", f"b16_{i}"))


def odd_jobs(sample):
    levels = () if sample else LEVELS
    jobs = [("r", ("dve", "log1")), ("rw", ("act", "xw")), ("nm", ("act", "xm"))]
    jobs += [(f"qk_{g}", ("dve", f"DM_{g}")) for g in range(2)]
    jobs += [("vct", ("act", "Vc")), ("vdt", ("act", "Vd")), ("kdt", ("dve", "KE"))]
    jobs += [(f"at_{g}", ("dve", f"AT_{g}")) for g in range(2)]
    jobs += [(f"at{w}_{g}", ("dve", f"L{w}_{g}")) for w in levels for g in range(2)]
    jobs += [("klt", ("act", "KL"))]
    if sample:
        jobs += [("co_s", ("act", "CO")), ("do_s", ("act", "DO")), ("dn_s", ("act", "DN"))]
    jobs += [("co", ("dve" if sample else "act", "Oc")), ("do", ("dve", "Od")), ("dn", ("dve", "den"))]
    if sample:
        for t in range(2):
            jobs += [(f"{n}{t}{x}", ("dve", f"{u}{t}{x}")) for n, u in (("sc", "SC"), ("sd", "SD")) for x in "ab"]
        jobs += [("sn", ("dve", "SN"))]
    else:
        jobs += [("sc", ("dve", "SC")), ("sd", ("dve", "SD"))]
    return jobs


def odd_chunks(k, sample):
    nc = k.nc
    n = NSEQ * TS if sample else CH
    chunks = [NCH] if sample else list(range(NCH))
    names = lambda base, c: f"{base}@{c}"
    levels = () if sample else LEVELS
    jobs = odd_jobs(sample)
    pe_steps, freed, act_steps, dve_steps = [], [], [], []
    for c in chunks:
        pe_steps += [names(j, c) for j, _ in jobs]
        freed += [(e, names(st, c)) for _, (e, st) in jobs]
        a = ["x16", "xn16", "xb", "xl"] + [x for w in levels for x in (f"abs{w}", f"F{w}")]
        a += ["xw", "xm", "xlog", "Vc", "Vd", "KL"] + (["CO", "DO", "DN"] if sample else ["Oc"]) + ["aden"]
        d = ["to_end", "Qb", "Qd", "Kd", "Kl"] + [x for w in levels for x in (f"rel{w}", f"Q{w}", f"K{w}")]
        d += ["log1", "log2", "qw", "DM_0", "DM_1", "KE", "AT_0", "AT_1"]
        d += [x for w in levels for g in range(2) for x in (f"L{w}_{g}", f"A{w}_{g}")]
        if sample:
            d += ["Nw", "Oc"]
        d += ["den", "max", "inv", "Od"] + (["Od2"] if sample else [])
        if sample:
            for t in range(2):
                for kind in ("C", "D"):
                    d += [f"V{kind}{t}", f"G{kind}{t}", f"S{kind}{t}a", f"S{kind}{t}b"]
            d += ["GN", "SN"]
        else:
            d += ["GC", "SC", "GD", "SD"]
        act_steps += [names(x, c) for x in a]
        dve_steps += [names(x, c) for x in d]
    if not sample:
        dve_steps.append("n_last")
    take = carve(k.arena[:, 0:ARENA - 3 * T])
    H, H2 = 4 * n, 2 * n
    x16, xn16, xb, xl = (take(H2) for _ in range(4))
    Qd, Kd, Qb, Kl = (take(H2) for _ in range(4))
    F = {w: take(H2) for w in levels}
    Q = {w: take(H2) for w in levels}
    K = {w: take(H2) for w in levels}
    L = {w: take(H) for w in levels}
    xw, qw = take(H2), take(H2)
    xm, lg, DM, AT, aden = (take(H) for _ in range(5))
    Vc, Vd, KE, KL = take(512), take(512), take(256), take(256)
    if sample:
        SC, SD, SN, Nw = take(2048), take(2048), take(16), take(2048)
        CO, DO, DN = take(H), take(H), take(H)
        Vw = {(kind, half): take(1024) for kind in "CD" for half in range(2)}
    else:
        n_last = take(2)
        SC, SD = take(256), take(512)
    v2 = lambda ap: ap.rearrange("p (t i) -> p t i", t=2)
    v4 = lambda ap, part=P: ap[0:part].rearrange("p (h n) -> p h n", h=4)
    par_of = lambda ap, g: ap[0:n].rearrange("p (t g i) -> p t g i", t=2, g=2)[:, :, g]
    bc = lambda m, cnt: m[:, None, :].to_broadcast([n, cnt, n])
    mask = lambda nm: k.mask(nm)[0:n, 0:n]
    sfx = "8" if sample else "16"

    with nc.cleanup_on_exit():
        ph = Phase(nc)
        sched = Schedule(ph, pe=pe_steps, act=act_steps, dve=dve_steps)
        number = {j: i for i, j in enumerate(pe_steps)}
        states_in, states_out, zeroed = ph.sem("states_in"), ph.sem("states_out"), ph.sem("zeroed")
        even_heads = ph.sem("even_heads")
        bank = lambda job, c: k.psum[number[names(job, c)] % 8]

        def tokens(t, c, count=4):
            return k.big_buf[:, t * T:(t + count) * T].rearrange("p (h t) -> p h t", t=T)[:, :, c * CH:c * CH + n]

        def col(c, r):
            v = k.cols[0:n].rearrange("p (c r h) -> p c r h", c=5, r=4)[:, c, r, :]
            return lambda w: v[:, :, None].to_broadcast([n, 4, w])

        with nc.Block() as block:
            @block.sync
            def _(sp):
                if sample:
                    sp.dma_start(SC, k.io["gla_in"]).then_inc(states_in, 16)
                    sp.dma_start(SD, k.io["mc_in"]).then_inc(states_in, 16)
                    sp.dma_start(SN, k.io["mn_in"]).then_inc(states_in, 16)
                    sp.wait_ge(*sched.after("dve", names("SN", NCH)))
                    sp.dma_start(k.io["gla_s_out"], SC).then_inc(states_out, 16)
                    sp.dma_start(k.io["mc_s_out"], SD).then_inc(states_out, 16)
                    sp.dma_start(k.io["mn_s_out"], SN).then_inc(states_out, 16)
                else:
                    sp.wait_ge(*sched.after("dve", names("SD", NCH - 1)))
                    sp.dma_start(k.io["gla_p_out"], SC).then_inc(states_out, 16)
                    sp.dma_start(k.io["mc_p_out"], SD[:, 0:256]).then_inc(states_out, 16)
                    sp.wait_ge(*sched.after("dve", "n_last"))
                    sp.dma_start(k.io["mn_p_out"], n_last).then_inc(states_out, 16)
                sp.wait_ge(states_out, 48)

            @block.gpsimd
            def _(pool):
                if not sample:
                    pool.memset(SC, 0.0).then_inc(zeroed, 1)
                    pool.memset(SD, 0.0).then_inc(zeroed, 1)

            @block.tensor
            def _(pe):
                for c in chunks:
                    after = lambda e, nm: sched.after(e, names(nm, c))

                    def claim(job):
                        i = number[names(job, c)]
                        if i >= 8:
                            pe.wait_ge(*sched.after(*freed[i - 8]))
                        return bank(job, c)

                    def done(job, ins):
                        ins.then_inc(*sched.did("pe", names(job, c)))

                    def rows(job, source, matrices):
                        b = claim(job)
                        for i, m in enumerate(matrices):
                            last = pe.matmul(b[:, i * n:(i + 1) * n], k.select(m)[0:4],
                                             source[:, c * CH:c * CH + n], start=True, stop=True)
                        done(job, last)
                    rfm, rw, rnm = (k.mrows[:, i * T:(i + 1) * T] for i in range(3))
                    rows("r", rfm, range(4))
                    rows("rw", rw, (4, 5))
                    rows("nm", rnm, range(4))
                    kd, qd = tokens(K_D, c, 2), tokens(Q_D, c, 2)

                    def pair(job, lhsT, rhs):
                        g = int(job[-1])
                        p = slice(64 * g, 64 * g + 64)
                        b = claim(job)
                        for t in range(2):
                            last = pe.matmul(b[0:n, t * n:(t + 1) * n], lhsT(p, t), rhs(p, t), start=True, stop=True)
                        done(job, last)

                    def transposes(job, source, count):
                        b = claim(job)
                        for i in range(count):
                            last = pe.transpose(b[0:n, i * P:(i + 1) * P], source(i), k.mask("ident"))
                        done(job, last)
                    for g in range(2):
                        pair(f"qk_{g}", lambda p, t: kd[p, t], lambda p, t: qd[p, t])
                    vc, vd = tokens(V_C, c), tokens(V_D, c)
                    transposes("vct", lambda i: vc[:, i], 4)
                    transposes("vdt", lambda i: vd[:, i], 4)
                    transposes("kdt", lambda i: kd[:, i], 2)
                    pe.wait_ge(*after("dve", "Kd"))
                    of = lambda buf: (lambda p, t: buf[p, t * n:(t + 1) * n])
                    for g in range(2):
                        pair(f"at_{g}", of(Kd), of(Qd))
                    for w in levels:
                        pe.wait_ge(*after("dve", f"K{w}"))
                        for g in range(2):
                            pair(f"at{w}_{g}", of(K[w]), of(Q[w]))
                    transposes("klt", lambda i: Kl[:, i * n:(i + 1) * n], 2)
                    last_a = f"A{levels[-1]}_1" if levels else "AT_1"
                    if sample:
                        pe.wait_ge(states_in, 48)
                        pe.wait_ge(*after("dve", "Nw"))
                        for turn, (job, state, right) in enumerate((
                                ("co_s", SC, Qb), ("do_s", SD, qw), ("dn_s", Nw, qw))):
                            b = claim(job)
                            for g in range(2):
                                if g:
                                    pe.wait_ge(even_heads, turn + 1)
                                for t in range(2):
                                    for q in range(NSEQ):
                                        h = 2 * t + g
                                        p = slice(64 * g, 64 * g + 64)
                                        last = pe.matmul(
                                            b[:, h * n + q * TS:h * n + (q + 1) * TS],
                                            state[p, (t * NSEQ + q) * P:(t * NSEQ + q + 1) * P],
                                            right[p, t * n + q * TS:t * n + (q + 1) * TS], start=True, stop=True)
                                if not g:
                                    last.then_inc(even_heads, 1)
                            done(job, last)
                    else:
                        if c == 0:
                            pe.wait_ge(zeroed, 2)
                        else:
                            pe.wait_ge(*sched.after("dve", names("SD", c - 1)))

                    def output(job, state, right, values, weights, ready):
                        pe.wait_ge(*ready)
                        b = claim(job)
                        for h in (0, 2, 1, 3):
                            t, g = h // 2, h % 2
                            out = b[:, h * n:(h + 1) * n]
                            if not sample and h == 1:
                                pe.wait_ge(even_heads, 3 * c + ("co", "do", "dn").index(job) + 1)
                            if not sample:
                                p = slice(64 * g, 64 * g + 64)
                                pe.matmul(out, state[p, t * P:(t + 1) * P], right[p, t * n:(t + 1) * n],
                                          start=True, stop=False)
                            last = pe.matmul(out, values(h), weights[0:n, h * n:(h + 1) * n],
                                             start=sample, stop=True)
                            if not sample and h == 2:
                                last.then_inc(even_heads, 1)
                        done(job, last)
                    pe.wait_ge(*after("act", "KL"))
                    output("co", SC, Qb, lambda h: Vc[0:n, h * P:(h + 1) * P], AT, after("dve", last_a))
                    output("do", SD, qw, lambda h: Vd[0:n, h * P:(h + 1) * P], DM, after("dve", "KE"))
                    output("dn", SD[:, 256:] if not sample else None, qw,
                           lambda h: k.mask("ones")[0:n], DM, after("dve", "KE"))
                    if not sample:
                        b = claim("sc")
                        for h in range(4):
                            t, p = h // 2, 64 * (h % 2)
                            last = pe.matmul(b[p:p + 64, t * P:(t + 1) * P], KL[:, h * 64:(h + 1) * 64],
                                             Vc[:, h * P:(h + 1) * P], start=True, stop=True)
                        done("sc", last)
                        b = claim("sd")
                        for h in range(4):
                            t, p = h // 2, 64 * (h % 2)
                            for part, values in ((0, Vd[:, h * P:(h + 1) * P]), (256, k.mask("ones"))):
                                last = pe.matmul(b[p:p + 64, part + t * P:part + (t + 1) * P],
                                                 KE[:, h * 64:(h + 1) * 64], values, start=True, stop=True)
                        done("sd", last)
                    else:
                        for t in range(2):
                            for kind, left in (("C", KL), ("D", KE)):
                                pe.wait_ge(*after("dve", f"V{kind}{t}"))
                                for part, x in enumerate("ab"):
                                    b = claim(f"s{kind.lower()}{t}{x}")
                                    for g in range(2):
                                        h = 2 * t + g
                                        last = pe.matmul(b[64 * g:64 * g + 64, :], left[0:n, h * 64:(h + 1) * 64],
                                                         Vw[kind, g][0:n, part * 512:(part + 1) * 512],
                                                         start=True, stop=True)
                                    done(f"s{kind.lower()}{t}{x}", last)
                        b = claim("sn")
                        for h in range(4):
                            t, p = h // 2, 64 * (h % 2)
                            last = pe.matmul(b[p:p + 64, t * NSEQ:(t + 1) * NSEQ], KE[0:n, h * 64:(h + 1) * 64],
                                             k.mask("block8")[0:n, 0:n:TS], start=True, stop=True)
                        done("sn", last)

            @block.scalar
            def _(act):
                for c in chunks:
                    after = lambda e, nm: sched.after(e, names(nm, c))
                    did = lambda nm: sched.did("act", names(nm, c))
                    psum = lambda job, part=n: bank(job, c)[0:part]
                    if c > chunks[0]:
                        act.wait_ge(*sched.after("dve", names("SD", c - 1)))
                        act.wait_ge(*sched.after("act", names("aden", c - 1)))
                    b16, bC = tokens(B16, c, 2), tokens(B_C, c, 2)
                    act.activation(v2(x16), b16, ACT.Exp).then_inc(*did("x16"))
                    act.activation(v2(xn16), b16, ACT.Exp, scale=-1.0).then_inc(*did("xn16"))
                    act.activation(v2(xb), bC, ACT.Exp).then_inc(*did("xb"))
                    act.wait_ge(*after("dve", "to_end"))
                    act.activation(xl, xl, ACT.Exp).then_inc(*did("xl"))
                    for w in levels:
                        act.wait_ge(*after("dve", f"rel{w}"))
                        act.activation(F[w], F[w], ACT.Abs).then_inc(*did(f"abs{w}"))
                        act.wait_ge(*after("act", f"abs{w}"))
                        act.activation(F[w], F[w], ACT.Exp, scale=-1.0).then_inc(*did(f"F{w}"))
                    act.wait_ge(*after("pe", "rw"))
                    act.activation(xw, psum("rw", P)[:, 0:H2], ACT.Exp).then_inc(*did("xw"))
                    act.wait_ge(*after("pe", "nm"))
                    act.activation(xm, psum("nm", P)[:, 0:H], ACT.Exp).then_inc(*did("xm"))
                    act.wait_ge(*after("dve", "log2"))
                    act.activation(lg[0:n], lg[0:n], ACT.Exp).then_inc(*did("xlog"))
                    for step, job, dst, cols in (("Vc", "vct", Vc, 512), ("Vd", "vdt", Vd, 512), ("KL", "klt", KL, 256)):
                        act.wait_ge(*after("pe", job))
                        act.activation(dst[0:n], psum(job)[:, 0:cols], ACT.Copy).then_inc(*did(step))
                    if sample:
                        for step, job, dst in (("CO", "co_s", CO), ("DO", "do_s", DO), ("DN", "dn_s", DN)):
                            act.wait_ge(*after("pe", job))
                            act.activation(dst, psum(job, P)[:, 0:H], ACT.Copy).then_inc(*did(step))
                        act.wait_ge(*after("dve", "den"))
                        act.activation(aden, aden, ACT.Abs).then_inc(*did("aden"))
                    else:
                        act.wait_ge(*after("pe", "co"))
                        act.activation(tokens(V_C, c), v4(psum("co", P)), ACT.Copy).then_inc(*did("Oc"))
                        act.wait_ge(*after("dve", "den"))
                        act.activation(aden, aden, ACT.Abs).then_inc(*did("aden"))

            @block.vector
            def _(dve):
                tt, ts, stt = dve.tensor_tensor, dve.tensor_scalar, dve.scalar_tensor_tensor
                for c in chunks:
                    after = lambda e, nm: sched.after(e, names(nm, c))
                    did = lambda nm: sched.did("dve", names(nm, c))
                    psum = lambda job, part=n: bank(job, c)[0:part]
                    w_ = lambda nm: dve.wait_ge(*after("dve", nm))
                    if c > chunks[0]:
                        dve.wait_ge(*sched.after("pe", names("sd", c - 1)))
                        dve.wait_ge(*sched.after("dve", names("SD", c - 1)))
                        dve.wait_ge(*sched.after("act", names("aden", c - 1)))
                    bC = tokens(B_C, c, 2)
                    if sample:
                        s8 = lambda ap: ap.rearrange("p t (s i) -> p t s i", s=NSEQ)
                        end = s8(bC)[:, :, :, TS - 1:TS].to_broadcast([P, 2, NSEQ, TS])
                        tt(s8(v2(xl)), end, s8(bC), ALU.subtract).then_inc(*did("to_end"))
                    else:
                        end = bC[:, :, n - 1:n].to_broadcast([P, 2, n])
                        tt(v2(xl), end, bC, ALU.subtract).then_inc(*did("to_end"))
                    q, kk = tokens(Q_C, c, 2), tokens(K_C, c, 2)
                    dve.wait_ge(*after("act", "xl"))
                    stt(out=v2(Qb), in0=q, scalar=SCALE_64, in1=v2(xb), op0=ALU.mult, op1=ALU.mult).then_inc(*did("Qb"))
                    stt(out=v2(Qd), in0=q, scalar=SCALE_64, in1=v2(x16), op0=ALU.mult, op1=ALU.mult)\
                        .then_inc(*did("Qd"))
                    tt(v2(Kd), kk, v2(xn16), ALU.mult).then_inc(*did("Kd"))
                    tt(v2(Kl), kk, v2(xl), ALU.mult).then_inc(*did("Kl"))
                    for w in levels:
                        blocks = n // (2 * w)
                        b4 = lambda ap: ap.rearrange("p t (b i) -> p t b i", b=blocks)
                        tt(b4(v2(F[w])), b4(bC), b4(bC)[:, :, :, w - 1:w].to_broadcast([P, 2, blocks, 2 * w]),
                           ALU.subtract).then_inc(*did(f"rel{w}"))
                        dve.wait_ge(*after("act", f"F{w}"))
                        stt(out=v2(Q[w]), in0=q, scalar=SCALE_64, in1=v2(F[w]), op0=ALU.mult, op1=ALU.mult)\
                            .then_inc(*did(f"Q{w}"))
                        tt(v2(K[w]), kk, v2(F[w]), ALU.mult).then_inc(*did(f"K{w}"))
                    dve.wait_ge(*after("pe", "r"))
                    nb = k.big("not_above_eq" + ("8" if sample else ""))[0:n, 0:n][:, None, :].to_broadcast([n, 4, n])
                    tt(v4(lg, n), v4(psum("r")[:, 0:H], n), nb, ALU.subtract).then_inc(*did("log1"))
                    w_("log1")
                    tt(v4(lg, n), v4(lg, n), col(c, 0)(n), ALU.add).then_inc(*did("log2"))
                    dve.wait_ge(*after("act", "xw"))
                    tt(v2(qw), tokens(Q_D, c, 2), v2(xw), ALU.mult).then_inc(*did("qw"))
                    dve.wait_ge(*after("act", "xlog"))
                    for g in range(2):
                        dve.wait_ge(*after("pe", f"qk_{g}"))
                        stt(out=par_of(DM, g), in0=v2(psum(f"qk_{g}")[:, 0:H2]), scalar=SCALE_64, in1=par_of(lg, g),
                            op0=ALU.mult, op1=ALU.mult).then_inc(*did(f"DM_{g}"))
                    dve.wait_ge(*after("pe", "kdt"))
                    stt(out=v4(KE, n), in0=v4(psum("kdt")[:, 0:256], n), scalar=SCALE_64, in1=col(c, 1)(64),
                        op0=ALU.mult, op1=ALU.mult).then_inc(*did("KE"))
                    for g in range(2):
                        dve.wait_ge(*after("pe", f"at_{g}"))
                        tt(par_of(AT, g), v2(psum(f"at_{g}")[:, 0:H2]), bc(mask("above_eq" + sfx), 2), ALU.mult)\
                            .then_inc(*did(f"AT_{g}"))
                    before = "AT"
                    for w in levels:
                        for g in range(2):
                            dve.wait_ge(*after("pe", f"at{w}_{g}"))
                            tt(par_of(L[w], g), v2(psum(f"at{w}_{g}")[:, 0:H2]), bc(mask(f"above_level{w}"), 2), ALU.mult)\
                                .then_inc(*did(f"L{w}_{g}"))
                            w_(f"L{w}_{g}")
                            tt(par_of(AT, g), par_of(AT, g), par_of(L[w], g), ALU.add).then_inc(*did(f"A{w}_{g}"))
                    if sample:
                        dve.wait_ge(states_in, 48)
                        dve.tensor_copy(Nw.rearrange("p (s v) -> p s v", v=P), SN[:, :, None].to_broadcast([P, 16, P]))\
                            .then_inc(*did("Nw"))
                        dve.wait_ge(*after("pe", "co"))
                        dve.wait_ge(*after("act", "CO"))
                        tt(tokens(V_C, c), v4(psum("co", P)[:, 0:H]), v4(CO), ALU.add).then_inc(*did("Oc"))
                        dve.wait_ge(*after("pe", "dn"))
                        dve.wait_ge(*after("act", "DN"))
                        tt(aden, psum("dn", P)[:, 0:H], DN, ALU.add).then_inc(*did("den"))
                    else:
                        dve.wait_ge(*after("pe", "dn"))
                        dve.tensor_copy(aden, psum("dn", P)[:, 0:H]).then_inc(*did("den"))
                    dve.wait_ge(*after("act", "aden"))
                    tt(aden, aden, xm, ALU.max).then_inc(*did("max"))
                    w_("max")
                    dve.reciprocal(aden, aden).then_inc(*did("inv"))
                    w_("inv")
                    if sample:
                        dve.wait_ge(*after("act", "DO"))
                        tt(DO, psum("do", P)[:, 0:H], DO, ALU.add).then_inc(*did("Od"))
                        w_("Od")
                        tt(tokens(V_D, c), v4(DO), v4(aden), ALU.mult).then_inc(*did("Od2"))
                        own = mask("block8")[:, 0:n:TS]
                        own_b = own[:, :, None].to_broadcast([n, NSEQ, P])
                        for t in range(2):
                            for kind, values, state in (("C", Vc, SC), ("D", Vd, SD)):
                                if t:
                                    dve.wait_ge(*after("pe", f"s{kind.lower()}{t - 1}b"))
                                for g in range(2):
                                    h = 2 * t + g
                                    last = tt(Vw[kind, g][0:n].rearrange("p (s v) -> p s v", s=NSEQ),
                                              values[0:n, None, h * P:(h + 1) * P].to_broadcast([n, NSEQ, P]),
                                              own_b, ALU.mult)
                                last.then_inc(*did(f"V{kind}{t}"))
                                St = state[:, t * 1024:(t + 1) * 1024]
                                ends = (xb if kind == "C" else xw)[:, t * n + TS - 1:(t + 1) * n:TS]
                                tt(St.rearrange("p (s v) -> p s v", s=NSEQ), St.rearrange("p (s v) -> p s v", s=NSEQ),
                                   ends[:, :, None].to_broadcast([P, NSEQ, P]), ALU.mult).then_inc(*did(f"G{kind}{t}"))
                                w_(f"G{kind}{t}")
                                for part, x in enumerate("ab"):
                                    dve.wait_ge(*after("pe", f"s{kind.lower()}{t}{x}"))
                                    cs = slice(part * 512, (part + 1) * 512)
                                    tt(St[:, cs], St[:, cs], psum(f"s{kind.lower()}{t}{x}", P), ALU.add)\
                                        .then_inc(*did(f"S{kind}{t}{x}"))
                        ends = xw.rearrange("p (t s i) -> p t s i", t=2, s=NSEQ)[:, :, :, TS - 1]
                        sn = SN.rearrange("p (t s) -> p t s", t=2)
                        tt(sn, sn, ends, ALU.mult).then_inc(*did("GN"))
                        w_("GN")
                        dve.wait_ge(*after("pe", "sn"))
                        tt(SN, SN, psum("sn", P)[:, 0:16], ALU.add).then_inc(*did("SN"))
                    else:
                        tt(tokens(V_D, c), v4(psum("do", P)), v4(aden), ALU.mult).then_inc(*did("Od"))
                        if c == 0:
                            dve.wait_ge(zeroed, 2)
                        dve.wait_ge(*after("pe", "sc"))
                        tt(v2(SC), v2(SC), v2(xb)[:, :, n - 1:n].to_broadcast([P, 2, P]), ALU.mult).then_inc(*did("GC"))
                        w_("GC")
                        tt(SC, SC, psum("sc", P)[:, 0:256], ALU.add).then_inc(*did("SC"))
                        dve.wait_ge(*after("pe", "sd"))
                        ends = v2(xw)[:, :, n - 1:n]
                        d4 = SD.rearrange("p (a t v) -> p a t v", a=2, t=2)
                        tt(d4, d4, ends[:, None].to_broadcast([P, 2, 2, P]), ALU.mult).then_inc(*did("GD"))
                        w_("GD")
                        tt(SD, SD, psum("sd", P), ALU.add).then_inc(*did("SD"))
                        if c == chunks[-1]:
                            w_("SD")
                            dve.tensor_copy(n_last, SD[:, 256:512:P]).then_inc(*sched.did("dve", "n_last"))


def finish_odd(k):
    nc = k.nc
    big = lambda t: k.big_buf[:, t * T:(t + 1) * T]
    sq = lambda i: k.arena[:, i * T:(i + 1) * T]
    N = range(8)
    src = lambda i: big(V_C + i) if i < 4 else big(V_D + i - 4)
    gate = lambda i: big(Z_C + i) if i < 4 else big(O_D + i - 4)
    with nc.cleanup_on_exit():
        s = Phase(nc)
        q = Schedule(s, pe=[f"{x}{i}" for x in ("sum", "spread") for i in N], act=[f"sq{i}" for i in N] + ["root"],
                     dve=["inverse"] + [f"{x}{i}" for i in N for x in ("gated", "out")])
        did, after = q.did, q.after
        norm = InverseRoots(k, s, "norm", len(N), P, k.arena[:, len(N) * T:])
        halves = lambda ap: ap.rearrange("p (a t) -> p a t", a=2)
        with nc.Block() as block:
            @block.tensor
            def _(pe):
                for i in N:
                    pe.wait_ge(*after("act", f"sq{i}"))
                    norm.sum_tile(pe, i, k.psum_pair(0), sq(i)).then_inc(*did("pe", f"sum{i}"))
                pe.wait_ge(*after("dve", "inverse"))
                for i in N:
                    if i >= 3:
                        pe.wait_ge(*after("dve", f"gated{i - 3}"))
                    norm.spread_tile(pe, i, k.psum_pair(1 + i % 3)).then_inc(*did("pe", f"spread{i}"))

            @block.gpsimd
            def _(pool):
                norm.constants(pool)

            @block.scalar
            def _(act):
                for i in N:
                    act.activation(sq(i), src(i), ACT.Square).then_inc(*did("act", f"sq{i}"))
                act.wait_ge(*after("pe", f"sum{N[-1]}"))
                norm.root(act, k.psum_pair(0), k.eps[:, 0:1], 1.0 / P).then_inc(*did("act", "root"))

            @block.vector
            def _(dve):
                dve.wait_ge(*after("act", "root"))
                norm.invert(dve).then_inc(*did("dve", "inverse"))
                for i in N:
                    dve.wait_ge(*after("pe", f"spread{i}"))
                    gain = k.par("gain_c") if i < 4 else k.par("gain_d")
                    dve.scalar_tensor_tensor(out=halves(sq(i)), in0=two_halves(k.psum_pair(1 + i % 3), HALF),
                                             scalar=gain, in1=halves(gate(i)), op0=ALU.mult, op1=ALU.mult)\
                        .then_inc(*did("dve", f"gated{i}"))
                    dve.wait_ge(*after("dve", f"gated{i}"))
                    dve.tensor_tensor(src(i), src(i), sq(i), ALU.mult).then_inc(*did("dve", f"out{i}"))


def odd_mixer(k, sublayer):
    project_odd(k, sublayer)
    prepare_odd(k)
    odd_chunks(k, sample=False)
    odd_chunks(k, sample=True)
    finish_odd(k)
    tile = lambda kt: V_C + kt if kt < 4 else V_D + kt - 4
    mixer_output(k, k.io["w_out_odd"], lambda kt: k.big_buf[:, tile(kt) * T:(tile(kt) + 1) * T], sublayer)


class Kernel:

    def __init__(self, nc, io):
        def sb(name, cols):
            return nc.alloc_sbuf_tensor(name, [P, cols], F32)[:]

        def rounded(name, cols, at=0):
            return nc.alloc_sbuf_tensor_at(name, [P, cols], F32R, offset=start + at * 4)[:]
        self.nc = nc
        self.io = io
        self.masks = sb("masks", N_MASK * P)
        self.bigs = sb("bigs", len(BIGS) * P)
        self.params = sb("params", N_PARAM)
        self.selection = sb("selection", 6 * P)
        self.work = sb("work", WORK)
        start = nc.sbuf_base - (WORK - KT * T) * 4
        self.weights_r = rounded("weights_r", H_LOW)
        self.low_r = rounded("low_r", ARENA - LOW, at=LOW)
        self.mixed_r = rounded("mixed_r", 2 * KT * T)
        self.x = self.work[:, 0:KT * T]
        self.arena = self.work[:, KT * T:]
        self.x_kept = nc.dram_tensor("x_kept", (P, KT * T), F32, kind="Internal").ap()
        self.h = sb("h", KT * TX)
        start = nc.sbuf_base - KT * TX * 4
        self.h_r = rounded("h_r", KT * TX)
        self.big_buf = sb("big_buf", 30 * T)
        start = nc.sbuf_base - 30 * T * 4
        self.big_r = rounded("big_r", 30 * T)
        self.h_low_ff = self.big_r[:, FT * T:]
        self.mods = [sb(f"mod{i}", MT * NC) for i in range(2)]
        self.cs = sb("cs", KT * NC)
        self.gated = sb("gated", 4 * (T - TP))
        self.resets = sb("resets", T)
        self.eps = sb("eps", 4)
        self.rows = sb("rows", T)
        self.cols = sb("cols", 5 * 16)
        self.pairs = [nc.alloc_psum_tensor(f"banks{b}", [P, 2, 512], F32)[:] for b in range(4)]
        self.psum = [self.pairs[b // 2][:, b % 2, :] for b in range(8)]
        self.cs_tmp = self.big_buf[:, 0:KT * NC]
        self.lc = self.arena[:, ARENA - 4 * T:]
        self.rows_b = self.arena[:, ARENA - 5 * T:ARENA - 4 * T]
        self.mrows = self.arena[0:4, ARENA - 3 * T:]

    def psum_pair(self, b):
        return self.pairs[b]

    def mask(self, name):
        at = MASKS.index(name) * P
        return self.masks[:, at:at + P]

    def big(self, name):
        at = BIGS.index(name) * P
        return self.bigs[:, at:at + P]

    def par(self, name):
        at, width = PARAM[name]
        return self.params[:, at:at + width]

    def select(self, h):
        return self.selection[:, h * P:(h + 1) * P]


def build(nc, io):
    k = Kernel(nc, io)
    setup(k)
    for layer in range(DEPTH):
        feed_forward(k, 3 * layer)
        if layer % 2 == 0:
            even_mixer(k, 3 * layer + 1)
        else:
            odd_mixer(k, 3 * layer + 1)
        feed_forward(k, 3 * layer + 2)
    final_norm(k)


def tile_weights(w):
    c, m = w.shape
    return w.reshape(c // P, P, m // P, P).transpose(2, 1, 0, 3).reshape(m // P, P, c)


def by_feature(v):
    n, f = v.shape
    return v.reshape(n, f // P, P).transpose(2, 0, 1).reshape(P, n * (f // P))


def pack(i):
    import numpy as np
    i = {n: np.asarray(v) for n, v in i.items()}
    cat = np.concatenate

    def column(v):
        out = np.zeros((P, 1), np.float32)
        out[:v.size, 0] = v.ravel()
        return out

    def padded(w, pieces):
        out = np.zeros((w.shape[0], P), np.float32)
        for at, lo, n in pieces:
            out[:, at:at + n] = w[:, lo:lo + n]
        return out

    x = cat([i["x_prompt"].reshape(TP, D), i["x_sample"].reshape(NSEQ * TS, D)])
    c = cat([i["c_prompt"], i["c_sample"]])
    we, wo = i["w_in_even"][0], i["w_in_odd"][0]
    a_end = 3 * 512
    b0 = 3 * 512 + 8 + 512
    even = cat([we[:, 0:a_end], we[:, b0:b0 + 1792], we[:, a_end + 8:b0], padded(we, [(0, a_end, 4), (32, a_end + 4, 4)])],
               axis=1)
    c_lr, c_z, d0 = 1024, 1040, 1552
    odd = cat([wo[:, 0:c_lr], wo[:, c_z:d0], wo[:, d0:d0 + 1024], wo[:, d0 + 1032:],
               padded(wo, [(0, c_lr, 16), (32, d0 + 1024, 4), (64, d0 + 1028, 4)])], axis=1)
    params = {
        "b_mod": by_feature(i["b_mod"].reshape(DEPTH * 9, D)),
        "norm_gain": by_feature(i["norm_gain"].reshape(DEPTH * 3, D)),
        "final_gain": by_feature(i["final_gain"][None]),
        "conv_w": i["conv_w"][0].reshape(CONV_W, 12, P).transpose(2, 1, 0).reshape(P, 48),
        "mu": by_feature(i["mu_b"]), "w0": by_feature(i["w0_b"]), "a0": by_feature(i["a0_b"]),
        "k_k": by_feature(i["k_k"]), "k_a": by_feature(i["k_a"]), "r_k": by_feature(i["r_k"].reshape(1, 512)),
        "lnx_gain": by_feature(i["lnx_gain"]), "lnx_bias": by_feature(i["lnx_bias"]),
        "gain_a": i["gain_a"].T, "a_log": column(i["a_log"]), "dt_bias": column(i["dt_bias"]),
        "b_gk": by_feature(i["b_gk"]), "gain_c": i["gain_c"].T, "gain_d": i["gain_d"].T,
        "b_i": column(i["b_i"]), "b_f": column(i["b_f"]),
    }
    selection = np.zeros((P, 6, P), np.float32)
    for h in range(4):
        selection[h, h] = 1.0
        selection[h, 4 + h // 2, 64 * (h % 2):64 * (h % 2) + 64] = 1.0
    ff = cat([tile_weights(i[n][l, s])[:, :, None] for l in range(DEPTH) for s in range(2) for n in ("w_ffn_gate",)])
    fu = cat([tile_weights(i["w_ffn_up"][l, s])[:, :, None] for l in range(DEPTH) for s in range(2)])
    pair_state = lambda v: v[0].reshape(NSEQ, -1, 2, v.shape[-2], v.shape[-1]).transpose(2, 3, 1, 0, 4)
    arrays = {
        "x_in": x.reshape(T, KT, P).transpose(2, 1, 0).reshape(P, KT * T),
        "c_in": c.reshape(NC, KT, P).transpose(2, 1, 0).reshape(P, KT * NC),
        "params_in": cat([params[n] for n, _ in PARAM_WIDTHS], axis=1),
        "selection_in": selection.reshape(P, 6 * P),
        "w_mod": i["w_mod"].reshape(DEPTH, KT, P, 3, 2, MOD_W).transpose(0, 3, 1, 4, 2, 5).reshape(-1, P, MOD_W),
        "w_ff": cat([ff, fu], axis=2).reshape(-1, P, 2 * D),
        "w_down": cat([tile_weights(i["w_ffn_down"][l, s]) for l in range(DEPTH) for s in range(2)]),
        "w_in_even": tile_weights(even), "w_out_even": tile_weights(i["w_out_even"][0]),
        "w_in_odd": tile_weights(odd), "w_out_odd": tile_weights(i["w_out_odd"][0]),
        "w_wa2": cat([i["w_w2"][0], i["w_a2"][0]]), "w_g2": i["w_g2"][0], "w_gk2": i["w_gk2"][0],
        "xbuf_in": i["state_xbuf_even"][0].reshape(NSEQ, PAD, KT, P).transpose(3, 2, 0, 1),
        "delta_in": i["state_delta"][0].transpose(2, 1, 0, 3).reshape(P, 32 * P),
        "rwkv_in": pair_state(i["state_rwkv"].swapaxes(-1, -2)).reshape(P, 4 * NSEQ * 64),
        "gla_in": pair_state(i["state_gla"]).reshape(P, 2 * NSEQ * P),
        "mc_in": pair_state(i["state_mlstm_c"]).reshape(P, 2 * NSEQ * P),
        "mn_in": pair_state(i["state_mlstm_n"][..., None]).reshape(P, 2 * NSEQ),
        "mm_in": i["state_mlstm_m"][0].T,
    }
    return {n: np.ascontiguousarray(a, dtype=np.float32) for n, a in arrays.items()}


OUTPUTS = {
    "y_out": (P, KT, T), "xbuf_p_out": (P, KT, PAD), "xbuf_s_out": (P, KT, NSEQ, PAD),
    "delta_p_out": (P, 512), "delta_s_out": (P, 32 * P), "rwkv_p_out": (P, 256), "rwkv_s_out": (P, 2048),
    "gla_p_out": (P, 256), "gla_s_out": (P, 2048), "mc_p_out": (P, 256), "mc_s_out": (P, 2048),
    "mn_p_out": (P, 2), "mn_s_out": (P, 16), "mm_p_out": (4, 1), "mm_s_out": (4, NSEQ),
}


def unpack(o):
    import numpy as np
    y = o["y_out"].transpose(2, 1, 0).reshape(T, D)

    def pair_state(v, seqs, rows, cols):
        v = v.reshape(2, rows, -1, seqs, cols).transpose(3, 2, 0, 1, 4)
        return v.reshape(1, seqs, -1, rows, cols)
    out = (
        y[:TP].reshape(1, TP, D), y[TP:].reshape(NSEQ, TS, D),
        o["xbuf_p_out"].transpose(2, 1, 0).reshape(1, 1, PAD, D),
        o["xbuf_s_out"].transpose(2, 3, 1, 0).reshape(1, NSEQ, PAD, D),
        o["delta_p_out"].reshape(P, 4, 1, P).transpose(2, 1, 0, 3)[None],
        o["delta_s_out"].reshape(P, 4, NSEQ, P).transpose(2, 1, 0, 3)[None],
        pair_state(o["rwkv_p_out"], 1, 64, 64).swapaxes(-1, -2),
        pair_state(o["rwkv_s_out"], NSEQ, 64, 64).swapaxes(-1, -2),
        pair_state(o["gla_p_out"], 1, 64, P), pair_state(o["gla_s_out"], NSEQ, 64, P),
        pair_state(o["mc_p_out"], 1, 64, P), pair_state(o["mc_s_out"], NSEQ, 64, P),
        pair_state(o["mn_p_out"], 1, 64, 1)[..., 0], pair_state(o["mn_s_out"], NSEQ, 64, 1)[..., 0],
        o["mm_p_out"].T[None], o["mm_s_out"].T[None],
    )
    return tuple(np.ascontiguousarray(v) for v in out)


def kernel(**inputs):
    import concourse.bacc as bacc
    from concourse.bass_utils import run_bass_kernel_spmd
    arrays = pack(inputs)
    nc = bacc.Bacc("TRN2", target_bir_lowering=False, num_devices=1)
    io = {n: nc.dram_tensor(n + "_dram", a.shape, F32, kind="ExternalInput").ap() for n, a in arrays.items()}
    io |= {n: nc.dram_tensor(n + "_dram", s, F32, kind="ExternalOutput").ap() for n, s in OUTPUTS.items()}
    build(nc, io)
    r = run_bass_kernel_spmd(nc, [{n + "_dram": a for n, a in arrays.items()}], core_ids=[0])
    return unpack({n: r.results[0][n + "_dram"] for n in OUTPUTS})
```
